# Optimizing a Trainium2 kernel written in Bass

```python
import math
import jax, jax.numpy as jnp
from jax import lax
import numpy as np
import jax
import jax.numpy as jnp

D_MODEL = 1024
BATCH = 1
SEQ = 1024
DEPTH = 1

CHUNK = 64
Q_BLOCK = 128
PLE_DIM = 256
D_FF = 4 * D_MODEL
EPS = 1e-6

GLA_HEADS = 4
GLA_DK = D_MODEL // 16
GLA_DV = D_MODEL // 8
GLA_GATE_RANK = 16
GLA_TAU = 16.0
GLA_WIDTH = GLA_HEADS * GLA_DV

MLA_HEADS = 8
MLA_NOPE = 64
MLA_ROPE = 32
MLA_V = 64
MLA_QK = MLA_NOPE + MLA_ROPE
MLA_Q_RANK = 256
MLA_KV_RANK = 128
MLA_WIDTH = MLA_HEADS * MLA_V
ROPE_THETA = 10000.0

D_MIX = GLA_WIDTH + MLA_WIDTH
IN_SPLITS = (GLA_HEADS * GLA_DK, GLA_HEADS * GLA_DK, GLA_WIDTH, GLA_GATE_RANK,
             GLA_WIDTH, MLA_Q_RANK, MLA_KV_RANK, MLA_ROPE)
D_IN = (GLA_HEADS * GLA_DK * 2 + GLA_WIDTH * 2 + GLA_GATE_RANK
        + MLA_Q_RANK + MLA_KV_RANK + MLA_ROPE)


def rms_norm(x, g):
    xf = x.astype(jnp.float32)
    y = xf * lax.rsqrt(jnp.mean(xf * xf, axis=-1, keepdims=True) + EPS)
    return (y * g.astype(jnp.float32)).astype(x.dtype)

def split_cols(t, sizes):
    out, start = [], 0
    for s in sizes:
        out.append(t[..., start:start + s])
        start += s
    return out

def rope_cos_sin(positions):
    inv_freq = ROPE_THETA ** (-jnp.arange(0, MLA_ROPE, 2, dtype=jnp.float32) / MLA_ROPE)
    ang = positions.astype(jnp.float32)[..., None] * inv_freq
    return jnp.cos(ang)[:, :, None, :], jnp.sin(ang)[:, :, None, :]

def apply_rope(x, cos, sin):
    half = x.shape[-1] // 2
    x1, x2 = x[..., :half], x[..., half:]
    c, s = cos.astype(x.dtype), sin.astype(x.dtype)
    return jnp.concatenate([x1 * c - x2 * s, x2 * c + x1 * s], axis=-1)

def gla_chunked(q, k, v, log_a):
    out_dtype = v.dtype
    B, S, H, DK = q.shape
    DV = v.shape[-1]
    NC = S // CHUNK

    def to_chunks(t):
        return t.astype(jnp.float32).reshape(B, NC, CHUNK, H, -1).transpose(1, 0, 3, 2, 4)

    qc, kc, vc, gc = to_chunks(q), to_chunks(k), to_chunks(v), to_chunks(log_a)
    causal = jnp.tril(jnp.ones((CHUNK, CHUNK), dtype=bool))[:, :, None]

    def step(state, inp):
        qi, ki, vi, gi = inp
        b = jnp.cumsum(gi, axis=2)
        b_last = b[:, :, -1:, :]
        o_inter = jnp.einsum('bhtk,bhkv->bhtv', qi * jnp.exp(b), state)
        diff = b[:, :, :, None, :] - b[:, :, None, :, :]
        decay = jnp.exp(jnp.where(causal, diff, -jnp.inf))
        scores = jnp.einsum('bhtk,bhsk,bhtsk->bhts', qi, ki, decay)
        o_intra = jnp.einsum('bhts,bhsv->bhtv', scores, vi)
        k_dec = ki * jnp.exp(b_last - b)
        state = state * jnp.exp(b_last[:, :, 0, :, None]) + jnp.einsum('bhsk,bhsv->bhkv', k_dec, vi)
        return state, o_inter + o_intra

    state0 = jnp.zeros((B, H, DK, DV), dtype=jnp.float32)
    _, oc = lax.scan(step, state0, (qc, kc, vc, gc))
    return oc.transpose(1, 0, 3, 2, 4).reshape(B, S, H, DV).astype(out_dtype)

def mla_attention(q, k, v):
    S = q.shape[1]
    scale = 1.0 / math.sqrt(MLA_QK)
    outs = []
    for blk in range(S // Q_BLOCK):
        qs, qe = blk * Q_BLOCK, (blk + 1) * Q_BLOCK
        qb, kb, vb = q[:, qs:qe], k[:, :qe], v[:, :qe]
        logits = jnp.einsum('bqhd,bkhd->bhqk', qb, kb).astype(jnp.float32) * scale
        q_chunk = (jnp.arange(qs, qe) // CHUNK)[:, None]
        k_chunk = (jnp.arange(qe) // CHUNK)[None, :]
        logits = jnp.where(k_chunk <= q_chunk, logits, -jnp.inf)
        probs = jax.nn.softmax(logits, axis=-1).astype(vb.dtype)
        outs.append(jnp.einsum('bhqk,bkhd->bqhd', probs, vb))
    return jnp.concatenate(outs, axis=1)

def first_inputs(seed: int = 0) -> dict:
    key = jax.random.key(seed)
    ks = jax.random.split(key, 24)
    f32 = jnp.float32

    def w(k, shape, fan_in):
        return jax.random.normal(k, shape, f32) * (fan_in ** -0.5)

    def gain(k, shape):
        return 1.0 + 0.1 * jax.random.normal(k, shape, f32)

    x = jax.random.normal(ks[0], (BATCH, SEQ, D_MODEL), f32)
    p = jax.random.normal(ks[1], (DEPTH, BATCH, SEQ, PLE_DIM), f32)
    offset = jax.random.randint(ks[2], (BATCH,), 0, 64, dtype=jnp.int32) * CHUNK
    positions = (offset[:, None] + jnp.arange(SEQ, dtype=jnp.int32)[None, :]).astype(jnp.int32)
    return {
        "x": x,
        "p": p,
        "positions": positions,
        "attn_norm": gain(ks[3], (DEPTH, D_MODEL)),
        "w_in": w(ks[4], (DEPTH, D_MODEL, D_IN), D_MODEL),
        "gla_gate_w2": w(ks[5], (DEPTH, GLA_GATE_RANK, GLA_HEADS * GLA_DK), GLA_GATE_RANK),
        "gla_gate_b": 0.1 * jax.random.normal(ks[6], (DEPTH, GLA_HEADS * GLA_DK), f32),
        "gla_out_norm": gain(ks[7], (DEPTH, GLA_DV)),
        "mla_q_norm": gain(ks[8], (DEPTH, MLA_Q_RANK)),
        "mla_w_uq": w(ks[9], (DEPTH, MLA_Q_RANK, MLA_HEADS * MLA_QK), MLA_Q_RANK),
        "mla_kv_norm": gain(ks[10], (DEPTH, MLA_KV_RANK)),
        "mla_w_ukv": w(ks[11], (DEPTH, MLA_KV_RANK, MLA_HEADS * (MLA_NOPE + MLA_V)), MLA_KV_RANK),
        "qk_norm_q": gain(ks[12], (DEPTH, MLA_QK)),
        "qk_norm_k": gain(ks[13], (DEPTH, MLA_QK)),
        "w_out": w(ks[14], (DEPTH, D_MIX, D_MODEL), D_MIX),
        "mlp_norm": gain(ks[15], (DEPTH, D_MODEL)),
        "w_mlp_up": w(ks[16], (DEPTH, D_MODEL, D_FF), D_MODEL),
        "w_mlp_down": w(ks[17], (DEPTH, D_FF, D_MODEL), D_FF),
        "ple_norm": gain(ks[18], (DEPTH, D_MODEL)),
        "w_ple_gate": w(ks[19], (DEPTH, D_MODEL, D_MODEL), D_MODEL),
        "b_ple_gate": 0.1 * jax.random.normal(ks[20], (DEPTH, D_MODEL), f32),
        "w_ple_proj": w(ks[21], (DEPTH, PLE_DIM, D_MODEL), PLE_DIM),
    }

def first_block(x, p, positions, attn_norm, w_in, gla_gate_w2, gla_gate_b, gla_out_norm,
              mla_q_norm, mla_w_uq, mla_kv_norm, mla_w_ukv, qk_norm_q, qk_norm_k,
              w_out, mlp_norm, w_mlp_up, w_mlp_down, ple_norm, w_ple_gate, b_ple_gate,
              w_ple_proj):
    B, S, _ = x.shape
    cos, sin = rope_cos_sin(positions)
    h = x
    for i in range(DEPTH):
        n = rms_norm(h, attn_norm[i])
        z = n @ w_in[i]
        gq, gk, gv, g_low, g_r, c_q, c_kv, k_r = split_cols(z, IN_SPLITS)

        q_g = gq.reshape(B, S, GLA_HEADS, GLA_DK) * (GLA_DK ** -0.5)
        k_g = gk.reshape(B, S, GLA_HEADS, GLA_DK)
        v_g = gv.reshape(B, S, GLA_HEADS, GLA_DV)
        log_a = jax.nn.log_sigmoid((g_low @ gla_gate_w2[i] + gla_gate_b[i]).astype(jnp.float32)) / GLA_TAU
        log_a = log_a.reshape(B, S, GLA_HEADS, GLA_DK)
        o_g = gla_chunked(q_g, k_g, v_g, log_a)
        o_g = rms_norm(o_g, gla_out_norm[i]).reshape(B, S, GLA_WIDTH) * jax.nn.silu(g_r)

        q_m = (rms_norm(c_q, mla_q_norm[i]) @ mla_w_uq[i]).reshape(B, S, MLA_HEADS, MLA_QK)
        kv = (rms_norm(c_kv, mla_kv_norm[i]) @ mla_w_ukv[i]).reshape(B, S, MLA_HEADS, MLA_NOPE + MLA_V)
        k_nope, v_m = kv[..., :MLA_NOPE], kv[..., MLA_NOPE:]
        k_rope = jnp.broadcast_to(k_r[:, :, None, :], (B, S, MLA_HEADS, MLA_ROPE))
        k_m = jnp.concatenate([k_nope, k_rope], axis=-1)
        q_m = rms_norm(q_m, qk_norm_q[i])
        k_m = rms_norm(k_m, qk_norm_k[i])
        q_m = jnp.concatenate([q_m[..., :MLA_NOPE], apply_rope(q_m[..., MLA_NOPE:], cos, sin)], axis=-1)
        k_m = jnp.concatenate([k_m[..., :MLA_NOPE], apply_rope(k_m[..., MLA_NOPE:], cos, sin)], axis=-1)
        o_m = mla_attention(q_m, k_m, v_m).reshape(B, S, MLA_WIDTH)

        h = h + jnp.concatenate([o_g, o_m], axis=-1) @ w_out[i]

        m = rms_norm(h, mlp_norm[i])
        h = h + jnp.square(jax.nn.relu(m @ w_mlp_up[i])) @ w_mlp_down[i]

        gate = jax.nn.sigmoid(rms_norm(h, ple_norm[i]) @ w_ple_gate[i] + b_ple_gate[i])
        h = h + (p[i] @ w_ple_proj[i]) * gate
    return h


CTX_LEN = 256
GRID_W = 64
N_MIXERS = 3
N_ATTN = (DEPTH + 2) // N_MIXERS
N_FNET = (DEPTH + 1) // N_MIXERS
N_RWKV = DEPTH // N_MIXERS
NORM_EPS = 1e-6

DA_HEADS = 8
DA_HEAD_DIM = D_MODEL // DA_HEADS // 2
ROPE_BASE = 10000.0
SUBLN_EPS = 1e-5

FN_GROUPS = 8
FN_GROUP_DIM = D_MODEL // FN_GROUPS

RW_HEAD_DIM = 64
RW_HEADS = D_MODEL // RW_HEAD_DIM
RW_DECAY_RANK = 64
RW_ICLR_RANK = 64
RW_GN_EPS = 64e-5


def rms_norm_2(x, gain, eps=NORM_EPS):
    xf = x.astype(jnp.float32)
    y = xf * lax.rsqrt(jnp.mean(xf * xf, axis=-1, keepdims=True) + eps)
    return (y * gain.astype(jnp.float32)).astype(x.dtype)

def ada_modulation(cond, w, b):
    m = jax.nn.silu(cond) @ w + b
    return jnp.split(m, 3, axis=-1)

def axial_rope_tables(n):
    rows = n // GRID_W
    row = jnp.repeat(jnp.arange(rows), GRID_W).astype(jnp.float32)
    col = jnp.tile(jnp.arange(GRID_W), rows).astype(jnp.float32)
    axis_dim = DA_HEAD_DIM // 2
    inv_freq = ROPE_BASE ** (-jnp.arange(0, axis_dim, 2, dtype=jnp.float32) / axis_dim)
    ang = jnp.stack([row[:, None] * inv_freq, col[:, None] * inv_freq], axis=1)
    return jnp.cos(ang), jnp.sin(ang)

def apply_axial_rope(t, cos, sin):
    quarter = DA_HEAD_DIM // 4
    tf = t.astype(jnp.float32).reshape(t.shape[:-1] + (2, 2, quarter))
    t1, t2 = tf[..., 0, :], tf[..., 1, :]
    c = cos[:, None, None]
    s = sin[:, None, None]
    out = jnp.stack([t1 * c - t2 * s, t2 * c + t1 * s], axis=-2)
    return out.reshape(t.shape).astype(t.dtype)

def diff_attend(q, k, v, lam):
    s = jnp.einsum('bqhzd,bkhzd->bhzqk', q, k).astype(jnp.float32)
    p = jax.nn.softmax(s, axis=-1)
    a = p[:, :, 0] - lam * p[:, :, 1]
    return jnp.einsum('bhqk,bkhe->bqhe', a.astype(v.dtype), v)

def diff_attention(h_lat, h_ctx, cos, sin, w_in, lam_q, lam_k, subln_gain, w_out, lambda_init, need_ctx_out):
    B, N, D = h_lat.shape
    H, d = DA_HEADS, DA_HEAD_DIM
    scale = d ** -0.5

    def project(h):
        L = h.shape[1]
        q, k, v, z = jnp.split(h @ w_in, 4, axis=-1)
        return (q.reshape(B, L, H, 2, d) * scale, k.reshape(B, L, H, 2, d),
                v.reshape(B, L, H, 2 * d), z)

    q_l, k_l, v_l, z_l = project(h_lat)
    q_c, k_c, v_c, z_c = project(h_ctx)
    q_l = apply_axial_rope(q_l, cos, sin)
    k_l = apply_axial_rope(k_l, cos, sin)
    lq = lam_q.astype(jnp.float32)
    lk = lam_k.astype(jnp.float32)
    lam = jnp.exp(jnp.sum(lq[0] * lk[0])) - jnp.exp(jnp.sum(lq[1] * lk[1])) + lambda_init

    def finish(o, z):
        L = o.shape[1]
        of = o.astype(jnp.float32)
        of = of * lax.rsqrt(jnp.mean(of * of, axis=-1, keepdims=True) + SUBLN_EPS)
        of = of * subln_gain.astype(jnp.float32) * (1.0 - lambda_init)
        return (of.reshape(B, L, D).astype(z.dtype) * jax.nn.silu(z)) @ w_out

    k_all = jnp.concatenate([k_c, k_l], axis=1)
    v_all = jnp.concatenate([v_c, v_l], axis=1)
    n_blocks = N // Q_BLOCK
    q_blocks = q_l.reshape(B, n_blocks, Q_BLOCK, H, 2, d).swapaxes(0, 1)
    o_l = lax.map(lambda qb: diff_attend(qb, k_all, v_all, lam), q_blocks)
    o_l = o_l.swapaxes(0, 1).reshape(B, N, H, 2 * d)
    y_l = finish(o_l, z_l)
    y_c = finish(diff_attend(q_c, k_c, v_c, lam), z_c) if need_ctx_out else None
    return y_l, y_c

def fourier_mix(h, w_in, w_group, w_out):
    B, L, D = h.shape
    u, z = jnp.split(h @ w_in, 2, axis=-1)
    ug = u.astype(jnp.float32).reshape(B, L, FN_GROUPS, FN_GROUP_DIM)
    f = jnp.fft.fftn(ug, axes=(1, 3), norm='ortho').real.astype(h.dtype)
    y = jnp.einsum('blgc,gce->blge', f, w_group).reshape(B, L, D)
    return (y * jax.nn.silu(z)) @ w_out

def centred_shift(s):
    sp = jnp.pad(s, ((0, 0), (1, 1), (0, 0)))
    return 0.5 * (sp[:, :-2] + sp[:, 2:])

def rwkv7_features(h, w_in, mu, w0, w_up, a0, a_up, k_k, k_a):
    B, L, D = h.shape
    p = h @ w_in
    s, z = p[..., :-D], p[..., -D:]
    s = s + mu * (centred_shift(s) - s)
    r, k, v = s[..., :D], s[..., D:2 * D], s[..., 2 * D:3 * D]
    wd = s[..., 3 * D:3 * D + 2 * RW_DECAY_RANK].reshape(B, L, 2, RW_DECAY_RANK)
    ad = s[..., 3 * D + 2 * RW_DECAY_RANK:].reshape(B, L, 2, RW_ICLR_RANK)
    w_pre = (w0 + jnp.einsum('blzr,zrd->blzd', jnp.tanh(wd), w_up)).astype(jnp.float32)
    decay = jnp.exp(-jnp.exp(-jax.nn.softplus(-w_pre) - 0.5))
    a = jax.nn.sigmoid((a0 + jnp.einsum('blzr,zrd->blzd', ad, a_up)).astype(jnp.float32))
    kk = (k * k_k).astype(jnp.float32).reshape(B, L, RW_HEADS, RW_HEAD_DIM)
    kk = (kk * lax.rsqrt(jnp.sum(kk * kk, axis=-1, keepdims=True) + 1e-12)).reshape(B, L, D)
    k_dir = k.astype(jnp.float32)[:, :, None] * (1.0 + (a - 1.0) * k_a.astype(jnp.float32))
    b = kk[:, :, None] * a
    return r.astype(jnp.float32), v.astype(jnp.float32), z, decay, kk, k_dir, b

def to_scan_layout(t):
    B, L = t.shape[:2]
    t = jnp.stack([t[:, :, 0], jnp.flip(t[:, :, 1], axis=1)], axis=0)
    return t.transpose(2, 0, 1, 3).reshape(L, 2, B, RW_HEADS, RW_HEAD_DIM)

def wkv7_step(S, inp):
    r, w, k, v, a, b = inp
    sa = jnp.einsum('zbhij,zbhj->zbhi', S, a)
    S = S * w[..., None, :] + sa[..., :, None] * b[..., None, :] + v[..., :, None] * k[..., None, :]
    return S, jnp.einsum('zbhij,zbhj->zbhi', S, r)

def wkv7_bidirectional(S0, r, decay, k_dir, v, kk, b):
    both = lambda t: jnp.stack([t, t], axis=2)
    seqs = (to_scan_layout(both(r)), to_scan_layout(decay), to_scan_layout(k_dir),
            to_scan_layout(both(v)), to_scan_layout(both(-kk)), to_scan_layout(b))
    S, y = lax.scan(wkv7_step, S0, seqs)
    y = y[:, 0] + jnp.flip(y[:, 1], axis=0)
    return S, y.transpose(1, 0, 2, 3)

def rwkv7_output(y, r, k_dir, v, z, r_k, ln_w, ln_b, w_out):
    B, L = y.shape[:2]
    yc = y - jnp.mean(y, axis=-1, keepdims=True)
    yn = yc * lax.rsqrt(jnp.mean(yc * yc, axis=-1, keepdims=True) + RW_GN_EPS)
    yn = yn.reshape(B, L, D_MODEL) * ln_w.astype(jnp.float32) + ln_b.astype(jnp.float32)
    heads = lambda t: t.reshape(B, L, RW_HEADS, RW_HEAD_DIM)
    bonus = jnp.sum(heads(r * jnp.mean(k_dir, axis=2) * r_k.astype(jnp.float32)), axis=-1, keepdims=True) * heads(v)
    o = (yn + bonus.reshape(B, L, D_MODEL)).astype(z.dtype) * jax.nn.silu(z)
    return o @ w_out

def rwkv7_mix(h_lat, h_ctx, w_in, mu, w0, w_up, a0, a_up, k_k, k_a, r_k, ln_w, ln_b, w_out, need_ctx_out):
    B = h_lat.shape[0]
    r_c, v_c, z_c, dec_c, kk_c, kd_c, b_c = rwkv7_features(h_ctx, w_in, mu, w0, w_up, a0, a_up, k_k, k_a)
    r_l, v_l, z_l, dec_l, kk_l, kd_l, b_l = rwkv7_features(h_lat, w_in, mu, w0, w_up, a0, a_up, k_k, k_a)
    S0 = jnp.zeros((2, B, RW_HEADS, RW_HEAD_DIM, RW_HEAD_DIM), jnp.float32)
    S_c, y_c = wkv7_bidirectional(S0, r_c, dec_c, kd_c, v_c, kk_c, b_c)
    _, y_l = wkv7_bidirectional(S_c, r_l, dec_l, kd_l, v_l, kk_l, b_l)
    out_l = rwkv7_output(y_l, r_l, kd_l, v_l, z_l, r_k, ln_w, ln_b, w_out)
    out_c = rwkv7_output(y_c, r_c, kd_c, v_c, z_c, r_k, ln_w, ln_b, w_out) if need_ctx_out else None
    return out_l, out_c

def second_inputs(seed: int = 0) -> dict:
    key = jax.random.key(seed)
    ks = iter(jax.random.split(key, 32))
    D = D_MODEL
    R_ALL = 2 * RW_DECAY_RANK + 2 * RW_ICLR_RANK

    def nrm(shape, scale):
        return jax.random.normal(next(ks), shape, jnp.float32) * scale

    inputs = {}
    inputs['x'] = nrm((BATCH, SEQ, D), 1.0)
    inputs['c'] = nrm((BATCH, D), 1.0)
    inputs['ctx'] = nrm((BATCH, CTX_LEN, D), 1.0)
    inputs['c_ctx'] = nrm((D,), 1.0)
    inputs['norm_gain'] = 1.0 + nrm((DEPTH, D), 0.02)
    inputs['ada_w'] = nrm((DEPTH, D, 3 * D), 0.3 * D ** -0.5)
    inputs['ada_b'] = nrm((DEPTH, 3 * D), 0.02)
    inputs['final_gain'] = 1.0 + nrm((D,), 0.02)
    inputs['da_w_in'] = nrm((N_ATTN, D, 4 * D), D ** -0.5)
    inputs['da_lam_q'] = nrm((N_ATTN, 2, DA_HEAD_DIM), 0.1)
    inputs['da_lam_k'] = nrm((N_ATTN, 2, DA_HEAD_DIM), 0.1)
    inputs['da_subln_gain'] = 1.0 + nrm((N_ATTN, 2 * DA_HEAD_DIM), 0.02)
    inputs['da_w_out'] = nrm((N_ATTN, D, D), D ** -0.5)
    inputs['fn_w_in'] = nrm((N_FNET, D, 2 * D), D ** -0.5)
    inputs['fn_w_group'] = nrm((N_FNET, FN_GROUPS, FN_GROUP_DIM, FN_GROUP_DIM), FN_GROUP_DIM ** -0.5)
    inputs['fn_w_out'] = nrm((N_FNET, D, D), D ** -0.5)
    inputs['rw_w_in'] = nrm((N_RWKV, D, 4 * D + R_ALL), D ** -0.5)
    inputs['rw_mu'] = jax.random.uniform(next(ks), (N_RWKV, 3 * D + R_ALL), jnp.float32, 0.0, 1.0)
    inputs['rw_w0'] = jax.random.uniform(next(ks), (N_RWKV, 2, D), jnp.float32, -6.5, -1.5)
    inputs['rw_w_up'] = nrm((N_RWKV, 2, RW_DECAY_RANK, D), 0.1)
    inputs['rw_a0'] = nrm((N_RWKV, 2, D), 0.1)
    inputs['rw_a_up'] = nrm((N_RWKV, 2, RW_ICLR_RANK, D), RW_ICLR_RANK ** -0.5)
    inputs['rw_k_k'] = 0.85 + nrm((N_RWKV, D), 0.02)
    inputs['rw_k_a'] = 1.0 + nrm((N_RWKV, D), 0.02)
    inputs['rw_r_k'] = nrm((N_RWKV, D), 0.1)
    inputs['rw_ln_w'] = 1.0 + nrm((N_RWKV, D), 0.02)
    inputs['rw_ln_b'] = nrm((N_RWKV, D), 0.02)
    inputs['rw_w_out'] = nrm((N_RWKV, D, D), D ** -0.5)
    return inputs

def second_block(x, c, ctx, c_ctx, norm_gain, ada_w, ada_b, final_gain,
              da_w_in, da_lam_q, da_lam_k, da_subln_gain, da_w_out,
              fn_w_in, fn_w_group, fn_w_out,
              rw_w_in, rw_mu, rw_w0, rw_w_up, rw_a0, rw_a_up, rw_k_k, rw_k_a, rw_r_k,
              rw_ln_w, rw_ln_b, rw_w_out):
    cos, sin = axial_rope_tables(x.shape[1])
    x_lat, x_ctx = x, ctx
    for i in range(DEPTH):
        last = i == DEPTH - 1
        kind = i % N_MIXERS
        j = i // N_MIXERS
        sh, sc, gt = ada_modulation(c, ada_w[i], ada_b[i])
        sh_c, sc_c, gt_c = ada_modulation(c_ctx, ada_w[i], ada_b[i])
        h_lat = rms_norm_2(x_lat, norm_gain[i]) * (1.0 + sc[:, None, :]) + sh[:, None, :]
        h_ctx = rms_norm_2(x_ctx, norm_gain[i]) * (1.0 + sc_c) + sh_c
        if kind == 0:
            lambda_init = 0.8 - 0.6 * math.exp(-0.3 * i)
            y_lat, y_ctx = diff_attention(h_lat, h_ctx, cos, sin, da_w_in[j], da_lam_q[j], da_lam_k[j],
                                          da_subln_gain[j], da_w_out[j], lambda_init, not last)
        elif kind == 1:
            y_lat = fourier_mix(h_lat, fn_w_in[j], fn_w_group[j], fn_w_out[j])
            y_ctx = None if last else fourier_mix(h_ctx, fn_w_in[j], fn_w_group[j], fn_w_out[j])
        else:
            y_lat, y_ctx = rwkv7_mix(h_lat, h_ctx, rw_w_in[j], rw_mu[j], rw_w0[j], rw_w_up[j], rw_a0[j],
                                     rw_a_up[j], rw_k_k[j], rw_k_a[j], rw_r_k[j], rw_ln_w[j], rw_ln_b[j],
                                     rw_w_out[j], not last)
        x_lat = x_lat + gt[:, None, :] * y_lat
        if not last:
            x_ctx = x_ctx + gt_c * y_ctx
    return rms_norm_2(x_lat, final_gain)


def setup_inputs(seed=0):
    out = dict(first_inputs(seed))
    for name, value in second_inputs(seed + 1).items():
        if name != "x":
            out[name + "_2"] = value
    return out


def reference(
    x, p, positions, attn_norm, w_in, gla_gate_w2, gla_gate_b, gla_out_norm, mla_q_norm,
    mla_w_uq, mla_kv_norm, mla_w_ukv, qk_norm_q, qk_norm_k, w_out, mlp_norm, w_mlp_up,
    w_mlp_down, ple_norm, w_ple_gate, b_ple_gate, w_ple_proj, c_2, ctx_2, c_ctx_2, norm_gain_2,
    ada_w_2, ada_b_2, final_gain_2, da_w_in_2, da_lam_q_2, da_lam_k_2, da_subln_gain_2,
    da_w_out_2, fn_w_in_2, fn_w_group_2, fn_w_out_2, rw_w_in_2, rw_mu_2, rw_w0_2, rw_w_up_2,
    rw_a0_2, rw_a_up_2, rw_k_k_2, rw_k_a_2, rw_r_k_2, rw_ln_w_2, rw_ln_b_2, rw_w_out_2,
):
    x = first_block(
        x, p, positions, attn_norm, w_in, gla_gate_w2, gla_gate_b, gla_out_norm, mla_q_norm,
        mla_w_uq, mla_kv_norm, mla_w_ukv, qk_norm_q, qk_norm_k, w_out, mlp_norm, w_mlp_up,
        w_mlp_down, ple_norm, w_ple_gate, b_ple_gate, w_ple_proj,
    )
    return second_block(
        x, c_2, ctx_2, c_ctx_2, norm_gain_2, ada_w_2, ada_b_2, final_gain_2, da_w_in_2,
        da_lam_q_2, da_lam_k_2, da_subln_gain_2, da_w_out_2, fn_w_in_2, fn_w_group_2,
        fn_w_out_2, rw_w_in_2, rw_mu_2, rw_w0_2, rw_w_up_2, rw_a0_2, rw_a_up_2, rw_k_k_2,
        rw_k_a_2, rw_r_k_2, rw_ln_w_2, rw_ln_b_2, rw_w_out_2,
    )


_drawn_inputs = setup_inputs


def setup_inputs(seed=0):
    import zlib

    import numpy as np

    out = dict(_drawn_inputs(seed))
    spreads = {}
    factors = {'gla_gate_b': 3.049,
     'mla_q_norm': 7.237,
     'mla_kv_norm': 3.843,
     'qk_norm_q': 6.832,
     'qk_norm_k': 6.745,
     'ple_norm': 4.795,
     'b_ple_gate': 4.874,
     'ctx_2': 8.0,
     'c_ctx_2': 7.507,
     'norm_gain_2': 8.0,
     'ada_b_2': 8.0,
     'final_gain_2': 7.722,
     'da_lam_q_2': 8.0,
     'da_lam_k_2': 8.0,
     'da_subln_gain_2': 22.15}
    for name, (base, spread) in spreads.items():
        noise = np.random.default_rng([zlib.crc32(name.encode()), seed]).standard_normal(out[name].shape)
        drawn = base * np.exp(spread * noise) if base else spread * noise
        out[name] = jnp.asarray(drawn.astype(out[name].dtype))
    for name, factor in factors.items():
        out[name] = (out[name] * factor).astype(out[name].dtype)
    return out
```

```python
from contextlib import ExitStack

import concourse.bass as bass
from concourse import mybir

F32 = mybir.dt.float32
F32R = mybir.dt.float32r
I32 = mybir.dt.int32
ALU = mybir.AluOpType
ACT = mybir.ActivationFunctionType
AX = mybir.AxisListType

P = 128
S = 1024
D = 1024
TT = S // P
KT = D // P
NCOL = 512
HALVES = S // NCOL
CTX = 256
CT = CTX // P
EPS = 1e-6

GH, GDK, GDV, GR = 4, 64, 128, 16
MH, MNOPE, MROPE, MV, MQK = 8, 64, 32, 64, 96
MQR, MKVR = 256, 128
DH, DD = 8, 64
D_FF = 4096
LAMBDA_INIT = 0.2

SLOTS = 4
RING = 4


class Chip:

    def __init__(self, nc, ctx):
        self.nc, self.ctx = nc, ctx
        self.used = []
        self.out_stored = nc.alloc_semaphore("out_stored")

    def sb(self, name, shape, dt=F32, ctx=None):
        return (ctx or self.ctx).enter_context(self.nc.sbuf_tensor(name, shape, dt))

    def hold_x(self, name, ctx):
        self.Xhi = self.sb(f"{name}_hi", [P, KT, S], F32R, ctx)
        self.Xlo = self.sb(f"{name}_lo", [P, KT, S], F32R, ctx)

    def banks(self, name, ctx, n=8):
        return [ctx.enter_context(self.nc.psum_tensor(f"{name}{i}", [P, NCOL], F32)) for i in range(n)]

    def sem(self, name, ctx):
        s = self.nc.alloc_semaphore(name)
        self.used.append(s)
        return s

    def renew_semaphores(self):
        nc, used = self.nc, self.used
        with nc.Block() as block:
            @block.gpsimd
            def _(pool):
                numbers = sorted(s.num for s in used)
                at = 0
                for i in range(1, len(numbers) + 1):
                    if i == len(numbers) or numbers[i] != numbers[i - 1] + 1:
                        nc.gpsimd.sem_clear(range(numbers[at], numbers[i - 1] + 1))
                        at = i
        for s in used:
            nc.release_semaphore(s)
        self.used = []


def constants(nc, chip, a):
    c = chip
    c.H = c.sb("residual", [P, TT, D])
    c.mod_bias = c.sb("mod_bias", [P, 2, KT])
    c.mod_gain = c.sb("mod_gain", [P, 2, KT])
    c.ident = c.sb("ident", [P, P])
    c.gains = c.sb("gains", [P, 4, KT])
    c.minus_half = c.sb("minus_half", [P, 64])
    with ExitStack() as ctx:
        ones_ready = c.sem("ones_ready", ctx)
        const_loaded = c.sem("const_loaded", ctx)
        block = ctx.enter_context(nc.Block())

        @block.gpsimd
        def _(pool):
            nc.gpsimd.memset(c.ident[:], 0.0).then_inc(ones_ready, 1)
            nc.gpsimd.memset(c.minus_half[:], -0.5).then_inc(ones_ready, 1)
            pool.wait_ge(ones_ready, 2)
            nc.gpsimd.affine_select(out=c.ident[:], in_=c.ident[:], compare_op=ALU.not_equal, fill=1.0,
                                    base=0, pattern=[[-1, P]], channel_multiplier=1).then_inc(ones_ready, 1)

        @block.sync
        def _(sp):
            for n, g in enumerate((a["attn_norm"][0], a["mlp_norm"][0], a["ple_norm"][0], a["norm_gain_2"][0])):
                sp.dma_start(c.gains[:, n, :], g.rearrange("(k p) -> p k", p=P)).then_inc(const_loaded, 16)
            sp.wait_ge(const_loaded, 64)


def norm_transpose(nc, chip, name, gain, bias=None, load=None, src=None, dst=None, tiles=TT):
    c = chip
    src = c.H if src is None else src
    Xhi, Xlo = dst or (c.Xhi, c.Xlo)
    per = min(4, tiles)
    n_half = tiles // per
    width = per * P
    with ExitStack() as ctx:
        scaled = c.sb(f"{name}_scaled", [P, per, D], ctx=ctx)
        junk = c.sb(f"{name}_squares", [P, D], ctx=ctx)
        ss = c.sb(f"{name}_ss", [P, TT], ctx=ctx)
        mean = c.sb(f"{name}_mean", [P, TT], ctx=ctx)
        rstd = c.sb(f"{name}_rstd", [P, TT], ctx=ctx)
        full = c.sb(f"{name}_full", [P, NCOL], ctx=ctx) if bias is not None else None
        banks = c.banks(f"{name}_ps", ctx)
        loaded = [c.sem(f"{name}_loaded{t}", ctx) for t in range(tiles)]
        ss_ready = c.sem(f"{name}_ss_ready", ctx)
        mean_ready = c.sem(f"{name}_mean_ready", ctx)
        rstd_ready = c.sem(f"{name}_rstd_ready", ctx)
        scaled_ready = c.sem(f"{name}_scaled_ready", ctx)
        turned = c.sem(f"{name}_turned", ctx)
        hi_ready = c.sem(f"{name}_hi_ready", ctx)
        full_ready = c.sem(f"{name}_full_ready", ctx)
        lo_ready = c.sem(f"{name}_lo_ready", ctx)
        block = ctx.enter_context(nc.Block())

        @block.sync
        def _(sp):
            if load is not None:
                for t in range(tiles):
                    sp.dma_start(src[:, t, :], load[t * P:(t + 1) * P, :]).then_inc(loaded[t], 16)

        @block.scalar
        def _(act):
            for t in range(tiles):
                if load is not None:
                    act.wait_ge(loaded[t], 16)
                if t:
                    act.wait_ge(ss_ready, t)
                nc.scalar.activation(junk[:], src[:, t, :], ACT.Square,
                                     accum_out=ss[:, t:t + 1]).then_inc(ss_ready, 1)
            for n in range(n_half * KT):
                h, k = divmod(n, KT)
                act.wait_ge(turned, n + 1)
                o = Xhi[:, k, h * width:(h + 1) * width]
                if bias is None:
                    nc.scalar.activation(o, banks[n % 8][:, 0:width], ACT.Copy,
                                         scale=gain[:, k:k + 1]).then_inc(hi_ready, 1)
                else:
                    nc.scalar.activation(o, banks[n % 8][:, 0:width], ACT.Identity, scale=gain[:, k:k + 1],
                                         bias=bias[:, k:k + 1]).then_inc(hi_ready, 1)

        @block.gpsimd
        def _(pool):
            for h in range(n_half):
                cols = slice(h * per, (h + 1) * per)
                pool.wait_ge(ss_ready, (h + 1) * per)
                nc.gpsimd.tensor_scalar(mean[:, cols], ss[:, cols], 1.0 / D, EPS, ALU.mult, ALU.add)\
                    .then_inc(mean_ready, 1)
                pool.wait_ge(mean_ready, h + 1)
                nc.gpsimd.tensor_tensor(rstd[:, cols], mean[:, cols], c.minus_half[:, 0:per], ALU.pow)\
                    .then_inc(rstd_ready, 1)

        @block.vector
        def _(dve):
            for h in range(n_half):
                dve.wait_ge(rstd_ready, h + 1)
                if h:
                    dve.wait_ge(turned, h * KT)
                for t in range(per):
                    nc.vector.tensor_scalar(scaled[:, t, :], src[:, h * per + t, :],
                                            rstd[:, h * per + t:h * per + t + 1], None, ALU.mult)\
                        .then_inc(scaled_ready, 1)
                for k in range(KT):
                    n = h * KT + k
                    dve.wait_ge(hi_ready, n + 1)
                    o = slice(h * width, (h + 1) * width)
                    if bias is None:
                        nc.vector.scalar_tensor_tensor(
                            out=Xlo[:, k, o], in0=banks[n % 8][:, 0:width], scalar=gain[:, k:k + 1],
                            in1=Xhi[:, k, o].bitcast(F32), op0=ALU.mult, op1=ALU.subtract).then_inc(lo_ready, 1)
                    else:
                        if n:
                            dve.wait_ge(lo_ready, n)
                        nc.vector.tensor_scalar(full[:, 0:width], banks[n % 8][:, 0:width], gain[:, k:k + 1],
                                                bias[:, k:k + 1], ALU.mult, ALU.add).then_inc(full_ready, 1)
                        dve.wait_ge(full_ready, n + 1)
                        nc.vector.tensor_tensor(Xlo[:, k, o], full[:, 0:width], Xhi[:, k, o].bitcast(F32),
                                                ALU.subtract).then_inc(lo_ready, 1)

        @block.tensor
        def _(pe):
            for h in range(n_half):
                pe.wait_ge(scaled_ready, (h + 1) * per)
                for k in range(KT):
                    n = h * KT + k
                    if n >= 8:
                        pe.wait_ge(lo_ready, n - 7)
                    for t in range(per):
                        last = nc.tensor.transpose(banks[n % 8][:, t * P:(t + 1) * P],
                                                   scaled[:, t, k * P:(k + 1) * P], c.ident[:])
                    last.then_inc(turned, 1)


class Weights:

    def __init__(self, chip, name, ctx, groups, done=None):
        c = chip
        self.nc = c.nc
        self.stage = c.sb(f"{name}_stage", [P, SLOTS, NCOL], ctx=ctx)
        self.hi = c.sb(f"{name}_w_hi", [P, 2, KT, NCOL], F32R, ctx=ctx)
        self.lo = c.sb(f"{name}_w_lo", [P, 2, KT, NCOL], F32R, ctx=ctx)
        self.loaded = [c.sem(f"{name}_w_loaded{i}", ctx) for i in range(SLOTS)]
        self.hi_ready = c.sem(f"{name}_w_hi_ready", ctx)
        self.lo_ready = c.sem(f"{name}_w_lo_ready", ctx)
        self.groups = groups
        self.done = done
        self.chunks = [(g, k, ap) for g, aps in enumerate(groups) for k, ap in enumerate(aps)]
        self.first = [sum(len(x) for x in groups[:g]) for g in range(len(groups) + 1)]

    def load(self, sp):
        for n, (g, k, ap) in enumerate(self.chunks):
            if n >= SLOTS:
                sp.wait_ge(self.lo_ready, n - SLOTS + 1)
            at = 0
            for piece in (ap if isinstance(ap, list) else [ap]):
                w = piece.shape[1]
                sp.dma_start(self.stage[:, n % SLOTS, at:at + w], piece).then_inc(self.loaded[n % SLOTS], 16)
                at += w

    def _loads(self, n):
        return sum(len(ap) if isinstance(ap, list) else 1 for m, (_, _, ap) in enumerate(self.chunks[:n + 1])
                   if m % SLOTS == n % SLOTS)

    def width(self, n):
        ap = self.chunks[n][2]
        return sum(x.shape[1] for x in ap) if isinstance(ap, list) else ap.shape[1]

    def split_hi(self, act, n):
        g, k, _ = self.chunks[n]
        act.wait_ge(self.loaded[n % SLOTS], 16 * self._loads(n))
        if g >= 2:
            act.wait_ge(self.done[0], self.done[1][g - 2])
        w = self.width(n)
        self.nc.scalar.activation(self.hi[:, g % 2, k, 0:w], self.stage[:, n % SLOTS, 0:w], ACT.Copy)\
            .then_inc(self.hi_ready, 1)

    def split_hi_group(self, act, g):
        for n in range(self.first[g], self.first[g + 1]):
            self.split_hi(act, n)

    def split_lo_chunk(self, pool, n):
        g, k, _ = self.chunks[n]
        pool.wait_ge(self.hi_ready, n + 1)
        w = self.width(n)
        self.nc.gpsimd.tensor_tensor(self.lo[:, g % 2, k, 0:w], self.stage[:, n % SLOTS, 0:w],
                                     self.hi[:, g % 2, k, 0:w].bitcast(F32), ALU.subtract)\
            .then_inc(self.lo_ready, 1)

    def split_lo(self, pool):
        for n in range(len(self.chunks)):
            self.split_lo_chunk(pool, n)


def product(nc, out, terms, cols, last_inc=None, ready=None):
    n = 0
    total = 3 * len(terms)
    for t, ((ah, al), (bh, bl)) in enumerate(terms):
        if ready:
            ready(t)
        for x, y in ((ah, bh), (ah, bl), (al, bh)):
            last = nc.tensor.matmul(out, x, y, start=(n == 0), stop=(n == total - 1))
            n += 1
    if last_inc is not None:
        last.then_inc(last_inc, 1)
    return last


def project_to_dram(nc, chip, name, groups):
    c = chip
    with ExitStack() as ctx:
        result_ready = c.sem(f"{name}_result_ready", ctx)
        w = Weights(c, name, ctx, [g[0] for g in groups], (result_ready, [TT * (g + 1) for g in range(len(groups))]))
        ring = c.sb(f"{name}_ring", [P, RING, NCOL], ctx=ctx)
        banks = c.banks(f"{name}_ps", ctx)
        copied = c.sem(f"{name}_copied", ctx)
        stored = [c.sem(f"{name}_stored{i}", ctx) for i in range(RING)]
        outs = [(g, o) for g in range(len(groups)) for o in range(TT)]
        stores = [len(groups[g][2](o)) for g, o in outs]
        upto = [sum(s for m, s in enumerate(stores[:n]) if m % RING == n % RING) for n in range(len(outs) + RING)]
        block = ctx.enter_context(nc.Block())

        @block.sync
        def _(sp):
            w.load(sp)

        @block.gpsimd
        def _(pool):
            w.split_lo(pool)

        @block.tensor
        def _(pe):
            for n, (g, o) in enumerate(outs):
                by_feature = groups[g][1]
                width = w.width(w.first[g])
                if n >= 8:
                    pe.wait_ge(copied, n - 7)
                terms = []
                for k in range(KT):
                    x = c.Xhi, c.Xlo
                    ww = w.hi[:, g % 2, k], w.lo[:, g % 2, k]
                    if by_feature:
                        f, h = divmod(o, HALVES)
                        terms.append((tuple(y[:, f * P:(f + 1) * P] for y in ww),
                                      tuple(y[:, k, h * NCOL:(h + 1) * NCOL] for y in x)))
                    else:
                        terms.append((tuple(y[:, k, o * P:(o + 1) * P] for y in x),
                                      tuple(y[:, 0:width] for y in ww)))
                out = banks[n % 8][:, 0:NCOL if by_feature else width]
                last = product(nc, out, terms, NCOL, result_ready,
                               (lambda k: pe.wait_ge(w.lo_ready, w.first[g] + k + 1)) if o == 0 else None)

        @block.scalar
        def _(act):
            def store(n):
                g, o = outs[n]
                act.wait_ge(copied, n + 1)
                for place, cols in groups[g][2](o):
                    act.dma_start(place, ring[:, n % RING, cols]).then_inc(stored[n % RING], 16)

            w.split_hi_group(act, 0)
            for n, (g, o) in enumerate(outs):
                _, by_feature, _, func, scale = groups[g]
                width = NCOL if by_feature else w.width(w.first[g])
                if n >= RING:
                    act.wait_ge(stored[n % RING], 16 * upto[n])
                act.wait_ge(result_ready, n + 1)
                nc.scalar.activation(ring[:, n % RING, 0:width], banks[n % 8][:, 0:width], func,
                                     scale=scale(o)).then_inc(copied, 1)
                if n:
                    store(n - 1)
                if g + 1 < len(groups):
                    w.split_hi(act, w.first[g + 1] + o)
            store(len(outs) - 1)
            for i in range(RING):
                n = max(m for m in range(len(outs)) if m % RING == i)
                act.wait_ge(stored[i], 16 * (upto[n] + stores[n]))


def split_small(nc, chip, name, ctx, parts):
    out = {}
    for pn, shape in parts:
        out[pn] = (chip.sb(f"{name}_{pn}_f", shape, ctx=ctx), chip.sb(f"{name}_{pn}_hi", shape, F32R, ctx=ctx),
                   chip.sb(f"{name}_{pn}_lo", shape, F32R, ctx=ctx))
    return out


def latent_prepare(nc, chip, a, d):
    c = chip
    QW = MH * MQK // 2
    KVW = MH * (MNOPE + MV) // 2
    TWO_PI_HI, TWO_PI_MID, TWO_PI_LO = 6.28125, 0.0019350051879882812, 3.0199159819e-07
    with ExitStack() as ctx:
        sb = lambda n, s, dt=F32: c.sb("mp_" + n, s, dt, ctx=ctx)
        sem = lambda n: c.sem("mp_" + n, ctx)
        zc = sb("zc", [P, TT, 432])
        cT_hi = sb("cT_hi", [P, 3, S], F32R)
        cT_lo = sb("cT_lo", [P, 3, S], F32R)
        w_f = sb("w_f", [P, 1, 1024])
        wq_hi, wq_lo = sb("wq_hi", [P, 2, 768], F32R), sb("wq_lo", [P, 2, 768], F32R)
        wk_hi, wk_lo = sb("wk_hi", [P, 1024], F32R), sb("wk_lo", [P, 1024], F32R)
        junk = sb("junk", [P, 1024])
        cn = sb("cn", [P, 2, 384])
        ss = sb("ss", [P, 3, TT])
        ssm = sb("ssm", [P, 2, TT])
        rstd = sb("rstd", [P, 2, TT])
        gc = sb("gc", [P, 3])
        gq, gk = sb("gq", [P, MQK]), sb("gk", [P, MQK])
        pos_i = sb("pos_i", [P, TT], I32)
        pos = sb("pos", [P, TT])
        freq = sb("freq", [P, 16])
        ang = sb("ang", [P, TT, 16])
        t1, t2 = sb("t1", [P, TT, 16]), sb("t2", [P, TT, 16])
        turn_i = sb("turn_i", [P, TT, 16], I32)
        cos, sin = sb("cos", [P, TT, 16]), sb("sin", [P, TT, 16])
        nrm = sb("nrm", [P, 2, 2, MH, MQK])
        rop = sb("rop", [P, 2, 4, MH, 16])
        ssh, msh, rsh = sb("ssh", [P, 2, 2, MH]), sb("msh", [P, 2, 2, MH]), sb("rsh", [P, 2, 2, MH])
        qk_hi = sb("qk_hi", [MQK, 2, MH, P], F32R)
        qk_lo = sb("qk_lo", [MQK, 2, MH, P], F32R)
        v_hi, v_lo = sb("v_hi", [P, MH, MV], F32R), sb("v_lo", [P, MH, MV], F32R)
        banks = c.banks("mp_ps", ctx)

        loaded = sem("loaded")
        wloaded = sem("wloaded")
        act_step, dve_step, pool_step = sem("act_step"), sem("dve_step"), sem("pool_step")
        c_scaled, c_hi, c_lo = sem("c_scaled"), sem("c_hi"), sem("c_lo")
        ss_ready, rstd_ready, w_split = sem("ss_ready"), sem("rstd_ready"), sem("w_split")
        w_hi_ready = sem("w_hi_ready")
        table_arg, table_ready = sem("table_arg"), sem("table_ready")
        up_ready = sem("up_ready")
        squares, head_ss, head_rstd, up_read, v_hi_ready, v_lo_ready = (
            sem("squares"), sem("head_ss"), sem("head_rstd"), sem("up_read"), sem("v_hi_ready"), sem("v_lo_ready"))
        roped, turned, hi_ready, lo_ready = sem("roped"), sem("turned"), sem("hi_ready"), sem("lo_ready")
        q_out, v_out = sem("q_out"), sem("v_out")
        head_ss_q, c_scaled_read = sem("head_ss_q"), sem("c_scaled_read")
        block = ctx.enter_context(nc.Block())

        w_rows = [a["mla_w_uq"][0, 0:P, :], a["mla_w_uq"][0, P:2 * P, :], a["mla_w_ukv"][0]]
        w_dst = [(wq_hi[:, 0], wq_lo[:, 0]), (wq_hi[:, 1], wq_lo[:, 1]), (wk_hi[:], wk_lo[:])]

        @block.sync
        def _(sp):
            sp.dma_start(zc[:], d["zc"].rearrange("t p n -> p t n")).then_inc(loaded, 16)
            sp.dma_start(gc[:, 0:2], a["mla_q_norm"][0].rearrange("(k p) -> p k", p=P)).then_inc(loaded, 16)
            sp.dma_start(gc[:, 2:3], a["mla_kv_norm"][0].rearrange("(k p) -> p k", p=P)).then_inc(loaded, 16)
            sp.dma_start(gq[:], a["qk_norm_q"].to_broadcast([P, MQK])).then_inc(loaded, 16)
            sp.dma_start(gk[:], a["qk_norm_k"].to_broadcast([P, MQK])).then_inc(loaded, 16)
            sp.dma_start(pos_i[:], a["positions"][0].rearrange("(t p) -> p t", p=P)).then_inc(loaded, 16)
            sp.dma_start(freq[:], a["inv_freq"].to_broadcast([P, 16])).then_inc(loaded, 16)
            for n, rows in enumerate(w_rows):
                if n:
                    sp.wait_ge(w_split, n)
                sp.dma_start(w_f[:, 0, 0:rows.shape[1]], rows).then_inc(wloaded, 16)
            for t in range(TT):
                sp.wait_ge(v_lo_ready, t + 1)
                sp.dma_start(d["mv_hi"][:, t].rearrange("h p v -> p h v"), v_hi[:].bitcast(F32)).then_inc(v_out, 16)
                sp.dma_start(d["mv_lo"][:, t].rearrange("h p v -> p h v"), v_lo[:].bitcast(F32)).then_inc(v_out, 16)
                for q in range(2):
                    sp.wait_ge(lo_ready, 4 * t + 2 * (q + 1))
                    cols = slice(t * P, (t + 1) * P)
                    sp.dma_start(d["mqk_hi"][q, :, :, cols].rearrange("h d s -> d h s"), qk_hi[:, q].bitcast(F32))\
                        .then_inc(q_out, 16)
                    sp.dma_start(d["mqk_lo"][q, :, :, cols].rearrange("h d s -> d h s"), qk_lo[:, q].bitcast(F32))\
                        .then_inc(q_out, 16)
            sp.wait_ge(q_out, 64 * TT)
            sp.wait_ge(v_out, 32 * TT)

        @block.gpsimd
        def _(pool):
            for n, rows in enumerate(w_rows):
                w = rows.shape[1]
                pool.wait_ge(w_hi_ready, n + 1)
                nc.gpsimd.tensor_tensor(w_dst[n][1], w_f[:, 0, 0:w], w_dst[n][0].bitcast(F32), ALU.subtract)\
                    .then_inc(w_split, 1)
            pool.wait_ge(ss_ready, 3 * TT)
            nc.gpsimd.tensor_scalar(ssm[:, 0], ss[:, 0], 1.0 / MQR, EPS, ALU.mult, ALU.add).then_inc(pool_step, 1)
            nc.gpsimd.tensor_scalar(ssm[:, 1], ss[:, 1], 1.0 / MKVR, EPS, ALU.mult, ALU.add).then_inc(pool_step, 1)
            pool.wait_ge(pool_step, 2)
            nc.gpsimd.tensor_tensor(rstd[:], ssm[:], c.minus_half[:, 0:16].rearrange("p (a b) -> p a b", a=2),
                                    ALU.pow).then_inc(rstd_ready, 1)
            for t in range(TT):
                b = t % 2
                pool.wait_ge(head_ss, t + 1)
                nc.gpsimd.tensor_scalar(msh[:, b], ssh[:, b], 1.0 / MQK, EPS, ALU.mult, ALU.add)\
                    .then_inc(pool_step, 1)
                pool.wait_ge(pool_step, 3 + t)
                nc.gpsimd.tensor_tensor(rsh[:, b], msh[:, b],
                                        c.minus_half[:, 0:16].rearrange("p (a b) -> p a b", a=2),
                                        ALU.pow).then_inc(head_rstd, 1)

        @block.scalar
        def _(act):
            for n, rows in enumerate(w_rows):
                act.wait_ge(wloaded, 16 * (n + 1))
                nc.scalar.activation(w_dst[n][0], w_f[:, 0, 0:rows.shape[1]], ACT.Copy).then_inc(w_hi_ready, 1)
            act.wait_ge(loaded, 16 * 7)
            n = 0
            for t in range(TT):
                for m, (lo, hi) in enumerate(((16, 272), (272, 400), (400, 432))):
                    if n:
                        act.wait_ge(ss_ready, n)
                    nc.scalar.activation(junk[:, 0:hi - lo], zc[:, t, lo:hi], ACT.Square,
                                         accum_out=ss[:, m, t:t + 1]).then_inc(ss_ready, 1)
                    n += 1
            for i, (arg, out) in enumerate(((t1, sin), (t2, cos))):
                act.wait_ge(table_arg, i + 1)
                nc.scalar.activation(out[:], arg[:], ACT.Sin).then_inc(table_ready, 1)
            for n in range(6):
                j = n % 3
                h = n // 3
                act.wait_ge(c_scaled_read, 4 * (h + 1))
                nc.scalar.activation(cT_hi[:, j, h * NCOL:(h + 1) * NCOL], banks[n][:], ACT.Copy,
                                     scale=gc[:, j:j + 1]).then_inc(c_hi, 1)
            for t in range(TT):
                act.wait_ge(up_ready, t + 1)
                if t:
                    act.wait_ge(head_ss, t)
                for g in range(2):
                    nc.scalar.activation(junk[:, g * QW:(g + 1) * QW], banks[g][:, 0:QW], ACT.Square)\
                        .then_inc(squares, 1)
                act.wait_ge(head_ss_q, t + 1)
                for g in range(2):
                    nc.scalar.activation(
                        junk[:, g * 256:(g + 1) * 256].rearrange("p (h n) -> p h n", h=4),
                        banks[2 + g][:].rearrange("p (h n) -> p h n", h=4)[:, :, 0:MNOPE], ACT.Square)\
                        .then_inc(squares, 1)
                if t:
                    act.wait_ge(v_out, 32 * t)
                for g in range(2):
                    nc.scalar.activation(v_hi[:, 4 * g:4 * g + 4, :],
                                         banks[2 + g][:].rearrange("p (h n) -> p h n", h=4)[:, :, MNOPE:],
                                         ACT.Copy).then_inc(v_hi_ready, 1)
                for m in range(4):
                    q, g = divmod(m, 2)
                    act.wait_ge(turned, 4 * t + m + 1)
                    if t:
                        act.wait_ge(q_out, 64 * t)
                    nc.scalar.activation(qk_hi[:, q, 4 * g:4 * g + 4, :],
                                         banks[4 + m][0:MQK].rearrange("p (h n) -> p h n", h=4),
                                         ACT.Copy).then_inc(hi_ready, 1)


        @block.vector
        def _(dve):
            steps = [0]

            def step(ins):
                steps[0] += 1
                ins.then_inc(dve_step, 1)
                dve.wait_ge(dve_step, steps[0])

            dve.wait_ge(loaded, 16 * 7)
            step(nc.vector.tensor_copy(pos[:], pos_i[:]))
            step(nc.vector.tensor_tensor(ang[:], pos[:].unsqueeze(2).to_broadcast([P, TT, 16]),
                                         freq[:].unsqueeze(1).to_broadcast([P, TT, 16]), ALU.mult))
            for i, (shift, out) in enumerate(((0.0, t1), (0.25, t2))):
                step(nc.vector.tensor_scalar(t1[:] if i == 0 else t2[:], ang[:], 0.15915494309189535, shift,
                                             ALU.mult, ALU.add))
                step(nc.vector.tensor_copy(turn_i[:], out[:]))
                step(nc.vector.tensor_copy(cos[:], turn_i[:]))
                step(nc.vector.scalar_tensor_tensor(out=out[:], in0=cos[:], scalar=-TWO_PI_HI, in1=ang[:],
                                                    op0=ALU.mult, op1=ALU.add))
                step(nc.vector.scalar_tensor_tensor(out=out[:], in0=cos[:], scalar=-TWO_PI_MID, in1=out[:],
                                                    op0=ALU.mult, op1=ALU.add))
                step(nc.vector.scalar_tensor_tensor(out=out[:], in0=cos[:], scalar=-TWO_PI_LO, in1=out[:],
                                                    op0=ALU.mult, op1=ALU.add))
                if i:
                    step(nc.vector.tensor_scalar(out[:], out[:], 1.5707963267948966, None, ALU.add))
                nc.vector.tensor_scalar(out[:], out[:], 3.1415925, -3.1415925, ALU.min, ALU.max)\
                    .then_inc(table_arg, 1)
                if i == 0:
                    dve.wait_ge(table_arg, 1)
            dve.wait_ge(rstd_ready, 1)
            for t in range(TT):
                if t >= 2:
                    dve.wait_ge(c_scaled_read, t - 1)
                nc.vector.tensor_scalar(cn[:, t % 2, 0:256], zc[:, t, 16:272], rstd[:, 0, t:t + 1], None, ALU.mult)\
                    .then_inc(c_scaled, 1)
                nc.vector.tensor_scalar(cn[:, t % 2, 256:384], zc[:, t, 272:400], rstd[:, 1, t:t + 1], None, ALU.mult)\
                    .then_inc(c_scaled, 1)
            for n in range(6):
                j, h = n % 3, n // 3
                dve.wait_ge(c_hi, n + 1)
                nc.vector.scalar_tensor_tensor(
                    out=cT_lo[:, j, h * NCOL:(h + 1) * NCOL], in0=banks[n][:], scalar=gc[:, j:j + 1],
                    in1=cT_hi[:, j, h * NCOL:(h + 1) * NCOL].bitcast(F32), op0=ALU.mult, op1=ALU.subtract)\
                    .then_inc(c_lo, 1)
            dve.wait_ge(table_ready, 2)
            for t in range(TT):
                b = t % 2
                dve.wait_ge(squares, 4 * t + 2)
                nc.vector.tensor_reduce(out=ssh[:, b, 0], in_=junk[:, 0:768].rearrange("p (h n) -> p h n", h=MH),
                                        op=ALU.add, axis=AX.X).then_inc(head_ss_q, 1)
                dve.wait_ge(squares, 4 * t + 4)
                step(nc.vector.tensor_reduce(out=ssh[:, b, 1], in_=junk[:, 0:512].rearrange("p (h n) -> p h n", h=MH),
                                             op=ALU.add, axis=AX.X))
                nc.vector.tensor_scalar(ssh[:, b, 1], ssh[:, b, 1], ss[:, 2, t:t + 1], None, ALU.add)\
                    .then_inc(head_ss, 1)
                dve.wait_ge(v_hi_ready, 2 * t + 2)
                for g in range(2):
                    last = nc.vector.tensor_tensor(
                        v_lo[:, 4 * g:4 * g + 4, :],
                        banks[2 + g][:].rearrange("p (h n) -> p h n", h=4)[:, :, MNOPE:],
                        v_hi[:, 4 * g:4 * g + 4, :].bitcast(F32), ALU.subtract)
                last.then_inc(v_lo_ready, 1)
                dve.wait_ge(head_rstd, t + 1)
                rs = rsh[:, b]
                for g in range(2):
                    hs = slice(4 * g, 4 * g + 4)
                    nc.vector.tensor_tensor(nrm[:, b, 0, hs], banks[g][:, 0:QW].rearrange("p (h n) -> p h n", h=4),
                                            rs[:, 0, hs].unsqueeze(2).to_broadcast([P, 4, MQK]), ALU.mult)\
                        .then_inc(dve_step, 1)
                    nc.vector.tensor_tensor(nrm[:, b, 1, hs, 0:MNOPE],
                                            banks[2 + g][:].rearrange("p (h n) -> p h n", h=4)[:, :, 0:MNOPE],
                                            rs[:, 1, hs].unsqueeze(2).to_broadcast([P, 4, MNOPE]), ALU.mult)\
                        .then_inc(dve_step, 1)
                steps[0] += 4
                step(nc.vector.tensor_tensor(nrm[:, b, 1, :, MNOPE:],
                                             zc[:, t, 400:432].unsqueeze(1).to_broadcast([P, MH, MROPE]),
                                             rs[:, 1].unsqueeze(2).to_broadcast([P, MH, MROPE]), ALU.mult))
                for q, g in ((0, gq), (1, gk)):
                    x = nrm[:, b, q]
                    step(nc.vector.tensor_tensor(x, x, g[:].unsqueeze(1).to_broadcast([P, MH, MQK]), ALU.mult))
                    x1, x2 = x[:, :, 64:80], x[:, :, 80:96]
                    cs = cos[:, t].unsqueeze(1).to_broadcast([P, MH, 16])
                    sn = sin[:, t].unsqueeze(1).to_broadcast([P, MH, 16])
                    for m, (u, v) in enumerate(((x1, cs), (x2, sn), (x2, cs), (x1, sn))):
                        nc.vector.tensor_tensor(rop[:, b, m], u, v, ALU.mult).then_inc(dve_step, 1)
                    steps[0] += 4
                    dve.wait_ge(dve_step, steps[0])
                    nc.vector.tensor_tensor(x1, rop[:, b, 0], rop[:, b, 1], ALU.subtract).then_inc(roped, 1)
                    nc.vector.tensor_tensor(x2, rop[:, b, 2], rop[:, b, 3], ALU.add).then_inc(roped, 1)
                for m in range(4):
                    q, g = divmod(m, 2)
                    dve.wait_ge(hi_ready, 4 * t + m + 1)
                    nc.vector.tensor_tensor(qk_lo[:, q, 4 * g:4 * g + 4, :],
                                            banks[4 + m][0:MQK].rearrange("p (h n) -> p h n", h=4),
                                            qk_hi[:, q, 4 * g:4 * g + 4, :].bitcast(F32), ALU.subtract)\
                        .then_inc(lo_ready, 1)


        @block.tensor
        def _(pe):
            for t in range(TT):
                pe.wait_ge(c_scaled, 2 * t + 2)
                h, u = divmod(t, 4)
                for j in range(3):
                    last = nc.tensor.transpose(banks[3 * h + j][:, u * P:(u + 1) * P],
                                               cn[:, t % 2, j * P:(j + 1) * P], c.ident[:])
                last.then_inc(c_scaled_read, 1)
            pe.wait_ge(c_lo, 6)
            pe.wait_ge(w_split, 3)

            def up(t):
                tok = slice(t * P, (t + 1) * P)
                if t:
                    pe.wait_ge(roped, 4 * t)
                    pe.wait_ge(v_lo_ready, t)
                for g in range(2):
                    product(nc, banks[g][:, 0:QW],
                            [((cT_hi[:, k, tok], cT_lo[:, k, tok]),
                              (wq_hi[:, k, g * QW:(g + 1) * QW], wq_lo[:, k, g * QW:(g + 1) * QW]))
                             for k in range(2)], QW)
                for g in range(2):
                    last = product(nc, banks[2 + g][:],
                                   [((cT_hi[:, 2, tok], cT_lo[:, 2, tok]),
                                     (wk_hi[:, g * KVW:(g + 1) * KVW], wk_lo[:, g * KVW:(g + 1) * KVW]))], KVW)
                last.then_inc(up_ready, 1)

            for t in range(TT):
                up(t)
                for q in range(2):
                    pe.wait_ge(roped, 4 * t + 2 * (q + 1))
                    for g in range(2):
                        if t:
                            pe.wait_ge(lo_ready, 4 * (t - 1) + 2 * q + g + 1)
                        for h in range(4):
                            last = nc.tensor.transpose(banks[4 + 2 * q + g][0:MQK, h * P:(h + 1) * P],
                                                       nrm[:, t % 2, q, 4 * g + h, :], c.ident[:])
                        last.then_inc(turned, 1)


def gated_linear_attention(nc, chip, a, d):
    c = chip
    CH = 4
    UT = CH * P
    UNITS = [(h, p) for h in range(TT // CH) for p in range(GH // 2)]
    LEVELS = (64, 32, 16)
    TAU = 16.0
    NQ = len(LEVELS) + 1
    with ExitStack() as ctx:
        sb = lambda n, s, dt=F32: c.sb("gla_" + n, s, dt, ctx=ctx)
        sem = lambda n: c.sem("gla_" + n, ctx)
        qT, kT = sb("qT", [P, 2, S]), sb("kT", [P, 2, S])
        v = c.H[:, 0:TT // 2, :].rearrange("p a (b n) -> p (a b) n", n=GH * GDV)
        gate = c.H[:, TT // 2:TT, :].rearrange("p a (b n) -> p (a b) n", n=GH * GDV)
        glow = sb("glow", [P, TT, GR])
        glowT = sb("glowT", [GR, S])
        w2 = sb("w2", [GR, 2 * P])
        gb = sb("gb", [P, 2])
        gain = sb("gain", [P, GDV])
        masks = sb("masks", [P, NQ, P])
        reset = sb("reset", [P, UT])
        low, mag, b = sb("low", [P, UT]), sb("mag", [P, UT]), sb("b", [P, UT])
        diff = sb("diff", [P, 2, UT])
        expo = sb("expo", [P, 2, UT])
        expn = sb("expn", [P, UT])
        qs = sb("qs", [P, 2, NQ + 1, UT])
        ks = sb("ks", [P, 2, NQ + 1, UT])
        dec = sb("dec", [P, 2, CH])
        state = sb("state", [P, 2, 2 * GDV])
        masked = sb("masked", [P, 2, NQ, P])
        st = sb("st", [P, 2, P])
        kdt = sb("kdt", [P, P])
        o_sq = sb("o_sq", [P, 2 * GDV])
        o_ss, o_ms, o_rs = sb("o_ss", [P, 2]), sb("o_ms", [P, 2]), sb("o_rs", [P, 2])
        on = sb("on", [P, CH, 2 * GDV])
        banks = c.banks("gla_ps", ctx)
        loaded = sem("loaded")
        ready0 = sem("ready0")
        gl_turned, gl_ready, pre_ready = sem("gl_turned"), sem("gl_ready"), sem("pre_ready")
        act_step, dve_step, pool_step = sem("act_step"), sem("dve_step"), sem("pool_step")
        mag_ready, low_ready, ln_ready, b_ready = sem("mag_ready"), sem("low_ready"), sem("ln_ready"), sem("b_ready")
        diff_ready, exp_ready, q_used, k_used = sem("diff_ready"), sem("exp_ready"), sem("q_used"), sem("k_used")
        scored, mask_ready, st_ready, st_used = sem("scored"), sem("mask_ready"), sem("st_ready"), sem("st_used")
        kd_turned, kdt_ready, update_ready, state_ready = (
            sem("kd_turned"), sem("kdt_ready"), sem("update_ready"), sem("state_ready"))
        o_squared, o_summed, o_rstd, o_done = (
            sem("o_squared"), sem("o_summed"), sem("o_rstd"), sem("o_done"))
        turned, hi_ready, lo_ready = sem("turned"), sem("hi_ready"), sem("lo_ready")
        block = ctx.enter_context(nc.Block())

        @block.sync
        def _(sp):
            for place, src in (
                (glow[:], d["zc"][:, :, 0:GR].rearrange("t p n -> p t n")), (w2[:], a["gla_gate_w2"][0]),
                (gb[:], a["gla_gate_b"][0].rearrange("(k p) -> p k", p=P)), (masks[:], a["gla_masks"]),
                (gain[:], a["gla_out_norm"].to_broadcast([P, GDV])),
                (qT[:], d["gqk"][0:2].rearrange("k p s -> p k s")), (kT[:], d["gqk"][2:4].rearrange("k p s -> p k s")),
                (v, d["gv"].rearrange("t p n -> p t n")), (gate, d["gr"].rearrange("t p n -> p t n")),
            ):
                sp.dma_start(place, src).then_inc(loaded, 16)

        @block.gpsimd
        def _(pool):
            steps = [0]

            def step(ins):
                steps[0] += 1
                ins.then_inc(pool_step, 1)
                pool.wait_ge(pool_step, steps[0])

            step(nc.gpsimd.memset(reset[:], 1.0))
            nc.gpsimd.memset(reset[:].rearrange("p (c t) -> p c t", t=P)[:, :, 0:1], 0.0).then_inc(ready0, 1)
            nc.gpsimd.memset(state[:], 0.0).then_inc(ready0, 1)
            pool.wait_ge(loaded, 16 * 9)
            for t in range(TT):
                last = nc.gpsimd.tensor_tensor(gate[:, t].rearrange("p (h n) -> p h n", h=GH),
                                               gate[:, t].rearrange("p (h n) -> p h n", h=GH),
                                               gain[:].unsqueeze(1).to_broadcast([P, GH, GDV]), ALU.mult)
            last.then_inc(ready0, 1)

            def prep(u):
                h, p = UNITS[u]
                kk = kT[:, p, h * UT:(h + 1) * UT]
                if u >= 2:
                    pool.wait_ge(st_used, 2 * CH * (u - 1))
                for i, (slot, dst) in enumerate(((0, 0), (1, 1), (0, 2), (2, 3), (1, 4))):
                    pool.wait_ge(exp_ready, 7 * u + (1, 2, 3, 5, 7)[i])
                    src = expn[:] if slot == 2 else expo[:, slot]
                    nc.gpsimd.tensor_tensor(ks[:, u % 2, dst], kk, src, ALU.mult).then_inc(k_used, 1)

            def chunk(n):
                pool.wait_ge(o_summed, n + 1)
                step(nc.gpsimd.tensor_scalar(o_ms[:], o_ss[:], 1.0 / GDV, EPS, ALU.mult, ALU.add))
                nc.gpsimd.tensor_tensor(o_rs[:], o_ms[:], c.minus_half[:, 0:2], ALU.pow).then_inc(o_rstd, 1)

            prep(0)
            for u in range(len(UNITS)):
                if u + 1 < len(UNITS):
                    prep(u + 1)
                for i in range(CH):
                    chunk(u * CH + i)

        @block.scalar
        def _(act):
            act.wait_ge(gl_turned, 1)
            nc.scalar.activation(glowT[:, 0:NCOL], banks[0][0:GR, :], ACT.Copy).then_inc(gl_ready, 1)
            nc.scalar.activation(glowT[:, NCOL:S], banks[1][0:GR, :], ACT.Copy).then_inc(gl_ready, 1)
            steps = [0]

            def step(ins):
                steps[0] += 1
                ins.then_inc(act_step, 1)
                act.wait_ge(act_step, steps[0])

            def prep(u):
                h, p = UNITS[u]
                act.wait_ge(pre_ready, u + 1)
                if u:
                    act.wait_ge(b_ready, u)
                nc.scalar.activation(mag[:], banks[0][:], ACT.Abs, bias=gb[:, p:p + 1]).then_inc(mag_ready, 1)
                act.wait_ge(mag_ready, u + 1)
                step(nc.scalar.activation(mag[:], mag[:], ACT.Exp, scale=-1.0))
                nc.scalar.activation(mag[:], mag[:], ACT.Ln, bias=1.0).then_inc(ln_ready, 1)
                e = 7 * u
                for i in range(3):
                    act.wait_ge(diff_ready, 5 * u + i + 1)
                    if i == 2:
                        act.wait_ge(q_used, 5 * u + 1)
                        act.wait_ge(k_used, 5 * u + 1)
                    elif u:
                        act.wait_ge(q_used, 5 * u)
                        act.wait_ge(k_used, 5 * u)
                    step(nc.scalar.activation(diff[:, i % 2], diff[:, i % 2], ACT.Abs))
                    nc.scalar.activation(expo[:, i % 2], diff[:, i % 2], ACT.Exp, scale=-1.0 / TAU).then_inc(exp_ready, 1)
                act.wait_ge(diff_ready, 5 * u + 4)
                act.wait_ge(q_used, 5 * u + 2)
                act.wait_ge(k_used, 5 * u + 2)
                nc.scalar.activation(expo[:, 1], diff[:, 1], ACT.Exp, scale=1.0 / TAU).then_inc(exp_ready, 1)
                nc.scalar.activation(expn[:], diff[:, 1], ACT.Exp, scale=-1.0 / TAU).then_inc(exp_ready, 1)
                act.wait_ge(q_used, 5 * u + 3)
                act.wait_ge(k_used, 5 * u + 3)
                nc.scalar.activation(expo[:, 0], b[:], ACT.Exp, scale=1.0 / TAU).then_inc(exp_ready, 1)
                act.wait_ge(diff_ready, 5 * u + 5)
                act.wait_ge(q_used, 5 * u + 4)
                nc.scalar.activation(expo[:, 1], diff[:, 0], ACT.Exp, scale=1.0 / TAU).then_inc(exp_ready, 1)

            def chunk(n):
                act.wait_ge(kd_turned, n + 1)
                if n:
                    act.wait_ge(update_ready, n)
                nc.scalar.activation(kdt[:], banks[5][:, 0:P], ACT.Copy).then_inc(kdt_ready, 1)
                act.wait_ge(st_used, 2 * (n + 1))
                if n:
                    act.wait_ge(o_summed, n)
                nc.scalar.activation(o_sq[:], banks[3 + n % 2][:, 0:2 * GDV], ACT.Square).then_inc(o_squared, 1)

            def out(u):
                h, p = UNITS[u]
                for i in range(2):
                    act.wait_ge(turned, 2 * u + i + 1)
                    nc.scalar.activation(c.Xhi[:, 2 * p + i, h * UT:(h + 1) * UT], banks[7][:], ACT.Copy)\
                        .then_inc(hi_ready, 1)

            prep(0)
            for u in range(len(UNITS)):
                if u + 1 < len(UNITS):
                    prep(u + 1)
                for i in range(CH):
                    chunk(u * CH + i)
                out(u)

        @block.vector
        def _(dve):
            steps = [0]

            def step(ins):
                steps[0] += 1
                ins.then_inc(dve_step, 1)
                dve.wait_ge(dve_step, steps[0])

            dve.wait_ge(loaded, 16 * 9)
            dve.wait_ge(ready0, 3)

            def difference(slot, block_len, ref, sign=1):
                bb = b[:].rearrange("p (n t) -> p n t", t=block_len)
                rr = bb[:, :, ref:ref + 1].to_broadcast([P, UT // block_len, block_len])
                o = diff[:, slot].rearrange("p (n t) -> p n t", t=block_len)
                return nc.vector.tensor_tensor(o, bb, rr, ALU.subtract) if sign > 0 else \
                    nc.vector.tensor_tensor(o, rr, bb, ALU.subtract)

            def prep(u):
                h, p = UNITS[u]
                qq = qT[:, p, h * UT:(h + 1) * UT]
                par = u % 2
                dve.wait_ge(mag_ready, u + 1)
                nc.vector.tensor_scalar(low[:], banks[0][:], gb[:, p:p + 1], 0.0, ALU.add, ALU.min)\
                    .then_inc(low_ready, 1)
                dve.wait_ge(low_ready, u + 1)
                dve.wait_ge(ln_ready, u + 1)
                step(nc.vector.tensor_tensor(low[:], low[:], mag[:], ALU.subtract))
                if u:
                    dve.wait_ge(exp_ready, 7 * u)
                nc.vector.tensor_tensor_scan(b[:], reset[:], low[:], 0.0, ALU.mult, ALU.add).then_inc(b_ready, 1)
                dve.wait_ge(b_ready, u + 1)
                if u >= 2:
                    dve.wait_ge(st_used, 2 * CH * (u - 1))
                difference(0, 2 * LEVELS[0], LEVELS[0] - 1).then_inc(diff_ready, 1)
                difference(1, 2 * LEVELS[1], LEVELS[1] - 1).then_inc(diff_ready, 1)

                def decayed(i, need, src):
                    dve.wait_ge(exp_ready, 7 * u + need)
                    nc.vector.tensor_tensor(qs[:, par, i], qq, src, ALU.mult).then_inc(q_used, 1)

                decayed(0, 1, expo[:, 0])
                difference(0, 2 * LEVELS[2], LEVELS[2] - 1).then_inc(diff_ready, 1)
                decayed(1, 2, expo[:, 1])
                step(difference(1, 16, 7))
                nc.vector.tensor_scalar(diff[:, 1], diff[:, 1], 80.0 * TAU, -80.0 * TAU, ALU.min, ALU.max)\
                    .then_inc(diff_ready, 1)
                decayed(2, 3, expo[:, 0])
                difference(0, P, P - 1, -1).then_inc(diff_ready, 1)
                decayed(3, 4, expo[:, 1])
                dve.wait_ge(exp_ready, 7 * u + 6)
                nc.vector.tensor_copy(dec[:, par], expo[:, 0].rearrange("p (c t) -> p c t", t=P)[:, :, P - 1])\
                    .then_inc(dve_step, 1)
                steps[0] += 1
                decayed(4, 6, expo[:, 0])

            def chunk(n):
                u, i = divmod(n, CH)
                h, p = UNITS[u]
                t = h * CH + i
                for hd in range(2):
                    m = 2 * n + hd
                    dve.wait_ge(scored, m + 1)
                    step(nc.vector.tensor_tensor(masked[:, m % 2].rearrange("p a b -> p (a b)"), banks[1 + m % 2][:],
                                                 masks[:].rearrange("p a b -> p (a b)"), ALU.mult))
                    if m >= 2:
                        dve.wait_ge(st_used, m - 1)
                    nc.vector.tensor_reduce(out=st[:, m % 2], in_=masked[:, m % 2].rearrange("p a b -> p b a"),
                                            op=ALU.add, axis=AX.X).then_inc(st_ready, 1)
                dve.wait_ge(update_ready, n + 1)
                dve.wait_ge(st_used, 2 * (n + 1))
                for hd in range(2):
                    rows, cols = slice(64 * hd, 64 * hd + 64), slice(GDV * hd, GDV * (hd + 1))
                    last = nc.vector.scalar_tensor_tensor(
                        out=state[rows, p, cols], in0=state[rows, p, cols], scalar=dec[rows, u % 2, i:i + 1],
                        in1=banks[6][rows, cols], op0=ALU.mult, op1=ALU.add)
                last.then_inc(state_ready, 1)
                dve.wait_ge(o_squared, n + 1)
                nc.vector.tensor_reduce(out=o_ss[:], in_=o_sq[:].rearrange("p (h n) -> p h n", h=2), op=ALU.add,
                                        axis=AX.X).then_inc(o_summed, 1)
                dve.wait_ge(o_rstd, n + 1)
                if i == 0 and u:
                    dve.wait_ge(turned, 2 * u)
                for hd in range(2):
                    cols = slice(GDV * hd, GDV * (hd + 1))
                    last = nc.vector.scalar_tensor_tensor(
                        out=on[:, i, cols], in0=banks[3 + n % 2][:, cols], scalar=o_rs[:, hd:hd + 1],
                        in1=gate[:, t, (2 * p + hd) * GDV:(2 * p + hd + 1) * GDV], op0=ALU.mult, op1=ALU.mult)
                last.then_inc(o_done, 1)

            def out(u):
                h, p = UNITS[u]
                for i in range(2):
                    dve.wait_ge(hi_ready, 2 * u + i + 1)
                    nc.vector.tensor_tensor(c.Xlo[:, 2 * p + i, h * UT:(h + 1) * UT], banks[7][:],
                                            c.Xhi[:, 2 * p + i, h * UT:(h + 1) * UT].bitcast(F32), ALU.subtract)\
                        .then_inc(lo_ready, 1)

            prep(0)
            for u in range(len(UNITS)):
                if u + 1 < len(UNITS):
                    prep(u + 1)
                for i in range(CH):
                    chunk(u * CH + i)
                out(u)

        @block.tensor
        def _(pe):
            pe.wait_ge(loaded, 16 * 9)
            for t in range(TT):
                last = nc.tensor.transpose(banks[t // 4][0:GR, (t % 4) * P:(t % 4 + 1) * P], glow[:, t, :], c.ident[:])
            last.then_inc(gl_turned, 1)
            pe.wait_ge(gl_ready, 2)
            pe.wait_ge(ready0, 2)

            def gates(u):
                h, p = UNITS[u]
                if u:
                    pe.wait_ge(low_ready, u)
                nc.tensor.matmul(banks[0][:], w2[:, p * P:(p + 1) * P], glowT[:, h * UT:(h + 1) * UT],
                                 start=True, stop=True).then_inc(pre_ready, 1)

            def chunk(n):
                u, i = divmod(n, CH)
                h, p = UNITS[u]
                t, par = h * CH + i, u % 2
                tok = slice(i * P, (i + 1) * P)
                vv = v[:, t, 2 * p * GDV:(2 * p + 2) * GDV]
                if i == 0:
                    pe.wait_ge(q_used, 5 * (u + 1))
                    pe.wait_ge(k_used, 5 * (u + 1))
                if n:
                    pe.wait_ge(kdt_ready, n)
                nc.tensor.transpose(banks[5][:, 0:P], ks[:, par, NQ, tok], c.ident[:]).then_inc(kd_turned, 1)
                for hd in range(2):
                    m = 2 * n + hd
                    rows = slice(64 * hd, 64 * hd + 64)
                    if m >= 2:
                        pe.wait_ge(st_ready, m - 1)
                    for lv in range(NQ):
                        last = nc.tensor.matmul(banks[1 + m % 2][:, lv * P:(lv + 1) * P], ks[rows, par, lv, tok],
                                                qs[rows, par, lv, tok], start=(lv == 0), stop=True,
                                                skip_group_check=True)
                    last.then_inc(scored, 1)
                pe.wait_ge(kdt_ready, n + 1)
                if n:
                    pe.wait_ge(state_ready, n)
                nc.tensor.matmul(banks[6][:, 0:2 * GDV], kdt[:], vv, start=True, stop=True).then_inc(update_ready, 1)
                if n >= 2:
                    pe.wait_ge(o_done, n - 1)
                ob = banks[3 + n % 2]
                nc.tensor.matmul(ob[:, 0:2 * GDV], qs[:, par, NQ, tok], state[:, p], start=True, stop=True,
                                 skip_group_check=True)
                for hd in range(2):
                    m = 2 * n + hd
                    pe.wait_ge(st_ready, m + 1)
                    last = nc.tensor.matmul(ob[:, GDV * hd:GDV * (hd + 1)], st[:, m % 2],
                                            vv[:, GDV * hd:GDV * (hd + 1)], start=False, stop=True,
                                            skip_group_check=True)
                    last.then_inc(st_used, 1)

            def out(u):
                pe.wait_ge(o_done, (u + 1) * CH)
                for hd in range(2):
                    if 2 * u + hd:
                        pe.wait_ge(lo_ready, 2 * u + hd)
                    for i in range(CH):
                        last = nc.tensor.transpose(banks[7][:, i * P:(i + 1) * P], on[:, i, GDV * hd:GDV * (hd + 1)],
                                                   c.ident[:])
                    last.then_inc(turned, 1)

            gates(0)
            for u in range(len(UNITS)):
                if u + 1 < len(UNITS):
                    gates(u + 1)
                for i in range(CH):
                    chunk(u * CH + i)
                out(u)


def latent_attention(nc, chip, a, d):
    c = chip
    SCALE = MQK ** -0.5
    HEADS_OUT = GH * GDV // P
    QT = S // P
    N = MH * QT
    first_chunk = []
    m = 0
    for n in range(N + 1):
        first_chunk.append(m)
        m += (n % QT) // 4 + 1
    with ExitStack() as ctx:
        sb = lambda n, s, dt=F32: c.sb("ma_" + n, s, dt, ctx=ctx)
        sem = lambda n: c.sem("ma_" + n, ctx)
        q_hi, q_lo = sb("q_hi", [MQK, 2, S], F32R), sb("q_lo", [MQK, 2, S], F32R)
        k_hi, k_lo = sb("k_hi", [MQK, 2, S], F32R), sb("k_lo", [MQK, 2, S], F32R)
        v_hi, v_lo = sb("v_hi", [P, 2, TT, MV], F32R), sb("v_lo", [P, 2, TT, MV], F32R)
        prob = sb("prob", [P, 2, S])
        pT_hi, pT_lo = sb("pT_hi", [P, TT, NCOL], F32R), sb("pT_lo", [P, TT, NCOL], F32R)
        mx, nb, sums, inv = (sb(x, [P, 2]) for x in ("mx", "nb", "sums", "inv"))
        mask_f = sb("mask_f", [1, 2, P])
        mask = sb("mask", [1, 2, P], F32R)
        scores = [ctx.enter_context(nc.psum_tensor(f"ma_scores{i}", [P, S], F32)) for i in range(2)]
        turn_bank = c.banks("ma_turn", ctx, 2)
        o_bank = c.banks("ma_o", ctx, 2)
        loaded = [sem(f"loaded{i}") for i in range(2)]
        mask_ready, scored, max_ready, nb_ready, exp_ready = (
            sem("mask_ready"), sem("scored"), sem("max_ready"), sem("nb_ready"), sem("exp_ready"))
        inv_ready, prob_ready, turned, hi_ready, lo_ready = (
            sem("inv_ready"), sem("prob_ready"), sem("turned"), sem("hi_ready"), sem("lo_ready"))
        x_loaded = sem("x_loaded")
        o_ready, o_hi, o_lo = sem("o_ready"), sem("o_hi"), sem("o_lo")
        block = ctx.enter_context(nc.Block())

        @block.sync
        def _(sp):
            sp.dma_start(c.H[:], a["x"][0].rearrange("(t p) n -> p t n", p=P)).then_inc(x_loaded, 16)
            for h in range(MH):
                if h >= 2:
                    sp.wait_ge(o_ready, 2 * (h - 1))
                for place, src in ((q_hi[:, h % 2], d["mqk_hi"][0, h]), (q_lo[:, h % 2], d["mqk_lo"][0, h]),
                                   (k_hi[:, h % 2], d["mqk_hi"][1, h]), (k_lo[:, h % 2], d["mqk_lo"][1, h]),
                                   (v_hi[:, h % 2], d["mv_hi"][h].rearrange("t p v -> p t v")),
                                   (v_lo[:, h % 2], d["mv_lo"][h].rearrange("t p v -> p t v"))):
                    sp.dma_start(place.bitcast(F32), src).then_inc(loaded[h % 2], 16)
            sp.wait_ge(x_loaded, 16)

        @block.gpsimd
        def _(pool):
            nc.gpsimd.memset(mask_f[:], 0.0).then_inc(mask_ready, 1)
            pool.wait_ge(mask_ready, 1)
            nc.gpsimd.memset(mask_f[:, 0, 0:64], -1e30).then_inc(mask_ready, 1)
            nc.gpsimd.memset(mask_f[:, 1, 64:P], 1.0).then_inc(mask_ready, 1)

        @block.tensor
        def _(pe):
            pe.wait_ge(mask_ready, 4)

            def score(n):
                h, qt = divmod(n, QT)
                s = h % 2
                if qt == 0:
                    pe.wait_ge(loaded[s], 96 * (h // 2 + 1))
                if n >= 2:
                    pe.wait_ge(exp_ready, n - 1)
                q = slice(qt * P, (qt + 1) * P)
                keys = (qt + 1) * P
                for at in range(0, keys, NCOL):
                    end = min(at + NCOL, keys)
                    out = scores[n % 2][:, at:end]
                    nc.tensor.matmul(out, q_hi[:, s, q], k_hi[:, s, at:end], start=True, stop=False)
                    nc.tensor.matmul(out, q_hi[:, s, q], k_lo[:, s, at:end], start=False, stop=False)
                    last = nc.tensor.matmul(out, q_lo[:, s, q], k_hi[:, s, at:end], start=False, stop=True)
                last = nc.tensor.matmul(scores[n % 2][:, keys - P:keys], mask[:, 0], mask[:, 1], start=False,
                                        stop=True, skip_group_check=True)
                last.then_inc(scored, 1)

            def turn(n):
                h, qt = divmod(n, QT)
                pe.wait_ge(prob_ready, n + 1)
                for i in range(qt // 4 + 1):
                    m = first_chunk[n] + i
                    if m >= 2:
                        pe.wait_ge(lo_ready, m - 1)
                    for j in range(4 * i, min(4 * i + 4, qt + 1)):
                        last = nc.tensor.transpose(turn_bank[m % 2][:, (j % 4) * P:(j % 4 + 1) * P],
                                                   prob[:, n % 2, j * P:(j + 1) * P], c.ident[:])
                    last.then_inc(turned, 1)

            def values(h, half):
                m = 2 * h + half
                pe.wait_ge(lo_ready, first_chunk[h * QT + 4 * half + 4])
                if m >= 2:
                    pe.wait_ge(o_lo, m - 1)
                n_k = 4 * half + 4
                for j in range(n_k):
                    at = max(0, j - 4 * half) * P
                    vs = v_hi[:, h % 2, j], v_lo[:, h % 2, j]
                    ps = pT_hi[:, j, at:], pT_lo[:, j, at:]
                    for i, (x, y) in enumerate(((0, 0), (0, 1), (1, 0))):
                        last = nc.tensor.matmul(o_bank[m % 2][0:MV, at:], vs[x], ps[y],
                                                start=(j == 0 and i == 0), stop=(i == 2),
                                                skip_group_check=True)
                last.then_inc(o_ready, 1)

            score(0)
            for n in range(N):
                if n + 1 < N:
                    score(n + 1)
                turn(n)
                if n % 4 == 3:
                    values(n // QT, (n % QT) // 4)

        @block.scalar
        def _(act):
            act.wait_ge(mask_ready, 3)
            nc.scalar.activation(mask[:], mask_f[:], ACT.Copy).then_inc(mask_ready, 1)

            def exp(n):
                keys = (n % QT + 1) * P
                act.wait_ge(nb_ready, n + 1)
                if n >= 2:
                    act.wait_ge(turned, first_chunk[n - 1])
                nc.scalar.activation(prob[:, n % 2, 0:keys], scores[n % 2][:, 0:keys], ACT.Exp, scale=SCALE,
                                     bias=nb[:, n % 2:n % 2 + 1], accum_out=sums[:, n % 2:n % 2 + 1])\
                    .then_inc(exp_ready, 1)

            def high(n):
                qt = n % QT
                q = slice((qt % 4) * P, (qt % 4 + 1) * P)
                for i in range(qt // 4 + 1):
                    m = first_chunk[n] + i
                    j, e = 4 * i, min(4 * i + 4, qt + 1)
                    act.wait_ge(turned, m + 1)
                    nc.scalar.activation(pT_hi[:, j:e, q],
                                         turn_bank[m % 2][:, 0:(e - j) * P].rearrange("p (j q) -> p j q", q=P),
                                         ACT.Copy).then_inc(hi_ready, 1)

            def out(h, half):
                m = 2 * h + half
                act.wait_ge(o_ready, m + 1)
                rows = slice(64 * (h % 2), 64 * (h % 2) + 64)
                nc.scalar.activation(c.Xhi[rows, HEADS_OUT + h // 2, half * NCOL:(half + 1) * NCOL],
                                     o_bank[m % 2][0:MV, :], ACT.Copy).then_inc(o_hi, 1)

            exp(0)
            for n in range(N):
                if n + 1 < N:
                    exp(n + 1)
                high(n)
                if n % 4 == 3:
                    out(n // QT, (n % QT) // 4)

        @block.vector
        def _(dve):
            def row_max(n):
                keys = (n % QT + 1) * P
                i = slice(n % 2, n % 2 + 1)
                dve.wait_ge(scored, n + 1)
                nc.vector.tensor_reduce(out=mx[:, i], in_=scores[n % 2][:, 0:keys], op=ALU.max, axis=AX.X)\
                    .then_inc(max_ready, 1)
                dve.wait_ge(max_ready, n + 1)
                nc.vector.tensor_scalar(nb[:, i], mx[:, i], -SCALE, None, ALU.mult).then_inc(nb_ready, 1)

            def normalise(n):
                keys = (n % QT + 1) * P
                i = slice(n % 2, n % 2 + 1)
                dve.wait_ge(exp_ready, n + 1)
                nc.vector.reciprocal(inv[:, i], sums[:, i]).then_inc(inv_ready, 1)
                dve.wait_ge(inv_ready, n + 1)
                nc.vector.tensor_scalar(prob[:, n % 2, 0:keys], prob[:, n % 2, 0:keys], inv[:, i], None, ALU.mult)\
                    .then_inc(prob_ready, 1)

            def low(n):
                qt = n % QT
                q = slice((qt % 4) * P, (qt % 4 + 1) * P)
                for i in range(qt // 4 + 1):
                    m = first_chunk[n] + i
                    j, e = 4 * i, min(4 * i + 4, qt + 1)
                    dve.wait_ge(hi_ready, m + 1)
                    nc.vector.tensor_tensor(pT_lo[:, j:e, q],
                                            turn_bank[m % 2][:, 0:(e - j) * P].rearrange("p (j q) -> p j q", q=P),
                                            pT_hi[:, j:e, q].bitcast(F32), ALU.subtract).then_inc(lo_ready, 1)

            def out(h, half):
                m = 2 * h + half
                dve.wait_ge(o_hi, m + 1)
                rows = slice(64 * (h % 2), 64 * (h % 2) + 64)
                cols = slice(half * NCOL, (half + 1) * NCOL)
                nc.vector.tensor_tensor(c.Xlo[rows, HEADS_OUT + h // 2, cols], o_bank[m % 2][0:MV, :],
                                        c.Xhi[rows, HEADS_OUT + h // 2, cols].bitcast(F32), ALU.subtract)\
                    .then_inc(o_lo, 1)

            row_max(0)
            normalise(0)
            for n in range(N):
                if n + 1 < N:
                    row_max(n + 1)
                low(n)
                if n + 1 < N:
                    normalise(n + 1)
                if n % 4 == 3:
                    out(n // QT, (n % QT) // 4)


def project_into_residual(nc, chip, name, weights, gate=None):
    c = chip
    groups = [[weights[k * P:(k + 1) * P, n * NCOL:(n + 1) * NCOL] for k in range(KT)] for n in range(HALVES)]
    with ExitStack() as ctx:
        result_ready = c.sem(f"{name}_result_ready", ctx)
        added = c.sem(f"{name}_added", ctx)
        gated = c.sem(f"{name}_gated", ctx)
        w = Weights(c, name, ctx, groups, (result_ready, [TT, 2 * TT]))
        gate_sb = c.sb(f"{name}_gate", [P, D], ctx=ctx) if gate is not None else None
        gate_loaded = c.sem(f"{name}_gate_loaded", ctx)
        part = c.sb(f"{name}_part", [P, 2, NCOL], ctx=ctx) if gate is not None else None
        banks = c.banks(f"{name}_ps", ctx)
        outs = [(g, t) for g in range(HALVES) for t in range(TT)]
        block = ctx.enter_context(nc.Block())

        @block.sync
        def _(sp):
            if gate is not None:
                sp.dma_start(gate_sb[:], gate).then_inc(gate_loaded, 16)
            w.load(sp)

        @block.gpsimd
        def _(pool):
            w.split_lo(pool)

        @block.scalar
        def _(act):
            for g in range(HALVES):
                w.split_hi_group(act, g)

        @block.tensor
        def _(pe):
            for n, (g, t) in enumerate(outs):
                if n >= 8:
                    pe.wait_ge(added, n - 7)
                tok = slice(t * P, (t + 1) * P)
                product(nc, banks[n % 8][:],
                        [((c.Xhi[:, k, tok], c.Xlo[:, k, tok]), (w.hi[:, g, k], w.lo[:, g, k])) for k in range(KT)],
                        NCOL, result_ready,
                        (lambda k: pe.wait_ge(w.lo_ready, w.first[g] + k + 1)) if t == 0 else None)

        @block.vector
        def _(dve):
            if gate is not None:
                dve.wait_ge(gate_loaded, 16)
            for n, (g, t) in enumerate(outs):
                cols = slice(g * NCOL, (g + 1) * NCOL)
                dve.wait_ge(result_ready, n + 1)
                src = banks[n % 8][:]
                if gate is not None:
                    nc.vector.tensor_tensor(part[:, n % 2], src, gate_sb[:, cols], ALU.mult).then_inc(gated, 1)
                    dve.wait_ge(gated, n + 1)
                    src = part[:, n % 2]
                nc.vector.tensor_tensor(c.H[:, t, cols], c.H[:, t, cols], src, ALU.add).then_inc(added, 1)


def mlp(nc, chip, a):
    c = chip
    G = D_FF // NCOL
    FT = NCOL // P
    with ExitStack() as ctx:
        sb = lambda n, s, dt=F32: c.sb("mlp_" + n, s, dt, ctx=ctx)
        sem = lambda n: c.sem("mlp_" + n, ctx)
        stage = sb("stage", [P, SLOTS, NCOL])
        w_hi, w_lo = sb("w_hi", [P, 2, KT, NCOL], F32R), sb("w_lo", [P, 2, KT, NCOL], F32R)
        h_hi, h_lo = sb("h_hi", [P, FT, S], F32R), sb("h_lo", [P, FT, S], F32R)
        act_r = sb("act_r", [P, 2, NCOL])
        loaded = [sem(f"loaded{i}") for i in range(SLOTS)]
        w_hi_ready, w_lo_ready = sem("w_hi_ready"), sem("w_lo_ready")
        up_ready, relu_ready, square_ready, h_hi_ready, h_lo_ready = (
            sem("up_ready"), sem("relu_ready"), sem("square_ready"), sem("h_hi_ready"), sem("h_lo_ready"))
        down_ready, added = sem("down_ready"), sem("added")
        up_bank = c.banks("mlp_up", ctx, 3)
        down_bank = c.banks("mlp_down", ctx, 5)
        UP, DOWN = FT * HALVES, TT * HALVES
        block = ctx.enter_context(nc.Block())

        def rows(n):
            g, x = divmod(n, 2 * KT)
            which, k = divmod(x, KT)
            if which == 0:
                return a["w_mlp_up"][0, k * P:(k + 1) * P, g * NCOL:(g + 1) * NCOL]
            j, half = divmod(k, HALVES)
            at = g * NCOL + j * P
            return a["w_mlp_down"][0, at:at + P, half * NCOL:(half + 1) * NCOL]

        @block.sync
        def _(sp):
            for n in range(G * 2 * KT):
                if n >= SLOTS:
                    sp.wait_ge(w_lo_ready, n - SLOTS + 1)
                sp.dma_start(stage[:, n % SLOTS], rows(n)).then_inc(loaded[n % SLOTS], 16)

        @block.gpsimd
        def _(pool):
            for n in range(G * 2 * KT):
                which, k = divmod(n % (2 * KT), KT)
                pool.wait_ge(w_hi_ready, n + 1)
                nc.gpsimd.tensor_tensor(w_lo[:, which, k], stage[:, n % SLOTS], w_hi[:, which, k].bitcast(F32),
                                        ALU.subtract).then_inc(w_lo_ready, 1)

        @block.scalar
        def _(act):
            def split(n):
                g, x = divmod(n, 2 * KT)
                which, k = divmod(x, KT)
                act.wait_ge(loaded[n % SLOTS], 16 * (n // SLOTS + 1))
                if g and k == 0:
                    act.wait_ge(*((up_ready, UP * g) if which == 0 else (down_ready, DOWN * g)))
                nc.scalar.activation(w_hi[:, which, k], stage[:, n % SLOTS], ACT.Copy).then_inc(w_hi_ready, 1)

            for n in range(KT):
                split(n)
            for g in range(G):
                for o in range(UP):
                    n = g * UP + o
                    f, h = divmod(o, HALVES)
                    act.wait_ge(up_ready, n + 1)
                    if n >= 2:
                        act.wait_ge(h_lo_ready, n - 1)
                    nc.scalar.activation(act_r[:, n % 2], up_bank[n % 3][:], ACT.Relu).then_inc(relu_ready, 1)
                    split(g * 2 * KT + KT + o)
                    act.wait_ge(square_ready, n + 1)
                    if g and o == 0:
                        act.wait_ge(down_ready, DOWN * g)
                    nc.scalar.activation(h_hi[:, f, h * NCOL:(h + 1) * NCOL], act_r[:, n % 2], ACT.Copy)\
                        .then_inc(h_hi_ready, 1)
                if g + 1 < G:
                    for k in range(KT):
                        split((g + 1) * 2 * KT + k)

        @block.vector
        def _(dve):
            for g in range(G):
                for o in range(UP):
                    n = g * UP + o
                    f, h = divmod(o, HALVES)
                    dve.wait_ge(relu_ready, n + 1)
                    nc.vector.tensor_tensor(act_r[:, n % 2], act_r[:, n % 2], act_r[:, n % 2], ALU.mult)\
                        .then_inc(square_ready, 1)
                    dve.wait_ge(h_hi_ready, n + 1)
                    nc.vector.tensor_tensor(h_lo[:, f, h * NCOL:(h + 1) * NCOL], act_r[:, n % 2],
                                            h_hi[:, f, h * NCOL:(h + 1) * NCOL].bitcast(F32), ALU.subtract)\
                        .then_inc(h_lo_ready, 1)
                for o in range(DOWN):
                    n = g * DOWN + o
                    t, half = divmod(o, HALVES)
                    cols = slice(half * NCOL, (half + 1) * NCOL)
                    dve.wait_ge(down_ready, n + 1)
                    nc.vector.tensor_tensor(c.H[:, t, cols], c.H[:, t, cols], down_bank[n % 5][:], ALU.add)\
                        .then_inc(added, 1)

        @block.tensor
        def _(pe):
            for g in range(G):
                for o in range(UP):
                    n = g * UP + o
                    f, h = divmod(o, HALVES)
                    if n >= 3:
                        pe.wait_ge(relu_ready, n - 2)
                    product(nc, up_bank[n % 3][:],
                            [((w_hi[:, 0, k, f * P:(f + 1) * P], w_lo[:, 0, k, f * P:(f + 1) * P]),
                              (c.Xhi[:, k, h * NCOL:(h + 1) * NCOL], c.Xlo[:, k, h * NCOL:(h + 1) * NCOL]))
                             for k in range(KT)], NCOL, up_ready,
                            (lambda k: pe.wait_ge(w_lo_ready, g * 2 * KT + k + 1)) if o == 0 else None)
                for o in range(DOWN):
                    n = g * DOWN + o
                    t, half = divmod(o, HALVES)
                    tok = slice(t * P, (t + 1) * P)
                    if o == 0:
                        pe.wait_ge(w_lo_ready, (g + 1) * 2 * KT)
                        pe.wait_ge(h_lo_ready, (g + 1) * UP)
                    if n >= 5:
                        pe.wait_ge(added, n - 4)
                    product(nc, down_bank[n % 5][:],
                            [((h_hi[:, j, tok], h_lo[:, j, tok]),
                              (w_hi[:, 1, HALVES * j + half], w_lo[:, 1, HALVES * j + half]))
                             for j in range(FT)], NCOL, down_ready)


def ple(nc, chip, a):
    c = chip
    PK = 2
    proj, gate_w = a["w_ple_proj"][0], a["w_ple_gate"][0]
    groups = []
    for half in range(HALVES):
        cols = slice(half * NCOL, (half + 1) * NCOL)
        groups.append([proj[k * P:(k + 1) * P, cols] for k in range(PK)])
        groups.append([gate_w[k * P:(k + 1) * P, cols] for k in range(KT)])
    with ExitStack() as ctx:
        sb = lambda n, s, dt=F32: c.sb("ple_" + n, s, dt, ctx=ctx)
        sem = lambda n: c.sem("ple_" + n, ctx)
        gate_ready = sem("gate_ready")
        w = Weights(c, "ple", ctx, groups, (gate_ready, [TT, TT, 2 * TT, 2 * TT]))
        pt = sb("pt", [P, 4, PK * P])
        pT_hi, pT_lo = sb("pT_hi", [P, PK, S], F32R), sb("pT_lo", [P, PK, S], F32R)
        bias = sb("bias", [P, D])
        logit = sb("logit", [P, 2, NCOL])
        banks = c.banks("ple_ps", ctx)
        loaded, bias_loaded = [sem(f"loaded{i}") for i in range(2)], sem("bias_loaded")
        turned, hi_ready, lo_ready = sem("turned"), sem("hi_ready"), sem("lo_ready")
        proj_ready = sem("proj_ready")
        logit_ready, sig_ready, mul_ready, added = sem("logit_ready"), sem("sig_ready"), sem("mul_ready"), sem("added")
        block = ctx.enter_context(nc.Block())

        @block.sync
        def _(sp):
            for h in range(2):
                if h:
                    sp.wait_ge(turned, 2)
                sp.dma_start(pt[:], a["p"][0, 0, h * NCOL:(h + 1) * NCOL, :].rearrange("(t p) n -> p t n", p=P))\
                    .then_inc(loaded[h], 16)
                if h == 0:
                    sp.dma_start(bias[:], a["b_ple_gate"].to_broadcast([P, D])).then_inc(bias_loaded, 16)
            w.load(sp)

        @block.gpsimd
        def _(pool):
            w.split_lo(pool)

        @block.tensor
        def _(pe):
            for h in range(2):
                pe.wait_ge(loaded[h], 16)
                for k in range(PK):
                    for t in range(4):
                        last = nc.tensor.transpose(banks[2 * h + k][:, t * P:(t + 1) * P],
                                                   pt[:, t, k * P:(k + 1) * P], c.ident[:])
                    last.then_inc(turned, 1)
            pe.wait_ge(lo_ready, 4)
            for half in range(HALVES):
                for t in range(TT):
                    n = half * TT + t
                    tok = slice(t * P, (t + 1) * P)
                    if n >= 4:
                        pe.wait_ge(added, n - 3)
                    for g, x, kt, ready, bank in ((2 * half, (pT_hi, pT_lo), PK, proj_ready, 2 * (n % 4)),
                                                  (2 * half + 1, (c.Xhi, c.Xlo), KT, gate_ready, 2 * (n % 4) + 1)):
                        product(nc, banks[bank][:],
                                [((x[0][:, k, tok], x[1][:, k, tok]), (w.hi[:, g % 2, k], w.lo[:, g % 2, k]))
                                 for k in range(kt)], NCOL, ready,
                                (lambda k: pe.wait_ge(w.lo_ready, w.first[g] + k + 1)) if t == 0 else None)

        @block.scalar
        def _(act):
            for n in range(4):
                h, k = divmod(n, PK)
                act.wait_ge(turned, n + 1)
                nc.scalar.activation(pT_hi[:, k, h * NCOL:(h + 1) * NCOL], banks[n][:], ACT.Copy).then_inc(hi_ready, 1)
            w.split_hi_group(act, 0)
            w.split_hi_group(act, 1)
            for n in range(2 * TT):
                act.wait_ge(logit_ready, n + 1)
                nc.scalar.activation(logit[:, n % 2], logit[:, n % 2], ACT.Sigmoid).then_inc(sig_ready, 1)
                if n == TT - 1:
                    w.split_hi_group(act, 2)
                    w.split_hi_group(act, 3)

        @block.vector
        def _(dve):
            for n in range(4):
                h, k = divmod(n, PK)
                dve.wait_ge(hi_ready, n + 1)
                nc.vector.tensor_tensor(pT_lo[:, k, h * NCOL:(h + 1) * NCOL], banks[n][:],
                                        pT_hi[:, k, h * NCOL:(h + 1) * NCOL].bitcast(F32), ALU.subtract)\
                    .then_inc(lo_ready, 1)
            dve.wait_ge(bias_loaded, 16)
            for n in range(2 * TT):
                half, t = divmod(n, TT)
                cols = slice(half * NCOL, (half + 1) * NCOL)
                dve.wait_ge(gate_ready, n + 1)
                nc.vector.tensor_tensor(logit[:, n % 2], banks[2 * (n % 4) + 1][:], bias[:, cols], ALU.add)\
                    .then_inc(logit_ready, 1)
                dve.wait_ge(sig_ready, n + 1)
                dve.wait_ge(proj_ready, n + 1)
                nc.vector.tensor_tensor(logit[:, n % 2], banks[2 * (n % 4)][:], logit[:, n % 2], ALU.mult)\
                    .then_inc(mul_ready, 1)
                dve.wait_ge(mul_ready, n + 1)
                nc.vector.tensor_tensor(c.H[:, t, cols], c.H[:, t, cols], logit[:, n % 2], ALU.add).then_inc(added, 1)


def modulation(nc, chip, a, d):
    c = chip
    MW = 3 * D
    G = MW // NCOL
    with ExitStack() as ctx:
        sb = lambda n, s, dt=F32: c.sb("mod_" + n, s, dt, ctx=ctx)
        sem = lambda n: c.sem("mod_" + n, ctx)
        cond_in, cond = sb("cond_in", [P, KT, 2]), sb("cond", [P, KT, 2])
        w = sb("w", [P, 2, KT, NCOL])
        rowb = sb("rowb", [2, MW])
        row = sb("row", [2, MW])
        ones = sb("ones", [1, P])
        banks = c.banks("mod_ps", ctx)
        cloaded, loaded = sem("cloaded"), [sem(f"loaded{i}") for i in range(2)]
        cond_ready, ones_ready, row_ps, row_ready, turned, wide_ready = (
            sem("cond_ready"), sem("ones_ready"), sem("row_ps"), sem("row_ready"), sem("turned"), sem("wide_ready"))
        done, wide_copied, wide_stored = sem("done"), sem("wide_copied"), sem("wide_stored")
        wide = sb("wide", [P, D])
        block = ctx.enter_context(nc.Block())

        @block.sync
        def _(sp):
            sp.dma_start(cond_in[:, :, 0], a["c_2"][0].rearrange("(k p) -> p k", p=P)).then_inc(cloaded, 16)
            sp.dma_start(cond_in[:, :, 1], a["c_ctx_2"].rearrange("(k p) -> p k", p=P)).then_inc(cloaded, 16)
            sp.dma_start(rowb[:], a["ada_b_2"].to_broadcast([2, MW])).then_inc(cloaded, 16)
            for g in range(G):
                if g >= 2:
                    sp.wait_ge(row_ps, g - 1)
                sp.dma_start(w[:, g % 2], a["ada_w_2"][0, :, g * NCOL:(g + 1) * NCOL]
                             .rearrange("(k p) n -> p k n", p=P)).then_inc(loaded[g % 2], 16)
            sp.wait_ge(wide_copied, HALVES)
            sp.dma_start(d["gate"], wide[:]).then_inc(wide_stored, 16)
            sp.wait_ge(wide_stored, 16)

        @block.gpsimd
        def _(pool):
            nc.gpsimd.memset(ones[:], 1.0).then_inc(ones_ready, 1)

        @block.scalar
        def _(act):
            act.wait_ge(cloaded, 48)
            nc.scalar.activation(cond[:], cond_in[:], ACT.Silu).then_inc(cond_ready, 1)

        @block.tensor
        def _(pe):
            pe.wait_ge(cond_ready, 1)
            for g in range(G):
                pe.wait_ge(loaded[g % 2], 16 * (g // 2 + 1))
                for k in range(KT):
                    last = nc.tensor.matmul(banks[g][0:2, :], cond[:, k, :], w[:, g % 2, k], start=(k == 0),
                                            stop=(k == KT - 1))
                last.then_inc(row_ps, 1)
            pe.wait_ge(row_ready, G)
            pe.wait_ge(ones_ready, 1)
            for j in range(2 * KT):
                last = nc.tensor.transpose(banks[6][:, 2 * j:2 * j + 2], row[:, j * P:(j + 1) * P], c.ident[0:2, 0:2])
            last.then_inc(turned, 1)
            for half in range(HALVES):
                at = 2 * D + half * NCOL
                last = nc.tensor.matmul(banks[half][:], ones[:], row[0:1, at:at + NCOL], start=True, stop=True)
            last.then_inc(wide_ready, 1)

        @block.vector
        def _(dve):
            dve.wait_ge(cloaded, 48)
            for g in range(G):
                cols = slice(g * NCOL, (g + 1) * NCOL)
                dve.wait_ge(row_ps, g + 1)
                nc.vector.tensor_tensor(row[:, cols], banks[g][0:2, :], rowb[:, cols], ALU.add).then_inc(row_ready, 1)
            dve.wait_ge(turned, 1)
            for i in range(2):
                nc.vector.tensor_copy(c.mod_bias[:, i], banks[6][:, i:2 * KT:2]).then_inc(done, 1)
                nc.vector.scalar_tensor_tensor(out=c.mod_gain[:, i], in0=banks[6][:, 2 * KT + i:4 * KT:2], scalar=1.0,
                                               in1=c.gains[:, 3], op0=ALU.add, op1=ALU.mult).then_inc(done, 1)
            dve.wait_ge(wide_ready, 1)
            for half in range(HALVES):
                nc.vector.tensor_copy(wide[:, half * NCOL:(half + 1) * NCOL], banks[half][:]).then_inc(wide_copied, 1)


def differential_project(nc, chip, a, d, ctx_hi, ctx_lo):
    c = chip
    WIN = a["da_w_in_2"][0]
    Q_G, K_G, V_G, Z_G = (0, 1), (2, 3), (4, 5), (6, 7)
    G = 8
    groups = [[WIN[k * P:(k + 1) * P, g * NCOL:(g + 1) * NCOL] for k in range(KT)] for g in range(G)]
    tiles = {g: TT + CT if g in K_G + V_G else TT for g in range(G)}
    outs = [(g, o) for g in range(G) for o in range(tiles[g])]
    done_at = [sum(tiles[x] for x in range(g + 1)) for g in range(G)]
    rope = [n for n, (g, o) in enumerate(outs) if g in Q_G + K_G]
    R = len(rope)
    BANKS = 4
    with ExitStack() as ctx:
        sb = lambda n, s, dt=F32: c.sb("dp_" + n, s, dt, ctx=ctx)
        sem = lambda n: c.sem("dp_" + n, ctx)
        result_ready = sem("result_ready")
        w = Weights(c, "dp", ctx, groups, (result_ready, done_at))
        cos, sin = sb("cos", [P, TT, 32]), sb("sin", [P, TT, 32])
        tmp = sb("tmp", [P, 4, NCOL // 2])
        turned_in = sb("turned_in", [P, 2, 8, 2, DD])
        out_hi, out_lo = sb("out_hi", [P, 2 * NCOL], F32R), sb("out_lo", [P, 2 * NCOL], F32R)
        banks = c.banks("dp_ps", ctx, BANKS)
        turn = [ctx.enter_context(nc.psum_tensor(f"dp_turn{i}", [P, 2 * NCOL], F32)) for i in range(2)]
        loaded = sem("loaded")
        dve_step, doubled, roped, turned, hi_ready, lo_ready, stored = (
            sem("dve_step"), sem("doubled"), sem("roped"), sem("turned"), sem("hi_ready"), sem("lo_ready"), sem("stored"))
        block = ctx.enter_context(nc.Block())
        N = len(outs)
        stores_upto = [0]
        for g, o in outs:
            stores_upto.append(stores_upto[-1] + (1 if g in Q_G + Z_G else 2))

        @block.sync
        def _(sp):
            sp.dma_start(cos[:], a["da_cos"].rearrange("(t p) n -> p t n", p=P)).then_inc(loaded, 16)
            sp.dma_start(sin[:], a["da_sin"].rearrange("(t p) n -> p t n", p=P)).then_inc(loaded, 16)
            w.load(sp)

        @block.gpsimd
        def _(pool):
            lo_at = 0
            for n in range(N):
                g, o = outs[n]
                while lo_at < len(w.chunks) and lo_at < w.first[min(g + 1, G - 1)] + min(o + 1, KT):
                    w.split_lo_chunk(pool, lo_at)
                    lo_at += 1
                if n < R:
                    pool.wait_ge(roped, n + 1)
                    nc.gpsimd.tensor_copy(turned_in[:, n % 2, :, 1], turned_in[:, n % 2, :, 0]).then_inc(doubled, 1)

        @block.tensor
        def _(pe):
            def turns(n):
                i = n % 2
                pe.wait_ge(doubled, n + 1)
                if n >= 2:
                    pe.wait_ge(lo_ready, n - 1)
                for m in range(8):
                    x = turned_in[:, i, m].rearrange("p a b -> p (a b)")
                    last = nc.tensor.transpose(turn[i][:, m * P:(m + 1) * P], x, c.ident[:])
                last.then_inc(turned, 1)

            for n, (g, o) in enumerate(outs):
                if n >= BANKS:
                    m = n - BANKS
                    pe.wait_ge(*((roped, m + 1) if m < R else (lo_ready, m + 1)))
                terms = []
                xs, tile = ((c.Xhi, c.Xlo), o) if o < TT else ((ctx_hi, ctx_lo), o - TT)
                for k in range(KT):
                    ww = w.hi[:, g % 2, k], w.lo[:, g % 2, k]
                    if g in Z_G:
                        f, h = divmod(o, HALVES)
                        terms.append((tuple(y[:, f * P:(f + 1) * P] for y in ww),
                                      tuple(y[:, k, h * NCOL:(h + 1) * NCOL] for y in xs)))
                    else:
                        terms.append((tuple(y[:, k, tile * P:(tile + 1) * P] for y in xs), ww))
                product(nc, banks[n % BANKS][:], terms, NCOL, result_ready,
                        (lambda k: pe.wait_ge(w.lo_ready, w.first[g] + k + 1)) if o == 0 else None)
                if 1 <= n <= R:
                    turns(n - 1)

        def places(n):
            g, o = outs[n]
            hs = slice(4 * (g % 2), 4 * (g % 2) + 4)
            if g in Q_G:
                return [(d["dq"][hs, :, :, o * P:(o + 1) * P].rearrange("h z p s -> p h z s"), 0)]
            if g in K_G:
                return [(d[x][hs, :, :, o * P:(o + 1) * P].rearrange("h z p s -> p h z s"), i)
                        for i, x in enumerate(("dk_hi", "dk_lo"))]
            if g in V_G:
                return [(d[x][hs, :, o, :].rearrange("h p n -> p h n"), i) for i, x in enumerate(("dv_hi", "dv_lo"))]
            f, h = divmod(o, HALVES)
            return [(d["dz"][4 * (g % 2) + f, :, h * NCOL:(h + 1) * NCOL], 0)]

        @block.scalar
        def _(act):
            def store(n):
                g, o = outs[n]
                act.wait_ge(lo_ready, n + 1)
                for place, which in places(n):
                    t = (out_hi, out_lo)[which]
                    if g in Q_G + K_G:
                        src = t[:].bitcast(F32).rearrange("p (h z s) -> p h z s", h=4, z=2)
                        for z in range(2):
                            act.dma_start(place[:, :, z], src[:, :, z]).then_inc(stored, 16)
                    elif g in V_G:
                        act.dma_start(place, t[:, 0:NCOL].bitcast(F32).rearrange("p (h n) -> p h n", h=4)).then_inc(stored, 16)
                    else:
                        act.dma_start(place, t[:, 0:NCOL].bitcast(F32)).then_inc(stored, 16)

            def n_stores(n):
                g, _ = outs[n]
                return {True: 2, False: 1}[g in Q_G + K_G] * len(places(n))

            total = [0]
            w.split_hi_group(act, 0)
            for n, (g, o) in enumerate(outs):
                if g + 1 < G and o < KT:
                    w.split_hi(act, w.first[g + 1] + o)
                if n:
                    store(n - 1)
                    total[0] += n_stores(n - 1)
                    act.wait_ge(stored, 16 * total[0])
                if g in Q_G + K_G:
                    act.wait_ge(turned, n + 1)
                    nc.scalar.activation(out_hi[:], turn[n % 2][:], ACT.Copy).then_inc(hi_ready, 1)
                else:
                    act.wait_ge(result_ready, n + 1)
                    nc.scalar.activation(out_hi[:, 0:NCOL] if g in V_G else out_hi[:, 0:NCOL].bitcast(F32),
                                         banks[n % BANKS][:], ACT.Copy if g in V_G else ACT.Silu).then_inc(hi_ready, 1)
            store(N - 1)
            total[0] += n_stores(N - 1)
            act.wait_ge(stored, 16 * total[0])

        @block.vector
        def _(dve):
            dve.wait_ge(loaded, 32)
            steps = [0]

            def step(ins):
                steps[0] += 1
                ins.then_inc(dve_step, 1)
                dve.wait_ge(dve_step, steps[0])

            def low(n):
                g, o = outs[n]
                dve.wait_ge(hi_ready, n + 1)
                if g in Q_G:
                    nc.vector.tensor_tensor(out_hi[64:P, :], turn[n % 2][64:P, :], out_hi[64:P, :].bitcast(F32),
                                            ALU.subtract).then_inc(lo_ready, 1)
                elif g in K_G:
                    nc.vector.tensor_tensor(out_lo[:], turn[n % 2][:], out_hi[:].bitcast(F32), ALU.subtract)\
                        .then_inc(lo_ready, 1)
                elif g in V_G:
                    nc.vector.tensor_tensor(out_lo[:, 0:NCOL], banks[n % BANKS][:], out_hi[:, 0:NCOL].bitcast(F32),
                                            ALU.subtract).then_inc(lo_ready, 1)
                else:
                    nc.vector.memset(tmp[0:1, 0, 0:1], 0.0).then_inc(lo_ready, 1)

            for n, (g, o) in enumerate(outs):
                if n < R:
                    dve.wait_ge(result_ready, n + 1)
                    dst = turned_in[:, n % 2, :, 0]
                    if n >= 2:
                        dve.wait_ge(turned, n - 1)
                    if o < TT:
                        x = banks[n % BANKS][:].rearrange("p (m a b q) -> p m a b q", a=2, b=2, q=16)
                        y = dst.rearrange("p m (a b q) -> p m a b q", a=2, b=2, q=16)
                        cs, sn = (t[:, o].rearrange("p (a q) -> p a q", a=2).unsqueeze(1).to_broadcast([P, 8, 2, 16])
                                  for t in (cos, sin))
                        if n:
                            dve.wait_ge(roped, n)
                        for i, (f0, f1, op) in enumerate(((cs, sn, ALU.subtract), (sn, cs, ALU.add))):
                            u, v = (tmp[:, 2 * i + j].rearrange("p (m a q) -> p m a q", a=2, q=16) for j in range(2))
                            nc.vector.tensor_tensor(u, x[:, :, :, 0], f0, ALU.mult).then_inc(dve_step, 1)
                            steps[0] += 1
                            step(nc.vector.tensor_tensor(v, x[:, :, :, 1], f1, ALU.mult))
                            last = nc.vector.tensor_tensor(y[:, :, :, i], u, v, op)
                            last.then_inc(*((roped, 1) if i else (dve_step, 1)))
                            steps[0] += 1 - i
                    else:
                        nc.vector.tensor_copy(dst, banks[n % BANKS][:].rearrange("p (m n) -> p m n", m=8)).then_inc(roped, 1)
                    if n:
                        low(n - 1)
                    if n == R - 1:
                        low(n)
                else:
                    low(n)


def differential_attention(nc, chip, a, d):
    c = chip
    K = S + CTX
    KB = K // P
    QT = S // P
    N = DH * QT
    SCALE = DD ** -0.5
    CHUNKS = -(-KB // 4)
    ITEMS = 4 * CHUNKS + 1
    PIECES = [(at, min(at + NCOL, K)) for at in range(0, K, NCOL)]
    with ExitStack() as ctx:
        sb = lambda n, s, dt=F32: c.sb("da_" + n, s, dt, ctx=ctx)
        sem = lambda n: c.sem("da_" + n, ctx)
        q = sb("q", [P, 2, 2, S], F32R)
        k_hi, k_lo = sb("k_hi", [P, 2, 2, K], F32R), sb("k_lo", [P, 2, 2, K], F32R)
        v_hi, v_lo = sb("v_hi", [P, 2, KB, P], F32R), sb("v_lo", [P, 2, KB, P], F32R)
        prob = sb("prob", [P, 2, 2, K])
        aT_hi, aT_lo = sb("aT_hi", [P, KB, NCOL], F32R), sb("aT_lo", [P, KB, NCOL], F32R)
        mx, nb, sums, inv = (sb(x, [P, 2, 2]) for x in ("mx", "nb", "sums", "inv"))
        lam_in, lam_prod = sb("lam_in", [P, 2, 2, DD]), sb("lam_prod", [P, 2, DD])
        lam_sum, lam_exp, lam = sb("lam_sum", [P, 2]), sb("lam_exp", [P, 2]), sb("lam", [P, 1])
        o_sb = sb("o_sb", [P, 2, NCOL])
        ratio, diag = sb("ratio", [P, 2, 1]), sb("diag", [P, 2, P])
        scores = [ctx.enter_context(nc.psum_tensor(f"da_scores{i}", [P, 3 * NCOL], F32)) for i in range(2)]
        turn_bank = c.banks("da_turn", ctx, 2)
        loaded = [sem(f"loaded{i}") for i in range(2)]
        lam_loaded, lam_step, lam_summed, lam_exped = (
            sem("lam_loaded"), sem("lam_step"), sem("lam_summed"), sem("lam_exped"))
        scored, max_ready, nb_ready, exp_ready = sem("scored"), sem("max_ready"), sem("nb_ready"), sem("exp_ready")
        inv_ready, ratio_ready, diag_ready, prob_ready = (
            sem("inv_ready"), sem("ratio_ready"), sem("diag_ready"), sem("prob_ready"))
        turned, hi_ready, lo_ready = sem("turned"), sem("hi_ready"), sem("lo_ready")
        o_ready, o_copied = sem("o_ready"), sem("o_copied")
        o_stored = [sem(f"o_stored{i}") for i in range(2)]
        block = ctx.enter_context(nc.Block())

        @block.sync
        def _(sp):
            sp.dma_start(lam_in[:, 0], a["da_lam_q_2"].to_broadcast([P, 2, DD])).then_inc(lam_loaded, 16)
            sp.dma_start(lam_in[:, 1], a["da_lam_k_2"].to_broadcast([P, 2, DD])).then_inc(lam_loaded, 16)
            for h in range(DH):
                s = h % 2
                if h >= 2:
                    sp.wait_ge(o_ready, 2 * (h - 1))
                for place, src in ((q[:, s], d["dq"][h].rearrange("z p s -> p z s")),
                                   (k_hi[:, s], d["dk_hi"][h].rearrange("z p s -> p z s")),
                                   (k_lo[:, s], d["dk_lo"][h].rearrange("z p s -> p z s")),
                                   (v_hi[:, s], d["dv_hi"][h]), (v_lo[:, s], d["dv_lo"][h])):
                    sp.dma_start(place.bitcast(F32), src).then_inc(loaded[s], 16)

        def emptied(engine, r):
            group, k = divmod(r, ITEMS)
            if k == ITEMS - 1:
                engine.wait_ge(o_copied, group + 1)
            else:
                engine.wait_ge(lo_ready, 4 * CHUNKS * group + k + 1)

        def chunk_item(n, i):
            return CHUNKS * n + i + n // 4

        @block.tensor
        def _(pe):
            def score(n, z):
                h, qt = divmod(n, QT)
                s = h % 2
                if qt == 0 and z == 0:
                    pe.wait_ge(loaded[s], 80 * (h // 2 + 1))
                if n:
                    pe.wait_ge(exp_ready, 2 * (n - 1) + z + 1)
                for at, end in PIECES:
                    for i, k in enumerate((k_hi, k_lo)):
                        last = nc.tensor.matmul(scores[z][:, at:end], q[:, s, z, qt * P:(qt + 1) * P],
                                                k[:, s, z, at:end], start=(i == 0), stop=(i == 1))
                last.then_inc(scored, 1)

            def turn(n, i):
                if i == 0:
                    pe.wait_ge(prob_ready, n + 1)
                r = chunk_item(n, i)
                if r >= 2:
                    emptied(pe, r - 2)
                for j in range(4 * i, min(4 * i + 4, KB)):
                    last = nc.tensor.matmul(turn_bank[r % 2][:, (j % 4) * P:(j % 4 + 1) * P],
                                            prob[:, n % 2, 0, j * P:(j + 1) * P], diag[:, n % 2],
                                            start=True, stop=True)
                last.then_inc(turned, 1)

            def values(m):
                s = m // 2 % 2
                r = ITEMS * m + ITEMS - 1
                emptied(pe, r - 2)
                product(nc, turn_bank[r % 2][:], [((v_hi[:, s, j], v_lo[:, s, j]), (aT_hi[:, j], aT_lo[:, j]))
                                                  for j in range(KB)], NCOL, o_ready,
                        lambda j: pe.wait_ge(lo_ready, CHUNKS * (4 * m + 3) + j // 4 + 1))

            for n in range(2):
                score(n, 0)
                score(n, 1)
            for n in range(N):
                turn(n, 0)
                if n + 2 < N:
                    score(n + 2, 0)
                turn(n, 1)
                if n + 2 < N:
                    score(n + 2, 1)
                turn(n, 2)
                if n % 4 == 3:
                    values(n // 4)

        @block.scalar
        def _(act):
            act.wait_ge(lam_summed, 1)
            nc.scalar.activation(lam_exp[:], lam_sum[:], ACT.Exp).then_inc(lam_exped, 1)

            def exp(n, z):
                act.wait_ge(nb_ready, 2 * n + z + 1)
                if n >= 2:
                    act.wait_ge(turned, CHUNKS * (n - 1))
                nc.scalar.activation(prob[:, n % 2, z], scores[z][:, 0:K], ACT.Exp, scale=SCALE,
                                     bias=nb[:, n % 2, z:z + 1], accum_out=sums[:, n % 2, z:z + 1])\
                    .then_inc(exp_ready, 1)

            def high(n, i):
                qs = slice((n % 4) * P, (n % 4 + 1) * P)
                j, e = 4 * i, min(4 * i + 4, KB)
                act.wait_ge(turned, CHUNKS * n + i + 1)
                nc.scalar.activation(aT_hi[:, j:e, qs],
                                     turn_bank[chunk_item(n, i) % 2][:, 0:(e - j) * P]
                                     .rearrange("p (j q) -> p j q", q=P), ACT.Copy).then_inc(hi_ready, 1)

            def out(m):
                act.wait_ge(o_ready, m + 1)
                if m >= 2:
                    act.wait_ge(o_stored[m % 2], 16 * (m // 2))
                nc.scalar.activation(o_sb[:, m % 2], turn_bank[(ITEMS * m + ITEMS - 1) % 2][:], ACT.Copy)\
                    .then_inc(o_copied, 1)

            exp(0, 0)
            exp(0, 1)
            for n in range(N):
                if n + 1 < N:
                    exp(n + 1, 0)
                if n % 4 == 0 and n:
                    out(n // 4 - 1)
                high(n, 0)
                if n + 1 < N:
                    exp(n + 1, 1)
                high(n, 1)
                high(n, 2)
            out(N // 4 - 1)

        @block.gpsimd
        def _(pool):
            for m in range(N // 4):
                h, half = divmod(m, 2)
                pool.wait_ge(o_copied, m + 1)
                pool.dma_start(d["do"][h, :, half * NCOL:(half + 1) * NCOL], o_sb[:, m % 2])\
                    .then_inc(o_stored[m % 2], 16)
            for i in range(2):
                pool.wait_ge(o_stored[i], 16 * (N // 8))

        @block.vector
        def _(dve):
            dve.wait_ge(lam_loaded, 32)
            nc.vector.tensor_tensor(lam_prod[:], lam_in[:, 0], lam_in[:, 1], ALU.mult).then_inc(lam_step, 1)
            dve.wait_ge(lam_step, 1)
            nc.vector.tensor_reduce(out=lam_sum[:], in_=lam_prod[:], op=ALU.add, axis=AX.X).then_inc(lam_summed, 1)
            dve.wait_ge(lam_exped, 1)
            nc.vector.tensor_tensor(lam[:], lam_exp[:, 1:2], lam_exp[:, 0:1], ALU.subtract).then_inc(lam_step, 1)
            dve.wait_ge(lam_step, 2)
            nc.vector.tensor_scalar(lam[:], lam[:], -LAMBDA_INIT, None, ALU.add).then_inc(lam_step, 1)
            dve.wait_ge(lam_step, 3)

            def row_max(n, z):
                dve.wait_ge(scored, 2 * n + z + 1)
                nc.vector.tensor_reduce(out=mx[:, n % 2, z:z + 1], in_=scores[z][:, 0:K], op=ALU.max, axis=AX.X)\
                    .then_inc(max_ready, 1)
                dve.wait_ge(max_ready, 2 * n + z + 1)
                nc.vector.tensor_scalar(nb[:, n % 2, z:z + 1], mx[:, n % 2, z:z + 1], -SCALE, None, ALU.mult)\
                    .then_inc(nb_ready, 1)

            def combine(n):
                i = n % 2
                dve.wait_ge(exp_ready, 2 * n + 2)
                nc.vector.reciprocal(inv[:, i], sums[:, i]).then_inc(inv_ready, 1)
                dve.wait_ge(inv_ready, n + 1)
                nc.vector.scalar_tensor_tensor(out=ratio[:, i], in0=sums[:, i, 0:1], scalar=lam[:],
                                               in1=inv[:, i, 1:2], op0=ALU.mult, op1=ALU.mult)\
                    .then_inc(ratio_ready, 1)
                nc.vector.tensor_scalar(diag[:, i], c.ident[:], inv[:, i, 0:1], None, ALU.mult)\
                    .then_inc(diag_ready, 1)
                dve.wait_ge(ratio_ready, n + 1)
                nc.vector.scalar_tensor_tensor(out=prob[:, i, 0], in0=prob[:, i, 1], scalar=ratio[:, i],
                                               in1=prob[:, i, 0], op0=ALU.mult, op1=ALU.add).then_inc(prob_ready, 1)

            def low(n, i):
                qs = slice((n % 4) * P, (n % 4 + 1) * P)
                j, e = 4 * i, min(4 * i + 4, KB)
                dve.wait_ge(hi_ready, CHUNKS * n + i + 1)
                nc.vector.tensor_tensor(aT_lo[:, j:e, qs],
                                        turn_bank[chunk_item(n, i) % 2][:, 0:(e - j) * P]
                                        .rearrange("p (j q) -> p j q", q=P),
                                        aT_hi[:, j:e, qs].bitcast(F32), ALU.subtract).then_inc(lo_ready, 1)

            row_max(0, 0)
            row_max(0, 1)
            combine(0)
            row_max(1, 0)
            row_max(1, 1)
            for n in range(N):
                low(n, 0)
                if n + 2 < N:
                    row_max(n + 2, 0)
                if n + 1 < N:
                    combine(n + 1)
                low(n, 1)
                if n + 2 < N:
                    row_max(n + 2, 1)
                low(n, 2)


def head_norm(nc, chip, a, d):
    c = chip
    SUB_EPS = 1e-5
    N = DH * HALVES
    with ExitStack() as ctx:
        sb = lambda n, s, dt=F32: c.sb("hn_" + n, s, dt, ctx=ctx)
        sem = lambda n: c.sem("hn_" + n, ctx)
        o, z = sb("o", [P, 3, NCOL]), sb("z", [P, 3, NCOL])
        sq, rs, y = sb("sq", [P, 2, NCOL]), sb("rs", [P, 2, NCOL]), sb("y", [P, 2, NCOL])
        gain, ones, eps = sb("gain", [P, 1]), sb("ones", [P, P]), sb("eps", [P, 1])
        banks = c.banks("hn_ps", ctx)
        gl, const = sem("gl"), sem("const")
        loaded = [sem(f"loaded{i}") for i in range(3)]
        squared, summed, logged, rstd_ready, scaled, y_ready, hi_ready, lo_ready, gain_ready = (
            sem(x) for x in ("squared", "summed", "logged", "rstd_ready", "scaled", "y_ready", "hi_ready",
                             "lo_ready", "gain_ready"))
        block = ctx.enter_context(nc.Block())

        @block.sync
        def _(sp):
            sp.dma_start(gain[:], a["da_subln_gain_2"][0].rearrange("(p a) -> p a", a=1)).then_inc(gl, 16)
            for n in range(N):
                half, h = divmod(n, DH)
                cols = slice(half * NCOL, (half + 1) * NCOL)
                if n >= 3:
                    sp.wait_ge(y_ready, n - 2)
                sp.dma_start(o[:, n % 3], d["do"][h, :, cols]).then_inc(loaded[n % 3], 16)
                sp.dma_start(z[:, n % 3], d["dz"][h, :, cols]).then_inc(loaded[n % 3], 16)

        @block.gpsimd
        def _(pool):
            nc.gpsimd.memset(ones[:], 1.0).then_inc(const, 1)
            nc.gpsimd.memset(eps[:], SUB_EPS).then_inc(const, 1)

        @block.tensor
        def _(pe):
            pe.wait_ge(const, 2)
            for n in range(N):
                pe.wait_ge(squared, n + 1)
                if n >= 8:
                    pe.wait_ge(logged, n - 7)
                nc.tensor.matmul(banks[n % 8][:], ones[:], sq[:, n % 2], start=True, stop=True).then_inc(summed, 1)

        @block.scalar
        def _(act):
            act.wait_ge(const, 2)

            def square(n):
                act.wait_ge(loaded[n % 3], 32 * (n // 3 + 1))
                if n >= 2:
                    act.wait_ge(summed, n - 1)
                nc.scalar.activation(sq[:, n % 2], o[:, n % 3], ACT.Square).then_inc(squared, 1)

            square(0)
            for n in range(N):
                if n + 1 < N:
                    square(n + 1)
                act.wait_ge(summed, n + 1)
                if n >= 2:
                    act.wait_ge(scaled, n - 1)
                nc.scalar.activation(rs[:, n % 2], banks[n % 8][:], ACT.Ln, scale=1.0 / P, bias=eps[:])\
                    .then_inc(logged, 1)
                act.wait_ge(logged, n + 1)
                nc.scalar.activation(rs[:, n % 2], rs[:, n % 2], ACT.Exp, scale=-0.5).then_inc(rstd_ready, 1)
                half, h = divmod(n, DH)
                act.wait_ge(y_ready, n + 1)
                nc.scalar.activation(c.Xhi[:, h, half * NCOL:(half + 1) * NCOL], y[:, n % 2], ACT.Copy)\
                    .then_inc(hi_ready, 1)

        @block.vector
        def _(dve):
            dve.wait_ge(gl, 16)
            nc.vector.tensor_scalar(gain[:], gain[:], 1.0 - LAMBDA_INIT, None, ALU.mult).then_inc(gain_ready, 1)
            dve.wait_ge(gain_ready, 1)
            for n in range(N):
                half, h = divmod(n, DH)
                cols = slice(half * NCOL, (half + 1) * NCOL)
                dve.wait_ge(rstd_ready, n + 1)
                nc.vector.scalar_tensor_tensor(out=y[:, n % 2], in0=o[:, n % 3], scalar=gain[:], in1=rs[:, n % 2],
                                               op0=ALU.mult, op1=ALU.mult).then_inc(scaled, 1)
                dve.wait_ge(scaled, n + 1)
                nc.vector.tensor_tensor(y[:, n % 2], y[:, n % 2], z[:, n % 3], ALU.mult).then_inc(y_ready, 1)
                dve.wait_ge(hi_ready, n + 1)
                nc.vector.tensor_tensor(c.Xlo[:, h, cols], y[:, n % 2], c.Xhi[:, h, cols].bitcast(F32),
                                        ALU.subtract).then_inc(lo_ready, 1)


def final_norm(nc, chip, a, out):
    c = chip
    with ExitStack() as ctx:
        sb = lambda n, s, dt=F32: c.sb("fn_" + n, s, dt, ctx=ctx)
        sem = lambda n: c.sem("fn_" + n, ctx)
        gain, junk, ss, ms, rs = (sb("gain", [P, D]), sb("junk", [P, D]), sb("ss", [P, TT]), sb("ms", [P, TT]),
                                  sb("rs", [P, TT]))
        loaded, ss_ready, ms_ready, rs_ready, y_ready = (
            sem(x) for x in ("loaded", "ss_ready", "ms_ready", "rs_ready", "y_ready"))
        block = ctx.enter_context(nc.Block())

        @block.scalar
        def _(act):
            for t in range(TT):
                if t:
                    act.wait_ge(ss_ready, t)
                nc.scalar.activation(junk[:], c.H[:, t, :], ACT.Square, accum_out=ss[:, t:t + 1]).then_inc(ss_ready, 1)

        @block.gpsimd
        def _(pool):
            for h in range(2):
                cols = slice(4 * h, 4 * h + 4)
                pool.wait_ge(ss_ready, 4 * h + 4)
                nc.gpsimd.tensor_scalar(ms[:, cols], ss[:, cols], 1.0 / D, EPS, ALU.mult, ALU.add).then_inc(ms_ready, 1)
                pool.wait_ge(ms_ready, h + 1)
                nc.gpsimd.tensor_tensor(rs[:, cols], ms[:, cols], c.minus_half[:, 0:4], ALU.pow).then_inc(rs_ready, 1)

        @block.vector
        def _(dve):
            dve.wait_ge(loaded, 16)
            for t in range(TT):
                dve.wait_ge(rs_ready, t // 4 + 1)
                nc.vector.scalar_tensor_tensor(out=c.H[:, t, :], in0=c.H[:, t, :], scalar=rs[:, t:t + 1], in1=gain[:],
                                               op0=ALU.mult, op1=ALU.mult).then_inc(y_ready, 1)

        @block.sync
        def _(sp):
            sp.dma_start(gain[:], a["final_gain_2"].rearrange("(a n) -> a n", a=1).to_broadcast([P, D]))\
                .then_inc(loaded, 16)
            for t in range(TT):
                sp.wait_ge(y_ready, t + 1)
                sp.dma_start(out[0, t * P:(t + 1) * P, :], c.H[:, t, :]).then_inc(c.out_stored, 16)
            sp.wait_ge(c.out_stored, 16 * TT)


def program(nc, a, out):
    with ExitStack() as ctx:
        ctx.enter_context(nc.allow_non_contiguous_dma(reason="gains and transposed results"))
        c = Chip(nc, ctx)

        def scratch(name, shape):
            return nc.dram_tensor(name, shape, F32, kind="Internal").ap()

        d = {
            "zc": scratch("zc", [TT, P, 432]), "gqk": scratch("gqk", [4, P, S]),
            "gv": scratch("gv", [TT, P, NCOL]), "gr": scratch("gr", [TT, P, NCOL]),
            "mqk_hi": scratch("mqk_hi", [2, MH, MQK, S]), "mqk_lo": scratch("mqk_lo", [2, MH, MQK, S]),
            "mv_hi": scratch("mv_hi", [MH, TT, P, MV]), "mv_lo": scratch("mv_lo", [MH, TT, P, MV]),
            "dq": scratch("dq", [DH, 2, P, S]),
            "dk_hi": scratch("dk_hi", [DH, 2, P, S + CTX]), "dk_lo": scratch("dk_lo", [DH, 2, P, S + CTX]),
            "dv_hi": scratch("dv_hi", [DH, P, TT + CT, P]), "dv_lo": scratch("dv_lo", [DH, P, TT + CT, P]),
            "dz": scratch("dz", [DH, P, S]), "do": scratch("do", [DH, P, S]),
            "gate": scratch("gate", [P, D]),
        }
        constants(nc, c, a)
        with ExitStack() as x_ctx:
            c.hold_x("x", x_ctx)
            norm_transpose(nc, c, "n1", c.gains[:, 0], load=a["x"][0])

            w_in = a["w_in"][0]
            rows = [slice(k * P, (k + 1) * P) for k in range(KT)]
            g_low = GH * GDK * 2 + GH * GDV
            g_r = g_low + GR
            c_q = g_r + GH * GDV
            one = lambda o: 1.0
            tok_place = lambda name, width: (lambda o: [(d[name][o], slice(0, width))])
            groups = [
                ([[w_in[r, g_low:g_r], w_in[r, c_q:c_q + MQR + MKVR + MROPE]] for r in rows], False,
                 tok_place("zc", 432), ACT.Copy, one),
                ([w_in[r, 0:NCOL] for r in rows], True,
                 lambda o: [(d["gqk"][o // HALVES, :, (o % HALVES) * NCOL:(o % HALVES + 1) * NCOL], slice(0, NCOL))],
                 ACT.Copy, lambda o: GDK ** -0.5 if o < TT // 2 else 1.0),
                ([w_in[r, NCOL:2 * NCOL] for r in rows], False, tok_place("gv", NCOL), ACT.Copy, one),
                ([w_in[r, g_r:c_q] for r in rows], False, tok_place("gr", NCOL), ACT.Silu, one),
            ]
            project_to_dram(nc, c, "p1", groups)
            latent_prepare(nc, c, a, d)
            gated_linear_attention(nc, c, a, d)
            c.renew_semaphores()
            latent_attention(nc, c, a, d)
            project_into_residual(nc, c, "wo", a["w_out"][0])
            norm_transpose(nc, c, "n2", c.gains[:, 1])
            c.renew_semaphores()
            mlp(nc, c, a)
            norm_transpose(nc, c, "n3", c.gains[:, 2])
            ple(nc, c, a)
            c.renew_semaphores()
            modulation(nc, c, a, d)
            with ExitStack() as inner:
                ctx_hi, ctx_lo = (c.sb(f"ctx_{x}", [P, KT, CTX], F32R, ctx=inner) for x in ("hi", "lo"))
                with ExitStack() as load_ctx:
                    raw = c.sb("ctx_raw", [P, CT, D], ctx=load_ctx)
                    norm_transpose(nc, c, "nc", c.mod_gain[:, 1], c.mod_bias[:, 1], load=a["ctx_2"][0], src=raw,
                                   dst=(ctx_hi, ctx_lo), tiles=CT)
                norm_transpose(nc, c, "n4", c.mod_gain[:, 0], c.mod_bias[:, 0])
                differential_project(nc, c, a, d, ctx_hi, ctx_lo)
        c.renew_semaphores()
        differential_attention(nc, c, a, d)
        with ExitStack() as x_ctx:
            c.hold_x("x2", x_ctx)
            head_norm(nc, c, a, d)
            project_into_residual(nc, c, "do", a["da_w_out_2"][0], gate=d["gate"])
            final_norm(nc, c, a, out)


_INS = ["x", "p", "positions", "attn_norm", "w_in", "gla_gate_w2", "gla_gate_b", "gla_out_norm", "mla_q_norm",
        "mla_w_uq", "mla_kv_norm", "mla_w_ukv", "qk_norm_q", "qk_norm_k", "w_out", "mlp_norm", "w_mlp_up",
        "w_mlp_down", "ple_norm", "w_ple_gate", "b_ple_gate", "w_ple_proj", "c_2", "ctx_2", "c_ctx_2",
        "norm_gain_2", "ada_w_2", "ada_b_2", "final_gain_2", "da_w_in_2", "da_lam_q_2", "da_lam_k_2",
        "da_subln_gain_2", "da_w_out_2"]


def shape_constants():
    import numpy as np
    f = np.float32
    inv = (f(10000.0) ** (-np.arange(0, MROPE, 2, dtype=f) / f(MROPE))).astype(f)
    n = np.arange(S)
    axis = (f(10000.0) ** (-np.arange(0, 32, 2, dtype=f) / f(32))).astype(f)
    ang = np.concatenate([(n // 64).astype(f)[:, None] * axis, (n % 64).astype(f)[:, None] * axis], axis=1)
    s, t = np.arange(P)[:, None], np.arange(P)[None, :]
    masks = [(s // (2 * h) == t // (2 * h)) & (s % (2 * h) < h) & (t % (2 * h) >= h) for h in (64, 32, 16)]
    masks.append((s // 16 == t // 16) & (s <= t))
    return {"inv_freq": inv[None], "da_cos": np.cos(ang).astype(f), "da_sin": np.sin(ang).astype(f),
            "gla_masks": np.stack(masks, axis=1).astype(f)}


def kernel(**inputs):
    import numpy as np
    import concourse.bacc as bacc
    from concourse.bass_utils import run_bass_kernel_spmd

    nc = bacc.Bacc("TRN2", target_bir_lowering=False, num_devices=1)
    arrays, args = {}, {}
    for name, array in [(n, inputs[n]) for n in _INS] + list(shape_constants().items()):
        array = np.ascontiguousarray(array)
        arrays[f"in_{name}"] = array
        args[name] = nc.dram_tensor(f"in_{name}", array.shape, mybir.dt.from_np(array.dtype),
                                    kind="ExternalInput").ap()
    out = nc.dram_tensor("out", (1, S, D), F32, kind="ExternalOutput").ap()
    program(nc, args, out)
    result = run_bass_kernel_spmd(nc, [arrays], core_ids=[0])
    return result.results[0]["out"]
```

```python
from contextlib import ExitStack

import concourse.bass as bass
from concourse import mybir

F32 = mybir.dt.float32
F32R = mybir.dt.float32r
I32 = mybir.dt.int32
ALU = mybir.AluOpType
ACT = mybir.ActivationFunctionType
AX = mybir.AxisListType

P = 128
S = 1024
D = 1024
TT = S // P
KT = D // P
NCOL = 512
HALVES = S // NCOL
CTX = 256
CT = CTX // P
EPS = 1e-6

GH, GDK, GDV, GR = 4, 64, 128, 16
MH, MNOPE, MROPE, MV, MQK = 8, 64, 32, 64, 96
MQR, MKVR = 256, 128
DH, DD = 8, 64
D_FF = 4096
LAMBDA_INIT = 0.2

SLOTS = 4
RING = 4


class Chip:

    def __init__(self, nc, ctx):
        self.nc, self.ctx = nc, ctx
        self.used = []
        self.out_stored = nc.alloc_semaphore("out_stored")

    def sb(self, name, shape, dt=F32, ctx=None):
        return (ctx or self.ctx).enter_context(self.nc.sbuf_tensor(name, shape, dt))

    def hold_x(self, name, ctx):
        self.Xhi = self.sb(f"{name}_hi", [P, KT, S], F32R, ctx)
        self.Xlo = self.sb(f"{name}_lo", [P, KT, S], F32R, ctx)

    def banks(self, name, ctx, n=8):
        return [ctx.enter_context(self.nc.psum_tensor(f"{name}{i}", [P, NCOL], F32)) for i in range(n)]

    def sem(self, name, ctx):
        s = self.nc.alloc_semaphore(name)
        self.used.append(s)
        return s

    def renew_semaphores(self):
        nc, used = self.nc, self.used
        with nc.Block() as block:
            @block.gpsimd
            def _(pool):
                numbers = sorted(s.num for s in used)
                at = 0
                for i in range(1, len(numbers) + 1):
                    if i == len(numbers) or numbers[i] != numbers[i - 1] + 1:
                        nc.gpsimd.sem_clear(range(numbers[at], numbers[i - 1] + 1))
                        at = i
        for s in used:
            nc.release_semaphore(s)
        self.used = []


def constants(nc, chip, a):
    c = chip
    c.H = c.sb("residual", [P, TT, D])
    c.mod_bias = c.sb("mod_bias", [P, 2, KT])
    c.mod_gain = c.sb("mod_gain", [P, 2, KT])
    c.ident = c.sb("ident", [P, P])
    c.gains = c.sb("gains", [P, 4, KT])
    c.minus_half = c.sb("minus_half", [P, 64])
    with ExitStack() as ctx:
        ones_ready = c.sem("ones_ready", ctx)
        const_loaded = c.sem("const_loaded", ctx)
        block = ctx.enter_context(nc.Block())

        @block.gpsimd
        def _(pool):
            nc.gpsimd.memset(c.ident[:], 0.0).then_inc(ones_ready, 1)
            nc.gpsimd.memset(c.minus_half[:], -0.5).then_inc(ones_ready, 1)
            pool.wait_ge(ones_ready, 2)
            nc.gpsimd.affine_select(out=c.ident[:], in_=c.ident[:], compare_op=ALU.not_equal, fill=1.0,
                                    base=0, pattern=[[-1, P]], channel_multiplier=1).then_inc(ones_ready, 1)

        @block.sync
        def _(sp):
            for n, g in enumerate((a["attn_norm"][0], a["mlp_norm"][0], a["ple_norm"][0], a["norm_gain_2"][0])):
                sp.dma_start(c.gains[:, n, :], g.rearrange("(k p) -> p k", p=P)).then_inc(const_loaded, 16)
            sp.wait_ge(const_loaded, 64)


def norm_transpose(nc, chip, name, gain, bias=None, load=None, src=None, dst=None, tiles=TT):
    c = chip
    src = c.H if src is None else src
    Xhi, Xlo = dst or (c.Xhi, c.Xlo)
    per = min(4, tiles)
    n_half = tiles // per
    width = per * P
    with ExitStack() as ctx:
        scaled = c.sb(f"{name}_scaled", [P, per, D], ctx=ctx)
        junk = c.sb(f"{name}_squares", [P, D], ctx=ctx)
        ss = c.sb(f"{name}_ss", [P, TT], ctx=ctx)
        mean = c.sb(f"{name}_mean", [P, TT], ctx=ctx)
        rstd = c.sb(f"{name}_rstd", [P, TT], ctx=ctx)
        full = c.sb(f"{name}_full", [P, NCOL], ctx=ctx) if bias is not None else None
        banks = c.banks(f"{name}_ps", ctx)
        loaded = [c.sem(f"{name}_loaded{t}", ctx) for t in range(tiles)]
        ss_ready = c.sem(f"{name}_ss_ready", ctx)
        mean_ready = c.sem(f"{name}_mean_ready", ctx)
        rstd_ready = c.sem(f"{name}_rstd_ready", ctx)
        scaled_ready = c.sem(f"{name}_scaled_ready", ctx)
        turned = c.sem(f"{name}_turned", ctx)
        hi_ready = c.sem(f"{name}_hi_ready", ctx)
        full_ready = c.sem(f"{name}_full_ready", ctx)
        lo_ready = c.sem(f"{name}_lo_ready", ctx)
        block = ctx.enter_context(nc.Block())

        @block.sync
        def _(sp):
            if load is not None:
                for t in range(tiles):
                    sp.dma_start(src[:, t, :], load[t * P:(t + 1) * P, :]).then_inc(loaded[t], 16)

        @block.scalar
        def _(act):
            for t in range(tiles):
                if load is not None:
                    act.wait_ge(loaded[t], 16)
                if t:
                    act.wait_ge(ss_ready, t)
                nc.scalar.activation(junk[:], src[:, t, :], ACT.Square,
                                     accum_out=ss[:, t:t + 1]).then_inc(ss_ready, 1)
            for n in range(n_half * KT):
                h, k = divmod(n, KT)
                act.wait_ge(turned, n + 1)
                o = Xhi[:, k, h * width:(h + 1) * width]
                if bias is None:
                    nc.scalar.activation(o, banks[n % 8][:, 0:width], ACT.Copy,
                                         scale=gain[:, k:k + 1]).then_inc(hi_ready, 1)
                else:
                    nc.scalar.activation(o, banks[n % 8][:, 0:width], ACT.Identity, scale=gain[:, k:k + 1],
                                         bias=bias[:, k:k + 1]).then_inc(hi_ready, 1)

        @block.gpsimd
        def _(pool):
            for h in range(n_half):
                cols = slice(h * per, (h + 1) * per)
                pool.wait_ge(ss_ready, (h + 1) * per)
                nc.gpsimd.tensor_scalar(mean[:, cols], ss[:, cols], 1.0 / D, EPS, ALU.mult, ALU.add)\
                    .then_inc(mean_ready, 1)
                pool.wait_ge(mean_ready, h + 1)
                nc.gpsimd.tensor_tensor(rstd[:, cols], mean[:, cols], c.minus_half[:, 0:per], ALU.pow)\
                    .then_inc(rstd_ready, 1)

        @block.vector
        def _(dve):
            for h in range(n_half):
                dve.wait_ge(rstd_ready, h + 1)
                if h:
                    dve.wait_ge(turned, h * KT)
                for t in range(per):
                    nc.vector.tensor_scalar(scaled[:, t, :], src[:, h * per + t, :],
                                            rstd[:, h * per + t:h * per + t + 1], None, ALU.mult)\
                        .then_inc(scaled_ready, 1)
                for k in range(KT):
                    n = h * KT + k
                    dve.wait_ge(hi_ready, n + 1)
                    o = slice(h * width, (h + 1) * width)
                    if bias is None:
                        nc.vector.scalar_tensor_tensor(
                            out=Xlo[:, k, o], in0=banks[n % 8][:, 0:width], scalar=gain[:, k:k + 1],
                            in1=Xhi[:, k, o].bitcast(F32), op0=ALU.mult, op1=ALU.subtract).then_inc(lo_ready, 1)
                    else:
                        if n:
                            dve.wait_ge(lo_ready, n)
                        nc.vector.tensor_scalar(full[:, 0:width], banks[n % 8][:, 0:width], gain[:, k:k + 1],
                                                bias[:, k:k + 1], ALU.mult, ALU.add).then_inc(full_ready, 1)
                        dve.wait_ge(full_ready, n + 1)
                        nc.vector.tensor_tensor(Xlo[:, k, o], full[:, 0:width], Xhi[:, k, o].bitcast(F32),
                                                ALU.subtract).then_inc(lo_ready, 1)

        @block.tensor
        def _(pe):
            for h in range(n_half):
                pe.wait_ge(scaled_ready, (h + 1) * per)
                for k in range(KT):
                    n = h * KT + k
                    if n >= 8:
                        pe.wait_ge(lo_ready, n - 7)
                    for t in range(per):
                        last = nc.tensor.transpose(banks[n % 8][:, t * P:(t + 1) * P],
                                                   scaled[:, t, k * P:(k + 1) * P], c.ident[:])
                    last.then_inc(turned, 1)


class Weights:

    def __init__(self, chip, name, ctx, groups, done=None):
        c = chip
        self.nc = c.nc
        self.stage = c.sb(f"{name}_stage", [P, SLOTS, NCOL], ctx=ctx)
        self.hi = c.sb(f"{name}_w_hi", [P, 2, KT, NCOL], F32R, ctx=ctx)
        self.lo = c.sb(f"{name}_w_lo", [P, 2, KT, NCOL], F32R, ctx=ctx)
        self.loaded = [c.sem(f"{name}_w_loaded{i}", ctx) for i in range(SLOTS)]
        self.hi_ready = c.sem(f"{name}_w_hi_ready", ctx)
        self.lo_ready = c.sem(f"{name}_w_lo_ready", ctx)
        self.groups = groups
        self.done = done
        self.chunks = [(g, k, ap) for g, aps in enumerate(groups) for k, ap in enumerate(aps)]
        self.first = [sum(len(x) for x in groups[:g]) for g in range(len(groups) + 1)]

    def load(self, sp):
        for n in range(len(self.chunks)):
            self.load_chunk(sp, n)

    def load_chunk(self, sp, n):
        ap = self.chunks[n][2]
        if n >= SLOTS:
            sp.wait_ge(self.lo_ready, n - SLOTS + 1)
        at = 0
        for piece in (ap if isinstance(ap, list) else [ap]):
            w = piece.shape[1]
            sp.dma_start(self.stage[:, n % SLOTS, at:at + w], piece).then_inc(self.loaded[n % SLOTS], 16)
            at += w

    def _loads(self, n):
        return sum(len(ap) if isinstance(ap, list) else 1 for m, (_, _, ap) in enumerate(self.chunks[:n + 1])
                   if m % SLOTS == n % SLOTS)

    def width(self, n):
        ap = self.chunks[n][2]
        return sum(x.shape[1] for x in ap) if isinstance(ap, list) else ap.shape[1]

    def split_hi(self, act, n):
        g, k, _ = self.chunks[n]
        act.wait_ge(self.loaded[n % SLOTS], 16 * self._loads(n))
        if g >= 2:
            act.wait_ge(self.done[0], self.done[1][g - 2])
        w = self.width(n)
        self.nc.scalar.activation(self.hi[:, g % 2, k, 0:w], self.stage[:, n % SLOTS, 0:w], ACT.Copy)\
            .then_inc(self.hi_ready, 1)

    def split_hi_group(self, act, g):
        for n in range(self.first[g], self.first[g + 1]):
            self.split_hi(act, n)

    def split_lo_chunk(self, pool, n):
        g, k, _ = self.chunks[n]
        pool.wait_ge(self.hi_ready, n + 1)
        w = self.width(n)
        self.nc.gpsimd.tensor_tensor(self.lo[:, g % 2, k, 0:w], self.stage[:, n % SLOTS, 0:w],
                                     self.hi[:, g % 2, k, 0:w].bitcast(F32), ALU.subtract)\
            .then_inc(self.lo_ready, 1)

    def split_lo(self, pool):
        for n in range(len(self.chunks)):
            self.split_lo_chunk(pool, n)


def product(nc, out, terms, cols, last_inc=None, ready=None):
    n = 0
    total = 3 * len(terms)
    for t, ((ah, al), (bh, bl)) in enumerate(terms):
        if ready:
            ready(t)
        for x, y in ((ah, bh), (ah, bl), (al, bh)):
            last = nc.tensor.matmul(out, x, y, start=(n == 0), stop=(n == total - 1))
            n += 1
    if last_inc is not None:
        last.then_inc(last_inc, 1)
    return last


def project_to_dram(nc, chip, name, groups):
    c = chip
    with ExitStack() as ctx:
        result_ready = c.sem(f"{name}_result_ready", ctx)
        w = Weights(c, name, ctx, [g[0] for g in groups], (result_ready, [TT * (g + 1) for g in range(len(groups))]))
        ring = c.sb(f"{name}_ring", [P, RING, NCOL], ctx=ctx)
        banks = c.banks(f"{name}_ps", ctx)
        copied = c.sem(f"{name}_copied", ctx)
        stored = [c.sem(f"{name}_stored{i}", ctx) for i in range(RING)]
        outs = [(g, o) for g in range(len(groups)) for o in range(TT)]
        stores = [len(groups[g][2](o)) for g, o in outs]
        upto = [sum(s for m, s in enumerate(stores[:n]) if m % RING == n % RING) for n in range(len(outs) + RING)]
        block = ctx.enter_context(nc.Block())

        @block.sync
        def _(sp):
            w.load(sp)

        @block.gpsimd
        def _(pool):
            w.split_lo(pool)

        @block.tensor
        def _(pe):
            for n, (g, o) in enumerate(outs):
                by_feature = groups[g][1]
                width = w.width(w.first[g])
                if n >= 8:
                    pe.wait_ge(copied, n - 7)
                terms = []
                for k in range(KT):
                    x = c.Xhi, c.Xlo
                    ww = w.hi[:, g % 2, k], w.lo[:, g % 2, k]
                    if by_feature:
                        f, h = divmod(o, HALVES)
                        terms.append((tuple(y[:, f * P:(f + 1) * P] for y in ww),
                                      tuple(y[:, k, h * NCOL:(h + 1) * NCOL] for y in x)))
                    else:
                        terms.append((tuple(y[:, k, o * P:(o + 1) * P] for y in x),
                                      tuple(y[:, 0:width] for y in ww)))
                out = banks[n % 8][:, 0:NCOL if by_feature else width]
                last = product(nc, out, terms, NCOL, result_ready,
                               (lambda k: pe.wait_ge(w.lo_ready, w.first[g] + k + 1)) if o == 0 else None)

        @block.scalar
        def _(act):
            def store(n):
                g, o = outs[n]
                act.wait_ge(copied, n + 1)
                for place, cols in groups[g][2](o):
                    act.dma_start(place, ring[:, n % RING, cols]).then_inc(stored[n % RING], 16)

            w.split_hi_group(act, 0)
            for n, (g, o) in enumerate(outs):
                _, by_feature, _, func, scale = groups[g]
                width = NCOL if by_feature else w.width(w.first[g])
                if n >= RING:
                    act.wait_ge(stored[n % RING], 16 * upto[n])
                act.wait_ge(result_ready, n + 1)
                nc.scalar.activation(ring[:, n % RING, 0:width], banks[n % 8][:, 0:width], func,
                                     scale=scale(o)).then_inc(copied, 1)
                if n:
                    store(n - 1)
                if g + 1 < len(groups):
                    w.split_hi(act, w.first[g + 1] + o)
            store(len(outs) - 1)
            for i in range(RING):
                n = max(m for m in range(len(outs)) if m % RING == i)
                act.wait_ge(stored[i], 16 * (upto[n] + stores[n]))


def split_small(nc, chip, name, ctx, parts):
    out = {}
    for pn, shape in parts:
        out[pn] = (chip.sb(f"{name}_{pn}_f", shape, ctx=ctx), chip.sb(f"{name}_{pn}_hi", shape, F32R, ctx=ctx),
                   chip.sb(f"{name}_{pn}_lo", shape, F32R, ctx=ctx))
    return out


def latent_prepare(nc, chip, a, d):
    c = chip
    QW = MH * MQK // 2
    KVW = MH * (MNOPE + MV) // 2
    TWO_PI_HI, TWO_PI_MID, TWO_PI_LO = 6.28125, 0.0019350051879882812, 3.0199159819e-07
    with ExitStack() as ctx:
        sb = lambda n, s, dt=F32: c.sb("mp_" + n, s, dt, ctx=ctx)
        sem = lambda n: c.sem("mp_" + n, ctx)
        zc = sb("zc", [P, TT, 432])
        cT_hi = sb("cT_hi", [P, 3, S], F32R)
        cT_lo = sb("cT_lo", [P, 3, S], F32R)
        w_f = sb("w_f", [P, 1, 1024])
        wq_hi, wq_lo = sb("wq_hi", [P, 2, 768], F32R), sb("wq_lo", [P, 2, 768], F32R)
        wk_hi, wk_lo = sb("wk_hi", [P, 1024], F32R), sb("wk_lo", [P, 1024], F32R)
        junk = sb("junk", [P, 1280])
        cn = sb("cn", [P, 2, 384])
        ss = sb("ss", [P, 3, TT])
        ssm = sb("ssm", [P, 2, TT])
        rstd = sb("rstd", [P, 2, TT])
        gc = sb("gc", [P, 3])
        gq, gk = sb("gq", [P, MQK]), sb("gk", [P, MQK])
        pos_i = sb("pos_i", [P, TT], I32)
        pos = sb("pos", [P, TT])
        freq = sb("freq", [P, 16])
        ang = sb("ang", [P, TT, 16])
        t1, t2 = sb("t1", [P, TT, 16]), sb("t2", [P, TT, 16])
        turn_i = sb("turn_i", [P, TT, 16], I32)
        cos, sin = sb("cos", [P, TT, 16]), sb("sin", [P, TT, 16])
        nrm = sb("nrm", [P, 2, 2, MH, MQK])
        rop = sb("rop", [P, 2, 4, MH, 16])
        ssh, msh, rsh = sb("ssh", [P, 2, 2, MH]), sb("msh", [P, 2, 2, MH]), sb("rsh", [P, 2, 2, MH])
        qk_hi = sb("qk_hi", [MQK, 2, MH, P], F32R)
        qk_lo = sb("qk_lo", [MQK, 2, MH, P], F32R)
        v_hi, v_lo = sb("v_hi", [P, MH, MV], F32R), sb("v_lo", [P, MH, MV], F32R)
        banks = c.banks("mp_ps", ctx)

        loaded = sem("loaded")
        wloaded = sem("wloaded")
        act_step, dve_step, pool_step = sem("act_step"), sem("dve_step"), sem("pool_step")
        c_scaled, c_hi, c_lo = sem("c_scaled"), sem("c_hi"), sem("c_lo")
        ss_ready, rstd_ready, w_split = sem("ss_ready"), sem("rstd_ready"), sem("w_split")
        w_hi_ready = sem("w_hi_ready")
        table_arg, table_ready = sem("table_arg"), sem("table_ready")
        up_ready = sem("up_ready")
        squares, head_ss, head_rstd, up_read, v_hi_ready, v_lo_ready = (
            sem("squares"), sem("head_ss"), sem("head_rstd"), sem("up_read"), sem("v_hi_ready"), sem("v_lo_ready"))
        roped, turned, hi_ready, lo_ready = sem("roped"), sem("turned"), sem("hi_ready"), sem("lo_ready")
        q_out, v_out = sem("q_out"), sem("v_out")
        c_scaled_read = sem("c_scaled_read")
        block = ctx.enter_context(nc.Block())

        w_rows = [a["mla_w_uq"][0, 0:P, :], a["mla_w_uq"][0, P:2 * P, :], a["mla_w_ukv"][0]]
        w_dst = [(wq_hi[:, 0], wq_lo[:, 0]), (wq_hi[:, 1], wq_lo[:, 1]), (wk_hi[:], wk_lo[:])]

        @block.sync
        def _(sp):
            sp.dma_start(zc[:], d["zc"].rearrange("t p n -> p t n")).then_inc(loaded, 16)
            sp.dma_start(gc[:, 0:2], a["mla_q_norm"][0].rearrange("(k p) -> p k", p=P)).then_inc(loaded, 16)
            sp.dma_start(gc[:, 2:3], a["mla_kv_norm"][0].rearrange("(k p) -> p k", p=P)).then_inc(loaded, 16)
            sp.dma_start(gq[:], a["qk_norm_q"].to_broadcast([P, MQK])).then_inc(loaded, 16)
            sp.dma_start(gk[:], a["qk_norm_k"].to_broadcast([P, MQK])).then_inc(loaded, 16)
            sp.dma_start(pos_i[:], a["positions"][0].rearrange("(t p) -> p t", p=P)).then_inc(loaded, 16)
            sp.dma_start(freq[:], a["inv_freq"].to_broadcast([P, 16])).then_inc(loaded, 16)
            for n, rows in enumerate(w_rows):
                if n:
                    sp.wait_ge(w_split, n)
                sp.dma_start(w_f[:, 0, 0:rows.shape[1]], rows).then_inc(wloaded, 16)
            for t in range(TT):
                sp.wait_ge(v_lo_ready, t + 1)
                sp.dma_start(d["mv_hi"][:, t].rearrange("h p v -> p h v"), v_hi[:].bitcast(F32)).then_inc(v_out, 16)
                sp.dma_start(d["mv_lo"][:, t].rearrange("h p v -> p h v"), v_lo[:].bitcast(F32)).then_inc(v_out, 16)
                for q in range(2):
                    sp.wait_ge(lo_ready, 4 * t + 2 * (q + 1))
                    cols = slice(t * P, (t + 1) * P)
                    sp.dma_start(d["mqk_hi"][q, :, :, cols].rearrange("h d s -> d h s"), qk_hi[:, q].bitcast(F32))\
                        .then_inc(q_out, 16)
                    sp.dma_start(d["mqk_lo"][q, :, :, cols].rearrange("h d s -> d h s"), qk_lo[:, q].bitcast(F32))\
                        .then_inc(q_out, 16)
            sp.wait_ge(q_out, 64 * TT)
            sp.wait_ge(v_out, 32 * TT)

        @block.gpsimd
        def _(pool):
            for n, rows in enumerate(w_rows):
                w = rows.shape[1]
                pool.wait_ge(w_hi_ready, n + 1)
                nc.gpsimd.tensor_tensor(w_dst[n][1], w_f[:, 0, 0:w], w_dst[n][0].bitcast(F32), ALU.subtract)\
                    .then_inc(w_split, 1)
            pool.wait_ge(ss_ready, 3 * TT)
            nc.gpsimd.tensor_scalar(ssm[:, 0], ss[:, 0], 1.0 / MQR, EPS, ALU.mult, ALU.add).then_inc(pool_step, 1)
            nc.gpsimd.tensor_scalar(ssm[:, 1], ss[:, 1], 1.0 / MKVR, EPS, ALU.mult, ALU.add).then_inc(pool_step, 1)
            pool.wait_ge(pool_step, 2)
            nc.gpsimd.tensor_tensor(rstd[:], ssm[:], c.minus_half[:, 0:16].rearrange("p (a b) -> p a b", a=2),
                                    ALU.pow).then_inc(rstd_ready, 1)
            for t in range(TT):
                b = t % 2
                pool.wait_ge(head_ss, t + 1)
                nc.gpsimd.tensor_scalar(msh[:, b], ssh[:, b], 1.0 / MQK, EPS, ALU.mult, ALU.add)\
                    .then_inc(pool_step, 1)
                pool.wait_ge(pool_step, 3 + t)
                nc.gpsimd.tensor_tensor(rsh[:, b], msh[:, b],
                                        c.minus_half[:, 0:16].rearrange("p (a b) -> p a b", a=2),
                                        ALU.pow).then_inc(head_rstd, 1)

        @block.scalar
        def _(act):
            for n, rows in enumerate(w_rows):
                act.wait_ge(wloaded, 16 * (n + 1))
                nc.scalar.activation(w_dst[n][0], w_f[:, 0, 0:rows.shape[1]], ACT.Copy).then_inc(w_hi_ready, 1)
            act.wait_ge(loaded, 16 * 7)
            n = 0
            for t in range(TT):
                for m, (lo, hi) in enumerate(((16, 272), (272, 400), (400, 432))):
                    if n:
                        act.wait_ge(ss_ready, n)
                    nc.scalar.activation(junk[:, 0:hi - lo], zc[:, t, lo:hi], ACT.Square,
                                         accum_out=ss[:, m, t:t + 1]).then_inc(ss_ready, 1)
                    n += 1
            for i, (arg, out) in enumerate(((t1, sin), (t2, cos))):
                act.wait_ge(table_arg, i + 1)
                nc.scalar.activation(out[:], arg[:], ACT.Sin).then_inc(table_ready, 1)
            for n in range(6):
                j = n % 3
                h = n // 3
                act.wait_ge(c_scaled_read, 4 * (h + 1))
                nc.scalar.activation(cT_hi[:, j, h * NCOL:(h + 1) * NCOL], banks[n][:], ACT.Copy,
                                     scale=gc[:, j:j + 1]).then_inc(c_hi, 1)

            def squares_of(t):
                bank = banks[4 * (t % 2):4 * (t % 2) + 4]
                act.wait_ge(up_ready, t + 1)
                if t:
                    act.wait_ge(head_ss, t)
                for g in range(2):
                    nc.scalar.activation(junk[:, g * QW:(g + 1) * QW], bank[g][:, 0:QW], ACT.Square)\
                        .then_inc(squares, 1)
                for g in range(2):
                    nc.scalar.activation(
                        junk[:, 768 + g * 256:768 + (g + 1) * 256].rearrange("p (h n) -> p h n", h=4),
                        bank[2 + g][:].rearrange("p (h n) -> p h n", h=4)[:, :, 0:MNOPE], ACT.Square)\
                        .then_inc(squares, 1)
                if t:
                    act.wait_ge(v_out, 32 * t)
                for g in range(2):
                    nc.scalar.activation(v_hi[:, 4 * g:4 * g + 4, :],
                                         bank[2 + g][:].rearrange("p (h n) -> p h n", h=4)[:, :, MNOPE:],
                                         ACT.Copy).then_inc(v_hi_ready, 1)

            def high(t):
                for m in range(4):
                    q, g = divmod(m, 2)
                    act.wait_ge(turned, 4 * t + m + 1)
                    if t:
                        act.wait_ge(q_out, 64 * t)
                    nc.scalar.activation(qk_hi[:, q, 4 * g:4 * g + 4, :],
                                         banks[4 * (t % 2) + m][0:MQK].rearrange("p (h n) -> p h n", h=4),
                                         ACT.Copy).then_inc(hi_ready, 1)

            squares_of(0)
            for t in range(TT):
                if t:
                    high(t - 1)
                if t + 1 < TT:
                    squares_of(t + 1)
            high(TT - 1)

        @block.vector
        def _(dve):
            steps = [0]

            def step(ins):
                steps[0] += 1
                ins.then_inc(dve_step, 1)
                dve.wait_ge(dve_step, steps[0])

            dve.wait_ge(loaded, 16 * 7)
            step(nc.vector.tensor_copy(pos[:], pos_i[:]))
            step(nc.vector.tensor_tensor(ang[:], pos[:].unsqueeze(2).to_broadcast([P, TT, 16]),
                                         freq[:].unsqueeze(1).to_broadcast([P, TT, 16]), ALU.mult))
            for i, (shift, out) in enumerate(((0.0, t1), (0.25, t2))):
                step(nc.vector.tensor_scalar(t1[:] if i == 0 else t2[:], ang[:], 0.15915494309189535, shift,
                                             ALU.mult, ALU.add))
                step(nc.vector.tensor_copy(turn_i[:], out[:]))
                step(nc.vector.tensor_copy(cos[:], turn_i[:]))
                step(nc.vector.scalar_tensor_tensor(out=out[:], in0=cos[:], scalar=-TWO_PI_HI, in1=ang[:],
                                                    op0=ALU.mult, op1=ALU.add))
                step(nc.vector.scalar_tensor_tensor(out=out[:], in0=cos[:], scalar=-TWO_PI_MID, in1=out[:],
                                                    op0=ALU.mult, op1=ALU.add))
                step(nc.vector.scalar_tensor_tensor(out=out[:], in0=cos[:], scalar=-TWO_PI_LO, in1=out[:],
                                                    op0=ALU.mult, op1=ALU.add))
                if i:
                    step(nc.vector.tensor_scalar(out[:], out[:], 1.5707963267948966, None, ALU.add))
                nc.vector.tensor_scalar(out[:], out[:], 3.1415925, -3.1415925, ALU.min, ALU.max)\
                    .then_inc(table_arg, 1)
                if i == 0:
                    dve.wait_ge(table_arg, 1)
            dve.wait_ge(rstd_ready, 1)
            for t in range(TT):
                if t >= 2:
                    dve.wait_ge(c_scaled_read, t - 1)
                nc.vector.tensor_scalar(cn[:, t % 2, 0:256], zc[:, t, 16:272], rstd[:, 0, t:t + 1], None, ALU.mult)\
                    .then_inc(c_scaled, 1)
                nc.vector.tensor_scalar(cn[:, t % 2, 256:384], zc[:, t, 272:400], rstd[:, 1, t:t + 1], None, ALU.mult)\
                    .then_inc(c_scaled, 1)
            for n in range(6):
                j, h = n % 3, n // 3
                dve.wait_ge(c_hi, n + 1)
                nc.vector.scalar_tensor_tensor(
                    out=cT_lo[:, j, h * NCOL:(h + 1) * NCOL], in0=banks[n][:], scalar=gc[:, j:j + 1],
                    in1=cT_hi[:, j, h * NCOL:(h + 1) * NCOL].bitcast(F32), op0=ALU.mult, op1=ALU.subtract)\
                    .then_inc(c_lo, 1)
            dve.wait_ge(table_ready, 2)

            def sums_of(t):
                b = t % 2
                bank = banks[4 * b:4 * b + 4]
                dve.wait_ge(squares, 4 * t + 2)
                nc.vector.tensor_reduce(out=ssh[:, b, 0], in_=junk[:, 0:768].rearrange("p (h n) -> p h n", h=MH),
                                        op=ALU.add, axis=AX.X).then_inc(dve_step, 1)
                steps[0] += 1
                dve.wait_ge(squares, 4 * t + 4)
                step(nc.vector.tensor_reduce(out=ssh[:, b, 1], in_=junk[:, 768:1280].rearrange("p (h n) -> p h n", h=MH),
                                             op=ALU.add, axis=AX.X))
                nc.vector.tensor_scalar(ssh[:, b, 1], ssh[:, b, 1], ss[:, 2, t:t + 1], None, ALU.add)\
                    .then_inc(head_ss, 1)
                dve.wait_ge(v_hi_ready, 2 * t + 2)
                for g in range(2):
                    last = nc.vector.tensor_tensor(
                        v_lo[:, 4 * g:4 * g + 4, :],
                        bank[2 + g][:].rearrange("p (h n) -> p h n", h=4)[:, :, MNOPE:],
                        v_hi[:, 4 * g:4 * g + 4, :].bitcast(F32), ALU.subtract)
                last.then_inc(v_lo_ready, 1)

            def norm_rope(t):
                b = t % 2
                bank = banks[4 * b:4 * b + 4]
                dve.wait_ge(head_rstd, t + 1)
                rs = rsh[:, b]
                for g in range(2):
                    hs = slice(4 * g, 4 * g + 4)
                    nc.vector.tensor_tensor(nrm[:, b, 0, hs], bank[g][:, 0:QW].rearrange("p (h n) -> p h n", h=4),
                                            rs[:, 0, hs].unsqueeze(2).to_broadcast([P, 4, MQK]), ALU.mult)\
                        .then_inc(dve_step, 1)
                    nc.vector.tensor_tensor(nrm[:, b, 1, hs, 0:MNOPE],
                                            bank[2 + g][:].rearrange("p (h n) -> p h n", h=4)[:, :, 0:MNOPE],
                                            rs[:, 1, hs].unsqueeze(2).to_broadcast([P, 4, MNOPE]), ALU.mult)\
                        .then_inc(dve_step, 1)
                steps[0] += 4
                step(nc.vector.tensor_tensor(nrm[:, b, 1, :, MNOPE:],
                                             zc[:, t, 400:432].unsqueeze(1).to_broadcast([P, MH, MROPE]),
                                             rs[:, 1].unsqueeze(2).to_broadcast([P, MH, MROPE]), ALU.mult))
                for q, g in ((0, gq), (1, gk)):
                    x = nrm[:, b, q]
                    step(nc.vector.tensor_tensor(x, x, g[:].unsqueeze(1).to_broadcast([P, MH, MQK]), ALU.mult))
                    x1, x2 = x[:, :, 64:80], x[:, :, 80:96]
                    cs = cos[:, t].unsqueeze(1).to_broadcast([P, MH, 16])
                    sn = sin[:, t].unsqueeze(1).to_broadcast([P, MH, 16])
                    for m, (u, v) in enumerate(((x1, cs), (x2, sn), (x2, cs), (x1, sn))):
                        nc.vector.tensor_tensor(rop[:, b, m], u, v, ALU.mult).then_inc(dve_step, 1)
                    steps[0] += 4
                    dve.wait_ge(dve_step, steps[0])
                    nc.vector.tensor_tensor(x1, rop[:, b, 0], rop[:, b, 1], ALU.subtract).then_inc(roped, 1)
                    nc.vector.tensor_tensor(x2, rop[:, b, 2], rop[:, b, 3], ALU.add).then_inc(roped, 1)

            def low(t):
                for m in range(4):
                    q, g = divmod(m, 2)
                    dve.wait_ge(hi_ready, 4 * t + m + 1)
                    nc.vector.tensor_tensor(qk_lo[:, q, 4 * g:4 * g + 4, :],
                                            banks[4 * (t % 2) + m][0:MQK].rearrange("p (h n) -> p h n", h=4),
                                            qk_hi[:, q, 4 * g:4 * g + 4, :].bitcast(F32), ALU.subtract)\
                        .then_inc(lo_ready, 1)

            sums_of(0)
            for t in range(TT):
                if t:
                    low(t - 1)
                norm_rope(t)
                if t + 1 < TT:
                    sums_of(t + 1)
            low(TT - 1)

        @block.tensor
        def _(pe):
            for t in range(TT):
                pe.wait_ge(c_scaled, 2 * t + 2)
                h, u = divmod(t, 4)
                for j in range(3):
                    last = nc.tensor.transpose(banks[3 * h + j][:, u * P:(u + 1) * P],
                                               cn[:, t % 2, j * P:(j + 1) * P], c.ident[:])
                last.then_inc(c_scaled_read, 1)
            pe.wait_ge(c_lo, 6)
            pe.wait_ge(w_split, 3)

            def up(t):
                tok = slice(t * P, (t + 1) * P)
                bank = banks[4 * (t % 2):4 * (t % 2) + 4]
                if t >= 2:
                    pe.wait_ge(lo_ready, 4 * (t - 1))
                for g in range(2):
                    product(nc, bank[g][:, 0:QW],
                            [((cT_hi[:, k, tok], cT_lo[:, k, tok]),
                              (wq_hi[:, k, g * QW:(g + 1) * QW], wq_lo[:, k, g * QW:(g + 1) * QW]))
                             for k in range(2)], QW)
                for g in range(2):
                    last = product(nc, bank[2 + g][:],
                                   [((cT_hi[:, 2, tok], cT_lo[:, 2, tok]),
                                     (wk_hi[:, g * KVW:(g + 1) * KVW], wk_lo[:, g * KVW:(g + 1) * KVW]))], KVW)
                last.then_inc(up_ready, 1)

            def turn(t):
                for q in range(2):
                    pe.wait_ge(roped, 4 * t + 2 * (q + 1))
                    if q:
                        pe.wait_ge(v_lo_ready, t + 1)
                    for g in range(2):
                        for h in range(4):
                            last = nc.tensor.transpose(banks[4 * (t % 2) + 2 * q + g][0:MQK, h * P:(h + 1) * P],
                                                       nrm[:, t % 2, q, 4 * g + h, :], c.ident[:])
                        last.then_inc(turned, 1)

            up(0)
            for t in range(TT):
                if t + 1 < TT:
                    up(t + 1)
                turn(t)


def gated_linear_attention(nc, chip, a, d):
    c = chip
    CH = 4
    UT = CH * P
    UNITS = [(h, p) for h in range(TT // CH) for p in range(GH // 2)]
    LEVELS = (64, 32, 16)
    TAU = 16.0
    NQ = len(LEVELS) + 1
    CHUNKS = len(UNITS) * CH
    with ExitStack() as ctx:
        sb = lambda n, s, dt=F32: c.sb("gla_" + n, s, dt, ctx=ctx)
        sem = lambda n: c.sem("gla_" + n, ctx)
        qT, kT = sb("qT", [P, 2, S]), sb("kT", [P, 2, S])
        v = c.H[:, 0:TT // 2, :].rearrange("p a (b n) -> p (a b) n", n=GH * GDV)
        gate = c.H[:, TT // 2:TT, :].rearrange("p a (b n) -> p (a b) n", n=GH * GDV)
        glow = sb("glow", [P, TT, GR])
        glowT = sb("glowT", [GR, S])
        w2 = sb("w2", [GR, 2 * P])
        gb = sb("gb", [P, 2])
        gain = sb("gain", [P, GDV])
        masks = sb("masks", [P, NQ, P])
        reset = sb("reset", [P, UT])
        low, mag, b = sb("low", [P, UT]), sb("mag", [P, UT]), sb("b", [P, UT])
        diff = sb("diff", [P, 2, UT])
        expo = sb("expo", [P, 2, UT])
        expn = sb("expn", [P, UT])
        qs = sb("qs", [P, 2, NQ + 1, UT])
        ks = sb("ks", [P, 2, NQ + 1, UT])
        dec = sb("dec", [P, 2, CH])
        state = sb("state", [P, 2, 2 * GDV])
        masked = sb("masked", [P, 2, NQ, P])
        st = sb("st", [P, 4, P])
        kdt = sb("kdt", [P, 2, P])
        o_sq = sb("o_sq", [P, 2 * GDV])
        o_ss, o_ms, o_rs = sb("o_ss", [P, 2]), sb("o_ms", [P, 2]), sb("o_rs", [P, 2, 2])
        on = sb("on", [P, 2, CH, 2 * GDV])
        banks = c.banks("gla_ps", ctx)
        loaded = sem("loaded")
        ready0 = sem("ready0")
        gl_turned, gl_ready, pre_ready = sem("gl_turned"), sem("gl_ready"), sem("pre_ready")
        act_step, dve_step, pool_step = sem("act_step"), sem("dve_step"), sem("pool_step")
        mag_ready, low_ready, ln_ready, b_ready = sem("mag_ready"), sem("low_ready"), sem("ln_ready"), sem("b_ready")
        diff_ready, exp_ready, q_used, k_used = sem("diff_ready"), sem("exp_ready"), sem("q_used"), sem("k_used")
        scored, mask_ready, st_ready, st_used = sem("scored"), sem("mask_ready"), sem("st_ready"), sem("st_used")
        kd_turned, kdt_ready, update_ready, state_ready = (
            sem("kd_turned"), sem("kdt_ready"), sem("update_ready"), sem("state_ready"))
        o_squared, o_summed, o_rstd, o_done = (
            sem("o_squared"), sem("o_summed"), sem("o_rstd"), sem("o_done"))
        turned, hi_ready, lo_ready = sem("turned"), sem("hi_ready"), sem("lo_ready")
        block = ctx.enter_context(nc.Block())

        @block.sync
        def _(sp):
            for place, src in (
                (glow[:], d["zc"][:, :, 0:GR].rearrange("t p n -> p t n")), (w2[:], a["gla_gate_w2"][0]),
                (gb[:], a["gla_gate_b"][0].rearrange("(k p) -> p k", p=P)), (masks[:], a["gla_masks"]),
                (gain[:], a["gla_out_norm"].to_broadcast([P, GDV])),
                (qT[:], d["gqk"][0:2].rearrange("k p s -> p k s")), (kT[:], d["gqk"][2:4].rearrange("k p s -> p k s")),
                (v, d["gv"].rearrange("t p n -> p t n")), (gate, d["gr"].rearrange("t p n -> p t n")),
            ):
                sp.dma_start(place, src).then_inc(loaded, 16)

        @block.gpsimd
        def _(pool):
            steps = [0]

            def step(ins):
                steps[0] += 1
                ins.then_inc(pool_step, 1)
                pool.wait_ge(pool_step, steps[0])

            step(nc.gpsimd.memset(reset[:], 1.0))
            nc.gpsimd.memset(reset[:].rearrange("p (c t) -> p c t", t=P)[:, :, 0:1], 0.0).then_inc(ready0, 1)
            nc.gpsimd.memset(state[:], 0.0).then_inc(ready0, 1)
            pool.wait_ge(loaded, 16 * 9)
            for t in range(TT):
                last = nc.gpsimd.tensor_tensor(gate[:, t].rearrange("p (h n) -> p h n", h=GH),
                                               gate[:, t].rearrange("p (h n) -> p h n", h=GH),
                                               gain[:].unsqueeze(1).to_broadcast([P, GH, GDV]), ALU.mult)
            last.then_inc(ready0, 1)

            def prep(u, part):
                h, p = UNITS[u]
                kk = kT[:, p, h * UT:(h + 1) * UT]
                if u >= 2 and part == 1:
                    pool.wait_ge(st_used, 2 * CH * (u - 1))
                for need, src, dst in ((), ((1, expo[:, 0], 0), (2, expo[:, 1], 1)), ((3, expo[:, 0], 2), (5, expn[:], 3)),
                                       ((7, expo[:, 1], 4),))[part]:
                    pool.wait_ge(exp_ready, 7 * u + need)
                    nc.gpsimd.tensor_tensor(ks[:, u % 2, dst], kk, src, ALU.mult).then_inc(k_used, 1)

            def chunk(n):
                pool.wait_ge(o_summed, n + 1)
                step(nc.gpsimd.tensor_scalar(o_ms[:], o_ss[:], 1.0 / GDV, EPS, ALU.mult, ALU.add))
                if n >= 2:
                    pool.wait_ge(o_done, n - 1)
                nc.gpsimd.tensor_tensor(o_rs[:, n % 2], o_ms[:], c.minus_half[:, 0:2], ALU.pow).then_inc(o_rstd, 1)

            for i in range(CH):
                prep(0, i)
            for n in range(CHUNKS):
                u, i = divmod(n, CH)
                if u + 1 < len(UNITS):
                    prep(u + 1, i)
                chunk(n)

        @block.scalar
        def _(act):
            act.wait_ge(gl_turned, 1)
            nc.scalar.activation(glowT[:, 0:NCOL], banks[0][0:GR, :], ACT.Copy).then_inc(gl_ready, 1)
            nc.scalar.activation(glowT[:, NCOL:S], banks[1][0:GR, :], ACT.Copy).then_inc(gl_ready, 1)
            steps = [0]

            def step(ins):
                steps[0] += 1
                ins.then_inc(act_step, 1)
                act.wait_ge(act_step, steps[0])

            def prep(u, part):
                h, p = UNITS[u]
                if part == 0:
                    act.wait_ge(pre_ready, u + 1)
                    if u:
                        act.wait_ge(b_ready, u)
                    nc.scalar.activation(mag[:], banks[0][:], ACT.Abs, bias=gb[:, p:p + 1]).then_inc(mag_ready, 1)
                    act.wait_ge(mag_ready, u + 1)
                    step(nc.scalar.activation(mag[:], mag[:], ACT.Exp, scale=-1.0))
                    nc.scalar.activation(mag[:], mag[:], ACT.Ln, bias=1.0).then_inc(ln_ready, 1)

                def level(i):
                    act.wait_ge(diff_ready, 5 * u + i + 1)
                    if i == 2:
                        act.wait_ge(q_used, 5 * u + 1)
                        act.wait_ge(k_used, 5 * u + 1)
                    elif u:
                        act.wait_ge(q_used, 5 * u)
                        act.wait_ge(k_used, 5 * u)
                    step(nc.scalar.activation(diff[:, i % 2], diff[:, i % 2], ACT.Abs))
                    nc.scalar.activation(expo[:, i % 2], diff[:, i % 2], ACT.Exp, scale=-1.0 / TAU).then_inc(exp_ready, 1)

                if part == 1:
                    level(0)
                    level(1)
                if part == 2:
                    level(2)
                    act.wait_ge(diff_ready, 5 * u + 4)
                    act.wait_ge(q_used, 5 * u + 2)
                    act.wait_ge(k_used, 5 * u + 2)
                    nc.scalar.activation(expo[:, 1], diff[:, 1], ACT.Exp, scale=1.0 / TAU).then_inc(exp_ready, 1)
                    nc.scalar.activation(expn[:], diff[:, 1], ACT.Exp, scale=-1.0 / TAU).then_inc(exp_ready, 1)
                if part == 3:
                    act.wait_ge(q_used, 5 * u + 3)
                    act.wait_ge(k_used, 5 * u + 3)
                    nc.scalar.activation(expo[:, 0], b[:], ACT.Exp, scale=1.0 / TAU).then_inc(exp_ready, 1)
                    act.wait_ge(diff_ready, 5 * u + 5)
                    act.wait_ge(q_used, 5 * u + 4)
                    nc.scalar.activation(expo[:, 1], diff[:, 0], ACT.Exp, scale=1.0 / TAU).then_inc(exp_ready, 1)

            def keys(n):
                act.wait_ge(kd_turned, n + 1)
                if n >= 2:
                    act.wait_ge(update_ready, n - 1)
                nc.scalar.activation(kdt[:, n % 2], banks[5][:, 0:P], ACT.Copy).then_inc(kdt_ready, 1)

            def square(n):
                act.wait_ge(st_used, 2 * (n + 1))
                if n:
                    act.wait_ge(o_summed, n)
                nc.scalar.activation(o_sq[:], banks[3 + n % 2][:, 0:2 * GDV], ACT.Square).then_inc(o_squared, 1)

            def out(u):
                h, p = UNITS[u]
                for i in range(2):
                    act.wait_ge(turned, 2 * u + i + 1)
                    nc.scalar.activation(c.Xhi[:, 2 * p + i, h * UT:(h + 1) * UT], banks[7][:], ACT.Copy)\
                        .then_inc(hi_ready, 1)

            for i in range(CH):
                prep(0, i)
            keys(0)
            for n in range(CHUNKS):
                u, i = divmod(n, CH)
                if u + 1 < len(UNITS):
                    prep(u + 1, i)
                if n + 1 < CHUNKS:
                    keys(n + 1)
                square(n)
                if i == 1 and u:
                    out(u - 1)
            out(len(UNITS) - 1)

        @block.vector
        def _(dve):
            steps = [0]

            def step(ins):
                steps[0] += 1
                ins.then_inc(dve_step, 1)
                dve.wait_ge(dve_step, steps[0])

            dve.wait_ge(loaded, 16 * 9)
            dve.wait_ge(ready0, 3)

            def difference(slot, block_len, ref, sign=1):
                bb = b[:].rearrange("p (n t) -> p n t", t=block_len)
                rr = bb[:, :, ref:ref + 1].to_broadcast([P, UT // block_len, block_len])
                o = diff[:, slot].rearrange("p (n t) -> p n t", t=block_len)
                return nc.vector.tensor_tensor(o, bb, rr, ALU.subtract) if sign > 0 else \
                    nc.vector.tensor_tensor(o, rr, bb, ALU.subtract)

            def prep(u, part):
                h, p = UNITS[u]
                qq = qT[:, p, h * UT:(h + 1) * UT]
                par = u % 2

                def decayed(i, need, src):
                    dve.wait_ge(exp_ready, 7 * u + need)
                    nc.vector.tensor_tensor(qs[:, par, i], qq, src, ALU.mult).then_inc(q_used, 1)

                if part == 0:
                    dve.wait_ge(mag_ready, u + 1)
                    nc.vector.tensor_scalar(low[:], banks[0][:], gb[:, p:p + 1], 0.0, ALU.add, ALU.min)\
                        .then_inc(low_ready, 1)
                    dve.wait_ge(low_ready, u + 1)
                    dve.wait_ge(ln_ready, u + 1)
                    step(nc.vector.tensor_tensor(low[:], low[:], mag[:], ALU.subtract))
                    if u:
                        dve.wait_ge(exp_ready, 7 * u)
                    nc.vector.tensor_tensor_scan(b[:], reset[:], low[:], 0.0, ALU.mult, ALU.add).then_inc(b_ready, 1)
                    dve.wait_ge(b_ready, u + 1)
                    if u >= 2:
                        dve.wait_ge(st_used, 2 * CH * (u - 1))
                    difference(0, 2 * LEVELS[0], LEVELS[0] - 1).then_inc(diff_ready, 1)
                    difference(1, 2 * LEVELS[1], LEVELS[1] - 1).then_inc(diff_ready, 1)
                if part == 1:
                    decayed(0, 1, expo[:, 0])
                    difference(0, 2 * LEVELS[2], LEVELS[2] - 1).then_inc(diff_ready, 1)
                    decayed(1, 2, expo[:, 1])
                    step(difference(1, 16, 7))
                    nc.vector.tensor_scalar(diff[:, 1], diff[:, 1], 80.0 * TAU, -80.0 * TAU, ALU.min, ALU.max)\
                        .then_inc(diff_ready, 1)
                if part == 2:
                    decayed(2, 3, expo[:, 0])
                    difference(0, P, P - 1, -1).then_inc(diff_ready, 1)
                if part == 3:
                    decayed(3, 4, expo[:, 1])
                    dve.wait_ge(exp_ready, 7 * u + 6)
                    nc.vector.tensor_copy(dec[:, par], expo[:, 0].rearrange("p (c t) -> p c t", t=P)[:, :, P - 1])\
                        .then_inc(dve_step, 1)
                    steps[0] += 1
                    decayed(4, 6, expo[:, 0])

            def mask(n):
                for hd in range(2):
                    m = 2 * n + hd
                    dve.wait_ge(scored, m + 1)
                    step(nc.vector.tensor_tensor(masked[:, m % 2].rearrange("p a b -> p (a b)"), banks[1 + m % 2][:],
                                                 masks[:].rearrange("p a b -> p (a b)"), ALU.mult))
                    if m >= 4:
                        dve.wait_ge(st_used, m - 3)
                    nc.vector.tensor_reduce(out=st[:, m % 4], in_=masked[:, m % 2].rearrange("p a b -> p b a"),
                                            op=ALU.add, axis=AX.X).then_inc(st_ready, 1)

            def advance(n):
                u, i = divmod(n, CH)
                h, p = UNITS[u]
                dve.wait_ge(update_ready, n + 1)
                dve.wait_ge(st_used, 2 * (n + 1))
                for hd in range(2):
                    rows, cols = slice(64 * hd, 64 * hd + 64), slice(GDV * hd, GDV * (hd + 1))
                    last = nc.vector.scalar_tensor_tensor(
                        out=state[rows, p, cols], in0=state[rows, p, cols], scalar=dec[rows, u % 2, i:i + 1],
                        in1=banks[6][rows, cols], op0=ALU.mult, op1=ALU.add)
                last.then_inc(state_ready, 1)
                dve.wait_ge(o_squared, n + 1)
                if n:
                    dve.wait_ge(o_rstd, n)
                nc.vector.tensor_reduce(out=o_ss[:], in_=o_sq[:].rearrange("p (h n) -> p h n", h=2), op=ALU.add,
                                        axis=AX.X).then_inc(o_summed, 1)

            def finish(n):
                u, i = divmod(n, CH)
                h, p = UNITS[u]
                t = h * CH + i
                dve.wait_ge(o_rstd, n + 1)
                if i == 0 and u >= 2:
                    dve.wait_ge(turned, 2 * (u - 1))
                for hd in range(2):
                    cols = slice(GDV * hd, GDV * (hd + 1))
                    last = nc.vector.scalar_tensor_tensor(
                        out=on[:, u % 2, i, cols], in0=banks[3 + n % 2][:, cols], scalar=o_rs[:, n % 2, hd:hd + 1],
                        in1=gate[:, t, (2 * p + hd) * GDV:(2 * p + hd + 1) * GDV], op0=ALU.mult, op1=ALU.mult)
                last.then_inc(o_done, 1)

            def out(u):
                h, p = UNITS[u]
                for i in range(2):
                    dve.wait_ge(hi_ready, 2 * u + i + 1)
                    nc.vector.tensor_tensor(c.Xlo[:, 2 * p + i, h * UT:(h + 1) * UT], banks[7][:],
                                            c.Xhi[:, 2 * p + i, h * UT:(h + 1) * UT].bitcast(F32), ALU.subtract)\
                        .then_inc(lo_ready, 1)

            for i in range(CH):
                prep(0, i)
            mask(0)
            for n in range(CHUNKS):
                u, i = divmod(n, CH)
                if u + 1 < len(UNITS):
                    prep(u + 1, i)
                if n + 1 < CHUNKS:
                    mask(n + 1)
                if n:
                    finish(n - 1)
                advance(n)
                if i == 1 and u:
                    out(u - 1)
            finish(CHUNKS - 1)
            out(len(UNITS) - 1)

        @block.tensor
        def _(pe):
            pe.wait_ge(loaded, 16 * 9)
            for t in range(TT):
                last = nc.tensor.transpose(banks[t // 4][0:GR, (t % 4) * P:(t % 4 + 1) * P], glow[:, t, :], c.ident[:])
            last.then_inc(gl_turned, 1)
            pe.wait_ge(gl_ready, 2)
            pe.wait_ge(ready0, 2)

            def gates(u):
                h, p = UNITS[u]
                if u:
                    pe.wait_ge(low_ready, u)
                nc.tensor.matmul(banks[0][:], w2[:, p * P:(p + 1) * P], glowT[:, h * UT:(h + 1) * UT],
                                 start=True, stop=True).then_inc(pre_ready, 1)

            def scores(n):
                u, i = divmod(n, CH)
                par = u % 2
                tok = slice(i * P, (i + 1) * P)
                if i == 0:
                    pe.wait_ge(q_used, 5 * (u + 1))
                    pe.wait_ge(k_used, 5 * (u + 1))
                if n:
                    pe.wait_ge(kdt_ready, n)
                nc.tensor.transpose(banks[5][:, 0:P], ks[:, par, NQ, tok], c.ident[:]).then_inc(kd_turned, 1)
                for hd in range(2):
                    m = 2 * n + hd
                    rows = slice(64 * hd, 64 * hd + 64)
                    if m >= 2:
                        pe.wait_ge(st_ready, m - 1)
                    for lv in range(NQ):
                        last = nc.tensor.matmul(banks[1 + m % 2][:, lv * P:(lv + 1) * P], ks[rows, par, lv, tok],
                                                qs[rows, par, lv, tok], start=(lv == 0), stop=True,
                                                skip_group_check=True)
                    last.then_inc(scored, 1)

            def outputs(n):
                u, i = divmod(n, CH)
                h, p = UNITS[u]
                t, par = h * CH + i, u % 2
                tok = slice(i * P, (i + 1) * P)
                vv = v[:, t, 2 * p * GDV:(2 * p + 2) * GDV]
                pe.wait_ge(kdt_ready, n + 1)
                if n:
                    pe.wait_ge(state_ready, n)
                nc.tensor.matmul(banks[6][:, 0:2 * GDV], kdt[:, n % 2], vv, start=True, stop=True)\
                    .then_inc(update_ready, 1)
                if n >= 2:
                    pe.wait_ge(o_done, n - 1)
                ob = banks[3 + n % 2]
                nc.tensor.matmul(ob[:, 0:2 * GDV], qs[:, par, NQ, tok], state[:, p], start=True, stop=True,
                                 skip_group_check=True)
                for hd in range(2):
                    m = 2 * n + hd
                    pe.wait_ge(st_ready, m + 1)
                    last = nc.tensor.matmul(ob[:, GDV * hd:GDV * (hd + 1)], st[:, m % 4],
                                            vv[:, GDV * hd:GDV * (hd + 1)], start=False, stop=True,
                                            skip_group_check=True)
                    last.then_inc(st_used, 1)

            def out(u):
                pe.wait_ge(o_done, (u + 1) * CH)
                for hd in range(2):
                    if 2 * u + hd:
                        pe.wait_ge(lo_ready, 2 * u + hd)
                    for i in range(CH):
                        last = nc.tensor.transpose(banks[7][:, i * P:(i + 1) * P], on[:, u % 2, i, GDV * hd:GDV * (hd + 1)],
                                                   c.ident[:])
                    last.then_inc(turned, 1)

            gates(0)
            scores(0)
            for n in range(CHUNKS):
                u, i = divmod(n, CH)
                if i == 0 and u + 1 < len(UNITS):
                    gates(u + 1)
                if i == 3 or n + 1 == CHUNKS:
                    outputs(n)
                if n + 1 < CHUNKS:
                    scores(n + 1)
                if i != 3:
                    outputs(n)
                if i == 1 and u:
                    out(u - 1)
            out(len(UNITS) - 1)


def latent_attention(nc, chip, a, d):
    c = chip
    SCALE = MQK ** -0.5
    HEADS_OUT = GH * GDV // P
    QT = S // P
    N = MH * QT
    first_chunk = []
    m = 0
    for n in range(N + 1):
        first_chunk.append(m)
        m += (n % QT) // 4 + 1
    with ExitStack() as ctx:
        sb = lambda n, s, dt=F32: c.sb("ma_" + n, s, dt, ctx=ctx)
        sem = lambda n: c.sem("ma_" + n, ctx)
        q_hi, q_lo = sb("q_hi", [MQK, 2, S], F32R), sb("q_lo", [MQK, 2, S], F32R)
        k_hi, k_lo = sb("k_hi", [MQK, 2, S], F32R), sb("k_lo", [MQK, 2, S], F32R)
        v = sb("v", [P, 2, TT, 2, MV], F32R)
        prob = sb("prob", [P, 3, S])
        diag = sb("diag", [P, 3, P])
        o_low = sb("o_low", [MV, NCOL])
        o_sum = sb("o_sum", [MV, NCOL])
        pT_hi, pT_lo = sb("pT_hi", [P, TT, NCOL], F32R), sb("pT_lo", [P, TT, NCOL], F32R)
        mx, nb, sums, inv = (sb(x, [P, 2]) for x in ("mx", "nb", "sums", "inv"))
        mask_f = sb("mask_f", [1, 2, P])
        mask = sb("mask", [1, 2, P], F32R)
        scores = [ctx.enter_context(nc.psum_tensor(f"ma_scores{i}", [P, S], F32)) for i in range(2)]
        turn_bank = c.banks("ma_turn", ctx, 3)
        o_bank = c.banks("ma_o", ctx, 1)
        loaded = [sem(f"loaded{i}") for i in range(2)]
        mask_ready, scored, max_ready, nb_ready, exp_ready = (
            sem("mask_ready"), sem("scored"), sem("max_ready"), sem("nb_ready"), sem("exp_ready"))
        inv_ready, diag_ready, turned, hi_ready, lo_ready = (
            sem("inv_ready"), sem("diag_ready"), sem("turned"), sem("hi_ready"), sem("lo_ready"))
        x_loaded = sem("x_loaded")
        o_ready, o_low_ready, o_sum_ready, o_hi, o_lo = (
            sem(x) for x in ("o_ready", "o_low_ready", "o_sum_ready", "o_hi", "o_lo"))
        block = ctx.enter_context(nc.Block())

        @block.sync
        def _(sp):
            sp.dma_start(c.H[:], a["x"][0].rearrange("(t p) n -> p t n", p=P)).then_inc(x_loaded, 16)
            for h in range(MH):
                if h >= 2:
                    sp.wait_ge(o_ready, 2 * (h - 1))
                for place, src in ((q_hi[:, h % 2], d["mqk_hi"][0, h]), (q_lo[:, h % 2], d["mqk_lo"][0, h]),
                                   (k_hi[:, h % 2], d["mqk_hi"][1, h]), (k_lo[:, h % 2], d["mqk_lo"][1, h]),
                                   (v[:, h % 2, :, 0], d["mv_hi"][h].rearrange("t p v -> p t v")),
                                   (v[:, h % 2, :, 1], d["mv_lo"][h].rearrange("t p v -> p t v"))):
                    sp.dma_start(place.bitcast(F32), src).then_inc(loaded[h % 2], 16)
            sp.wait_ge(x_loaded, 16)

        @block.gpsimd
        def _(pool):
            nc.gpsimd.memset(mask_f[:], 0.0).then_inc(mask_ready, 1)
            pool.wait_ge(mask_ready, 1)
            nc.gpsimd.memset(mask_f[:, 0, 0:64], -1e30).then_inc(mask_ready, 1)
            nc.gpsimd.memset(mask_f[:, 1, 64:P], 1.0).then_inc(mask_ready, 1)

        @block.tensor
        def _(pe):
            pe.wait_ge(mask_ready, 4)

            def score(n):
                h, qt = divmod(n, QT)
                s = h % 2
                if qt == 0:
                    pe.wait_ge(loaded[s], 96 * (h // 2 + 1))
                if n >= 2:
                    pe.wait_ge(exp_ready, n - 1)
                q = slice(qt * P, (qt + 1) * P)
                keys = (qt + 1) * P
                for at in range(0, keys, NCOL):
                    end = min(at + NCOL, keys)
                    out = scores[n % 2][:, at:end]
                    nc.tensor.matmul(out, q_hi[:, s, q], k_hi[:, s, at:end], start=True, stop=False)
                    nc.tensor.matmul(out, q_hi[:, s, q], k_lo[:, s, at:end], start=False, stop=False)
                    last = nc.tensor.matmul(out, q_lo[:, s, q], k_hi[:, s, at:end], start=False, stop=True)
                last = nc.tensor.matmul(scores[n % 2][:, keys - P:keys], mask[:, 0], mask[:, 1], start=False,
                                        stop=True, skip_group_check=True)
                last.then_inc(scored, 1)

            def turn(n, i):
                qt = n % QT
                if i == 0:
                    pe.wait_ge(diag_ready, n + 1)
                m = first_chunk[n] + i
                if m >= 3:
                    pe.wait_ge(lo_ready, m - 2)
                for j in range(4 * i, min(4 * i + 4, qt + 1)):
                    last = nc.tensor.matmul(turn_bank[m % 3][:, (j % 4) * P:(j % 4 + 1) * P],
                                            prob[:, n % 3, j * P:(j + 1) * P], diag[:, n % 3], start=True, stop=True)
                last.then_inc(turned, 1)

            def values(m):
                h, half = divmod(m, 2)
                pe.wait_ge(lo_ready, first_chunk[4 * m + 4])
                if m:
                    pe.wait_ge(o_sum_ready, m)
                n_k = 4 * half + 4
                for j in range(n_k):
                    at = max(0, j - 4 * half) * P
                    both = v[:, h % 2, j].rearrange("p a v -> p (a v)")
                    nc.tensor.matmul(o_bank[0][:, at:], both, pT_hi[:, j, at:], start=(j == 0), stop=True,
                                     skip_group_check=True)
                    last = nc.tensor.matmul(o_bank[0][0:MV, at:], v[:, h % 2, j, 0], pT_lo[:, j, at:],
                                            start=False, stop=True, skip_group_check=True)
                last.then_inc(o_ready, 1)

            for n in range(3):
                score(n)
            for n in range(N + 1):
                chunks = n % QT // 4 + 1
                if n + 3 < N:
                    score(n + 3)
                if n and n % 4 == 0:
                    values(n // 4 - 1)
                if n < N:
                    turn(n, 0)
                if n < N and chunks == 2:
                    turn(n, 1)

        @block.scalar
        def _(act):
            act.wait_ge(mask_ready, 3)
            nc.scalar.activation(mask[:], mask_f[:], ACT.Copy).then_inc(mask_ready, 1)

            def exp(n):
                keys = (n % QT + 1) * P
                act.wait_ge(nb_ready, n + 1)
                if n >= 3:
                    act.wait_ge(turned, first_chunk[n - 2])
                nc.scalar.activation(prob[:, n % 3, 0:keys], scores[n % 2][:, 0:keys], ACT.Exp, scale=SCALE,
                                     bias=nb[:, n % 2:n % 2 + 1], accum_out=sums[:, n % 2:n % 2 + 1])\
                    .then_inc(exp_ready, 1)

            def high(n):
                qt = n % QT
                q = slice((qt % 4) * P, (qt % 4 + 1) * P)
                for i in range(qt // 4 + 1):
                    m = first_chunk[n] + i
                    j, e = 4 * i, min(4 * i + 4, qt + 1)
                    act.wait_ge(turned, m + 1)
                    nc.scalar.activation(pT_hi[:, j:e, q],
                                         turn_bank[m % 3][:, 0:(e - j) * P].rearrange("p (j q) -> p j q", q=P),
                                         ACT.Copy).then_inc(hi_ready, 1)

            def out(m):
                h, half = divmod(m, 2)
                act.wait_ge(o_ready, m + 1)
                if m:
                    act.wait_ge(o_sum_ready, m)
                nc.scalar.activation(o_low[:], o_bank[0][MV:2 * MV, :], ACT.Copy).then_inc(o_low_ready, 1)
                act.wait_ge(o_sum_ready, m + 1)
                rows = slice(64 * (h % 2), 64 * (h % 2) + 64)
                nc.scalar.activation(c.Xhi[rows, HEADS_OUT + h // 2, half * NCOL:(half + 1) * NCOL], o_sum[:],
                                     ACT.Copy).then_inc(o_hi, 1)

            exp(0)
            exp(1)
            for n in range(N):
                if n + 2 < N:
                    exp(n + 2)
                high(n)
                if n % 4 == 0 and n:
                    out(n // 4 - 1)
            out(N // 4 - 1)

        @block.vector
        def _(dve):
            def row_max(n):
                keys = (n % QT + 1) * P
                i = slice(n % 2, n % 2 + 1)
                dve.wait_ge(scored, n + 1)
                nc.vector.tensor_reduce(out=mx[:, i], in_=scores[n % 2][:, 0:keys], op=ALU.max, axis=AX.X)\
                    .then_inc(max_ready, 1)
                dve.wait_ge(max_ready, n + 1)
                nc.vector.tensor_scalar(nb[:, i], mx[:, i], -SCALE, None, ALU.mult).then_inc(nb_ready, 1)

            def invert(n):
                i = slice(n % 2, n % 2 + 1)
                dve.wait_ge(exp_ready, n + 1)
                nc.vector.reciprocal(inv[:, i], sums[:, i]).then_inc(inv_ready, 1)
                dve.wait_ge(inv_ready, n + 1)
                nc.vector.tensor_scalar(diag[:, n % 3], c.ident[:], inv[:, i], None, ALU.mult).then_inc(diag_ready, 1)

            def low(n):
                qt = n % QT
                q = slice((qt % 4) * P, (qt % 4 + 1) * P)
                for i in range(qt // 4 + 1):
                    m = first_chunk[n] + i
                    j, e = 4 * i, min(4 * i + 4, qt + 1)
                    dve.wait_ge(hi_ready, m + 1)
                    nc.vector.tensor_tensor(pT_lo[:, j:e, q],
                                            turn_bank[m % 3][:, 0:(e - j) * P].rearrange("p (j q) -> p j q", q=P),
                                            pT_hi[:, j:e, q].bitcast(F32), ALU.subtract).then_inc(lo_ready, 1)

            def out(m):
                h, half = divmod(m, 2)
                dve.wait_ge(o_low_ready, m + 1)
                if m:
                    dve.wait_ge(o_lo, m)
                nc.vector.tensor_tensor(o_sum[:], o_bank[0][0:MV, :], o_low[:], ALU.add).then_inc(o_sum_ready, 1)
                dve.wait_ge(o_hi, m + 1)
                rows = slice(64 * (h % 2), 64 * (h % 2) + 64)
                cols = slice(half * NCOL, (half + 1) * NCOL)
                nc.vector.tensor_tensor(c.Xlo[rows, HEADS_OUT + h // 2, cols], o_sum[:],
                                        c.Xhi[rows, HEADS_OUT + h // 2, cols].bitcast(F32), ALU.subtract)\
                    .then_inc(o_lo, 1)

            row_max(0)
            row_max(1)
            invert(0)
            row_max(2)
            invert(1)
            for n in range(N):
                if n + 3 < N:
                    row_max(n + 3)
                if n + 2 < N:
                    invert(n + 2)
                low(n)
                if n % 4 == 0 and n:
                    out(n // 4 - 1)
            out(N // 4 - 1)


def project_into_residual(nc, chip, name, weights, gate=None):
    c = chip
    groups = [[weights[k * P:(k + 1) * P, n * NCOL:(n + 1) * NCOL] for k in range(KT)] for n in range(HALVES)]
    with ExitStack() as ctx:
        result_ready = c.sem(f"{name}_result_ready", ctx)
        added = c.sem(f"{name}_added", ctx)
        gated = c.sem(f"{name}_gated", ctx)
        w = Weights(c, name, ctx, groups, (result_ready, [TT, 2 * TT]))
        gate_sb = c.sb(f"{name}_gate", [P, D], ctx=ctx) if gate is not None else None
        gate_loaded = c.sem(f"{name}_gate_loaded", ctx)
        part = c.sb(f"{name}_part", [P, 2, NCOL], ctx=ctx) if gate is not None else None
        banks = c.banks(f"{name}_ps", ctx)
        outs = [(g, t) for g in range(HALVES) for t in range(TT)]
        block = ctx.enter_context(nc.Block())

        @block.sync
        def _(sp):
            if gate is not None:
                sp.dma_start(gate_sb[:], gate).then_inc(gate_loaded, 16)
            w.load(sp)

        @block.gpsimd
        def _(pool):
            w.split_lo(pool)

        @block.scalar
        def _(act):
            for g in range(HALVES):
                w.split_hi_group(act, g)

        @block.tensor
        def _(pe):
            for n, (g, t) in enumerate(outs):
                if n >= 8:
                    pe.wait_ge(added, n - 7)
                tok = slice(t * P, (t + 1) * P)
                product(nc, banks[n % 8][:],
                        [((c.Xhi[:, k, tok], c.Xlo[:, k, tok]), (w.hi[:, g, k], w.lo[:, g, k])) for k in range(KT)],
                        NCOL, result_ready,
                        (lambda k: pe.wait_ge(w.lo_ready, w.first[g] + k + 1)) if t == 0 else None)

        @block.vector
        def _(dve):
            if gate is not None:
                dve.wait_ge(gate_loaded, 16)
            for n, (g, t) in enumerate(outs):
                cols = slice(g * NCOL, (g + 1) * NCOL)
                dve.wait_ge(result_ready, n + 1)
                src = banks[n % 8][:]
                if gate is not None:
                    nc.vector.tensor_tensor(part[:, n % 2], src, gate_sb[:, cols], ALU.mult).then_inc(gated, 1)
                    dve.wait_ge(gated, n + 1)
                    src = part[:, n % 2]
                nc.vector.tensor_tensor(c.H[:, t, cols], c.H[:, t, cols], src, ALU.add).then_inc(added, 1)


def mlp(nc, chip, a):
    c = chip
    G = D_FF // NCOL
    FT = NCOL // P
    with ExitStack() as ctx:
        sb = lambda n, s, dt=F32: c.sb("mlp_" + n, s, dt, ctx=ctx)
        sem = lambda n: c.sem("mlp_" + n, ctx)
        stage = sb("stage", [P, SLOTS, NCOL])
        w_hi, w_lo = sb("w_hi", [P, 2, KT, NCOL], F32R), sb("w_lo", [P, 2, KT, NCOL], F32R)
        h_hi, h_lo = sb("h_hi", [P, FT, S], F32R), sb("h_lo", [P, FT, S], F32R)
        act_r = sb("act_r", [P, 2, NCOL])
        loaded = [sem(f"loaded{i}") for i in range(SLOTS)]
        w_hi_ready, w_lo_ready = sem("w_hi_ready"), sem("w_lo_ready")
        up_ready, relu_ready, square_ready, h_hi_ready, h_lo_ready = (
            sem("up_ready"), sem("relu_ready"), sem("square_ready"), sem("h_hi_ready"), sem("h_lo_ready"))
        down_ready, added = sem("down_ready"), sem("added")
        up_bank = c.banks("mlp_up", ctx, 3)
        down_bank = c.banks("mlp_down", ctx, 5)
        UP, DOWN = FT * HALVES, TT * HALVES
        block = ctx.enter_context(nc.Block())

        def rows(n):
            g, x = divmod(n, 2 * KT)
            which, k = divmod(x, KT)
            if which == 0:
                return a["w_mlp_up"][0, k * P:(k + 1) * P, g * NCOL:(g + 1) * NCOL]
            j, half = divmod(k, HALVES)
            at = g * NCOL + j * P
            return a["w_mlp_down"][0, at:at + P, half * NCOL:(half + 1) * NCOL]

        @block.sync
        def _(sp):
            for n in range(G * 2 * KT):
                if n >= SLOTS:
                    sp.wait_ge(w_lo_ready, n - SLOTS + 1)
                sp.dma_start(stage[:, n % SLOTS], rows(n)).then_inc(loaded[n % SLOTS], 16)

        @block.gpsimd
        def _(pool):
            for n in range(G * 2 * KT):
                which, k = divmod(n % (2 * KT), KT)
                pool.wait_ge(w_hi_ready, n + 1)
                nc.gpsimd.tensor_tensor(w_lo[:, which, k], stage[:, n % SLOTS], w_hi[:, which, k].bitcast(F32),
                                        ALU.subtract).then_inc(w_lo_ready, 1)

        @block.scalar
        def _(act):
            def split(n):
                g, x = divmod(n, 2 * KT)
                which, k = divmod(x, KT)
                act.wait_ge(loaded[n % SLOTS], 16 * (n // SLOTS + 1))
                if g and k == 0:
                    act.wait_ge(*((up_ready, UP * g) if which == 0 else (down_ready, DOWN * g)))
                nc.scalar.activation(w_hi[:, which, k], stage[:, n % SLOTS], ACT.Copy).then_inc(w_hi_ready, 1)

            for n in range(KT):
                split(n)
            for g in range(G):
                for o in range(UP):
                    n = g * UP + o
                    f, h = divmod(o, HALVES)
                    act.wait_ge(up_ready, n + 1)
                    if n >= 2:
                        act.wait_ge(h_lo_ready, n - 1)
                    nc.scalar.activation(act_r[:, n % 2], up_bank[n % 3][:], ACT.Relu).then_inc(relu_ready, 1)
                    split(g * 2 * KT + KT + o)
                    act.wait_ge(square_ready, n + 1)
                    if g and o == 0:
                        act.wait_ge(down_ready, DOWN * g)
                    nc.scalar.activation(h_hi[:, f, h * NCOL:(h + 1) * NCOL], act_r[:, n % 2], ACT.Copy)\
                        .then_inc(h_hi_ready, 1)
                if g + 1 < G:
                    for k in range(KT):
                        split((g + 1) * 2 * KT + k)

        @block.vector
        def _(dve):
            for g in range(G):
                for o in range(UP):
                    n = g * UP + o
                    f, h = divmod(o, HALVES)
                    dve.wait_ge(relu_ready, n + 1)
                    nc.vector.tensor_tensor(act_r[:, n % 2], act_r[:, n % 2], act_r[:, n % 2], ALU.mult)\
                        .then_inc(square_ready, 1)
                    dve.wait_ge(h_hi_ready, n + 1)
                    nc.vector.tensor_tensor(h_lo[:, f, h * NCOL:(h + 1) * NCOL], act_r[:, n % 2],
                                            h_hi[:, f, h * NCOL:(h + 1) * NCOL].bitcast(F32), ALU.subtract)\
                        .then_inc(h_lo_ready, 1)
                for o in range(DOWN):
                    n = g * DOWN + o
                    t, half = divmod(o, HALVES)
                    cols = slice(half * NCOL, (half + 1) * NCOL)
                    dve.wait_ge(down_ready, n + 1)
                    nc.vector.tensor_tensor(c.H[:, t, cols], c.H[:, t, cols], down_bank[n % 5][:], ALU.add)\
                        .then_inc(added, 1)

        @block.tensor
        def _(pe):
            for g in range(G):
                for o in range(UP):
                    n = g * UP + o
                    f, h = divmod(o, HALVES)
                    if n >= 3:
                        pe.wait_ge(relu_ready, n - 2)
                    product(nc, up_bank[n % 3][:],
                            [((w_hi[:, 0, k, f * P:(f + 1) * P], w_lo[:, 0, k, f * P:(f + 1) * P]),
                              (c.Xhi[:, k, h * NCOL:(h + 1) * NCOL], c.Xlo[:, k, h * NCOL:(h + 1) * NCOL]))
                             for k in range(KT)], NCOL, up_ready,
                            (lambda k: pe.wait_ge(w_lo_ready, g * 2 * KT + k + 1)) if o == 0 else None)
                for o in range(DOWN):
                    n = g * DOWN + o
                    t, half = divmod(o, HALVES)
                    tok = slice(t * P, (t + 1) * P)
                    if o == 0:
                        pe.wait_ge(w_lo_ready, (g + 1) * 2 * KT)
                        pe.wait_ge(h_lo_ready, (g + 1) * UP)
                    if n >= 5:
                        pe.wait_ge(added, n - 4)
                    product(nc, down_bank[n % 5][:],
                            [((h_hi[:, j, tok], h_lo[:, j, tok]),
                              (w_hi[:, 1, HALVES * j + half], w_lo[:, 1, HALVES * j + half]))
                             for j in range(FT)], NCOL, down_ready)


def ple(nc, chip, a):
    c = chip
    PK = 2
    proj, gate_w = a["w_ple_proj"][0], a["w_ple_gate"][0]
    groups = []
    for half in range(HALVES):
        cols = slice(half * NCOL, (half + 1) * NCOL)
        groups.append([proj[k * P:(k + 1) * P, cols] for k in range(PK)])
        groups.append([gate_w[k * P:(k + 1) * P, cols] for k in range(KT)])
    with ExitStack() as ctx:
        sb = lambda n, s, dt=F32: c.sb("ple_" + n, s, dt, ctx=ctx)
        sem = lambda n: c.sem("ple_" + n, ctx)
        gate_ready = sem("gate_ready")
        w = Weights(c, "ple", ctx, groups, (gate_ready, [TT, TT, 2 * TT, 2 * TT]))
        pt = sb("pt", [P, 4, PK * P])
        pT_hi, pT_lo = sb("pT_hi", [P, PK, S], F32R), sb("pT_lo", [P, PK, S], F32R)
        bias = sb("bias", [P, D])
        logit = sb("logit", [P, 2, NCOL])
        banks = c.banks("ple_ps", ctx)
        loaded, bias_loaded = [sem(f"loaded{i}") for i in range(2)], sem("bias_loaded")
        turned, hi_ready, lo_ready = sem("turned"), sem("hi_ready"), sem("lo_ready")
        proj_ready = sem("proj_ready")
        logit_ready, sig_ready, mul_ready, added = sem("logit_ready"), sem("sig_ready"), sem("mul_ready"), sem("added")
        block = ctx.enter_context(nc.Block())

        @block.sync
        def _(sp):
            for h in range(2):
                if h:
                    sp.wait_ge(turned, 2)
                sp.dma_start(pt[:], a["p"][0, 0, h * NCOL:(h + 1) * NCOL, :].rearrange("(t p) n -> p t n", p=P))\
                    .then_inc(loaded[h], 16)
                if h == 0:
                    sp.dma_start(bias[:], a["b_ple_gate"].to_broadcast([P, D])).then_inc(bias_loaded, 16)
            w.load(sp)

        @block.gpsimd
        def _(pool):
            w.split_lo(pool)

        @block.tensor
        def _(pe):
            for h in range(2):
                pe.wait_ge(loaded[h], 16)
                for k in range(PK):
                    for t in range(4):
                        last = nc.tensor.transpose(banks[2 * h + k][:, t * P:(t + 1) * P],
                                                   pt[:, t, k * P:(k + 1) * P], c.ident[:])
                    last.then_inc(turned, 1)
            pe.wait_ge(lo_ready, 4)
            for half in range(HALVES):
                for t in range(TT):
                    n = half * TT + t
                    tok = slice(t * P, (t + 1) * P)
                    if n >= 4:
                        pe.wait_ge(added, n - 3)
                    for g, x, kt, ready, bank in ((2 * half, (pT_hi, pT_lo), PK, proj_ready, 2 * (n % 4)),
                                                  (2 * half + 1, (c.Xhi, c.Xlo), KT, gate_ready, 2 * (n % 4) + 1)):
                        product(nc, banks[bank][:],
                                [((x[0][:, k, tok], x[1][:, k, tok]), (w.hi[:, g % 2, k], w.lo[:, g % 2, k]))
                                 for k in range(kt)], NCOL, ready,
                                (lambda k: pe.wait_ge(w.lo_ready, w.first[g] + k + 1)) if t == 0 else None)

        @block.scalar
        def _(act):
            for n in range(4):
                h, k = divmod(n, PK)
                act.wait_ge(turned, n + 1)
                nc.scalar.activation(pT_hi[:, k, h * NCOL:(h + 1) * NCOL], banks[n][:], ACT.Copy).then_inc(hi_ready, 1)
            w.split_hi_group(act, 0)
            w.split_hi_group(act, 1)
            for n in range(2 * TT):
                act.wait_ge(logit_ready, n + 1)
                nc.scalar.activation(logit[:, n % 2], logit[:, n % 2], ACT.Sigmoid).then_inc(sig_ready, 1)
                if n == TT - 1:
                    w.split_hi_group(act, 2)
                    w.split_hi_group(act, 3)

        @block.vector
        def _(dve):
            for n in range(4):
                h, k = divmod(n, PK)
                dve.wait_ge(hi_ready, n + 1)
                nc.vector.tensor_tensor(pT_lo[:, k, h * NCOL:(h + 1) * NCOL], banks[n][:],
                                        pT_hi[:, k, h * NCOL:(h + 1) * NCOL].bitcast(F32), ALU.subtract)\
                    .then_inc(lo_ready, 1)
            dve.wait_ge(bias_loaded, 16)
            for n in range(2 * TT):
                half, t = divmod(n, TT)
                cols = slice(half * NCOL, (half + 1) * NCOL)
                dve.wait_ge(gate_ready, n + 1)
                nc.vector.tensor_tensor(logit[:, n % 2], banks[2 * (n % 4) + 1][:], bias[:, cols], ALU.add)\
                    .then_inc(logit_ready, 1)
                dve.wait_ge(sig_ready, n + 1)
                dve.wait_ge(proj_ready, n + 1)
                nc.vector.tensor_tensor(logit[:, n % 2], banks[2 * (n % 4)][:], logit[:, n % 2], ALU.mult)\
                    .then_inc(mul_ready, 1)
                dve.wait_ge(mul_ready, n + 1)
                nc.vector.tensor_tensor(c.H[:, t, cols], c.H[:, t, cols], logit[:, n % 2], ALU.add).then_inc(added, 1)


def modulation(nc, chip, a, d):
    c = chip
    MW = 3 * D
    G = MW // NCOL
    with ExitStack() as ctx:
        sb = lambda n, s, dt=F32: c.sb("mod_" + n, s, dt, ctx=ctx)
        sem = lambda n: c.sem("mod_" + n, ctx)
        cond_in, cond = sb("cond_in", [P, KT, 2]), sb("cond", [P, KT, 2])
        w = sb("w", [P, 2, KT, NCOL])
        rowb = sb("rowb", [2, MW])
        row = sb("row", [2, MW])
        ones = sb("ones", [1, P])
        banks = c.banks("mod_ps", ctx)
        cloaded, loaded = sem("cloaded"), [sem(f"loaded{i}") for i in range(2)]
        cond_ready, ones_ready, row_ps, row_ready, turned, wide_ready = (
            sem("cond_ready"), sem("ones_ready"), sem("row_ps"), sem("row_ready"), sem("turned"), sem("wide_ready"))
        done, wide_copied, wide_stored = sem("done"), sem("wide_copied"), sem("wide_stored")
        wide = sb("wide", [P, D])
        block = ctx.enter_context(nc.Block())

        @block.sync
        def _(sp):
            sp.dma_start(cond_in[:, :, 0], a["c_2"][0].rearrange("(k p) -> p k", p=P)).then_inc(cloaded, 16)
            sp.dma_start(cond_in[:, :, 1], a["c_ctx_2"].rearrange("(k p) -> p k", p=P)).then_inc(cloaded, 16)
            sp.dma_start(rowb[:], a["ada_b_2"].to_broadcast([2, MW])).then_inc(cloaded, 16)
            for g in range(G):
                if g >= 2:
                    sp.wait_ge(row_ps, g - 1)
                sp.dma_start(w[:, g % 2], a["ada_w_2"][0, :, g * NCOL:(g + 1) * NCOL]
                             .rearrange("(k p) n -> p k n", p=P)).then_inc(loaded[g % 2], 16)
            sp.wait_ge(wide_copied, HALVES)
            sp.dma_start(d["gate"], wide[:]).then_inc(wide_stored, 16)
            sp.wait_ge(wide_stored, 16)

        @block.gpsimd
        def _(pool):
            nc.gpsimd.memset(ones[:], 1.0).then_inc(ones_ready, 1)

        @block.scalar
        def _(act):
            act.wait_ge(cloaded, 48)
            nc.scalar.activation(cond[:], cond_in[:], ACT.Silu).then_inc(cond_ready, 1)

        @block.tensor
        def _(pe):
            pe.wait_ge(cond_ready, 1)
            for g in range(G):
                pe.wait_ge(loaded[g % 2], 16 * (g // 2 + 1))
                for k in range(KT):
                    last = nc.tensor.matmul(banks[g][0:2, :], cond[:, k, :], w[:, g % 2, k], start=(k == 0),
                                            stop=(k == KT - 1))
                last.then_inc(row_ps, 1)
            pe.wait_ge(row_ready, G)
            pe.wait_ge(ones_ready, 1)
            for j in range(2 * KT):
                last = nc.tensor.transpose(banks[6][:, 2 * j:2 * j + 2], row[:, j * P:(j + 1) * P], c.ident[0:2, 0:2])
            last.then_inc(turned, 1)
            for half in range(HALVES):
                at = 2 * D + half * NCOL
                last = nc.tensor.matmul(banks[half][:], ones[:], row[0:1, at:at + NCOL], start=True, stop=True)
            last.then_inc(wide_ready, 1)

        @block.vector
        def _(dve):
            dve.wait_ge(cloaded, 48)
            for g in range(G):
                cols = slice(g * NCOL, (g + 1) * NCOL)
                dve.wait_ge(row_ps, g + 1)
                nc.vector.tensor_tensor(row[:, cols], banks[g][0:2, :], rowb[:, cols], ALU.add).then_inc(row_ready, 1)
            dve.wait_ge(turned, 1)
            for i in range(2):
                nc.vector.tensor_copy(c.mod_bias[:, i], banks[6][:, i:2 * KT:2]).then_inc(done, 1)
                nc.vector.scalar_tensor_tensor(out=c.mod_gain[:, i], in0=banks[6][:, 2 * KT + i:4 * KT:2], scalar=1.0,
                                               in1=c.gains[:, 3], op0=ALU.add, op1=ALU.mult).then_inc(done, 1)
            dve.wait_ge(wide_ready, 1)
            for half in range(HALVES):
                nc.vector.tensor_copy(wide[:, half * NCOL:(half + 1) * NCOL], banks[half][:]).then_inc(wide_copied, 1)


def differential_project(nc, chip, a, d, ctx_hi, ctx_lo):
    c = chip
    WIN = a["da_w_in_2"][0]
    Q_G, K_G, V_G, Z_G = (0, 1), (2, 3), (4, 5), (6, 7)
    G = 8
    groups = [[WIN[k * P:(k + 1) * P, g * NCOL:(g + 1) * NCOL] for k in range(KT)] for g in range(G)]
    tiles = {g: TT + CT if g in K_G + V_G else TT for g in range(G)}
    outs = [(g, o) for g in range(G) for o in range(tiles[g])]
    done_at = [sum(tiles[x] for x in range(g + 1)) for g in range(G)]
    rope = [n for n, (g, o) in enumerate(outs) if g in Q_G + K_G]
    R = len(rope)
    BANKS = 4
    with ExitStack() as ctx:
        sb = lambda n, s, dt=F32: c.sb("dp_" + n, s, dt, ctx=ctx)
        sem = lambda n: c.sem("dp_" + n, ctx)
        result_ready = sem("result_ready")
        w = Weights(c, "dp", ctx, groups, (result_ready, done_at))
        cos, sin = sb("cos", [P, TT, 32]), sb("sin", [P, TT, 32])
        tmp = sb("tmp", [P, 4, NCOL // 2])
        turned_in = sb("turned_in", [P, 2, 8, 2, DD])
        out_hi, out_lo = sb("out_hi", [P, 2 * NCOL], F32R), sb("out_lo", [P, 2 * NCOL], F32R)
        banks = c.banks("dp_ps", ctx, BANKS)
        turn = [ctx.enter_context(nc.psum_tensor(f"dp_turn{i}", [P, 2 * NCOL], F32)) for i in range(2)]
        loaded = sem("loaded")
        dve_step, doubled, roped, turned, hi_ready, lo_ready, stored = (
            sem("dve_step"), sem("doubled"), sem("roped"), sem("turned"), sem("hi_ready"), sem("lo_ready"), sem("stored"))
        block = ctx.enter_context(nc.Block())
        N = len(outs)
        stores_upto = [0]
        for g, o in outs:
            stores_upto.append(stores_upto[-1] + (1 if g in Q_G + Z_G else 2))

        @block.sync
        def _(sp):
            sp.dma_start(cos[:], a["da_cos"].rearrange("(t p) n -> p t n", p=P)).then_inc(loaded, 16)
            sp.dma_start(sin[:], a["da_sin"].rearrange("(t p) n -> p t n", p=P)).then_inc(loaded, 16)
            w.load(sp)

        @block.gpsimd
        def _(pool):
            lo_at = 0
            for n in range(N):
                g, o = outs[n]
                while lo_at < len(w.chunks) and lo_at < w.first[min(g + 1, G - 1)] + min(o + 1, KT):
                    w.split_lo_chunk(pool, lo_at)
                    lo_at += 1
                if n < R:
                    pool.wait_ge(roped, n + 1)
                    nc.gpsimd.tensor_copy(turned_in[:, n % 2, :, 1], turned_in[:, n % 2, :, 0]).then_inc(doubled, 1)

        @block.tensor
        def _(pe):
            def turns(n):
                i = n % 2
                pe.wait_ge(doubled, n + 1)
                if n >= 2:
                    pe.wait_ge(lo_ready, n - 1)
                for m in range(8):
                    x = turned_in[:, i, m].rearrange("p a b -> p (a b)")
                    last = nc.tensor.transpose(turn[i][:, m * P:(m + 1) * P], x, c.ident[:])
                last.then_inc(turned, 1)

            for n, (g, o) in enumerate(outs):
                if n >= BANKS:
                    m = n - BANKS
                    pe.wait_ge(*((roped, m + 1) if m < R else (lo_ready, m + 1)))
                terms = []
                xs, tile = ((c.Xhi, c.Xlo), o) if o < TT else ((ctx_hi, ctx_lo), o - TT)
                for k in range(KT):
                    ww = w.hi[:, g % 2, k], w.lo[:, g % 2, k]
                    if g in Z_G:
                        f, h = divmod(o, HALVES)
                        terms.append((tuple(y[:, f * P:(f + 1) * P] for y in ww),
                                      tuple(y[:, k, h * NCOL:(h + 1) * NCOL] for y in xs)))
                    else:
                        terms.append((tuple(y[:, k, tile * P:(tile + 1) * P] for y in xs), ww))
                product(nc, banks[n % BANKS][:], terms, NCOL, result_ready,
                        (lambda k: pe.wait_ge(w.lo_ready, w.first[g] + k + 1)) if o == 0 else None)
                if 1 <= n <= R:
                    turns(n - 1)

        def places(n):
            g, o = outs[n]
            hs = slice(4 * (g % 2), 4 * (g % 2) + 4)
            if g in Q_G:
                return [(d["dq"][hs, :, :, o * P:(o + 1) * P].rearrange("h z p s -> p h z s"), 0)]
            if g in K_G:
                return [(d[x][hs, :, :, o * P:(o + 1) * P].rearrange("h z p s -> p h z s"), i)
                        for i, x in enumerate(("dk_hi", "dk_lo"))]
            if g in V_G:
                return [(d[x][hs, :, o, :].rearrange("h p n -> p h n"), i) for i, x in enumerate(("dv_hi", "dv_lo"))]
            f, h = divmod(o, HALVES)
            return [(d["dz"][4 * (g % 2) + f, :, h * NCOL:(h + 1) * NCOL], 0)]

        @block.scalar
        def _(act):
            def store(n):
                g, o = outs[n]
                act.wait_ge(lo_ready, n + 1)
                for place, which in places(n):
                    t = (out_hi, out_lo)[which]
                    if g in Q_G + K_G:
                        src = t[:].bitcast(F32).rearrange("p (h z s) -> p h z s", h=4, z=2)
                        for z in range(2):
                            act.dma_start(place[:, :, z], src[:, :, z]).then_inc(stored, 16)
                    elif g in V_G:
                        act.dma_start(place, t[:, 0:NCOL].bitcast(F32).rearrange("p (h n) -> p h n", h=4)).then_inc(stored, 16)
                    else:
                        act.dma_start(place, t[:, 0:NCOL].bitcast(F32)).then_inc(stored, 16)

            def n_stores(n):
                g, _ = outs[n]
                return {True: 2, False: 1}[g in Q_G + K_G] * len(places(n))

            total = [0]
            w.split_hi_group(act, 0)
            for n, (g, o) in enumerate(outs):
                if g + 1 < G and o < KT:
                    w.split_hi(act, w.first[g + 1] + o)
                if n:
                    store(n - 1)
                    total[0] += n_stores(n - 1)
                    act.wait_ge(stored, 16 * total[0])
                if g in Q_G + K_G:
                    act.wait_ge(turned, n + 1)
                    nc.scalar.activation(out_hi[:], turn[n % 2][:], ACT.Copy).then_inc(hi_ready, 1)
                else:
                    act.wait_ge(result_ready, n + 1)
                    nc.scalar.activation(out_hi[:, 0:NCOL] if g in V_G else out_hi[:, 0:NCOL].bitcast(F32),
                                         banks[n % BANKS][:], ACT.Copy if g in V_G else ACT.Silu).then_inc(hi_ready, 1)
            store(N - 1)
            total[0] += n_stores(N - 1)
            act.wait_ge(stored, 16 * total[0])

        @block.vector
        def _(dve):
            dve.wait_ge(loaded, 32)
            steps = [0]

            def step(ins):
                steps[0] += 1
                ins.then_inc(dve_step, 1)
                dve.wait_ge(dve_step, steps[0])

            def low(n):
                g, o = outs[n]
                dve.wait_ge(hi_ready, n + 1)
                if g in Q_G:
                    nc.vector.tensor_tensor(out_hi[64:P, :], turn[n % 2][64:P, :], out_hi[64:P, :].bitcast(F32),
                                            ALU.subtract).then_inc(lo_ready, 1)
                elif g in K_G:
                    nc.vector.tensor_tensor(out_lo[:], turn[n % 2][:], out_hi[:].bitcast(F32), ALU.subtract)\
                        .then_inc(lo_ready, 1)
                elif g in V_G:
                    nc.vector.tensor_tensor(out_lo[:, 0:NCOL], banks[n % BANKS][:], out_hi[:, 0:NCOL].bitcast(F32),
                                            ALU.subtract).then_inc(lo_ready, 1)
                else:
                    nc.vector.memset(tmp[0:1, 0, 0:1], 0.0).then_inc(lo_ready, 1)

            for n, (g, o) in enumerate(outs):
                if n < R:
                    dve.wait_ge(result_ready, n + 1)
                    dst = turned_in[:, n % 2, :, 0]
                    if n >= 2:
                        dve.wait_ge(turned, n - 1)
                    if o < TT:
                        x = banks[n % BANKS][:].rearrange("p (m a b q) -> p m a b q", a=2, b=2, q=16)
                        y = dst.rearrange("p m (a b q) -> p m a b q", a=2, b=2, q=16)
                        cs, sn = (t[:, o].rearrange("p (a q) -> p a q", a=2).unsqueeze(1).to_broadcast([P, 8, 2, 16])
                                  for t in (cos, sin))
                        if n:
                            dve.wait_ge(roped, n)
                        for i, (f0, f1, op) in enumerate(((cs, sn, ALU.subtract), (sn, cs, ALU.add))):
                            u, v = (tmp[:, 2 * i + j].rearrange("p (m a q) -> p m a q", a=2, q=16) for j in range(2))
                            nc.vector.tensor_tensor(u, x[:, :, :, 0], f0, ALU.mult).then_inc(dve_step, 1)
                            steps[0] += 1
                            step(nc.vector.tensor_tensor(v, x[:, :, :, 1], f1, ALU.mult))
                            last = nc.vector.tensor_tensor(y[:, :, :, i], u, v, op)
                            last.then_inc(*((roped, 1) if i else (dve_step, 1)))
                            steps[0] += 1 - i
                    else:
                        nc.vector.tensor_copy(dst, banks[n % BANKS][:].rearrange("p (m n) -> p m n", m=8)).then_inc(roped, 1)
                    if n:
                        low(n - 1)
                    if n == R - 1:
                        low(n)
                else:
                    low(n)


def differential_attention(nc, chip, a, d):
    c = chip
    K = S + CTX
    KB = K // P
    QT = S // P
    N = DH * QT
    SCALE = DD ** -0.5
    CHUNKS = -(-KB // 4)
    SHARE = 6 * P
    PIECES = [(at, min(at + NCOL, K)) for at in range(0, K, NCOL)]
    with ExitStack() as ctx:
        sb = lambda n, s, dt=F32: c.sb("da_" + n, s, dt, ctx=ctx)
        sem = lambda n: c.sem("da_" + n, ctx)
        q = sb("q", [P, 2, 2, S], F32R)
        k_hi, k_lo = sb("k_hi", [P, 2, 2, K], F32R), sb("k_lo", [P, 2, 2, K], F32R)
        v_hi, v_lo = sb("v_hi", [P, 2, KB, P], F32R), sb("v_lo", [P, 2, KB, P], F32R)
        prob = sb("prob", [P, 2, 2, K])
        aT_hi, aT_lo = sb("aT_hi", [P, KB, NCOL], F32R), sb("aT_lo", [P, KB, NCOL], F32R)
        mx, nb, sums, inv = (sb(x, [P, 2, 2]) for x in ("mx", "nb", "sums", "inv"))
        lam_in, lam_prod = sb("lam_in", [P, 2, 2, DD]), sb("lam_prod", [P, 2, DD])
        lam_sum, lam_exp, lam = sb("lam_sum", [P, 2]), sb("lam_exp", [P, 2]), sb("lam", [P, 1])
        o_sb = sb("o_sb", [P, 2, NCOL])
        ratio, diag = sb("ratio", [P, 2, 1]), sb("diag", [P, 2, P])
        scores = [ctx.enter_context(nc.psum_tensor(f"da_scores{i}", [P, 3 * NCOL], F32)) for i in range(2)]
        turn_bank = c.banks("da_turn", ctx, 2)
        loaded = [sem(f"loaded{i}") for i in range(2)]
        lam_loaded, lam_step, lam_summed, lam_exped = (
            sem("lam_loaded"), sem("lam_step"), sem("lam_summed"), sem("lam_exped"))
        scored, max_ready, nb_ready, exp_ready = sem("scored"), sem("max_ready"), sem("nb_ready"), sem("exp_ready")
        inv_ready, ratio_ready, diag_ready, prob_ready, rest_scaled, rest_ready = (
            sem(x) for x in ("inv_ready", "ratio_ready", "diag_ready", "prob_ready", "rest_scaled", "rest_ready"))
        turned, hi_ready, lo_ready = sem("turned"), sem("hi_ready"), sem("lo_ready")
        o_ready, o_copied = sem("o_ready"), sem("o_copied")
        o_stored = [sem(f"o_stored{i}") for i in range(2)]
        block = ctx.enter_context(nc.Block())

        @block.sync
        def _(sp):
            sp.dma_start(lam_in[:, 0], a["da_lam_q_2"].to_broadcast([P, 2, DD])).then_inc(lam_loaded, 16)
            sp.dma_start(lam_in[:, 1], a["da_lam_k_2"].to_broadcast([P, 2, DD])).then_inc(lam_loaded, 16)
            for h in range(DH):
                s = h % 2
                if h >= 2:
                    sp.wait_ge(o_ready, 2 * (h - 1))
                for place, src in ((q[:, s], d["dq"][h].rearrange("z p s -> p z s")),
                                   (k_hi[:, s], d["dk_hi"][h].rearrange("z p s -> p z s")),
                                   (k_lo[:, s], d["dk_lo"][h].rearrange("z p s -> p z s")),
                                   (v_hi[:, s], d["dv_hi"][h]), (v_lo[:, s], d["dv_lo"][h])):
                    sp.dma_start(place.bitcast(F32), src).then_inc(loaded[s], 16)

        def chunk_bank(m):
            g, k = divmod(m, 4 * CHUNKS)
            return turn_bank[(g + max(k, 2)) % 2]

        def wait_bank_read(pe, m):
            g, k = divmod(m, 4 * CHUNKS)
            if k == 3:
                if g:
                    pe.wait_ge(o_copied, g)
            elif m:
                pe.wait_ge(lo_ready, m if k < 3 else m - 1)

        @block.tensor
        def _(pe):
            def score(n, z):
                h, qt = divmod(n, QT)
                s = h % 2
                if qt == 0 and z == 0:
                    pe.wait_ge(loaded[s], 80 * (h // 2 + 1))
                if n:
                    pe.wait_ge(exp_ready, 2 * (n - 1) + z + 1)
                for at, end in PIECES:
                    for i, k in enumerate((k_hi, k_lo)):
                        last = nc.tensor.matmul(scores[z][:, at:end], q[:, s, z, qt * P:(qt + 1) * P],
                                                k[:, s, z, at:end], start=(i == 0), stop=(i == 1))
                last.then_inc(scored, 1)

            def turn(n, i):
                if i == 0:
                    pe.wait_ge(prob_ready, n + 1)
                if (i + 1) * NCOL > SHARE >= i * NCOL:
                    pe.wait_ge(rest_ready, n + 1)
                bank = chunk_bank(CHUNKS * n + i)
                wait_bank_read(pe, CHUNKS * n + i)
                for j in range(4 * i, min(4 * i + 4, KB)):
                    last = nc.tensor.matmul(bank[:, (j % 4) * P:(j % 4 + 1) * P],
                                            prob[:, n % 2, 0, j * P:(j + 1) * P], diag[:, n % 2],
                                            start=True, stop=True)
                last.then_inc(turned, 1)

            def values(n, i):
                m = n // 4
                v = m // 2 % 2
                pe.wait_ge(lo_ready, CHUNKS * n + i + 1)
                if i == 0:
                    pe.wait_ge(lo_ready, CHUNKS * n + 2)
                for j in range(4 * i, min(4 * i + 4, KB)):
                    for x, y in ((v_hi, aT_hi), (v_hi, aT_lo), (v_lo, aT_hi)):
                        last = nc.tensor.matmul(turn_bank[m % 2][:], x[:, v, j], y[:, j],
                                                start=(j == 0 and x is v_hi and y is aT_hi),
                                                stop=(j == KB - 1 and x is v_lo))
                if i == CHUNKS - 1:
                    last.then_inc(o_ready, 1)

            for n in range(2):
                score(n, 0)
                score(n, 1)
            for n in range(N + 1):
                for i in range(CHUNKS):
                    if n % 4 == 0 and n:
                        values(n - 1, i)
                    if n < N:
                        turn(n, i)
                    if n + 2 < N and i < 2:
                        score(n + 2, i)

        @block.scalar
        def _(act):
            act.wait_ge(lam_summed, 1)
            nc.scalar.activation(lam_exp[:], lam_sum[:], ACT.Exp).then_inc(lam_exped, 1)

            def exp(n, z):
                act.wait_ge(nb_ready, 2 * n + z + 1)
                if n >= 2:
                    act.wait_ge(turned, CHUNKS * (n - 1))
                nc.scalar.activation(prob[:, n % 2, z], scores[z][:, 0:K], ACT.Exp, scale=SCALE,
                                     bias=nb[:, n % 2, z:z + 1], accum_out=sums[:, n % 2, z:z + 1])\
                    .then_inc(exp_ready, 1)

            def high(n, i):
                qs = slice((n % 4) * P, (n % 4 + 1) * P)
                j, e = 4 * i, min(4 * i + 4, KB)
                act.wait_ge(turned, CHUNKS * n + i + 1)
                nc.scalar.activation(aT_hi[:, j:e, qs],
                                     chunk_bank(CHUNKS * n + i)[:, 0:(e - j) * P]
                                     .rearrange("p (j q) -> p j q", q=P), ACT.Copy).then_inc(hi_ready, 1)

            def out(m):
                act.wait_ge(o_ready, m + 1)
                if m >= 2:
                    act.wait_ge(o_stored[m % 2], 16 * (m // 2))
                nc.scalar.activation(o_sb[:, m % 2], turn_bank[m % 2][:], ACT.Copy)\
                    .then_inc(o_copied, 1)

            exp(0, 0)
            exp(0, 1)
            for n in range(N):
                if n + 1 < N:
                    exp(n + 1, 0)
                high(n, 0)
                if n + 1 < N:
                    exp(n + 1, 1)
                high(n, 1)
                if n % 4 == 0 and n:
                    out(n // 4 - 1)
                high(n, 2)
            out(N // 4 - 1)

        @block.gpsimd
        def _(pool):
            for n in range(N + 1):
                if n < N:
                    i = n % 2
                    pool.wait_ge(ratio_ready, n + 1)
                    p0, p1 = prob[:, i, 0, SHARE:], prob[:, i, 1, SHARE:]
                    nc.gpsimd.tensor_tensor(p1, p1, ratio[:, i].to_broadcast([P, K - SHARE]), ALU.mult)\
                        .then_inc(rest_scaled, 1)
                    pool.wait_ge(rest_scaled, n + 1)
                    nc.gpsimd.tensor_tensor(p0, p0, p1, ALU.add).then_inc(rest_ready, 1)
                if n % 4 == 3 and n > 4 or n == N:
                    m = n // 4 - 1
                    h, half = divmod(m, 2)
                    pool.wait_ge(o_copied, m + 1)
                    pool.dma_start(d["do"][h, :, half * NCOL:(half + 1) * NCOL], o_sb[:, m % 2])\
                        .then_inc(o_stored[m % 2], 16)
            for i in range(2):
                pool.wait_ge(o_stored[i], 16 * (N // 8))

        @block.vector
        def _(dve):
            dve.wait_ge(lam_loaded, 32)
            nc.vector.tensor_tensor(lam_prod[:], lam_in[:, 0], lam_in[:, 1], ALU.mult).then_inc(lam_step, 1)
            dve.wait_ge(lam_step, 1)
            nc.vector.tensor_reduce(out=lam_sum[:], in_=lam_prod[:], op=ALU.add, axis=AX.X).then_inc(lam_summed, 1)
            dve.wait_ge(lam_exped, 1)
            nc.vector.tensor_tensor(lam[:], lam_exp[:, 1:2], lam_exp[:, 0:1], ALU.subtract).then_inc(lam_step, 1)
            dve.wait_ge(lam_step, 2)
            nc.vector.tensor_scalar(lam[:], lam[:], -LAMBDA_INIT, None, ALU.add).then_inc(lam_step, 1)
            dve.wait_ge(lam_step, 3)

            def row_max(n, z):
                dve.wait_ge(scored, 2 * n + z + 1)
                nc.vector.tensor_reduce(out=mx[:, n % 2, z:z + 1], in_=scores[z][:, 0:K], op=ALU.max, axis=AX.X)\
                    .then_inc(max_ready, 1)
                dve.wait_ge(max_ready, 2 * n + z + 1)
                nc.vector.tensor_scalar(nb[:, n % 2, z:z + 1], mx[:, n % 2, z:z + 1], -SCALE, None, ALU.mult)\
                    .then_inc(nb_ready, 1)

            def combine(n):
                i = n % 2
                dve.wait_ge(exp_ready, 2 * n + 2)
                nc.vector.reciprocal(inv[:, i], sums[:, i]).then_inc(inv_ready, 1)
                dve.wait_ge(inv_ready, n + 1)
                nc.vector.scalar_tensor_tensor(out=ratio[:, i], in0=sums[:, i, 0:1], scalar=lam[:],
                                               in1=inv[:, i, 1:2], op0=ALU.mult, op1=ALU.mult)\
                    .then_inc(ratio_ready, 1)
                nc.vector.tensor_scalar(diag[:, i], c.ident[:], inv[:, i, 0:1], None, ALU.mult)\
                    .then_inc(diag_ready, 1)
                dve.wait_ge(ratio_ready, n + 1)
                nc.vector.scalar_tensor_tensor(out=prob[:, i, 0, :SHARE], in0=prob[:, i, 1, :SHARE], scalar=ratio[:, i],
                                               in1=prob[:, i, 0, :SHARE], op0=ALU.mult, op1=ALU.add)\
                    .then_inc(prob_ready, 1)

            def low(n, i):
                qs = slice((n % 4) * P, (n % 4 + 1) * P)
                j, e = 4 * i, min(4 * i + 4, KB)
                dve.wait_ge(hi_ready, CHUNKS * n + i + 1)
                nc.vector.tensor_tensor(aT_lo[:, j:e, qs],
                                        chunk_bank(CHUNKS * n + i)[:, 0:(e - j) * P]
                                        .rearrange("p (j q) -> p j q", q=P),
                                        aT_hi[:, j:e, qs].bitcast(F32), ALU.subtract).then_inc(lo_ready, 1)

            row_max(0, 0)
            row_max(0, 1)
            combine(0)
            row_max(1, 0)
            row_max(1, 1)
            for n in range(N):
                low(n, 0)
                if n + 2 < N:
                    row_max(n + 2, 0)
                low(n, 1)
                if n + 1 < N:
                    combine(n + 1)
                if n + 2 < N:
                    row_max(n + 2, 1)
                low(n, 2)


def head_norm_project(nc, chip, a, d):
    c = chip
    SUB_EPS = 1e-5
    QT2 = TT // HALVES
    weights = a["da_w_out_2"][0]
    groups = [[weights[k * P:(k + 1) * P, n * NCOL:(n + 1) * NCOL] for k in range(KT)] for n in range(HALVES)]
    outs = [(half, g, half * QT2 + t) for half in range(HALVES) for g in range(HALVES) for t in range(QT2)]
    PER = len(outs) // HALVES
    EARLY = 3
    BANKS = 5
    with ExitStack() as ctx:
        sb = lambda n, s, dt=F32: c.sb("hp_" + n, s, dt, ctx=ctx)
        sem = lambda n: c.sem("hp_" + n, ctx)
        w = Weights(c, "hp", ctx, groups)
        o, z, sq = sb("o", [P, DH, NCOL]), sb("z", [P, 2, NCOL]), sb("sq", [P, 2, NCOL])
        rs = sb("rs", [DH, NCOL])
        eps = sb("eps", [DH, 1])
        gain = sb("gain", [P, 1])
        band = sb("band", [P, 2 * DH])
        rows = sb("rows", [DH, DH, P])
        gate, part = sb("gate", [P, D]), sb("part", [P, NCOL])
        sum_bank = c.banks("hp_sum", ctx, 1)[0]
        wide_bank = c.banks("hp_wide", ctx, 2)
        banks = c.banks("hp_ps", ctx, BANKS)
        gain_loaded, gain_ready, gate_loaded, band_ready, eps_ready, rows_ready = (
            sem(x) for x in ("gain_loaded", "gain_ready", "gate_loaded", "band_ready", "eps_ready", "rows_ready"))
        o_loaded = [sem(f"o_loaded{h}") for h in range(DH)]
        z_loaded = [sem(f"z_loaded{i}") for i in range(2)]
        squared, summed, logged, rstd_ready, wide_ready, scaled, y_ready, hi_ready, lo_ready = (
            sem(x) for x in ("squared", "summed", "logged", "rstd_ready", "wide_ready", "scaled", "y_ready",
                             "hi_ready", "lo_ready"))
        result_ready, gated, added = sem("result_ready"), sem("gated"), sem("added")
        block = ctx.enter_context(nc.Block())

        @block.sync
        def _(sp):
            def load_o(half, h):
                if half:
                    sp.wait_ge(lo_ready, h + 1)
                sp.dma_start(o[:, h], d["do"][h, :, half * NCOL:(half + 1) * NCOL]).then_inc(o_loaded[h], 16)

            def load_z(n):
                half, h = divmod(n, DH)
                if n >= 2:
                    sp.wait_ge(y_ready, n - 1)
                sp.dma_start(z[:, n % 2], d["dz"][h, :, half * NCOL:(half + 1) * NCOL]).then_inc(z_loaded[n % 2], 16)

            sp.dma_start(gain[:], a["da_subln_gain_2"][0].rearrange("(p a) -> p a", a=1)).then_inc(gain_loaded, 16)
            for h in range(DH):
                load_o(0, h)
            load_z(0)
            load_z(1)
            for n in range(SLOTS):
                w.load_chunk(sp, n)
            sp.dma_start(gate[:], d["gate"]).then_inc(gate_loaded, 16)
            for h in range(DH):
                load_z(h + 2)
                w.load_chunk(sp, SLOTS + h)
                load_o(1, h)
            for n in range(SLOTS + DH, len(w.chunks)):
                w.load_chunk(sp, n)
            for n in range(DH + 2, 2 * DH):
                load_z(n)

        @block.gpsimd
        def _(pool):
            nc.gpsimd.memset(band[:], 0.0).then_inc(band_ready, 1)
            pool.wait_ge(band_ready, 1)
            nc.gpsimd.memset(band[:, DH:DH + 1], 1.0).then_inc(band_ready, 1)
            nc.gpsimd.memset(eps[:], SUB_EPS).then_inc(eps_ready, 1)

            def by_z(n):
                pool.wait_ge(scaled, n + 1)
                pool.wait_ge(z_loaded[n % 2], 16 * (n // 2 + 1))
                nc.gpsimd.tensor_tensor(o[:, n % DH], o[:, n % DH], z[:, n % 2], ALU.mult).then_inc(y_ready, 1)

            for n in range(SLOTS):
                w.split_lo_chunk(pool, n)
            for h in range(DH):
                by_z(h)
                w.split_lo_chunk(pool, SLOTS + h)
            for n in range(SLOTS + DH, len(w.chunks)):
                w.split_lo_chunk(pool, n)
            for h in range(DH):
                by_z(DH + h)

        @block.scalar
        def _(act):
            def square(n):
                half, h = divmod(n, DH)
                act.wait_ge(o_loaded[h], 16 * (half + 1))
                if n >= 2:
                    act.wait_ge(summed, n - 1)
                nc.scalar.activation(sq[:, n % 2], o[:, h], ACT.Square).then_inc(squared, 1)

            def high(n):
                half, h = divmod(n, DH)
                act.wait_ge(y_ready, n + 1)
                nc.scalar.activation(c.Xhi[:, h, half * NCOL:(half + 1) * NCOL], o[:, h], ACT.Copy)\
                    .then_inc(hi_ready, 1)

            def rstd(half):
                act.wait_ge(summed, DH * (half + 1))
                if half:
                    act.wait_ge(wide_ready, DH)
                nc.scalar.activation(rs[:], sum_bank[0:DH, :], ACT.Ln, scale=1.0 / P, bias=eps[:])\
                    .then_inc(logged, 1)
                act.wait_ge(logged, half + 1)
                nc.scalar.activation(rs[:], rs[:], ACT.Exp, scale=-0.5).then_inc(rstd_ready, 1)

            for h in range(DH):
                square(h)
            act.wait_ge(eps_ready, 1)
            rstd(0)
            for n in range(SLOTS):
                w.split_hi(act, n)
            for h in range(DH):
                high(h)
                w.split_hi(act, SLOTS + h)
            for n in range(SLOTS + DH, len(w.chunks)):
                w.split_hi(act, n)
            for h in range(DH):
                square(DH + h)
            rstd(1)
            for h in range(DH):
                high(DH + h)

        @block.tensor
        def _(pe):
            def sums(half):
                if half:
                    pe.wait_ge(logged, 1)
                for h in range(DH):
                    pe.wait_ge(squared, half * DH + h + 1)
                    nc.tensor.matmul(sum_bank[0:DH, :], band[:, DH - h:2 * DH - h], sq[:, h % 2],
                                     start=(h == 0), stop=(h == DH - 1)).then_inc(summed, 1)

            def wide(n):
                half, h = divmod(n, DH)
                pe.wait_ge(rstd_ready, half + 1)
                if n >= 2:
                    pe.wait_ge(scaled, n - 1)
                nc.tensor.matmul(wide_bank[n % 2][:], rows[:, h, :], rs[:], start=True, stop=True)\
                    .then_inc(wide_ready, 1)

            def result(n):
                half, g, t = outs[n]
                if n % PER == 0:
                    pe.wait_ge(lo_ready, DH * (half + 1))
                if n >= BANKS:
                    pe.wait_ge(added, n - BANKS + 1)
                tok = slice(t * P, (t + 1) * P)
                product(nc, banks[n % BANKS][:],
                        [((c.Xhi[:, k, tok], c.Xlo[:, k, tok]), (w.hi[:, g, k], w.lo[:, g, k])) for k in range(KT)],
                        NCOL, result_ready,
                        (lambda k: pe.wait_ge(w.lo_ready, w.first[g] + k + 1)) if n < PER and t == 0 else None)

            pe.wait_ge(band_ready, 2)
            sums(0)
            pe.wait_ge(rows_ready, 1)
            for h in range(DH):
                wide(h)
            result(0)
            result(1)
            sums(1)
            result(2)
            for h in range(DH):
                wide(DH + h)
                if h % 2:
                    result(EARLY + h // 2)
            for n in range(EARLY + DH // 2, len(outs)):
                result(n)

        @block.vector
        def _(dve):
            dve.wait_ge(gain_loaded, 16)
            nc.vector.tensor_scalar(gain[:], gain[:], 1.0 - LAMBDA_INIT, None, ALU.mult).then_inc(gain_ready, 1)
            nc.vector.tensor_copy(rows[:], c.ident[0:DH, 0:DH].unsqueeze(2).to_broadcast([DH, DH, P]))\
                .then_inc(rows_ready, 1)
            dve.wait_ge(gain_ready, 1)

            def scale(n):
                dve.wait_ge(wide_ready, n + 1)
                nc.vector.scalar_tensor_tensor(out=o[:, n % DH], in0=o[:, n % DH], scalar=gain[:],
                                               in1=wide_bank[n % 2][:], op0=ALU.mult, op1=ALU.mult)\
                    .then_inc(scaled, 1)

            def low(n):
                half, h = divmod(n, DH)
                cols = slice(half * NCOL, (half + 1) * NCOL)
                dve.wait_ge(hi_ready, n + 1)
                nc.vector.tensor_tensor(c.Xlo[:, h, cols], o[:, h], c.Xhi[:, h, cols].bitcast(F32), ALU.subtract)\
                    .then_inc(lo_ready, 1)

            def add(n):
                half, g, t = outs[n]
                cols = slice(g * NCOL, (g + 1) * NCOL)
                dve.wait_ge(result_ready, n + 1)
                if n:
                    dve.wait_ge(added, n)
                nc.vector.tensor_tensor(part[:], banks[n % BANKS][:], gate[:, cols], ALU.mult).then_inc(gated, 1)
                dve.wait_ge(gated, n + 1)
                nc.vector.tensor_tensor(c.H[:, t, cols], c.H[:, t, cols], part[:], ALU.add).then_inc(added, 1)

            for h in range(DH):
                scale(h)
                if h:
                    low(h - 1)
            low(DH - 1)
            dve.wait_ge(gate_loaded, 16)
            add(0)
            add(1)
            add(2)
            for h in range(DH):
                scale(DH + h)
                if h:
                    low(DH + h - 1)
                if h % 2:
                    add(EARLY + h // 2)
            low(2 * DH - 1)
            for n in range(EARLY + DH // 2, len(outs)):
                add(n)


def final_norm(nc, chip, a, out):
    c = chip
    with ExitStack() as ctx:
        sb = lambda n, s, dt=F32: c.sb("fn_" + n, s, dt, ctx=ctx)
        sem = lambda n: c.sem("fn_" + n, ctx)
        gain, junk, ss, ms, rs = (sb("gain", [P, D]), sb("junk", [P, D]), sb("ss", [P, TT]), sb("ms", [P, TT]),
                                  sb("rs", [P, TT]))
        loaded, ss_ready, ms_ready, rs_ready, y_ready = (
            sem(x) for x in ("loaded", "ss_ready", "ms_ready", "rs_ready", "y_ready"))
        block = ctx.enter_context(nc.Block())

        @block.scalar
        def _(act):
            for t in range(TT):
                if t:
                    act.wait_ge(ss_ready, t)
                nc.scalar.activation(junk[:], c.H[:, t, :], ACT.Square, accum_out=ss[:, t:t + 1]).then_inc(ss_ready, 1)

        @block.gpsimd
        def _(pool):
            for h in range(2):
                cols = slice(4 * h, 4 * h + 4)
                pool.wait_ge(ss_ready, 4 * h + 4)
                nc.gpsimd.tensor_scalar(ms[:, cols], ss[:, cols], 1.0 / D, EPS, ALU.mult, ALU.add).then_inc(ms_ready, 1)
                pool.wait_ge(ms_ready, h + 1)
                nc.gpsimd.tensor_tensor(rs[:, cols], ms[:, cols], c.minus_half[:, 0:4], ALU.pow).then_inc(rs_ready, 1)

        @block.vector
        def _(dve):
            dve.wait_ge(loaded, 16)
            for t in range(TT):
                dve.wait_ge(rs_ready, t // 4 + 1)
                nc.vector.scalar_tensor_tensor(out=c.H[:, t, :], in0=c.H[:, t, :], scalar=rs[:, t:t + 1], in1=gain[:],
                                               op0=ALU.mult, op1=ALU.mult).then_inc(y_ready, 1)

        @block.sync
        def _(sp):
            sp.dma_start(gain[:], a["final_gain_2"].rearrange("(a n) -> a n", a=1).to_broadcast([P, D]))\
                .then_inc(loaded, 16)
            for t in range(TT):
                sp.wait_ge(y_ready, t + 1)
                sp.dma_start(out[0, t * P:(t + 1) * P, :], c.H[:, t, :]).then_inc(c.out_stored, 16)
            sp.wait_ge(c.out_stored, 16 * TT)


def program(nc, a, out):
    with ExitStack() as ctx:
        ctx.enter_context(nc.allow_non_contiguous_dma(reason="gains and transposed results"))
        c = Chip(nc, ctx)

        def scratch(name, shape):
            return nc.dram_tensor(name, shape, F32, kind="Internal").ap()

        d = {
            "zc": scratch("zc", [TT, P, 432]), "gqk": scratch("gqk", [4, P, S]),
            "gv": scratch("gv", [TT, P, NCOL]), "gr": scratch("gr", [TT, P, NCOL]),
            "mqk_hi": scratch("mqk_hi", [2, MH, MQK, S]), "mqk_lo": scratch("mqk_lo", [2, MH, MQK, S]),
            "mv_hi": scratch("mv_hi", [MH, TT, P, MV]), "mv_lo": scratch("mv_lo", [MH, TT, P, MV]),
            "dq": scratch("dq", [DH, 2, P, S]),
            "dk_hi": scratch("dk_hi", [DH, 2, P, S + CTX]), "dk_lo": scratch("dk_lo", [DH, 2, P, S + CTX]),
            "dv_hi": scratch("dv_hi", [DH, P, TT + CT, P]), "dv_lo": scratch("dv_lo", [DH, P, TT + CT, P]),
            "dz": scratch("dz", [DH, P, S]), "do": scratch("do", [DH, P, S]),
            "gate": scratch("gate", [P, D]),
        }
        constants(nc, c, a)
        with ExitStack() as x_ctx:
            c.hold_x("x", x_ctx)
            norm_transpose(nc, c, "n1", c.gains[:, 0], load=a["x"][0])

            w_in = a["w_in"][0]
            rows = [slice(k * P, (k + 1) * P) for k in range(KT)]
            g_low = GH * GDK * 2 + GH * GDV
            g_r = g_low + GR
            c_q = g_r + GH * GDV
            one = lambda o: 1.0
            tok_place = lambda name, width: (lambda o: [(d[name][o], slice(0, width))])
            groups = [
                ([[w_in[r, g_low:g_r], w_in[r, c_q:c_q + MQR + MKVR + MROPE]] for r in rows], False,
                 tok_place("zc", 432), ACT.Copy, one),
                ([w_in[r, 0:NCOL] for r in rows], True,
                 lambda o: [(d["gqk"][o // HALVES, :, (o % HALVES) * NCOL:(o % HALVES + 1) * NCOL], slice(0, NCOL))],
                 ACT.Copy, lambda o: GDK ** -0.5 if o < TT // 2 else 1.0),
                ([w_in[r, NCOL:2 * NCOL] for r in rows], False, tok_place("gv", NCOL), ACT.Copy, one),
                ([w_in[r, g_r:c_q] for r in rows], False, tok_place("gr", NCOL), ACT.Silu, one),
            ]
            project_to_dram(nc, c, "p1", groups)
            latent_prepare(nc, c, a, d)
            gated_linear_attention(nc, c, a, d)
            c.renew_semaphores()
            latent_attention(nc, c, a, d)
            project_into_residual(nc, c, "wo", a["w_out"][0])
            norm_transpose(nc, c, "n2", c.gains[:, 1])
            c.renew_semaphores()
            mlp(nc, c, a)
            norm_transpose(nc, c, "n3", c.gains[:, 2])
            ple(nc, c, a)
            c.renew_semaphores()
            modulation(nc, c, a, d)
            with ExitStack() as inner:
                ctx_hi, ctx_lo = (c.sb(f"ctx_{x}", [P, KT, CTX], F32R, ctx=inner) for x in ("hi", "lo"))
                with ExitStack() as load_ctx:
                    raw = c.sb("ctx_raw", [P, CT, D], ctx=load_ctx)
                    norm_transpose(nc, c, "nc", c.mod_gain[:, 1], c.mod_bias[:, 1], load=a["ctx_2"][0], src=raw,
                                   dst=(ctx_hi, ctx_lo), tiles=CT)
                norm_transpose(nc, c, "n4", c.mod_gain[:, 0], c.mod_bias[:, 0])
                differential_project(nc, c, a, d, ctx_hi, ctx_lo)
        c.renew_semaphores()
        differential_attention(nc, c, a, d)
        with ExitStack() as x_ctx:
            c.hold_x("x2", x_ctx)
            head_norm_project(nc, c, a, d)
            final_norm(nc, c, a, out)


_INS = ["x", "p", "positions", "attn_norm", "w_in", "gla_gate_w2", "gla_gate_b", "gla_out_norm", "mla_q_norm",
        "mla_w_uq", "mla_kv_norm", "mla_w_ukv", "qk_norm_q", "qk_norm_k", "w_out", "mlp_norm", "w_mlp_up",
        "w_mlp_down", "ple_norm", "w_ple_gate", "b_ple_gate", "w_ple_proj", "c_2", "ctx_2", "c_ctx_2",
        "norm_gain_2", "ada_w_2", "ada_b_2", "final_gain_2", "da_w_in_2", "da_lam_q_2", "da_lam_k_2",
        "da_subln_gain_2", "da_w_out_2"]


def shape_constants():
    import numpy as np
    f = np.float32
    inv = (f(10000.0) ** (-np.arange(0, MROPE, 2, dtype=f) / f(MROPE))).astype(f)
    n = np.arange(S)
    axis = (f(10000.0) ** (-np.arange(0, 32, 2, dtype=f) / f(32))).astype(f)
    ang = np.concatenate([(n // 64).astype(f)[:, None] * axis, (n % 64).astype(f)[:, None] * axis], axis=1)
    s, t = np.arange(P)[:, None], np.arange(P)[None, :]
    masks = [(s // (2 * h) == t // (2 * h)) & (s % (2 * h) < h) & (t % (2 * h) >= h) for h in (64, 32, 16)]
    masks.append((s // 16 == t // 16) & (s <= t))
    return {"inv_freq": inv[None], "da_cos": np.cos(ang).astype(f), "da_sin": np.sin(ang).astype(f),
            "gla_masks": np.stack(masks, axis=1).astype(f)}


def kernel(**inputs):
    import numpy as np
    import concourse.bacc as bacc
    from concourse.bass_utils import run_bass_kernel_spmd

    nc = bacc.Bacc("TRN2", target_bir_lowering=False, num_devices=1)
    arrays, args = {}, {}
    for name, array in [(n, inputs[n]) for n in _INS] + list(shape_constants().items()):
        array = np.ascontiguousarray(array)
        arrays[f"in_{name}"] = array
        args[name] = nc.dram_tensor(f"in_{name}", array.shape, mybir.dt.from_np(array.dtype),
                                    kind="ExternalInput").ap()
    out = nc.dram_tensor("out", (1, S, D), F32, kind="ExternalOutput").ap()
    program(nc, args, out)
    result = run_bass_kernel_spmd(nc, [arrays], core_ids=[0])
    return result.results[0]["out"]
```

```python
from contextlib import ExitStack

import concourse.bass as bass
from concourse import mybir

F32 = mybir.dt.float32
F32R = mybir.dt.float32r
I32 = mybir.dt.int32
ALU = mybir.AluOpType
ACT = mybir.ActivationFunctionType
AX = mybir.AxisListType

P = 128
S = 1024
D = 1024
TT = S // P
KT = D // P
NCOL = 512
HALVES = S // NCOL
CTX = 256
CT = CTX // P
EPS = 1e-6

GH, GDK, GDV, GR = 4, 64, 128, 16
MH, MNOPE, MROPE, MV, MQK = 8, 64, 32, 64, 96
MQR, MKVR = 256, 128
DH, DD = 8, 64
D_FF = 4096
LAMBDA_INIT = 0.2

SLOTS = 4
RING = 4


class Tiles:

    def __init__(self):
        self.halves = [None, None]

    def __getitem__(self, at):
        rows, k, cols = at
        half, i = divmod(k, KT // 2)
        return self.halves[half][rows, i, cols]


class Chip:

    def __init__(self, nc, ctx):
        self.nc, self.ctx = nc, ctx
        self.used = []
        self.Xhi, self.Xlo = Tiles(), Tiles()
        self.out_stored = nc.alloc_semaphore("out_stored")

    def sb(self, name, shape, dt=F32, ctx=None):
        return (ctx or self.ctx).enter_context(self.nc.sbuf_tensor(name, shape, dt))

    def hold_x(self, name, ctx, halves=(0, 1)):
        for i in halves:
            self.Xhi.halves[i] = self.sb(f"{name}_hi{i}", [P, KT // 2, S], F32R, ctx)
            self.Xlo.halves[i] = self.sb(f"{name}_lo{i}", [P, KT // 2, S], F32R, ctx)

    def banks(self, name, ctx, n=8):
        return [ctx.enter_context(self.nc.psum_tensor(f"{name}{i}", [P, NCOL], F32)) for i in range(n)]

    def sem(self, name, ctx):
        s = self.nc.alloc_semaphore(name)
        self.used.append(s)
        return s

    def renew_semaphores(self):
        nc, used = self.nc, self.used
        with nc.Block() as block:
            @block.gpsimd
            def _(pool):
                numbers = sorted(s.num for s in used)
                at = 0
                for i in range(1, len(numbers) + 1):
                    if i == len(numbers) or numbers[i] != numbers[i - 1] + 1:
                        nc.gpsimd.sem_clear(range(numbers[at], numbers[i - 1] + 1))
                        at = i
        for s in used:
            nc.release_semaphore(s)
        self.used = []


def constants(nc, chip, a):
    c = chip
    c.H = c.sb("residual", [P, TT, D])
    c.sums = c.sb("sums", [P, TT])
    c.mod_bias = c.sb("mod_bias", [P, 2, KT])
    c.mod_gain = c.sb("mod_gain", [P, 2, KT])
    c.ident = c.sb("ident", [P, P])
    c.gains = c.sb("gains", [P, 4, KT])
    c.minus_half = c.sb("minus_half", [P, 64])
    with ExitStack() as ctx:
        ones_ready = c.sem("ones_ready", ctx)
        const_loaded = c.sem("const_loaded", ctx)
        block = ctx.enter_context(nc.Block())

        @block.gpsimd
        def _(pool):
            nc.gpsimd.memset(c.ident[:], 0.0).then_inc(ones_ready, 1)
            nc.gpsimd.memset(c.minus_half[:], -0.5).then_inc(ones_ready, 1)
            pool.wait_ge(ones_ready, 2)
            nc.gpsimd.affine_select(out=c.ident[:], in_=c.ident[:], compare_op=ALU.not_equal, fill=1.0,
                                    base=0, pattern=[[-1, P]], channel_multiplier=1).then_inc(ones_ready, 1)

        @block.sync
        def _(sp):
            for n, g in enumerate((a["attn_norm"][0], a["mlp_norm"][0], a["ple_norm"][0], a["norm_gain_2"][0])):
                sp.dma_start(c.gains[:, n, :], g.rearrange("(k p) -> p k", p=P)).then_inc(const_loaded, 16)
            sp.wait_ge(const_loaded, 64)


def half_parts(c, gain, bias=None, load=None):
    per = TT // HALVES
    return [([(c.H[:, t, :], load[t * P:(t + 1) * P, :] if load is not None else None)
              for t in range(h * per, (h + 1) * per)], gain, bias, (c.Xhi, c.Xlo), h * NCOL) for h in range(HALVES)]


def norm_transpose(nc, chip, name, parts):
    c = chip
    tiles = [x for part in parts for x in part[0]]
    first = [sum(len(part[0]) for part in parts[:h]) for h in range(len(parts) + 1)]
    loads = [t for t, (_, place) in enumerate(tiles) if place is not None]
    N = len(parts) * KT
    with ExitStack() as ctx:
        scaled = c.sb(f"{name}_scaled", [P, len(tiles), D], ctx=ctx)
        junk = c.sb(f"{name}_squares", [P, D], ctx=ctx)
        ss = c.sb(f"{name}_ss", [P, len(tiles)], ctx=ctx)
        mean = c.sb(f"{name}_mean", [P, len(tiles)], ctx=ctx)
        rstd = c.sb(f"{name}_rstd", [P, len(tiles)], ctx=ctx)
        full = c.sb(f"{name}_full", [P, 3, NCOL], ctx=ctx) if parts[0][2] is not None else None
        banks = c.banks(f"{name}_ps", ctx)
        loaded = {t: c.sem(f"{name}_loaded{t}", ctx) for t in loads}
        ss_ready, mean_ready, rstd_ready, scaled_ready, turned, hi_ready, full_ready, lo_ready = (
            c.sem(f"{name}_{x}", ctx) for x in ("ss_ready", "mean_ready", "rstd_ready", "scaled_ready", "turned",
                                                "hi_ready", "full_ready", "lo_ready"))
        block = ctx.enter_context(nc.Block())

        loaded_before = lambda t: sum(x < t for x in loads)

        def sums_of(h):
            source = ss if first[h] in loaded else c.sums
            return source[:, first[h]:first[h + 1]]

        def bank_of(n):
            h, k = divmod(n, KT)
            tile_list, gain, bias, out, at = parts[h]
            width = len(tile_list) * P
            return banks[n % 8][:, 0:width], k, slice(at, at + width), gain, bias, out

        @block.sync
        def _(sp):
            for t in loads:
                sp.dma_start(*tiles[t]).then_inc(loaded[t], 16)

        @block.scalar
        def _(act):
            for i, t in enumerate(loads):
                act.wait_ge(loaded[t], 16)
                if i:
                    act.wait_ge(ss_ready, i)
                nc.scalar.activation(junk[:], tiles[t][0], ACT.Square, accum_out=ss[:, t:t + 1]).then_inc(ss_ready, 1)
            for n in range(N):
                bank, k, cols, gain, bias, (hi, _) = bank_of(n)
                act.wait_ge(turned, n + 1)
                if bias is None:
                    nc.scalar.activation(hi[:, k, cols], bank, ACT.Copy, scale=gain[:, k:k + 1]).then_inc(hi_ready, 1)
                else:
                    nc.scalar.activation(hi[:, k, cols], bank, ACT.Identity, scale=gain[:, k:k + 1],
                                         bias=bias[:, k:k + 1]).then_inc(hi_ready, 1)

        @block.gpsimd
        def _(pool):
            for h in range(len(parts)):
                cols = slice(first[h], first[h + 1])
                if first[h] in loaded:
                    pool.wait_ge(ss_ready, loaded_before(first[h + 1]))
                nc.gpsimd.tensor_scalar(mean[:, cols], sums_of(h), 1.0 / D, EPS, ALU.mult, ALU.add)\
                    .then_inc(mean_ready, 1)
                pool.wait_ge(mean_ready, h + 1)
                nc.gpsimd.tensor_tensor(rstd[:, cols], mean[:, cols], c.minus_half[:, 0:first[h + 1] - first[h]],
                                        ALU.pow).then_inc(rstd_ready, 1)
            for n in range(N if full is not None else 0):
                bank, k, cols, _, _, (hi, lo) = bank_of(n)
                pool.wait_ge(full_ready, n + 1)
                nc.gpsimd.tensor_tensor(lo[:, k, cols], full[:, n % 3, 0:bank.shape[1]], hi[:, k, cols].bitcast(F32),
                                        ALU.subtract).then_inc(lo_ready, 1)

        @block.vector
        def _(dve):
            def shifted(n):
                bank, k, cols, gain, bias, _ = bank_of(n)
                dve.wait_ge(hi_ready, n + 1)
                if n >= 3:
                    dve.wait_ge(lo_ready, n - 2)
                nc.vector.tensor_scalar(full[:, n % 3, 0:bank.shape[1]], bank, gain[:, k:k + 1], bias[:, k:k + 1],
                                        ALU.mult, ALU.add).then_inc(full_ready, 1)

            for h in range(len(parts)):
                dve.wait_ge(rstd_ready, h + 1)
                for t in range(first[h], first[h + 1]):
                    nc.vector.tensor_scalar(scaled[:, t, :], tiles[t][0], rstd[:, t:t + 1], None, ALU.mult)\
                        .then_inc(scaled_ready, 1)
            for h in range(len(parts)):
                for n in range(h * KT, (h + 1) * KT):
                    bank, k, cols, gain, bias, (hi, lo) = bank_of(n)
                    if bias is not None:
                        shifted(n)
                        continue
                    dve.wait_ge(hi_ready, n + 1)
                    nc.vector.scalar_tensor_tensor(out=lo[:, k, cols], in0=bank, scalar=gain[:, k:k + 1],
                                                   in1=hi[:, k, cols].bitcast(F32), op0=ALU.mult,
                                                   op1=ALU.subtract).then_inc(lo_ready, 1)

        @block.tensor
        def _(pe):
            for h in range(len(parts)):
                pe.wait_ge(scaled_ready, first[h + 1])
                for n in range(h * KT, (h + 1) * KT):
                    k = n % KT
                    if n >= 8:
                        pe.wait_ge(lo_ready, n - 7)
                    for t in range(first[h + 1] - first[h]):
                        last = nc.tensor.transpose(banks[n % 8][:, t * P:(t + 1) * P],
                                                   scaled[:, first[h] + t, k * P:(k + 1) * P], c.ident[:])
                    last.then_inc(turned, 1)


class Weights:

    def __init__(self, chip, name, ctx, groups, done=None):
        c = chip
        self.nc = c.nc
        self.stage = c.sb(f"{name}_stage", [P, SLOTS, NCOL], ctx=ctx)
        self.hi = c.sb(f"{name}_w_hi", [P, 2, KT, NCOL], F32R, ctx=ctx)
        self.lo = c.sb(f"{name}_w_lo", [P, 2, KT, NCOL], F32R, ctx=ctx)
        self.loaded = [c.sem(f"{name}_w_loaded{i}", ctx) for i in range(SLOTS)]
        self.hi_ready = c.sem(f"{name}_w_hi_ready", ctx)
        self.lo_ready = c.sem(f"{name}_w_lo_ready", ctx)
        self.groups = groups
        self.done = done
        self.chunks = [(g, k, ap) for g, aps in enumerate(groups) for k, ap in enumerate(aps)]
        self.first = [sum(len(x) for x in groups[:g]) for g in range(len(groups) + 1)]

    def load(self, sp):
        for n in range(len(self.chunks)):
            self.load_chunk(sp, n)

    def load_chunk(self, sp, n):
        ap = self.chunks[n][2]
        if n >= SLOTS:
            sp.wait_ge(self.lo_ready, n - SLOTS + 1)
        at = 0
        for piece in (ap if isinstance(ap, list) else [ap]):
            w = piece.shape[1]
            sp.dma_start(self.stage[:, n % SLOTS, at:at + w], piece).then_inc(self.loaded[n % SLOTS], 16)
            at += w

    def _loads(self, n):
        return sum(len(ap) if isinstance(ap, list) else 1 for m, (_, _, ap) in enumerate(self.chunks[:n + 1])
                   if m % SLOTS == n % SLOTS)

    def width(self, n):
        ap = self.chunks[n][2]
        return sum(x.shape[1] for x in ap) if isinstance(ap, list) else ap.shape[1]

    def split_hi(self, act, n):
        g, k, _ = self.chunks[n]
        act.wait_ge(self.loaded[n % SLOTS], 16 * self._loads(n))
        if g >= 2:
            act.wait_ge(self.done[0], self.done[1][g - 2])
        w = self.width(n)
        self.nc.scalar.activation(self.hi[:, g % 2, k, 0:w], self.stage[:, n % SLOTS, 0:w], ACT.Copy)\
            .then_inc(self.hi_ready, 1)

    def split_hi_group(self, act, g):
        for n in range(self.first[g], self.first[g + 1]):
            self.split_hi(act, n)

    def split_lo_chunk(self, pool, n):
        g, k, _ = self.chunks[n]
        pool.wait_ge(self.hi_ready, n + 1)
        w = self.width(n)
        self.nc.gpsimd.tensor_tensor(self.lo[:, g % 2, k, 0:w], self.stage[:, n % SLOTS, 0:w],
                                     self.hi[:, g % 2, k, 0:w].bitcast(F32), ALU.subtract)\
            .then_inc(self.lo_ready, 1)

    def split_lo(self, pool):
        for n in range(len(self.chunks)):
            self.split_lo_chunk(pool, n)


def product(nc, out, terms, cols, last_inc=None, ready=None):
    n = 0
    total = 3 * len(terms)
    for t, ((ah, al), (bh, bl)) in enumerate(terms):
        if ready:
            ready(t)
        for x, y in ((ah, bh), (ah, bl), (al, bh)):
            last = nc.tensor.matmul(out, x, y, start=(n == 0), stop=(n == total - 1))
            n += 1
    if last_inc is not None:
        last.then_inc(last_inc, 1)
    return last


def project_to_dram(nc, chip, name, groups):
    c = chip
    with ExitStack() as ctx:
        result_ready = c.sem(f"{name}_result_ready", ctx)
        w = Weights(c, name, ctx, [g[0] for g in groups], (result_ready, [TT * (g + 1) for g in range(len(groups))]))
        ring = c.sb(f"{name}_ring", [P, RING, NCOL], ctx=ctx)
        banks = c.banks(f"{name}_ps", ctx)
        copied = c.sem(f"{name}_copied", ctx)
        stored = [c.sem(f"{name}_stored{i}", ctx) for i in range(RING)]
        outs = [(g, o) for g in range(len(groups)) for o in range(TT)]
        stores = [len(groups[g][2](o)) for g, o in outs]
        upto = [sum(s for m, s in enumerate(stores[:n]) if m % RING == n % RING) for n in range(len(outs) + RING)]
        block = ctx.enter_context(nc.Block())

        @block.sync
        def _(sp):
            w.load(sp)

        @block.gpsimd
        def _(pool):
            w.split_lo(pool)

        @block.tensor
        def _(pe):
            for n, (g, o) in enumerate(outs):
                by_feature = groups[g][1]
                width = w.width(w.first[g])
                if n >= 8:
                    pe.wait_ge(copied, n - 7)
                terms = []
                for k in range(KT):
                    x = c.Xhi, c.Xlo
                    ww = w.hi[:, g % 2, k], w.lo[:, g % 2, k]
                    if by_feature:
                        f, h = divmod(o, HALVES)
                        terms.append((tuple(y[:, f * P:(f + 1) * P] for y in ww),
                                      tuple(y[:, k, h * NCOL:(h + 1) * NCOL] for y in x)))
                    else:
                        terms.append((tuple(y[:, k, o * P:(o + 1) * P] for y in x),
                                      tuple(y[:, 0:width] for y in ww)))
                out = banks[n % 8][:, 0:NCOL if by_feature else width]
                product(nc, out, terms, NCOL, result_ready,
                        (lambda k: pe.wait_ge(w.lo_ready, w.first[g] + k + 1)) if o == 0 else None)

        @block.scalar
        def _(act):
            def store(n):
                g, o = outs[n]
                act.wait_ge(copied, n + 1)
                for place, cols in groups[g][2](o):
                    act.dma_start(place, ring[:, n % RING, cols]).then_inc(stored[n % RING], 16)

            w.split_hi_group(act, 0)
            for n, (g, o) in enumerate(outs):
                _, by_feature, _, func, scale = groups[g]
                width = NCOL if by_feature else w.width(w.first[g])
                if n >= RING:
                    act.wait_ge(stored[n % RING], 16 * upto[n])
                act.wait_ge(result_ready, n + 1)
                nc.scalar.activation(ring[:, n % RING, 0:width], banks[n % 8][:, 0:width], func,
                                     scale=scale(o)).then_inc(copied, 1)
                if n:
                    store(n - 1)
                if g + 1 < len(groups):
                    w.split_hi(act, w.first[g + 1] + o)
            store(len(outs) - 1)
            for i in range(RING):
                n = max(m for m in range(len(outs)) if m % RING == i)
                act.wait_ge(stored[i], 16 * (upto[n] + stores[n]))


def latent_prepare(nc, chip, a, d):
    c = chip
    QW = MH * MQK // 2
    KVW = MH * (MNOPE + MV) // 2
    TWO_PI_HI, TWO_PI_MID, TWO_PI_LO = 6.28125, 0.0019350051879882812, 3.0199159819e-07
    with ExitStack() as ctx:
        sb = lambda n, s, dt=F32: c.sb("mp_" + n, s, dt, ctx=ctx)
        sem = lambda n: c.sem("mp_" + n, ctx)
        zc = sb("zc", [P, TT, 432])
        cT_hi = sb("cT_hi", [P, 3, S], F32R)
        cT_lo = sb("cT_lo", [P, 3, S], F32R)
        w_f = sb("w_f", [P, 3, 1024])
        wq_hi, wq_lo = sb("wq_hi", [P, 2, 768], F32R), sb("wq_lo", [P, 2, 768], F32R)
        wk_hi, wk_lo = sb("wk_hi", [P, 1024], F32R), sb("wk_lo", [P, 1024], F32R)
        junk = sb("junk", [P, 1280])
        cn = sb("cn", [P, 2, 384])
        ss = sb("ss", [P, 3, TT])
        ssm = sb("ssm", [P, 2, TT])
        rstd = sb("rstd", [P, 2, TT])
        gc = sb("gc", [P, 3])
        gq, gk = sb("gq", [P, MQK]), sb("gk", [P, MQK])
        pos_i = sb("pos_i", [P, TT], I32)
        pos = sb("pos", [P, TT])
        freq = sb("freq", [P, 16])
        ang = sb("ang", [P, TT, 16])
        t1, t2 = sb("t1", [P, TT, 16]), sb("t2", [P, TT, 16])
        turn_i = sb("turn_i", [P, TT, 16], I32)
        cos, sin = sb("cos", [P, TT, 16]), sb("sin", [P, TT, 16])
        nrm = sb("nrm", [P, 2, 2, MH, MQK])
        rop = sb("rop", [P, 2, 4, MH, 16])
        ssh, msh, rsh = sb("ssh", [P, 2, 2, MH]), sb("msh", [P, 2, 2, MH]), sb("rsh", [P, 2, 2, MH])
        qk_hi = sb("qk_hi", [MQK, 2, MH, P], F32R)
        qk_lo = sb("qk_lo", [MQK, 2, MH, P], F32R)
        v_hi, v_lo = sb("v_hi", [P, MH, MV], F32R), sb("v_lo", [P, MH, MV], F32R)
        banks = c.banks("mp_ps", ctx)

        loaded = sem("loaded")
        wloaded = [sem(f"wloaded{n}") for n in range(3)]
        dve_step, pool_step = sem("dve_step"), sem("pool_step")
        c_scaled, c_hi, c_lo = sem("c_scaled"), sem("c_hi"), sem("c_lo")
        ss_ready, rstd_ready, w_split = sem("ss_ready"), sem("rstd_ready"), sem("w_split")
        w_hi_ready = sem("w_hi_ready")
        table_arg, table_ready = sem("table_arg"), sem("table_ready")
        up_ready = sem("up_ready")
        squares, head_ss, head_rstd, v_hi_ready, v_lo_ready = (
            sem("squares"), sem("head_ss"), sem("head_rstd"), sem("v_hi_ready"), sem("v_lo_ready"))
        roped, turned, hi_ready, lo_ready = sem("roped"), sem("turned"), sem("hi_ready"), sem("lo_ready")
        q_out, v_out = sem("q_out"), sem("v_out")
        c_scaled_read = sem("c_scaled_read")
        block = ctx.enter_context(nc.Block())

        w_rows = [a["mla_w_uq"][0, 0:P, :], a["mla_w_uq"][0, P:2 * P, :], a["mla_w_ukv"][0]]
        w_dst = [(wq_hi[:, 0], wq_lo[:, 0]), (wq_hi[:, 1], wq_lo[:, 1]), (wk_hi[:], wk_lo[:])]

        @block.sync
        def _(sp):
            sp.dma_start(zc[:], d["zc"].rearrange("t p n -> p t n")).then_inc(loaded, 16)
            sp.dma_start(gc[:, 0:2], a["mla_q_norm"][0].rearrange("(k p) -> p k", p=P)).then_inc(loaded, 16)
            sp.dma_start(gc[:, 2:3], a["mla_kv_norm"][0].rearrange("(k p) -> p k", p=P)).then_inc(loaded, 16)
            sp.dma_start(gq[:], a["qk_norm_q"].to_broadcast([P, MQK])).then_inc(loaded, 16)
            sp.dma_start(gk[:], a["qk_norm_k"].to_broadcast([P, MQK])).then_inc(loaded, 16)
            sp.dma_start(pos_i[:], a["positions"][0].rearrange("(t p) -> p t", p=P)).then_inc(loaded, 16)
            sp.dma_start(freq[:], a["inv_freq"].to_broadcast([P, 16])).then_inc(loaded, 16)
            for n, rows in enumerate(w_rows):
                sp.dma_start(w_f[:, n, 0:rows.shape[1]], rows).then_inc(wloaded[n], 16)
            for t in range(TT):
                sp.wait_ge(v_lo_ready, t + 1)
                sp.dma_start(d["mv_hi"][:, t].rearrange("h p v -> p h v"), v_hi[:].bitcast(F32)).then_inc(v_out, 16)
                sp.dma_start(d["mv_lo"][:, t].rearrange("h p v -> p h v"), v_lo[:].bitcast(F32)).then_inc(v_out, 16)
                for q in range(2):
                    sp.wait_ge(lo_ready, 4 * t + 2 * (q + 1))
                    cols = slice(t * P, (t + 1) * P)
                    sp.dma_start(d["mqk_hi"][q, :, :, cols].rearrange("h d s -> d h s"), qk_hi[:, q].bitcast(F32))\
                        .then_inc(q_out, 16)
                    sp.dma_start(d["mqk_lo"][q, :, :, cols].rearrange("h d s -> d h s"), qk_lo[:, q].bitcast(F32))\
                        .then_inc(q_out, 16)
            sp.wait_ge(q_out, 64 * TT)
            sp.wait_ge(v_out, 32 * TT)

        @block.gpsimd
        def _(pool):
            pool.wait_ge(ss_ready, 3 * TT)
            nc.gpsimd.tensor_scalar(ssm[:, 0], ss[:, 0], 1.0 / MQR, EPS, ALU.mult, ALU.add).then_inc(pool_step, 1)
            nc.gpsimd.tensor_scalar(ssm[:, 1], ss[:, 1], 1.0 / MKVR, EPS, ALU.mult, ALU.add).then_inc(pool_step, 1)
            pool.wait_ge(pool_step, 2)
            nc.gpsimd.tensor_tensor(rstd[:], ssm[:], c.minus_half[:, 0:16].rearrange("p (a b) -> p a b", a=2),
                                    ALU.pow).then_inc(rstd_ready, 1)
            for n, rows in enumerate(w_rows):
                w = rows.shape[1]
                pool.wait_ge(w_hi_ready, n + 1)
                nc.gpsimd.tensor_tensor(w_dst[n][1], w_f[:, n, 0:w], w_dst[n][0].bitcast(F32), ALU.subtract)\
                    .then_inc(w_split, 1)
            for t in range(TT):
                b = t % 2
                pool.wait_ge(head_ss, t + 1)
                nc.gpsimd.tensor_scalar(msh[:, b], ssh[:, b], 1.0 / MQK, EPS, ALU.mult, ALU.add)\
                    .then_inc(pool_step, 1)
                pool.wait_ge(pool_step, 3 + t)
                nc.gpsimd.tensor_tensor(rsh[:, b], msh[:, b],
                                        c.minus_half[:, 0:16].rearrange("p (a b) -> p a b", a=2),
                                        ALU.pow).then_inc(head_rstd, 1)

        @block.scalar
        def _(act):
            act.wait_ge(loaded, 16 * 7)
            n = 0
            for t in range(TT):
                for m, (lo, hi) in enumerate(((16, 272), (272, 400), (400, 432))):
                    if n:
                        act.wait_ge(ss_ready, n)
                    nc.scalar.activation(junk[:, 0:hi - lo], zc[:, t, lo:hi], ACT.Square,
                                         accum_out=ss[:, m, t:t + 1]).then_inc(ss_ready, 1)
                    n += 1
            for n, rows in enumerate(w_rows):
                act.wait_ge(wloaded[n], 16)
                nc.scalar.activation(w_dst[n][0], w_f[:, n, 0:rows.shape[1]], ACT.Copy).then_inc(w_hi_ready, 1)
            for i, (arg, out) in enumerate(((t1, sin), (t2, cos))):
                act.wait_ge(table_arg, i + 1)
                nc.scalar.activation(out[:], arg[:], ACT.Sin).then_inc(table_ready, 1)
            for n in range(6):
                j = n % 3
                h = n // 3
                act.wait_ge(c_scaled_read, 4 * (h + 1))
                nc.scalar.activation(cT_hi[:, j, h * NCOL:(h + 1) * NCOL], banks[n][:], ACT.Copy,
                                     scale=gc[:, j:j + 1]).then_inc(c_hi, 1)

            def squares_of(t):
                bank = banks[4 * (t % 2):4 * (t % 2) + 4]
                act.wait_ge(up_ready, t + 1)
                if t:
                    act.wait_ge(head_ss, t)
                for g in range(2):
                    nc.scalar.activation(junk[:, g * QW:(g + 1) * QW], bank[g][:, 0:QW], ACT.Square)\
                        .then_inc(squares, 1)
                for g in range(2):
                    nc.scalar.activation(
                        junk[:, 768 + g * 256:768 + (g + 1) * 256].rearrange("p (h n) -> p h n", h=4),
                        bank[2 + g][:].rearrange("p (h n) -> p h n", h=4)[:, :, 0:MNOPE], ACT.Square)\
                        .then_inc(squares, 1)
                if t:
                    act.wait_ge(v_out, 32 * t)
                for g in range(2):
                    nc.scalar.activation(v_hi[:, 4 * g:4 * g + 4, :],
                                         bank[2 + g][:].rearrange("p (h n) -> p h n", h=4)[:, :, MNOPE:],
                                         ACT.Copy).then_inc(v_hi_ready, 1)

            def high(t):
                for m in range(4):
                    q, g = divmod(m, 2)
                    act.wait_ge(turned, 4 * t + m + 1)
                    if t:
                        act.wait_ge(q_out, 64 * t)
                    nc.scalar.activation(qk_hi[:, q, 4 * g:4 * g + 4, :],
                                         banks[4 * (t % 2) + m][0:MQK].rearrange("p (h n) -> p h n", h=4),
                                         ACT.Copy).then_inc(hi_ready, 1)

            squares_of(0)
            for t in range(TT):
                if t:
                    high(t - 1)
                if t + 1 < TT:
                    squares_of(t + 1)
            high(TT - 1)

        @block.vector
        def _(dve):
            steps = [0]

            def step(ins):
                steps[0] += 1
                ins.then_inc(dve_step, 1)
                dve.wait_ge(dve_step, steps[0])

            dve.wait_ge(loaded, 16 * 7)
            step(nc.vector.tensor_scalar(gq[:], gq[:], -MQK ** -0.5, None, ALU.mult))
            step(nc.vector.tensor_copy(pos[:], pos_i[:]))
            step(nc.vector.tensor_tensor(ang[:], pos[:].unsqueeze(2).to_broadcast([P, TT, 16]),
                                         freq[:].unsqueeze(1).to_broadcast([P, TT, 16]), ALU.mult))
            for i, (shift, out) in enumerate(((0.0, t1), (0.25, t2))):
                step(nc.vector.tensor_scalar(t1[:] if i == 0 else t2[:], ang[:], 0.15915494309189535, shift,
                                             ALU.mult, ALU.add))
                step(nc.vector.tensor_copy(turn_i[:], out[:]))
                step(nc.vector.tensor_copy(cos[:], turn_i[:]))
                step(nc.vector.scalar_tensor_tensor(out=out[:], in0=cos[:], scalar=-TWO_PI_HI, in1=ang[:],
                                                    op0=ALU.mult, op1=ALU.add))
                step(nc.vector.scalar_tensor_tensor(out=out[:], in0=cos[:], scalar=-TWO_PI_MID, in1=out[:],
                                                    op0=ALU.mult, op1=ALU.add))
                step(nc.vector.scalar_tensor_tensor(out=out[:], in0=cos[:], scalar=-TWO_PI_LO, in1=out[:],
                                                    op0=ALU.mult, op1=ALU.add))
                if i:
                    step(nc.vector.tensor_scalar(out[:], out[:], 1.5707963267948966, None, ALU.add))
                nc.vector.tensor_scalar(out[:], out[:], 3.1415925, -3.1415925, ALU.min, ALU.max)\
                    .then_inc(table_arg, 1)
                if i == 0:
                    dve.wait_ge(table_arg, 1)
            dve.wait_ge(rstd_ready, 1)
            for t in range(TT):
                if t >= 2:
                    dve.wait_ge(c_scaled_read, t - 1)
                nc.vector.tensor_scalar(cn[:, t % 2, 0:256], zc[:, t, 16:272], rstd[:, 0, t:t + 1], None, ALU.mult)\
                    .then_inc(c_scaled, 1)
                nc.vector.tensor_scalar(cn[:, t % 2, 256:384], zc[:, t, 272:400], rstd[:, 1, t:t + 1], None, ALU.mult)\
                    .then_inc(c_scaled, 1)
            for n in range(6):
                j, h = n % 3, n // 3
                dve.wait_ge(c_hi, n + 1)
                nc.vector.scalar_tensor_tensor(
                    out=cT_lo[:, j, h * NCOL:(h + 1) * NCOL], in0=banks[n][:], scalar=gc[:, j:j + 1],
                    in1=cT_hi[:, j, h * NCOL:(h + 1) * NCOL].bitcast(F32), op0=ALU.mult, op1=ALU.subtract)\
                    .then_inc(c_lo, 1)
            dve.wait_ge(table_ready, 2)

            def sums_of(t):
                b = t % 2
                bank = banks[4 * b:4 * b + 4]
                dve.wait_ge(squares, 4 * t + 2)
                nc.vector.tensor_reduce(out=ssh[:, b, 0], in_=junk[:, 0:768].rearrange("p (h n) -> p h n", h=MH),
                                        op=ALU.add, axis=AX.X).then_inc(dve_step, 1)
                steps[0] += 1
                dve.wait_ge(squares, 4 * t + 4)
                step(nc.vector.tensor_reduce(out=ssh[:, b, 1], in_=junk[:, 768:1280].rearrange("p (h n) -> p h n", h=MH),
                                             op=ALU.add, axis=AX.X))
                nc.vector.tensor_scalar(ssh[:, b, 1], ssh[:, b, 1], ss[:, 2, t:t + 1], None, ALU.add)\
                    .then_inc(head_ss, 1)
                dve.wait_ge(v_hi_ready, 2 * t + 2)
                for g in range(2):
                    last = nc.vector.tensor_tensor(
                        v_lo[:, 4 * g:4 * g + 4, :],
                        bank[2 + g][:].rearrange("p (h n) -> p h n", h=4)[:, :, MNOPE:],
                        v_hi[:, 4 * g:4 * g + 4, :].bitcast(F32), ALU.subtract)
                last.then_inc(v_lo_ready, 1)

            def norm_rope(t):
                b = t % 2
                bank = banks[4 * b:4 * b + 4]
                dve.wait_ge(head_rstd, t + 1)
                rs = rsh[:, b]
                for g in range(2):
                    hs = slice(4 * g, 4 * g + 4)
                    nc.vector.tensor_tensor(nrm[:, b, 0, hs], bank[g][:, 0:QW].rearrange("p (h n) -> p h n", h=4),
                                            rs[:, 0, hs].unsqueeze(2).to_broadcast([P, 4, MQK]), ALU.mult)\
                        .then_inc(dve_step, 1)
                    nc.vector.tensor_tensor(nrm[:, b, 1, hs, 0:MNOPE],
                                            bank[2 + g][:].rearrange("p (h n) -> p h n", h=4)[:, :, 0:MNOPE],
                                            rs[:, 1, hs].unsqueeze(2).to_broadcast([P, 4, MNOPE]), ALU.mult)\
                        .then_inc(dve_step, 1)
                steps[0] += 4
                step(nc.vector.tensor_tensor(nrm[:, b, 1, :, MNOPE:],
                                             zc[:, t, 400:432].unsqueeze(1).to_broadcast([P, MH, MROPE]),
                                             rs[:, 1].unsqueeze(2).to_broadcast([P, MH, MROPE]), ALU.mult))
                for q, g in ((0, gq), (1, gk)):
                    x = nrm[:, b, q]
                    step(nc.vector.tensor_tensor(x, x, g[:].unsqueeze(1).to_broadcast([P, MH, MQK]), ALU.mult))
                    x1, x2 = x[:, :, 64:80], x[:, :, 80:96]
                    cs = cos[:, t].unsqueeze(1).to_broadcast([P, MH, 16])
                    sn = sin[:, t].unsqueeze(1).to_broadcast([P, MH, 16])
                    for m, (u, v) in enumerate(((x1, cs), (x2, sn), (x2, cs), (x1, sn))):
                        nc.vector.tensor_tensor(rop[:, b, m], u, v, ALU.mult).then_inc(dve_step, 1)
                    steps[0] += 4
                    dve.wait_ge(dve_step, steps[0])
                    nc.vector.tensor_tensor(x1, rop[:, b, 0], rop[:, b, 1], ALU.subtract).then_inc(roped, 1)
                    nc.vector.tensor_tensor(x2, rop[:, b, 2], rop[:, b, 3], ALU.add).then_inc(roped, 1)

            def low(t):
                for m in range(4):
                    q, g = divmod(m, 2)
                    dve.wait_ge(hi_ready, 4 * t + m + 1)
                    nc.vector.tensor_tensor(qk_lo[:, q, 4 * g:4 * g + 4, :],
                                            banks[4 * (t % 2) + m][0:MQK].rearrange("p (h n) -> p h n", h=4),
                                            qk_hi[:, q, 4 * g:4 * g + 4, :].bitcast(F32), ALU.subtract)\
                        .then_inc(lo_ready, 1)

            sums_of(0)
            for t in range(TT):
                if t:
                    low(t - 1)
                norm_rope(t)
                if t + 1 < TT:
                    sums_of(t + 1)
            low(TT - 1)

        @block.tensor
        def _(pe):
            for t in range(TT):
                pe.wait_ge(c_scaled, 2 * t + 2)
                h, u = divmod(t, 4)
                for j in range(3):
                    last = nc.tensor.transpose(banks[3 * h + j][:, u * P:(u + 1) * P],
                                               cn[:, t % 2, j * P:(j + 1) * P], c.ident[:])
                last.then_inc(c_scaled_read, 1)
            pe.wait_ge(c_lo, 6)
            pe.wait_ge(w_split, 3)

            def up(t):
                tok = slice(t * P, (t + 1) * P)
                bank = banks[4 * (t % 2):4 * (t % 2) + 4]
                if t >= 2:
                    pe.wait_ge(lo_ready, 4 * (t - 1))
                for g in range(2):
                    product(nc, bank[g][:, 0:QW],
                            [((cT_hi[:, k, tok], cT_lo[:, k, tok]),
                              (wq_hi[:, k, g * QW:(g + 1) * QW], wq_lo[:, k, g * QW:(g + 1) * QW]))
                             for k in range(2)], QW)
                for g in range(2):
                    last = product(nc, bank[2 + g][:],
                                   [((cT_hi[:, 2, tok], cT_lo[:, 2, tok]),
                                     (wk_hi[:, g * KVW:(g + 1) * KVW], wk_lo[:, g * KVW:(g + 1) * KVW]))], KVW)
                last.then_inc(up_ready, 1)

            def turn(t):
                for q in range(2):
                    pe.wait_ge(roped, 4 * t + 2 * (q + 1))
                    if q:
                        pe.wait_ge(v_lo_ready, t + 1)
                    for g in range(2):
                        for h in range(4):
                            last = nc.tensor.transpose(banks[4 * (t % 2) + 2 * q + g][0:MQK, h * P:(h + 1) * P],
                                                       nrm[:, t % 2, q, 4 * g + h, :], c.ident[:])
                        last.then_inc(turned, 1)

            up(0)
            for t in range(TT):
                if t + 1 < TT:
                    up(t + 1)
                turn(t)


def gated_linear_attention(nc, chip, a, d):
    c = chip
    CH = 4
    UT = CH * P
    UNITS = [(h, p) for h in range(TT // CH) for p in range(GH // 2)]
    LEVELS = (64, 32, 16)
    TAU = 16.0
    NQ = len(LEVELS) + 1
    CHUNKS = len(UNITS) * CH
    with ExitStack() as ctx:
        sb = lambda n, s, dt=F32: c.sb("gla_" + n, s, dt, ctx=ctx)
        sem = lambda n: c.sem("gla_" + n, ctx)
        qT, kT = sb("qT", [P, 2, S]), sb("kT", [P, 2, S])
        v = c.H[:, 0:TT // 2, :].rearrange("p a (b n) -> p (a b) n", n=GH * GDV)
        gate = c.H[:, TT // 2:TT, :].rearrange("p a (b n) -> p (a b) n", n=GH * GDV)
        glow = sb("glow", [P, TT, GR])
        glowT = sb("glowT", [GR, S])
        w2 = sb("w2", [GR, 2 * P])
        gb = sb("gb", [P, 2])
        gain = sb("gain", [P, GDV])
        masks = sb("masks", [P, NQ, P])
        reset = sb("reset", [P, UT])
        low, mag, b = sb("low", [P, UT]), sb("mag", [P, UT]), sb("b", [P, UT])
        diff = sb("diff", [P, 2, UT])
        expo = sb("expo", [P, 2, UT])
        expn = sb("expn", [P, UT])
        qs = sb("qs", [P, 2, NQ + 1, UT])
        ks = sb("ks", [P, 2, NQ + 1, UT])
        dec = sb("dec", [P, 2, CH])
        state = sb("state", [P, 2, 2 * GDV])
        masked = sb("masked", [P, 2, NQ, P])
        st = sb("st", [P, 4, P])
        kdt = sb("kdt", [P, 2, P])
        o_sq = sb("o_sq", [P, 2 * GDV])
        o_ss, o_ms, o_rs = sb("o_ss", [P, 2]), sb("o_ms", [P, 2]), sb("o_rs", [P, 2, 2])
        on = sb("on", [P, 2, CH, 2 * GDV])
        banks = c.banks("gla_ps", ctx)
        PIECES = 2 * (3 * D // NCOL)
        ada_w = sb("ada_w", [P, 4, KT // 2, NCOL])
        cond_in, cond = sb("cond_in", [P, KT, 2]), sb("cond", [P, KT, 2])
        ada_b, ada_row = sb("ada_b", [2, 2, NCOL]), sb("ada_row", [2, 2, NCOL])
        cond_loaded, cond_ready, ada_w_used, ada_row_ready = (
            sem(x) for x in ("cond_loaded", "cond_ready", "ada_w_used", "ada_row_ready"))
        ada_w_loaded = [sem(f"ada_w_loaded{i}") for i in range(4)]
        ada_b_loaded, ada_stored = [[sem(f"{x}{i}") for i in range(2)] for x in ("ada_b_loaded", "ada_stored")]
        loaded, mask_loaded, v_loaded, gate_loaded = (
            sem(x) for x in ("loaded", "mask_loaded", "v_loaded", "gate_loaded"))
        qk_loaded = [sem(f"qk_loaded{i}") for i in range(2)]
        gate_ready = sem("gate_ready")
        ready0 = sem("ready0")
        gl_turned, gl_ready, pre_ready = sem("gl_turned"), sem("gl_ready"), sem("pre_ready")
        act_step, dve_step, pool_step = sem("act_step"), sem("dve_step"), sem("pool_step")
        mag_ready, low_ready, ln_ready, b_ready = sem("mag_ready"), sem("low_ready"), sem("ln_ready"), sem("b_ready")
        diff_ready, exp_ready, q_used, k_used = sem("diff_ready"), sem("exp_ready"), sem("q_used"), sem("k_used")
        scored, st_ready, st_used = sem("scored"), sem("st_ready"), sem("st_used")
        kd_turned, kdt_ready, update_ready, state_ready = (
            sem("kd_turned"), sem("kdt_ready"), sem("update_ready"), sem("state_ready"))
        o_squared, o_summed, o_rstd, o_done = (
            sem("o_squared"), sem("o_summed"), sem("o_rstd"), sem("o_done"))
        turned, hi_ready, lo_ready = sem("turned"), sem("hi_ready"), sem("lo_ready")
        block = ctx.enter_context(nc.Block())

        @block.sync
        def _(sp):
            first, second = slice(0, UT), slice(UT, S)
            for place, src, s in (
                (glow[:], d["zc"][:, :, 0:GR].rearrange("t p n -> p t n"), loaded), (w2[:], a["gla_gate_w2"][0], loaded),
                (gb[:], a["gla_gate_b"][0].rearrange("(k p) -> p k", p=P), loaded),
                (qT[:, :, first], d["gqk"][0:2, :, first].rearrange("k p s -> p k s"), qk_loaded[0]),
                (kT[:, :, first], d["gqk"][2:4, :, first].rearrange("k p s -> p k s"), qk_loaded[0]),
                (masks[:], a["gla_masks"], mask_loaded),
                (v, d["gv"].rearrange("t p n -> p t n"), v_loaded),
                (gain[:], a["gla_out_norm"].to_broadcast([P, GDV]), gate_loaded),
                (gate, d["gr"].rearrange("t p n -> p t n"), gate_loaded),
                (qT[:, :, second], d["gqk"][0:2, :, second].rearrange("k p s -> p k s"), qk_loaded[1]),
                (kT[:, :, second], d["gqk"][2:4, :, second].rearrange("k p s -> p k s"), qk_loaded[1]),
            ):
                sp.dma_start(place, src).then_inc(s, 16)
            sp.dma_start(cond_in[:, :, 0], a["c_2"][0].rearrange("(k p) -> p k", p=P)).then_inc(cond_loaded, 16)
            sp.dma_start(cond_in[:, :, 1], a["c_ctx_2"].rearrange("(k p) -> p k", p=P)).then_inc(cond_loaded, 16)

            def store_row(g):
                sp.wait_ge(ada_row_ready, g + 1)
                sp.dma_start(d["mod_row"][:, g * NCOL:(g + 1) * NCOL], ada_row[:, g % 2]).then_inc(ada_stored[g % 2], 16)

            for m in range(PIECES):
                g, half = divmod(m, 2)
                cols = slice(g * NCOL, (g + 1) * NCOL)
                if m >= 4:
                    sp.wait_ge(ada_w_used, m - 3)
                sp.dma_start(ada_w[:, m % 4], a["ada_w_2"][0, half * NCOL:(half + 1) * NCOL, cols]
                             .rearrange("(k p) n -> p k n", p=P)).then_inc(ada_w_loaded[m % 4], 16)
                if half == 0:
                    if g >= 2:
                        store_row(g - 2)
                    sp.dma_start(ada_b[:, g % 2], a["ada_b_2"][:, cols].to_broadcast([2, NCOL]))\
                        .then_inc(ada_b_loaded[g % 2], 16)
            for g in (PIECES // 2 - 2, PIECES // 2 - 1):
                store_row(g)
            for i in range(2):
                sp.wait_ge(ada_stored[i], 16 * (PIECES // 4))

        @block.gpsimd
        def _(pool):
            steps = [0]

            def step(ins):
                steps[0] += 1
                ins.then_inc(pool_step, 1)
                pool.wait_ge(pool_step, steps[0])

            step(nc.gpsimd.memset(reset[:], 1.0))
            nc.gpsimd.memset(reset[:].rearrange("p (c t) -> p c t", t=P)[:, :, 0:1], 0.0).then_inc(ready0, 1)
            nc.gpsimd.memset(state[:], 0.0).then_inc(ready0, 1)
            def prep(u, part):
                h, p = UNITS[u]
                kk = kT[:, p, h * UT:(h + 1) * UT]
                pool.wait_ge(qk_loaded[h], 32)
                if u >= 2 and part == 1:
                    pool.wait_ge(st_used, 2 * CH * (u - 1))
                for need, src, dst in ((), ((1, expo[:, 0], 0), (2, expo[:, 1], 1)), ((3, expo[:, 0], 2), (5, expn[:], 3)),
                                       ((7, expo[:, 1], 4),))[part]:
                    pool.wait_ge(exp_ready, 7 * u + need)
                    nc.gpsimd.tensor_tensor(ks[:, u % 2, dst], kk, src, ALU.mult).then_inc(k_used, 1)

            def chunk(n):
                pool.wait_ge(o_summed, n + 1)
                step(nc.gpsimd.tensor_scalar(o_ms[:], o_ss[:], 1.0 / GDV, EPS, ALU.mult, ALU.add))
                if n >= 2:
                    pool.wait_ge(o_done, n - 1)
                nc.gpsimd.tensor_tensor(o_rs[:, n % 2], o_ms[:], c.minus_half[:, 0:2], ALU.pow).then_inc(o_rstd, 1)

            for i in range(CH):
                prep(0, i)
            pool.wait_ge(gate_loaded, 32)
            for n in range(CHUNKS):
                u, i = divmod(n, CH)
                if n < TT:
                    g = gate[:, n].rearrange("p (h n) -> p h n", h=GH)
                    nc.gpsimd.tensor_tensor(g, g, gain[:].unsqueeze(1).to_broadcast([P, GH, GDV]), ALU.mult)\
                        .then_inc(gate_ready, 1)
                if u + 1 < len(UNITS):
                    prep(u + 1, i)
                chunk(n)

        @block.scalar
        def _(act):
            act.wait_ge(gl_turned, 1)
            nc.scalar.activation(glowT[:, 0:NCOL], banks[0][0:GR, :], ACT.Copy).then_inc(gl_ready, 1)
            nc.scalar.activation(glowT[:, NCOL:S], banks[1][0:GR, :], ACT.Copy).then_inc(gl_ready, 1)
            steps = [0]

            def step(ins):
                steps[0] += 1
                ins.then_inc(act_step, 1)
                act.wait_ge(act_step, steps[0])

            def prep(u, part):
                h, p = UNITS[u]
                if part == 0:
                    act.wait_ge(pre_ready, u + 1)
                    if u:
                        act.wait_ge(b_ready, u)
                    nc.scalar.activation(mag[:], banks[0][:], ACT.Abs, bias=gb[:, p:p + 1]).then_inc(mag_ready, 1)
                    act.wait_ge(mag_ready, u + 1)
                    step(nc.scalar.activation(mag[:], mag[:], ACT.Exp, scale=-1.0))
                    nc.scalar.activation(mag[:], mag[:], ACT.Ln, bias=1.0).then_inc(ln_ready, 1)

                def level(i):
                    act.wait_ge(diff_ready, 5 * u + i + 1)
                    if i == 2:
                        act.wait_ge(q_used, 5 * u + 1)
                        act.wait_ge(k_used, 5 * u + 1)
                    elif u:
                        act.wait_ge(q_used, 5 * u)
                        act.wait_ge(k_used, 5 * u)
                    step(nc.scalar.activation(diff[:, i % 2], diff[:, i % 2], ACT.Abs))
                    nc.scalar.activation(expo[:, i % 2], diff[:, i % 2], ACT.Exp, scale=-1.0 / TAU).then_inc(exp_ready, 1)

                if part == 1:
                    level(0)
                    level(1)
                if part == 2:
                    level(2)
                    act.wait_ge(diff_ready, 5 * u + 4)
                    act.wait_ge(q_used, 5 * u + 2)
                    act.wait_ge(k_used, 5 * u + 2)
                    nc.scalar.activation(expo[:, 1], diff[:, 1], ACT.Exp, scale=1.0 / TAU).then_inc(exp_ready, 1)
                    nc.scalar.activation(expn[:], diff[:, 1], ACT.Exp, scale=-1.0 / TAU).then_inc(exp_ready, 1)
                if part == 3:
                    act.wait_ge(q_used, 5 * u + 3)
                    act.wait_ge(k_used, 5 * u + 3)
                    nc.scalar.activation(expo[:, 0], b[:], ACT.Exp, scale=1.0 / TAU).then_inc(exp_ready, 1)
                    act.wait_ge(diff_ready, 5 * u + 5)
                    act.wait_ge(q_used, 5 * u + 4)
                    nc.scalar.activation(expo[:, 1], diff[:, 0], ACT.Exp, scale=1.0 / TAU).then_inc(exp_ready, 1)

            def keys(n):
                act.wait_ge(kd_turned, n + 1)
                if n >= 2:
                    act.wait_ge(update_ready, n - 1)
                nc.scalar.activation(kdt[:, n % 2], banks[5][:, 0:P], ACT.Copy).then_inc(kdt_ready, 1)

            def square(n):
                act.wait_ge(st_used, 2 * (n + 1))
                if n:
                    act.wait_ge(o_summed, n)
                nc.scalar.activation(o_sq[:], banks[3 + n % 2][:, 0:2 * GDV], ACT.Square).then_inc(o_squared, 1)

            def out(u):
                h, p = UNITS[u]
                for i in range(2):
                    act.wait_ge(turned, 2 * u + i + 1)
                    nc.scalar.activation(c.Xhi[:, 2 * p + i, h * UT:(h + 1) * UT], banks[0][:], ACT.Copy)\
                        .then_inc(hi_ready, 1)

            for i in range(CH):
                prep(0, i)
            act.wait_ge(cond_loaded, 32)
            nc.scalar.activation(cond[:], cond_in[:], ACT.Silu).then_inc(cond_ready, 1)
            keys(0)
            for n in range(CHUNKS):
                u, i = divmod(n, CH)
                if u + 1 < len(UNITS):
                    prep(u + 1, i)
                if n + 1 < CHUNKS:
                    keys(n + 1)
                square(n)
                if i == 1 and u:
                    out(u - 1)
            out(len(UNITS) - 1)

        @block.vector
        def _(dve):
            steps = [0]

            def step(ins):
                steps[0] += 1
                ins.then_inc(dve_step, 1)
                dve.wait_ge(dve_step, steps[0])

            dve.wait_ge(loaded, 16 * 3)
            dve.wait_ge(ready0, 2)

            def difference(slot, block_len, ref, sign=1):
                bb = b[:].rearrange("p (n t) -> p n t", t=block_len)
                rr = bb[:, :, ref:ref + 1].to_broadcast([P, UT // block_len, block_len])
                o = diff[:, slot].rearrange("p (n t) -> p n t", t=block_len)
                return nc.vector.tensor_tensor(o, bb, rr, ALU.subtract) if sign > 0 else \
                    nc.vector.tensor_tensor(o, rr, bb, ALU.subtract)

            def prep(u, part):
                h, p = UNITS[u]
                qq = qT[:, p, h * UT:(h + 1) * UT]
                par = u % 2
                dve.wait_ge(qk_loaded[h], 32)

                def decayed(i, need, src):
                    dve.wait_ge(exp_ready, 7 * u + need)
                    nc.vector.tensor_tensor(qs[:, par, i], qq, src, ALU.mult).then_inc(q_used, 1)

                if part == 0:
                    dve.wait_ge(mag_ready, u + 1)
                    nc.vector.tensor_scalar(low[:], banks[0][:], gb[:, p:p + 1], 0.0, ALU.add, ALU.min)\
                        .then_inc(low_ready, 1)
                    dve.wait_ge(low_ready, u + 1)
                    dve.wait_ge(ln_ready, u + 1)
                    step(nc.vector.tensor_tensor(low[:], low[:], mag[:], ALU.subtract))
                    if u:
                        dve.wait_ge(exp_ready, 7 * u)
                    nc.vector.tensor_tensor_scan(b[:], reset[:], low[:], 0.0, ALU.mult, ALU.add).then_inc(b_ready, 1)
                    dve.wait_ge(b_ready, u + 1)
                    if u >= 2:
                        dve.wait_ge(st_used, 2 * CH * (u - 1))
                    difference(0, 2 * LEVELS[0], LEVELS[0] - 1).then_inc(diff_ready, 1)
                    difference(1, 2 * LEVELS[1], LEVELS[1] - 1).then_inc(diff_ready, 1)
                if part == 1:
                    decayed(0, 1, expo[:, 0])
                    difference(0, 2 * LEVELS[2], LEVELS[2] - 1).then_inc(diff_ready, 1)
                    decayed(1, 2, expo[:, 1])
                    step(difference(1, 16, 7))
                    nc.vector.tensor_scalar(diff[:, 1], diff[:, 1], 80.0 * TAU, -80.0 * TAU, ALU.min, ALU.max)\
                        .then_inc(diff_ready, 1)
                if part == 2:
                    decayed(2, 3, expo[:, 0])
                    difference(0, P, P - 1, -1).then_inc(diff_ready, 1)
                if part == 3:
                    decayed(3, 4, expo[:, 1])
                    dve.wait_ge(exp_ready, 7 * u + 6)
                    nc.vector.tensor_copy(dec[:, par], expo[:, 0].rearrange("p (c t) -> p c t", t=P)[:, :, P - 1])\
                        .then_inc(dve_step, 1)
                    steps[0] += 1
                    decayed(4, 6, expo[:, 0])

            def mask(n):
                for hd in range(2):
                    m = 2 * n + hd
                    dve.wait_ge(scored, m + 1)
                    step(nc.vector.tensor_tensor(masked[:, m % 2].rearrange("p a b -> p (a b)"), banks[1 + m % 2][:],
                                                 masks[:].rearrange("p a b -> p (a b)"), ALU.mult))
                    if m >= 4:
                        dve.wait_ge(st_used, m - 3)
                    nc.vector.tensor_reduce(out=st[:, m % 4], in_=masked[:, m % 2].rearrange("p a b -> p b a"),
                                            op=ALU.add, axis=AX.X).then_inc(st_ready, 1)

            def advance(n):
                u, i = divmod(n, CH)
                h, p = UNITS[u]
                dve.wait_ge(update_ready, n + 1)
                dve.wait_ge(st_used, 2 * (n + 1))
                for hd in range(2):
                    rows, cols = slice(64 * hd, 64 * hd + 64), slice(GDV * hd, GDV * (hd + 1))
                    last = nc.vector.scalar_tensor_tensor(
                        out=state[rows, p, cols], in0=state[rows, p, cols], scalar=dec[rows, u % 2, i:i + 1],
                        in1=banks[6][rows, cols], op0=ALU.mult, op1=ALU.add)
                last.then_inc(state_ready, 1)
                dve.wait_ge(o_squared, n + 1)
                if n:
                    dve.wait_ge(o_rstd, n)
                nc.vector.tensor_reduce(out=o_ss[:], in_=o_sq[:].rearrange("p (h n) -> p h n", h=2), op=ALU.add,
                                        axis=AX.X).then_inc(o_summed, 1)

            def finish(n):
                u, i = divmod(n, CH)
                h, p = UNITS[u]
                t = h * CH + i
                dve.wait_ge(gate_ready, t + 1)
                dve.wait_ge(o_rstd, n + 1)
                if i == 0 and u >= 2:
                    dve.wait_ge(turned, 2 * (u - 1))
                for hd in range(2):
                    cols = slice(GDV * hd, GDV * (hd + 1))
                    last = nc.vector.scalar_tensor_tensor(
                        out=on[:, u % 2, i, cols], in0=banks[3 + n % 2][:, cols], scalar=o_rs[:, n % 2, hd:hd + 1],
                        in1=gate[:, t, (2 * p + hd) * GDV:(2 * p + hd + 1) * GDV], op0=ALU.mult, op1=ALU.mult)
                last.then_inc(o_done, 1)

            def out(u):
                h, p = UNITS[u]
                for i in range(2):
                    dve.wait_ge(hi_ready, 2 * u + i + 1)
                    nc.vector.tensor_tensor(c.Xlo[:, 2 * p + i, h * UT:(h + 1) * UT], banks[0][:],
                                            c.Xhi[:, 2 * p + i, h * UT:(h + 1) * UT].bitcast(F32), ALU.subtract)\
                        .then_inc(lo_ready, 1)

            def row(g):
                dve.wait_ge(ada_w_used, 2 * (g + 1))
                dve.wait_ge(ada_b_loaded[g % 2], 16 * (g // 2 + 1))
                if g >= 2:
                    dve.wait_ge(ada_stored[g % 2], 16 * (g // 2))
                nc.vector.tensor_tensor(ada_row[:, g % 2], banks[7][0:2, :], ada_b[:, g % 2], ALU.add)\
                    .then_inc(ada_row_ready, 1)

            for i in range(CH):
                prep(0, i)
            dve.wait_ge(mask_loaded, 16)
            mask(0)
            for n in range(CHUNKS):
                u, i = divmod(n, CH)
                if n % 2 == 0 and 0 < n <= PIECES:
                    row(n // 2 - 1)
                if u + 1 < len(UNITS):
                    prep(u + 1, i)
                if n + 1 < CHUNKS:
                    mask(n + 1)
                if n:
                    finish(n - 1)
                advance(n)
                if i == 1 and u:
                    out(u - 1)
            finish(CHUNKS - 1)
            out(len(UNITS) - 1)

        @block.tensor
        def _(pe):
            pe.wait_ge(loaded, 16 * 3)
            for t in range(TT):
                last = nc.tensor.transpose(banks[t // 4][0:GR, (t % 4) * P:(t % 4 + 1) * P], glow[:, t, :], c.ident[:])
            last.then_inc(gl_turned, 1)
            pe.wait_ge(gl_ready, 2)
            pe.wait_ge(ready0, 2)

            def gates(u):
                h, p = UNITS[u]
                if u:
                    pe.wait_ge(low_ready, u)
                if u >= 3:
                    pe.wait_ge(lo_ready, 2 * (u - 2))
                nc.tensor.matmul(banks[0][:], w2[:, p * P:(p + 1) * P], glowT[:, h * UT:(h + 1) * UT],
                                 start=True, stop=True).then_inc(pre_ready, 1)

            def scores(n):
                u, i = divmod(n, CH)
                par = u % 2
                tok = slice(i * P, (i + 1) * P)
                if i == 0:
                    pe.wait_ge(q_used, 5 * (u + 1))
                    pe.wait_ge(k_used, 5 * (u + 1))
                if n:
                    pe.wait_ge(kdt_ready, n)
                nc.tensor.transpose(banks[5][:, 0:P], ks[:, par, NQ, tok], c.ident[:]).then_inc(kd_turned, 1)
                for hd in range(2):
                    m = 2 * n + hd
                    rows = slice(64 * hd, 64 * hd + 64)
                    if m >= 2:
                        pe.wait_ge(st_ready, m - 1)
                    for lv in range(NQ):
                        last = nc.tensor.matmul(banks[1 + m % 2][:, lv * P:(lv + 1) * P], ks[rows, par, lv, tok],
                                                qs[rows, par, lv, tok], start=(lv == 0), stop=True,
                                                skip_group_check=True)
                    last.then_inc(scored, 1)

            def outputs(n):
                u, i = divmod(n, CH)
                h, p = UNITS[u]
                t, par = h * CH + i, u % 2
                tok = slice(i * P, (i + 1) * P)
                vv = v[:, t, 2 * p * GDV:(2 * p + 2) * GDV]
                pe.wait_ge(kdt_ready, n + 1)
                if n:
                    pe.wait_ge(state_ready, n)
                nc.tensor.matmul(banks[6][:, 0:2 * GDV], kdt[:, n % 2], vv, start=True, stop=True)\
                    .then_inc(update_ready, 1)
                if n >= 2:
                    pe.wait_ge(o_done, n - 1)
                ob = banks[3 + n % 2]
                nc.tensor.matmul(ob[:, 0:2 * GDV], qs[:, par, NQ, tok], state[:, p], start=True, stop=True,
                                 skip_group_check=True)
                for hd in range(2):
                    m = 2 * n + hd
                    pe.wait_ge(st_ready, m + 1)
                    last = nc.tensor.matmul(ob[:, GDV * hd:GDV * (hd + 1)], st[:, m % 4],
                                            vv[:, GDV * hd:GDV * (hd + 1)], start=False, stop=True,
                                            skip_group_check=True)
                    last.then_inc(st_used, 1)

            def out(u):
                pe.wait_ge(o_done, (u + 1) * CH)
                ahead = min(u + 3, len(UNITS))
                pe.wait_ge(mag_ready, ahead)
                pe.wait_ge(low_ready, ahead)
                for hd in range(2):
                    if 2 * u + hd:
                        pe.wait_ge(lo_ready, 2 * u + hd)
                    for i in range(CH):
                        last = nc.tensor.transpose(banks[0][:, i * P:(i + 1) * P], on[:, u % 2, i, GDV * hd:GDV * (hd + 1)],
                                                   c.ident[:])
                    last.then_inc(turned, 1)

            def modulate(m):
                g, half = divmod(m, 2)
                if half == 0:
                    pe.wait_ge(cond_ready, 1)
                    if g:
                        pe.wait_ge(ada_row_ready, g)
                pe.wait_ge(ada_w_loaded[m % 4], 16 * (m // 4 + 1))
                for k in range(KT // 2):
                    last = nc.tensor.matmul(banks[7][0:2, :], cond[:, half * (KT // 2) + k, :], ada_w[:, m % 4, k],
                                            start=(half == 0 and k == 0), stop=(half == 1 and k == KT // 2 - 1))
                last.then_inc(ada_w_used, 1)

            gates(0)
            scores(0)
            pe.wait_ge(v_loaded, 16)
            for n in range(CHUNKS):
                u, i = divmod(n, CH)
                if i == 0 and u + 1 < len(UNITS):
                    gates(u + 1)
                if i == 3 or n + 1 == CHUNKS:
                    outputs(n)
                if n + 1 < CHUNKS:
                    scores(n + 1)
                if i != 3:
                    outputs(n)
                if n < PIECES:
                    modulate(n)
                if i == 1 and u:
                    out(u - 1)
            out(len(UNITS) - 1)


def latent_attention(nc, chip, a, d):
    c = chip
    HEADS_OUT = GH * GDV // P
    QT = S // P
    N = MH * QT
    first_chunk = []
    m = 0
    for n in range(N + 1):
        first_chunk.append(m)
        m += (n % QT) // 4 + 1
    with ExitStack() as ctx:
        sb = lambda n, s, dt=F32: c.sb("ma_" + n, s, dt, ctx=ctx)
        sem = lambda n: c.sem("ma_" + n, ctx)
        q_hi, q_lo = sb("q_hi", [MQK, 2, S], F32R), sb("q_lo", [MQK, 2, S], F32R)
        k_hi, k_lo = sb("k_hi", [MQK, 2, S], F32R), sb("k_lo", [MQK, 2, S], F32R)
        v = sb("v", [P, 2, TT, 2, MV], F32R)
        prob = sb("prob", [P, 3, S])
        diag = sb("diag", [P, 3, P])
        o_low = sb("o_low", [MV, NCOL])
        o_sum = sb("o_sum", [MV, NCOL])
        pT_hi, pT_lo = sb("pT_hi", [P, TT, NCOL], F32R), sb("pT_lo", [P, TT, NCOL], F32R)
        low_score, sums, inv = (sb(x, [P, 2]) for x in ("low_score", "sums", "inv"))
        mask_f = sb("mask_f", [1, 2, P])
        mask = sb("mask", [1, 2, P], F32R)
        scores = [ctx.enter_context(nc.psum_tensor(f"ma_scores{i}", [P, S], F32)) for i in range(2)]
        turn_bank = c.banks("ma_turn", ctx, 3)
        o_bank = c.banks("ma_o", ctx, 1)
        loaded = [sem(f"loaded{i}") for i in range(2)]
        mask_ready, scored, low_score_ready, exp_ready = (
            sem("mask_ready"), sem("scored"), sem("low_score_ready"), sem("exp_ready"))
        inv_ready, diag_ready, turned, hi_ready, lo_ready = (
            sem("inv_ready"), sem("diag_ready"), sem("turned"), sem("hi_ready"), sem("lo_ready"))
        x_loaded = sem("x_loaded")
        mod_scale = sb("mod_scale", [P, 2, KT])
        mod_loaded, mod_ready = sem("mod_loaded"), sem("mod_ready")
        o_ready, o_low_ready, o_sum_ready, o_hi, o_lo = (
            sem(x) for x in ("o_ready", "o_low_ready", "o_sum_ready", "o_hi", "o_lo"))
        block = ctx.enter_context(nc.Block())

        @block.sync
        def _(sp):
            for h in range(MH):
                if h >= 2:
                    sp.wait_ge(o_ready, 2 * (h - 1))
                for place, src in ((q_hi[:, h % 2], d["mqk_hi"][0, h]), (q_lo[:, h % 2], d["mqk_lo"][0, h]),
                                   (k_hi[:, h % 2], d["mqk_hi"][1, h]), (k_lo[:, h % 2], d["mqk_lo"][1, h]),
                                   (v[:, h % 2, :, 0], d["mv_hi"][h].rearrange("t p v -> p t v")),
                                   (v[:, h % 2, :, 1], d["mv_lo"][h].rearrange("t p v -> p t v"))):
                    sp.dma_start(place.bitcast(F32), src).then_inc(loaded[h % 2], 16)
                if h == 1:
                    sp.dma_start(c.H[:], a["x"][0].rearrange("(t p) n -> p t n", p=P)).then_inc(x_loaded, 16)
            for i in range(2):
                for place, at in ((c.mod_bias[:, i], 0), (mod_scale[:, i], D)):
                    sp.dma_start(place, d["mod_row"][i, at:at + D].rearrange("(k p) -> p k", p=P)).then_inc(mod_loaded, 16)
            sp.wait_ge(x_loaded, 16)

        @block.gpsimd
        def _(pool):
            nc.gpsimd.memset(mask_f[:], 0.0).then_inc(mask_ready, 1)
            pool.wait_ge(mask_ready, 1)
            nc.gpsimd.memset(mask_f[:, 0, 0:64], 1e30).then_inc(mask_ready, 1)
            nc.gpsimd.memset(mask_f[:, 1, 64:P], 1.0).then_inc(mask_ready, 1)

        @block.tensor
        def _(pe):
            pe.wait_ge(mask_ready, 4)

            def score(n):
                h, qt = divmod(n, QT)
                s = h % 2
                if qt == 0:
                    pe.wait_ge(loaded[s], 96 * (h // 2 + 1))
                if n >= 2:
                    pe.wait_ge(exp_ready, n - 1)
                q = slice(qt * P, (qt + 1) * P)
                keys = (qt + 1) * P
                for at in range(0, keys, NCOL):
                    end = min(at + NCOL, keys)
                    out = scores[n % 2][:, at:end]
                    nc.tensor.matmul(out, q_hi[:, s, q], k_hi[:, s, at:end], start=True, stop=False)
                    nc.tensor.matmul(out, q_hi[:, s, q], k_lo[:, s, at:end], start=False, stop=False)
                    last = nc.tensor.matmul(out, q_lo[:, s, q], k_hi[:, s, at:end], start=False, stop=True)
                last = nc.tensor.matmul(scores[n % 2][:, keys - P:keys], mask[:, 0], mask[:, 1], start=False,
                                        stop=True, skip_group_check=True)
                last.then_inc(scored, 1)

            def turn(n, i):
                qt = n % QT
                if i == 0:
                    pe.wait_ge(diag_ready, n + 1)
                m = first_chunk[n] + i
                if m >= 3:
                    pe.wait_ge(lo_ready, m - 2)
                for j in range(4 * i, min(4 * i + 4, qt + 1)):
                    last = nc.tensor.matmul(turn_bank[m % 3][:, (j % 4) * P:(j % 4 + 1) * P],
                                            prob[:, n % 3, j * P:(j + 1) * P], diag[:, n % 3], start=True, stop=True)
                last.then_inc(turned, 1)

            def values(m):
                h, half = divmod(m, 2)
                pe.wait_ge(lo_ready, first_chunk[4 * m + 4])
                if m:
                    pe.wait_ge(o_sum_ready, m)
                n_k = 4 * half + 4
                for j in range(n_k):
                    at = max(0, j - 4 * half) * P
                    both = v[:, h % 2, j].rearrange("p a v -> p (a v)")
                    nc.tensor.matmul(o_bank[0][:, at:], both, pT_hi[:, j, at:], start=(j == 0), stop=True,
                                     skip_group_check=True)
                    last = nc.tensor.matmul(o_bank[0][0:MV, at:], v[:, h % 2, j, 0], pT_lo[:, j, at:],
                                            start=False, stop=True, skip_group_check=True)
                last.then_inc(o_ready, 1)

            for n in range(3):
                score(n)
            for n in range(N + 1):
                chunks = n % QT // 4 + 1
                if n + 3 < N:
                    score(n + 3)
                if n and n % 4 == 0:
                    values(n // 4 - 1)
                if n < N:
                    turn(n, 0)
                if n < N and chunks == 2:
                    turn(n, 1)

        @block.scalar
        def _(act):
            act.wait_ge(mask_ready, 3)
            nc.scalar.activation(mask[:], mask_f[:], ACT.Copy).then_inc(mask_ready, 1)

            def exp(n):
                keys = (n % QT + 1) * P
                act.wait_ge(low_score_ready, n + 1)
                if n >= 3:
                    act.wait_ge(turned, first_chunk[n - 2])
                nc.scalar.activation(prob[:, n % 3, 0:keys], scores[n % 2][:, 0:keys], ACT.Exp, scale=-1.0,
                                     bias=low_score[:, n % 2:n % 2 + 1], accum_out=sums[:, n % 2:n % 2 + 1])\
                    .then_inc(exp_ready, 1)

            def high(n):
                qt = n % QT
                q = slice((qt % 4) * P, (qt % 4 + 1) * P)
                for i in range(qt // 4 + 1):
                    m = first_chunk[n] + i
                    j, e = 4 * i, min(4 * i + 4, qt + 1)
                    act.wait_ge(turned, m + 1)
                    nc.scalar.activation(pT_hi[:, j:e, q],
                                         turn_bank[m % 3][:, 0:(e - j) * P].rearrange("p (j q) -> p j q", q=P),
                                         ACT.Copy).then_inc(hi_ready, 1)

            def out(m):
                h, half = divmod(m, 2)
                act.wait_ge(o_ready, m + 1)
                if m:
                    act.wait_ge(o_sum_ready, m)
                nc.scalar.activation(o_low[:], o_bank[0][MV:2 * MV, :], ACT.Copy).then_inc(o_low_ready, 1)
                act.wait_ge(o_sum_ready, m + 1)
                rows = slice(64 * (h % 2), 64 * (h % 2) + 64)
                nc.scalar.activation(c.Xhi[rows, HEADS_OUT + h // 2, half * NCOL:(half + 1) * NCOL], o_sum[:],
                                     ACT.Copy).then_inc(o_hi, 1)

            exp(0)
            exp(1)
            for n in range(N):
                if n + 2 < N:
                    exp(n + 2)
                if n % 4 == 0 and n:
                    out(n // 4 - 1)
                high(n)
            out(N // 4 - 1)

        @block.vector
        def _(dve):
            def row_min(n):
                keys = (n % QT + 1) * P
                i = slice(n % 2, n % 2 + 1)
                dve.wait_ge(scored, n + 1)
                nc.vector.tensor_reduce(out=low_score[:, i], in_=scores[n % 2][:, 0:keys], op=ALU.min, axis=AX.X)\
                    .then_inc(low_score_ready, 1)

            def invert(n):
                i = slice(n % 2, n % 2 + 1)
                dve.wait_ge(exp_ready, n + 1)
                nc.vector.reciprocal(inv[:, i], sums[:, i]).then_inc(inv_ready, 1)
                dve.wait_ge(inv_ready, n + 1)
                nc.vector.tensor_scalar(diag[:, n % 3], c.ident[:], inv[:, i], None, ALU.mult).then_inc(diag_ready, 1)

            def low(n):
                qt = n % QT
                q = slice((qt % 4) * P, (qt % 4 + 1) * P)
                for i in range(qt // 4 + 1):
                    m = first_chunk[n] + i
                    j, e = 4 * i, min(4 * i + 4, qt + 1)
                    dve.wait_ge(hi_ready, m + 1)
                    nc.vector.tensor_tensor(pT_lo[:, j:e, q],
                                            turn_bank[m % 3][:, 0:(e - j) * P].rearrange("p (j q) -> p j q", q=P),
                                            pT_hi[:, j:e, q].bitcast(F32), ALU.subtract).then_inc(lo_ready, 1)

            def out(m):
                h, half = divmod(m, 2)
                dve.wait_ge(o_low_ready, m + 1)
                if m:
                    dve.wait_ge(o_lo, m)
                nc.vector.tensor_tensor(o_sum[:], o_bank[0][0:MV, :], o_low[:], ALU.add).then_inc(o_sum_ready, 1)
                dve.wait_ge(o_hi, m + 1)
                rows = slice(64 * (h % 2), 64 * (h % 2) + 64)
                cols = slice(half * NCOL, (half + 1) * NCOL)
                nc.vector.tensor_tensor(c.Xlo[rows, HEADS_OUT + h // 2, cols], o_sum[:],
                                        c.Xhi[rows, HEADS_OUT + h // 2, cols].bitcast(F32), ALU.subtract)\
                    .then_inc(o_lo, 1)

            row_min(0)
            row_min(1)
            invert(0)
            row_min(2)
            invert(1)
            for n in range(N):
                if n + 3 < N:
                    row_min(n + 3)
                if n + 2 < N:
                    invert(n + 2)
                if n % 4 == 0 and n:
                    out(n // 4 - 1)
                low(n)
            out(N // 4 - 1)
            dve.wait_ge(mod_loaded, 64)
            for i in range(2):
                nc.vector.scalar_tensor_tensor(out=c.mod_gain[:, i], in0=mod_scale[:, i], scalar=1.0,
                                               in1=c.gains[:, 3], op0=ALU.add, op1=ALU.mult).then_inc(mod_ready, 1)


def project_into_residual(nc, chip, name, weights, gate=None):
    c = chip
    groups = [[weights[k * P:(k + 1) * P, n * NCOL:(n + 1) * NCOL] for k in range(KT)] for n in range(HALVES)]
    with ExitStack() as ctx:
        result_ready = c.sem(f"{name}_result_ready", ctx)
        added = c.sem(f"{name}_added", ctx)
        gated = c.sem(f"{name}_gated", ctx)
        w = Weights(c, name, ctx, groups, (result_ready, [TT, 2 * TT]))
        gate_sb = c.sb(f"{name}_gate", [P, D], ctx=ctx) if gate is not None else None
        gate_loaded = c.sem(f"{name}_gate_loaded", ctx)
        part = c.sb(f"{name}_part", [P, 2, NCOL], ctx=ctx) if gate is not None else None
        squares = c.sb(f"{name}_squares", [P, D], ctx=ctx)
        summed = c.sem(f"{name}_summed", ctx)
        banks = c.banks(f"{name}_ps", ctx)
        outs = [(g, t) for g in range(HALVES) for t in range(TT)]
        block = ctx.enter_context(nc.Block())

        @block.sync
        def _(sp):
            if gate is not None:
                sp.dma_start(gate_sb[:], gate).then_inc(gate_loaded, 16)
            w.load(sp)

        @block.gpsimd
        def _(pool):
            w.split_lo(pool)

        @block.scalar
        def _(act):
            for g in range(HALVES):
                w.split_hi_group(act, g)
            for t in range(TT):
                act.wait_ge(added, TT + t + 1)
                if t:
                    act.wait_ge(summed, t)
                nc.scalar.activation(squares[:], c.H[:, t, :], ACT.Square, accum_out=c.sums[:, t:t + 1])\
                    .then_inc(summed, 1)

        @block.tensor
        def _(pe):
            for n, (g, t) in enumerate(outs):
                if n >= 8:
                    pe.wait_ge(added, n - 7)
                tok = slice(t * P, (t + 1) * P)
                product(nc, banks[n % 8][:],
                        [((c.Xhi[:, k, tok], c.Xlo[:, k, tok]), (w.hi[:, g, k], w.lo[:, g, k])) for k in range(KT)],
                        NCOL, result_ready,
                        (lambda k: pe.wait_ge(w.lo_ready, w.first[g] + k + 1)) if t == 0 else None)

        @block.vector
        def _(dve):
            if gate is not None:
                dve.wait_ge(gate_loaded, 16)
            for n, (g, t) in enumerate(outs):
                cols = slice(g * NCOL, (g + 1) * NCOL)
                dve.wait_ge(result_ready, n + 1)
                src = banks[n % 8][:]
                if gate is not None:
                    nc.vector.tensor_tensor(part[:, n % 2], src, gate_sb[:, cols], ALU.mult).then_inc(gated, 1)
                    dve.wait_ge(gated, n + 1)
                    src = part[:, n % 2]
                nc.vector.tensor_tensor(c.H[:, t, cols], c.H[:, t, cols], src, ALU.add).then_inc(added, 1)


def mlp(nc, chip, a):
    c = chip
    G = D_FF // NCOL
    FT = NCOL // P
    with ExitStack() as ctx:
        sb = lambda n, s, dt=F32: c.sb("mlp_" + n, s, dt, ctx=ctx)
        sem = lambda n: c.sem("mlp_" + n, ctx)
        stage = sb("stage", [P, SLOTS, NCOL])
        w_hi, w_lo = sb("w_hi", [P, 2, KT, NCOL], F32R), sb("w_lo", [P, 2, KT, NCOL], F32R)
        h_hi, h_lo = sb("h_hi", [P, FT, S], F32R), sb("h_lo", [P, FT, S], F32R)
        act_r = sb("act_r", [P, 2, NCOL])
        loaded = [sem(f"loaded{i}") for i in range(SLOTS)]
        w_hi_ready, w_lo_ready = sem("w_hi_ready"), sem("w_lo_ready")
        up_ready, relu_ready, square_ready, h_hi_ready, h_lo_ready = (
            sem("up_ready"), sem("relu_ready"), sem("square_ready"), sem("h_hi_ready"), sem("h_lo_ready"))
        down_ready, added, summed = sem("down_ready"), sem("added"), sem("summed")
        up_bank = c.banks("mlp_up", ctx, 3)
        down_bank = c.banks("mlp_down", ctx, 5)
        UP, DOWN = FT * HALVES, TT * HALVES
        block = ctx.enter_context(nc.Block())

        def rows(n):
            g, x = divmod(n, 2 * KT)
            which, k = divmod(x, KT)
            if which == 0:
                return a["w_mlp_up"][0, k * P:(k + 1) * P, g * NCOL:(g + 1) * NCOL]
            j, half = divmod(k, HALVES)
            at = g * NCOL + j * P
            return a["w_mlp_down"][0, at:at + P, half * NCOL:(half + 1) * NCOL]

        @block.sync
        def _(sp):
            for n in range(G * 2 * KT):
                if n >= SLOTS:
                    sp.wait_ge(w_lo_ready, n - SLOTS + 1)
                sp.dma_start(stage[:, n % SLOTS], rows(n)).then_inc(loaded[n % SLOTS], 16)

        @block.gpsimd
        def _(pool):
            for n in range(G * 2 * KT):
                which, k = divmod(n % (2 * KT), KT)
                pool.wait_ge(w_hi_ready, n + 1)
                nc.gpsimd.tensor_tensor(w_lo[:, which, k], stage[:, n % SLOTS], w_hi[:, which, k].bitcast(F32),
                                        ALU.subtract).then_inc(w_lo_ready, 1)

        @block.scalar
        def _(act):
            def split(n):
                g, x = divmod(n, 2 * KT)
                which, k = divmod(x, KT)
                act.wait_ge(loaded[n % SLOTS], 16 * (n // SLOTS + 1))
                if g and k == 0:
                    act.wait_ge(*((up_ready, UP * g) if which == 0 else (down_ready, DOWN * g)))
                nc.scalar.activation(w_hi[:, which, k], stage[:, n % SLOTS], ACT.Copy).then_inc(w_hi_ready, 1)

            for n in range(KT):
                split(n)
            for g in range(G):
                for o in range(UP):
                    n = g * UP + o
                    h, f = divmod(o, FT)
                    split(g * 2 * KT + KT + o)
                    act.wait_ge(up_ready, n + 1)
                    if n >= 2:
                        act.wait_ge(h_lo_ready, n - 1)
                    nc.scalar.activation(act_r[:, n % 2], up_bank[n % 3][:], ACT.Relu).then_inc(relu_ready, 1)
                    act.wait_ge(square_ready, n + 1)
                    if g and o == 0:
                        act.wait_ge(down_ready, DOWN * g)
                    nc.scalar.activation(h_hi[:, f, h * NCOL:(h + 1) * NCOL], act_r[:, n % 2], ACT.Copy)\
                        .then_inc(h_hi_ready, 1)
                if g + 1 < G:
                    for k in range(KT):
                        split((g + 1) * 2 * KT + k)
            act.wait_ge(h_lo_ready, G * UP)
            for t in range(TT):
                act.wait_ge(added, (G - 1) * DOWN + HALVES * (t + 1))
                if t:
                    act.wait_ge(summed, t)
                nc.scalar.activation(act_r[:].rearrange("p a n -> p (a n)"), c.H[:, t, :], ACT.Square,
                                     accum_out=c.sums[:, t:t + 1]).then_inc(summed, 1)

        @block.vector
        def _(dve):
            for g in range(G):
                for o in range(UP):
                    n = g * UP + o
                    h, f = divmod(o, FT)
                    dve.wait_ge(relu_ready, n + 1)
                    nc.vector.tensor_tensor(act_r[:, n % 2], act_r[:, n % 2], act_r[:, n % 2], ALU.mult)\
                        .then_inc(square_ready, 1)
                    dve.wait_ge(h_hi_ready, n + 1)
                    nc.vector.tensor_tensor(h_lo[:, f, h * NCOL:(h + 1) * NCOL], act_r[:, n % 2],
                                            h_hi[:, f, h * NCOL:(h + 1) * NCOL].bitcast(F32), ALU.subtract)\
                        .then_inc(h_lo_ready, 1)
                for o in range(DOWN):
                    n = g * DOWN + o
                    t, half = divmod(o, HALVES)
                    cols = slice(half * NCOL, (half + 1) * NCOL)
                    dve.wait_ge(down_ready, n + 1)
                    nc.vector.tensor_tensor(c.H[:, t, cols], c.H[:, t, cols], down_bank[n % 5][:], ALU.add)\
                        .then_inc(added, 1)

        @block.tensor
        def _(pe):
            for g in range(G):
                for o in range(UP):
                    n = g * UP + o
                    h, f = divmod(o, FT)
                    if n >= 3:
                        pe.wait_ge(relu_ready, n - 2)
                    product(nc, up_bank[n % 3][:],
                            [((w_hi[:, 0, k, f * P:(f + 1) * P], w_lo[:, 0, k, f * P:(f + 1) * P]),
                              (c.Xhi[:, k, h * NCOL:(h + 1) * NCOL], c.Xlo[:, k, h * NCOL:(h + 1) * NCOL]))
                             for k in range(KT)], NCOL, up_ready,
                            (lambda k: pe.wait_ge(w_lo_ready, g * 2 * KT + k + 1)) if o == 0 else None)
                for o in range(DOWN):
                    n = g * DOWN + o
                    t, half = divmod(o, HALVES)
                    tok = slice(t * P, (t + 1) * P)
                    if o == 0:
                        pe.wait_ge(h_lo_ready, g * UP + FT)
                    if o == DOWN // 2:
                        pe.wait_ge(h_lo_ready, (g + 1) * UP)
                    if n >= 5:
                        pe.wait_ge(added, n - 4)
                    product(nc, down_bank[n % 5][:],
                            [((h_hi[:, j, tok], h_lo[:, j, tok]),
                              (w_hi[:, 1, HALVES * j + half], w_lo[:, 1, HALVES * j + half]))
                             for j in range(FT)], NCOL, down_ready,
                            (lambda j: pe.wait_ge(w_lo_ready, g * 2 * KT + KT + HALVES * j + half + 1))
                            if o < HALVES else None)


def ple(nc, chip, a):
    c = chip
    PK = 2
    proj, gate_w = a["w_ple_proj"][0], a["w_ple_gate"][0]
    groups = []
    for half in range(HALVES):
        cols = slice(half * NCOL, (half + 1) * NCOL)
        groups.append([proj[k * P:(k + 1) * P, cols] for k in range(PK)])
        groups.append([gate_w[k * P:(k + 1) * P, cols] for k in range(KT)])
    with ExitStack() as ctx:
        sb = lambda n, s, dt=F32: c.sb("ple_" + n, s, dt, ctx=ctx)
        sem = lambda n: c.sem("ple_" + n, ctx)
        gate_ready = sem("gate_ready")
        w = Weights(c, "ple", ctx, groups, (gate_ready, [TT, TT, 2 * TT, 2 * TT]))
        pt = sb("pt", [P, 4, PK * P])
        pT_hi, pT_lo = sb("pT_hi", [P, PK, S], F32R), sb("pT_lo", [P, PK, S], F32R)
        bias = sb("bias", [P, D])
        logit = sb("logit", [P, 2, NCOL])
        banks = c.banks("ple_ps", ctx)
        loaded, bias_loaded = [sem(f"loaded{i}") for i in range(2)], sem("bias_loaded")
        turned, hi_ready, lo_ready = sem("turned"), sem("hi_ready"), sem("lo_ready")
        proj_ready, summed = sem("proj_ready"), sem("summed")
        squares = pt[:].rearrange("p t n -> p (t n)")
        logit_ready, sig_ready, mul_ready, added = sem("logit_ready"), sem("sig_ready"), sem("mul_ready"), sem("added")
        block = ctx.enter_context(nc.Block())

        @block.sync
        def _(sp):
            for h in range(2):
                if h:
                    sp.wait_ge(turned, 2)
                sp.dma_start(pt[:], a["p"][0, 0, h * NCOL:(h + 1) * NCOL, :].rearrange("(t p) n -> p t n", p=P))\
                    .then_inc(loaded[h], 16)
                if h == 0:
                    sp.dma_start(bias[:], a["b_ple_gate"].to_broadcast([P, D])).then_inc(bias_loaded, 16)
            w.load(sp)

        @block.gpsimd
        def _(pool):
            w.split_lo(pool)

        @block.tensor
        def _(pe):
            for h in range(2):
                pe.wait_ge(loaded[h], 16)
                for k in range(PK):
                    for t in range(4):
                        last = nc.tensor.transpose(banks[2 * h + k][:, t * P:(t + 1) * P],
                                                   pt[:, t, k * P:(k + 1) * P], c.ident[:])
                    last.then_inc(turned, 1)
            pe.wait_ge(lo_ready, 4)
            for half in range(HALVES):
                for t in range(TT):
                    n = half * TT + t
                    tok = slice(t * P, (t + 1) * P)
                    if n >= 4:
                        pe.wait_ge(added, n - 3)
                    for g, x, kt, ready, bank in ((2 * half, (pT_hi, pT_lo), PK, proj_ready, 2 * (n % 4)),
                                                  (2 * half + 1, (c.Xhi, c.Xlo), KT, gate_ready, 2 * (n % 4) + 1)):
                        product(nc, banks[bank][:],
                                [((x[0][:, k, tok], x[1][:, k, tok]), (w.hi[:, g % 2, k], w.lo[:, g % 2, k]))
                                 for k in range(kt)], NCOL, ready,
                                (lambda k: pe.wait_ge(w.lo_ready, w.first[g] + k + 1)) if t == 0 else None)

        @block.scalar
        def _(act):
            for n in range(4):
                h, k = divmod(n, PK)
                act.wait_ge(turned, n + 1)
                nc.scalar.activation(pT_hi[:, k, h * NCOL:(h + 1) * NCOL], banks[n][:], ACT.Copy).then_inc(hi_ready, 1)
            w.split_hi_group(act, 0)
            w.split_hi_group(act, 1)

            def square(t):
                act.wait_ge(added, TT + t + 1)
                if t:
                    act.wait_ge(summed, t)
                nc.scalar.activation(squares, c.H[:, t, :], ACT.Square,
                                     accum_out=c.sums[:, t:t + 1]).then_inc(summed, 1)

            for n in range(2 * TT):
                act.wait_ge(logit_ready, n + 1)
                nc.scalar.activation(logit[:, n % 2], logit[:, n % 2], ACT.Sigmoid).then_inc(sig_ready, 1)
                if n == TT - 1:
                    w.split_hi_group(act, 2)
                    w.split_hi_group(act, 3)
                if n > TT:
                    square(n - TT - 1)
            square(TT - 1)

        @block.vector
        def _(dve):
            for n in range(4):
                h, k = divmod(n, PK)
                dve.wait_ge(hi_ready, n + 1)
                nc.vector.tensor_tensor(pT_lo[:, k, h * NCOL:(h + 1) * NCOL], banks[n][:],
                                        pT_hi[:, k, h * NCOL:(h + 1) * NCOL].bitcast(F32), ALU.subtract)\
                    .then_inc(lo_ready, 1)
            dve.wait_ge(bias_loaded, 16)
            for n in range(2 * TT):
                half, t = divmod(n, TT)
                cols = slice(half * NCOL, (half + 1) * NCOL)
                dve.wait_ge(gate_ready, n + 1)
                nc.vector.tensor_tensor(logit[:, n % 2], banks[2 * (n % 4) + 1][:], bias[:, cols], ALU.add)\
                    .then_inc(logit_ready, 1)
                dve.wait_ge(sig_ready, n + 1)
                dve.wait_ge(proj_ready, n + 1)
                nc.vector.tensor_tensor(logit[:, n % 2], banks[2 * (n % 4)][:], logit[:, n % 2], ALU.mult)\
                    .then_inc(mul_ready, 1)
                dve.wait_ge(mul_ready, n + 1)
                nc.vector.tensor_tensor(c.H[:, t, cols], c.H[:, t, cols], logit[:, n % 2], ALU.add).then_inc(added, 1)


def differential_project(nc, chip, a, d, ctx_hi, ctx_lo):
    c = chip
    WIN = a["da_w_in_2"][0]
    Q_G, K_G, V_G, Z_G = (0, 1), (2, 3), (4, 5), (6, 7)
    G = 8
    groups = [[WIN[k * P:(k + 1) * P, g * NCOL:(g + 1) * NCOL] for k in range(KT)] for g in range(G)]
    tiles = {g: TT + CT if g in K_G + V_G else TT for g in range(G)}
    outs = [(g, o) for g in range(G) for o in range(tiles[g])]
    done_at = [sum(tiles[x] for x in range(g + 1)) for g in range(G)]
    rope = [n for n, (g, o) in enumerate(outs) if g in Q_G + K_G]
    R = len(rope)
    BANKS = 4
    Q_SCALE = -DD ** -0.5
    with ExitStack() as ctx:
        sb = lambda n, s, dt=F32: c.sb("dp_" + n, s, dt, ctx=ctx)
        sem = lambda n: c.sem("dp_" + n, ctx)
        result_ready = sem("result_ready")
        w = Weights(c, "dp", ctx, groups, (result_ready, done_at))
        cos, sin = sb("cos", [P, TT, 32]), sb("sin", [P, TT, 32])
        tmp = sb("tmp", [P, 4, NCOL // 2])
        turned_in = sb("turned_in", [P, 2, 8, 2, DD])
        out_hi, out_lo = sb("out_hi", [P, 2 * NCOL], F32R), sb("out_lo", [P, 2 * NCOL], F32R)
        banks = c.banks("dp_ps", ctx, BANKS)
        turn = [ctx.enter_context(nc.psum_tensor(f"dp_turn{i}", [P, 2 * NCOL], F32)) for i in range(2)]
        loaded = sem("loaded")
        dve_step, doubled, roped, turned, hi_ready, lo_ready, stored = (
            sem("dve_step"), sem("doubled"), sem("roped"), sem("turned"), sem("hi_ready"), sem("lo_ready"), sem("stored"))
        block = ctx.enter_context(nc.Block())
        N = len(outs)
        stores_upto = [0]
        for g, o in outs:
            stores_upto.append(stores_upto[-1] + (1 if g in Q_G + Z_G else 2))

        @block.sync
        def _(sp):
            sp.dma_start(cos[:], a["da_cos"].rearrange("(t p) n -> p t n", p=P)).then_inc(loaded, 16)
            sp.dma_start(sin[:], a["da_sin"].rearrange("(t p) n -> p t n", p=P)).then_inc(loaded, 16)
            w.load(sp)

        @block.gpsimd
        def _(pool):
            w.split_lo(pool)

        @block.tensor
        def _(pe):
            def turns(n):
                i = n % 2
                is_q = outs[n][0] in Q_G
                pe.wait_ge(*((doubled, n + 1) if is_q else (roped, n + 1)))
                if n >= 2:
                    pe.wait_ge(lo_ready, n - 1)
                for m in range(8):
                    x = turned_in[:, i, m].rearrange("p a b -> p (a b)") if is_q else turned_in[:, i, m, 0]
                    last = nc.tensor.transpose(turn[i][0:x.shape[1], m * P:(m + 1) * P], x, c.ident[:])
                last.then_inc(turned, 1)

            for n, (g, o) in enumerate(outs):
                if n >= BANKS:
                    m = n - BANKS
                    pe.wait_ge(*((roped, m + 1) if m < R else (lo_ready, m + 1)))
                terms = []
                xs, tile = ((c.Xhi, c.Xlo), o) if o < TT else ((ctx_hi, ctx_lo), o - TT)
                for k in range(KT):
                    ww = w.hi[:, g % 2, k], w.lo[:, g % 2, k]
                    if g in Z_G:
                        f, h = divmod(o, HALVES)
                        terms.append((tuple(y[:, f * P:(f + 1) * P] for y in ww),
                                      tuple(y[:, k, h * NCOL:(h + 1) * NCOL] for y in xs)))
                    else:
                        terms.append((tuple(y[:, k, tile * P:(tile + 1) * P] for y in xs), ww))
                product(nc, banks[n % BANKS][:], terms, NCOL, result_ready,
                        (lambda k: pe.wait_ge(w.lo_ready, w.first[g] + k + 1)) if o == 0 else None)
                if 1 <= n <= R:
                    turns(n - 1)

        def rows_of(g):
            return P if g in Q_G else DD

        def places(n):
            g, o = outs[n]
            hs = slice(4 * (g % 2), 4 * (g % 2) + 4)
            if g in Q_G:
                return [(d["dq"][hs, :, :, o * P:(o + 1) * P].rearrange("h z p s -> p h z s"), 0)]
            if g in K_G:
                return [(d[x][hs, :, :, o * P:(o + 1) * P].rearrange("h z p s -> p h z s"), i)
                        for i, x in enumerate(("dk_hi", "dk_lo"))]
            if g in V_G:
                return [(d[x][hs, :, o, :].rearrange("h p n -> p h n"), i) for i, x in enumerate(("dv_hi", "dv_lo"))]
            f, h = divmod(o, HALVES)
            return [(d["dz"][4 * (g % 2) + f, :, h * NCOL:(h + 1) * NCOL], 0)]

        @block.scalar
        def _(act):
            def store(n):
                g, o = outs[n]
                act.wait_ge(lo_ready, n + 1)
                for place, which in places(n):
                    t = (out_hi, out_lo)[which]
                    if g in Q_G + K_G:
                        src = t[0:rows_of(g)].bitcast(F32).rearrange("p (h z s) -> p h z s", h=4, z=2)
                        for z in range(2):
                            act.dma_start(place[:, :, z], src[:, :, z]).then_inc(stored, 16)
                    elif g in V_G:
                        act.dma_start(place, t[:, 0:NCOL].bitcast(F32).rearrange("p (h n) -> p h n", h=4)).then_inc(stored, 16)
                    else:
                        act.dma_start(place, t[:, 0:NCOL].bitcast(F32)).then_inc(stored, 16)

            def n_stores(n):
                g, _ = outs[n]
                return {True: 2, False: 1}[g in Q_G + K_G] * len(places(n))

            total = [0]
            w.split_hi_group(act, 0)
            for n, (g, o) in enumerate(outs):
                if g + 1 < G and o < KT:
                    w.split_hi(act, w.first[g + 1] + o)
                if n:
                    store(n - 1)
                    total[0] += n_stores(n - 1)
                    act.wait_ge(stored, 16 * total[0])
                if g in Q_G + K_G:
                    act.wait_ge(turned, n + 1)
                    r = rows_of(g)
                    nc.scalar.activation(out_hi[0:r], turn[n % 2][0:r], ACT.Copy, scale=Q_SCALE if g in Q_G else 1.0)\
                        .then_inc(hi_ready, 1)
                else:
                    act.wait_ge(result_ready, n + 1)
                    nc.scalar.activation(out_hi[:, 0:NCOL] if g in V_G else out_hi[:, 0:NCOL].bitcast(F32),
                                         banks[n % BANKS][:], ACT.Copy if g in V_G else ACT.Silu).then_inc(hi_ready, 1)
            store(N - 1)
            total[0] += n_stores(N - 1)
            act.wait_ge(stored, 16 * total[0])

        @block.vector
        def _(dve):
            dve.wait_ge(loaded, 32)
            steps = [0]

            def step(ins):
                steps[0] += 1
                ins.then_inc(dve_step, 1)
                dve.wait_ge(dve_step, steps[0])

            def low(n):
                g, o = outs[n]
                dve.wait_ge(hi_ready, n + 1)
                if g in Q_G:
                    nc.vector.scalar_tensor_tensor(out=out_hi[64:P, :], in0=turn[n % 2][64:P, :], scalar=Q_SCALE,
                                                   in1=out_hi[64:P, :].bitcast(F32), op0=ALU.mult,
                                                   op1=ALU.subtract).then_inc(lo_ready, 1)
                elif g in K_G:
                    nc.vector.tensor_tensor(out_lo[0:DD], turn[n % 2][0:DD], out_hi[0:DD].bitcast(F32), ALU.subtract)\
                        .then_inc(lo_ready, 1)
                elif g in V_G:
                    nc.vector.tensor_tensor(out_lo[:, 0:NCOL], banks[n % BANKS][:], out_hi[:, 0:NCOL].bitcast(F32),
                                            ALU.subtract).then_inc(lo_ready, 1)
                else:
                    nc.vector.memset(tmp[0:1, 0, 0:1], 0.0).then_inc(lo_ready, 1)

            for n, (g, o) in enumerate(outs):
                if n < R:
                    dve.wait_ge(result_ready, n + 1)
                    dst = turned_in[:, n % 2, :, 0]
                    if n >= 2:
                        dve.wait_ge(turned, n - 1)
                    if o < TT:
                        x = banks[n % BANKS][:].rearrange("p (m a b q) -> p m a b q", a=2, b=2, q=16)
                        y = dst.rearrange("p m (a b q) -> p m a b q", a=2, b=2, q=16)
                        cs, sn = (t[:, o].rearrange("p (a q) -> p a q", a=2).unsqueeze(1).to_broadcast([P, 8, 2, 16])
                                  for t in (cos, sin))
                        if n:
                            dve.wait_ge(roped, n)
                        for i, (f0, f1, op) in enumerate(((cs, sn, ALU.subtract), (sn, cs, ALU.add))):
                            u, v = (tmp[:, 2 * i + j].rearrange("p (m a q) -> p m a q", a=2, q=16) for j in range(2))
                            nc.vector.tensor_tensor(u, x[:, :, :, 0], f0, ALU.mult).then_inc(dve_step, 1)
                            steps[0] += 1
                            step(nc.vector.tensor_tensor(v, x[:, :, :, 1], f1, ALU.mult))
                            last = nc.vector.tensor_tensor(y[:, :, :, i], u, v, op)
                            last.then_inc(*((roped, 1) if i else (dve_step, 1)))
                            steps[0] += 1 - i
                    else:
                        nc.vector.tensor_copy(dst, banks[n % BANKS][:].rearrange("p (m n) -> p m n", m=8)).then_inc(roped, 1)
                    if g in Q_G:
                        dve.wait_ge(roped, n + 1)
                        nc.vector.tensor_copy(turned_in[:, n % 2, :, 1], dst).then_inc(doubled, 1)
                    if n:
                        low(n - 1)
                    if n == R - 1:
                        low(n)
                else:
                    low(n)


def differential_attention(nc, chip, a, d):
    c = chip
    K = S + CTX
    KB = K // P
    QT = S // P
    N = DH * QT
    CHUNKS = -(-KB // 4)
    SHARE = 5 * P
    PIECES = [(at, min(at + NCOL, K)) for at in range(0, K, NCOL)]
    with ExitStack() as ctx:
        sb = lambda n, s, dt=F32: c.sb("da_" + n, s, dt, ctx=ctx)
        sem = lambda n: c.sem("da_" + n, ctx)
        q = sb("q", [P, 2, 2, S], F32R)
        k_hi, k_lo = sb("k_hi", [P, 2, 2, K], F32R), sb("k_lo", [P, 2, 2, K], F32R)
        v_hi, v_lo = sb("v_hi", [P, 2, KB, P], F32R), sb("v_lo", [P, 2, KB, P], F32R)
        prob = sb("prob", [P, 2, 2, K])
        aT_hi, aT_lo = sb("aT_hi", [P, KB, NCOL], F32R), sb("aT_lo", [P, KB, NCOL], F32R)
        low_score, sums, inv = (sb(x, [P, 2, 2]) for x in ("low_score", "sums", "inv"))
        lam_in, lam_prod = sb("lam_in", [P, 2, 2, DD]), sb("lam_prod", [P, 2, DD])
        lam_sum, lam_exp, lam = sb("lam_sum", [P, 2]), sb("lam_exp", [P, 2]), sb("lam", [P, 1])
        o_sb = sb("o_sb", [P, 2, NCOL])
        ratio, diag = sb("ratio", [P, 2, 1]), sb("diag", [P, 2, P])
        scores = [ctx.enter_context(nc.psum_tensor(f"da_scores{i}", [P, 3 * NCOL], F32)) for i in range(2)]
        turn_bank = c.banks("da_turn", ctx, 2)
        loaded = [sem(f"loaded{i}") for i in range(2)]
        lam_loaded, lam_step, lam_summed, lam_exped = (
            sem("lam_loaded"), sem("lam_step"), sem("lam_summed"), sem("lam_exped"))
        scored, low_score_ready, exp_ready = sem("scored"), sem("low_score_ready"), sem("exp_ready")
        inv_ready, ratio_ready, diag_ready, prob_ready, rest_scaled, rest_ready = (
            sem(x) for x in ("inv_ready", "ratio_ready", "diag_ready", "prob_ready", "rest_scaled", "rest_ready"))
        turned, hi_ready, lo_ready = sem("turned"), sem("hi_ready"), sem("lo_ready")
        o_ready, o_copied = sem("o_ready"), sem("o_copied")
        o_stored = [sem(f"o_stored{i}") for i in range(2)]
        block = ctx.enter_context(nc.Block())

        @block.sync
        def _(sp):
            sp.dma_start(lam_in[:, 0], a["da_lam_q_2"].to_broadcast([P, 2, DD])).then_inc(lam_loaded, 16)
            sp.dma_start(lam_in[:, 1], a["da_lam_k_2"].to_broadcast([P, 2, DD])).then_inc(lam_loaded, 16)
            for h in range(DH):
                s = h % 2
                if h >= 2:
                    sp.wait_ge(o_ready, 2 * (h - 1))
                hi, lo = (d[x][h].rearrange("z p s -> p z s") for x in ("dk_hi", "dk_lo"))
                for place, src in ((q[:, s], d["dq"][h].rearrange("z p s -> p z s")),
                                   (k_hi[0:DD, s], hi), (k_hi[DD:P, s], hi), (k_lo[0:DD, s], lo), (k_lo[DD:P, s], lo),
                                   (v_hi[:, s], d["dv_hi"][h]), (v_lo[:, s], d["dv_lo"][h])):
                    sp.dma_start(place.bitcast(F32), src).then_inc(loaded[s], 16)

        def chunk_bank(m):
            g, k = divmod(m, 4 * CHUNKS)
            return turn_bank[(g + max(k, 2)) % 2]

        def wait_bank_read(pe, m):
            g, k = divmod(m, 4 * CHUNKS)
            if k == 3:
                if g:
                    pe.wait_ge(o_copied, g)
            elif m:
                pe.wait_ge(lo_ready, m if k < 3 else m - 1)

        @block.tensor
        def _(pe):
            def score(n, z):
                h, qt = divmod(n, QT)
                s = h % 2
                if qt == 0 and z == 0:
                    pe.wait_ge(loaded[s], 16 * 7 * (h // 2 + 1))
                if n:
                    pe.wait_ge(exp_ready, 2 * (n - 1) + z + 1)
                for at, end in PIECES:
                    for i, k in enumerate((k_hi, k_lo)):
                        last = nc.tensor.matmul(scores[z][:, at:end], q[:, s, z, qt * P:(qt + 1) * P],
                                                k[:, s, z, at:end], start=(i == 0), stop=(i == 1))
                last.then_inc(scored, 1)

            def turn(n, i):
                if i == 0:
                    pe.wait_ge(prob_ready, n + 1)
                if (i + 1) * NCOL > SHARE >= i * NCOL:
                    pe.wait_ge(rest_ready, n + 1)
                bank = chunk_bank(CHUNKS * n + i)
                wait_bank_read(pe, CHUNKS * n + i)
                for j in range(4 * i, min(4 * i + 4, KB)):
                    last = nc.tensor.matmul(bank[:, (j % 4) * P:(j % 4 + 1) * P],
                                            prob[:, n % 2, 0, j * P:(j + 1) * P], diag[:, n % 2],
                                            start=True, stop=True)
                last.then_inc(turned, 1)

            def values(n, i):
                m = n // 4
                v = m // 2 % 2
                pe.wait_ge(lo_ready, CHUNKS * n + i + 1)
                if i == 0:
                    pe.wait_ge(lo_ready, CHUNKS * n + 2)
                for j in range(4 * i, min(4 * i + 4, KB)):
                    for x, y in ((v_hi, aT_hi), (v_hi, aT_lo), (v_lo, aT_hi)):
                        last = nc.tensor.matmul(turn_bank[m % 2][:], x[:, v, j], y[:, j],
                                                start=(j == 0 and x is v_hi and y is aT_hi),
                                                stop=(j == KB - 1 and x is v_lo))
                if i == CHUNKS - 1:
                    last.then_inc(o_ready, 1)

            for n in range(2):
                score(n, 0)
                score(n, 1)
            for n in range(N + 1):
                for i in range(CHUNKS):
                    if n % 4 == 0 and n:
                        values(n - 1, i)
                    if n < N:
                        turn(n, i)
                    if n + 2 < N and i != 1:
                        score(n + 2, i // 2)

        @block.scalar
        def _(act):
            act.wait_ge(lam_summed, 1)
            nc.scalar.activation(lam_exp[:], lam_sum[:], ACT.Exp).then_inc(lam_exped, 1)

            def exp(n, z):
                act.wait_ge(low_score_ready, 2 * n + z + 1)
                if n >= 2:
                    act.wait_ge(turned, CHUNKS * (n - 1))
                nc.scalar.activation(prob[:, n % 2, z], scores[z][:, 0:K], ACT.Exp, scale=-1.0,
                                     bias=low_score[:, n % 2, z:z + 1], accum_out=sums[:, n % 2, z:z + 1])\
                    .then_inc(exp_ready, 1)

            def high(n, i):
                qs = slice((n % 4) * P, (n % 4 + 1) * P)
                j, e = 4 * i, min(4 * i + 4, KB)
                act.wait_ge(turned, CHUNKS * n + i + 1)
                nc.scalar.activation(aT_hi[:, j:e, qs],
                                     chunk_bank(CHUNKS * n + i)[:, 0:(e - j) * P]
                                     .rearrange("p (j q) -> p j q", q=P), ACT.Copy).then_inc(hi_ready, 1)

            def out(m):
                act.wait_ge(o_ready, m + 1)
                if m >= 2:
                    act.wait_ge(o_stored[m % 2], 16 * (m // 2))
                nc.scalar.activation(o_sb[:, m % 2], turn_bank[m % 2][:], ACT.Copy)\
                    .then_inc(o_copied, 1)

            exp(0, 0)
            exp(0, 1)
            for n in range(N):
                if n + 1 < N:
                    exp(n + 1, 0)
                high(n, 0)
                if n + 1 < N:
                    exp(n + 1, 1)
                high(n, 1)
                if n % 4 == 0 and n:
                    out(n // 4 - 1)
                high(n, 2)
            out(N // 4 - 1)

        @block.gpsimd
        def _(pool):
            for n in range(N + 1):
                if n < N:
                    i = n % 2
                    pool.wait_ge(ratio_ready, n + 1)
                    p0, p1 = prob[:, i, 0, SHARE:], prob[:, i, 1, SHARE:]
                    nc.gpsimd.tensor_tensor(p1, p1, ratio[:, i].to_broadcast([P, K - SHARE]), ALU.mult)\
                        .then_inc(rest_scaled, 1)
                    pool.wait_ge(rest_scaled, n + 1)
                    nc.gpsimd.tensor_tensor(p0, p0, p1, ALU.add).then_inc(rest_ready, 1)
                if n % 4 == 3 and n > 4 or n == N:
                    m = n // 4 - 1
                    h, half = divmod(m, 2)
                    pool.wait_ge(o_copied, m + 1)
                    pool.dma_start(d["do"][h, :, half * NCOL:(half + 1) * NCOL], o_sb[:, m % 2])\
                        .then_inc(o_stored[m % 2], 16)
            for i in range(2):
                pool.wait_ge(o_stored[i], 16 * (N // 8))

        @block.vector
        def _(dve):
            dve.wait_ge(lam_loaded, 32)
            nc.vector.tensor_tensor(lam_prod[:], lam_in[:, 0], lam_in[:, 1], ALU.mult).then_inc(lam_step, 1)
            dve.wait_ge(lam_step, 1)
            nc.vector.tensor_reduce(out=lam_sum[:], in_=lam_prod[:], op=ALU.add, axis=AX.X).then_inc(lam_summed, 1)
            dve.wait_ge(lam_exped, 1)
            nc.vector.tensor_tensor(lam[:], lam_exp[:, 1:2], lam_exp[:, 0:1], ALU.subtract).then_inc(lam_step, 1)
            dve.wait_ge(lam_step, 2)
            nc.vector.tensor_scalar(lam[:], lam[:], -LAMBDA_INIT, None, ALU.add).then_inc(lam_step, 1)
            dve.wait_ge(lam_step, 3)

            def row_min(n, z):
                dve.wait_ge(scored, 2 * n + z + 1)
                nc.vector.tensor_reduce(out=low_score[:, n % 2, z:z + 1], in_=scores[z][:, 0:K], op=ALU.min,
                                        axis=AX.X).then_inc(low_score_ready, 1)

            def combine(n):
                i = n % 2
                dve.wait_ge(exp_ready, 2 * n + 2)
                nc.vector.reciprocal(inv[:, i], sums[:, i]).then_inc(inv_ready, 1)
                dve.wait_ge(inv_ready, n + 1)
                nc.vector.scalar_tensor_tensor(out=ratio[:, i], in0=sums[:, i, 0:1], scalar=lam[:],
                                               in1=inv[:, i, 1:2], op0=ALU.mult, op1=ALU.mult)\
                    .then_inc(ratio_ready, 1)
                nc.vector.tensor_scalar(diag[:, i], c.ident[:], inv[:, i, 0:1], None, ALU.mult)\
                    .then_inc(diag_ready, 1)
                dve.wait_ge(ratio_ready, n + 1)
                nc.vector.scalar_tensor_tensor(out=prob[:, i, 0, :SHARE], in0=prob[:, i, 1, :SHARE], scalar=ratio[:, i],
                                               in1=prob[:, i, 0, :SHARE], op0=ALU.mult, op1=ALU.add)\
                    .then_inc(prob_ready, 1)

            def low(n, i):
                qs = slice((n % 4) * P, (n % 4 + 1) * P)
                j, e = 4 * i, min(4 * i + 4, KB)
                dve.wait_ge(hi_ready, CHUNKS * n + i + 1)
                nc.vector.tensor_tensor(aT_lo[:, j:e, qs],
                                        chunk_bank(CHUNKS * n + i)[:, 0:(e - j) * P]
                                        .rearrange("p (j q) -> p j q", q=P),
                                        aT_hi[:, j:e, qs].bitcast(F32), ALU.subtract).then_inc(lo_ready, 1)

            row_min(0, 0)
            row_min(0, 1)
            combine(0)
            row_min(1, 0)
            row_min(1, 1)
            for n in range(N):
                low(n, 0)
                if n + 2 < N:
                    row_min(n + 2, 0)
                low(n, 1)
                if n + 1 < N:
                    combine(n + 1)
                low(n, 2)
                if n + 2 < N:
                    row_min(n + 2, 1)


def head_norm_project(nc, chip, a, d):
    c = chip
    SUB_EPS = 1e-5
    QT2 = TT // HALVES
    weights = a["da_w_out_2"][0]
    groups = [[weights[k * P:(k + 1) * P, n * NCOL:(n + 1) * NCOL] for k in range(KT)] for n in range(HALVES)]
    outs = [(half, g, half * QT2 + t) for half in range(HALVES) for g in range(HALVES) for t in range(QT2)]
    PER = len(outs) // HALVES
    EARLY = 3
    BANKS = 5
    ZS = 4
    with ExitStack() as ctx:
        sb = lambda n, s, dt=F32: c.sb("hp_" + n, s, dt, ctx=ctx)
        sem = lambda n: c.sem("hp_" + n, ctx)
        w = Weights(c, "hp", ctx, groups)
        o, z, sq = sb("o", [P, DH, NCOL]), sb("z", [P, ZS, NCOL]), sb("sq", [P, 2, NCOL])
        rs = sb("rs", [DH, NCOL])
        eps = sb("eps", [DH, 1])
        gain = sb("gain", [P, 1])
        band = sb("band", [P, 2 * DH])
        rows = sb("rows", [DH, DH, P])
        gate = sb("gate", [P, D])
        sum_bank = c.banks("hp_sum", ctx, 1)[0]
        wide_bank = c.banks("hp_wide", ctx, 2)
        banks = c.banks("hp_ps", ctx, BANKS)
        gain_loaded, gain_ready, gate_loaded, band_ready, eps_ready, rows_ready = (
            sem(x) for x in ("gain_loaded", "gain_ready", "gate_loaded", "band_ready", "eps_ready", "rows_ready"))
        o_loaded = [sem(f"o_loaded{h}") for h in range(DH)]
        z_loaded = [sem(f"z_loaded{i}") for i in range(ZS)]
        squared, summed, logged, rstd_ready, wide_ready, scaled, y_ready, hi_ready, lo_ready = (
            sem(x) for x in ("squared", "summed", "logged", "rstd_ready", "wide_ready", "scaled", "y_ready",
                             "hi_ready", "lo_ready"))
        result_ready, gated, added, norm_summed = (
            sem(x) for x in ("result_ready", "gated", "added", "norm_summed"))
        block = ctx.enter_context(nc.Block())

        @block.sync
        def _(sp):
            def load_o(half, h):
                if half:
                    sp.wait_ge(lo_ready, h + 1)
                sp.dma_start(o[:, h], d["do"][h, :, half * NCOL:(half + 1) * NCOL]).then_inc(o_loaded[h], 16)

            def load_z(n):
                half, h = divmod(n, DH)
                if n >= ZS:
                    sp.wait_ge(y_ready, n - ZS + 1)
                sp.dma_start(z[:, n % ZS], d["dz"][h, :, half * NCOL:(half + 1) * NCOL]).then_inc(z_loaded[n % ZS], 16)

            sp.dma_start(gain[:], a["da_subln_gain_2"][0].rearrange("(p a) -> p a", a=1)).then_inc(gain_loaded, 16)
            for h in range(DH):
                load_o(0, h)
            for n in range(SLOTS):
                w.load_chunk(sp, n)
            for n in range(ZS):
                load_z(n)
            for n in range(SLOTS, 2 * SLOTS):
                w.load_chunk(sp, n)
            sp.dma_start(gate[:], d["mod_row"][0:1, 2 * D:3 * D].to_broadcast([P, D])).then_inc(gate_loaded, 16)
            for h in range(DH):
                load_z(h + ZS)
                w.load_chunk(sp, 2 * SLOTS + h)
                load_o(1, h)
            for n in range(DH + ZS, 2 * DH):
                load_z(n)

        @block.gpsimd
        def _(pool):
            nc.gpsimd.memset(band[:], 0.0).then_inc(band_ready, 1)
            pool.wait_ge(band_ready, 1)
            nc.gpsimd.memset(band[:, DH:DH + 1], 1.0).then_inc(band_ready, 1)
            nc.gpsimd.memset(eps[:], SUB_EPS).then_inc(eps_ready, 1)

            def by_z(n):
                pool.wait_ge(scaled, n + 1)
                pool.wait_ge(z_loaded[n % ZS], 16 * (n // ZS + 1))
                nc.gpsimd.tensor_tensor(o[:, n % DH], o[:, n % DH], z[:, n % ZS], ALU.mult).then_inc(y_ready, 1)

            for n in range(SLOTS):
                w.split_lo_chunk(pool, n)
            for h in range(DH):
                by_z(h)
                w.split_lo_chunk(pool, SLOTS + h)
            for n in range(SLOTS + DH, len(w.chunks)):
                w.split_lo_chunk(pool, n)
            for h in range(DH):
                by_z(DH + h)

        @block.scalar
        def _(act):
            def square(n):
                half, h = divmod(n, DH)
                act.wait_ge(o_loaded[h], 16 * (half + 1))
                if n >= 2:
                    act.wait_ge(summed, n - 1)
                nc.scalar.activation(sq[:, n % 2], o[:, h], ACT.Square).then_inc(squared, 1)

            def high(n):
                half, h = divmod(n, DH)
                act.wait_ge(y_ready, n + 1)
                nc.scalar.activation(c.Xhi[:, h, half * NCOL:(half + 1) * NCOL], o[:, h], ACT.Copy)\
                    .then_inc(hi_ready, 1)

            def rstd(half):
                act.wait_ge(summed, DH * (half + 1))
                if half:
                    act.wait_ge(wide_ready, DH)
                nc.scalar.activation(rs[:], sum_bank[0:DH, :], ACT.Ln, scale=1.0 / P, bias=eps[:])\
                    .then_inc(logged, 1)
                act.wait_ge(logged, half + 1)
                nc.scalar.activation(rs[:], rs[:], ACT.Exp, scale=-0.5).then_inc(rstd_ready, 1)

            for h in range(DH):
                square(h)
            act.wait_ge(eps_ready, 1)
            rstd(0)
            for n in range(SLOTS):
                w.split_hi(act, n)
            for h in range(DH):
                high(h)
                w.split_hi(act, SLOTS + h)
            for n in range(SLOTS + DH, len(w.chunks)):
                w.split_hi(act, n)
            for h in range(DH):
                square(DH + h)
            rstd(1)
            for h in range(DH):
                high(DH + h)
            for t in range(TT):
                half, i = divmod(t, QT2)
                act.wait_ge(added, half * PER + QT2 + i + 1)
                if t:
                    act.wait_ge(norm_summed, t)
                nc.scalar.activation(sq[:].rearrange("p a n -> p (a n)"), c.H[:, t, :], ACT.Square,
                                     accum_out=c.sums[:, t:t + 1]).then_inc(norm_summed, 1)

        @block.tensor
        def _(pe):
            def sums(half):
                if half:
                    pe.wait_ge(logged, 1)
                for h in range(DH):
                    pe.wait_ge(squared, half * DH + h + 1)
                    nc.tensor.matmul(sum_bank[0:DH, :], band[:, DH - h:2 * DH - h], sq[:, h % 2],
                                     start=(h == 0), stop=(h == DH - 1)).then_inc(summed, 1)

            def wide(n):
                half, h = divmod(n, DH)
                pe.wait_ge(rstd_ready, half + 1)
                if n >= 2:
                    pe.wait_ge(scaled, n - 1)
                nc.tensor.matmul(wide_bank[n % 2][:], rows[:, h, :], rs[:], start=True, stop=True)\
                    .then_inc(wide_ready, 1)

            def result(n):
                half, g, t = outs[n]
                if n % PER == 0:
                    pe.wait_ge(lo_ready, DH * (half + 1))
                if n >= BANKS:
                    pe.wait_ge(added, n - BANKS + 1)
                tok = slice(t * P, (t + 1) * P)
                product(nc, banks[n % BANKS][:],
                        [((c.Xhi[:, k, tok], c.Xlo[:, k, tok]), (w.hi[:, g, k], w.lo[:, g, k])) for k in range(KT)],
                        NCOL, result_ready,
                        (lambda k: pe.wait_ge(w.lo_ready, w.first[g] + k + 1)) if n < PER and t == 0 else None)

            pe.wait_ge(band_ready, 2)
            sums(0)
            pe.wait_ge(rows_ready, 1)
            for h in range(DH):
                wide(h)
            result(0)
            result(1)
            sums(1)
            result(2)
            for h in range(DH):
                wide(DH + h)
                if h % 2:
                    result(EARLY + h // 2)
            for n in range(EARLY + DH // 2, len(outs)):
                result(n)

        @block.vector
        def _(dve):
            dve.wait_ge(gain_loaded, 16)
            nc.vector.tensor_scalar(gain[:], gain[:], 1.0 - LAMBDA_INIT, None, ALU.mult).then_inc(gain_ready, 1)
            nc.vector.tensor_copy(rows[:], c.ident[0:DH, 0:DH].unsqueeze(2).to_broadcast([DH, DH, P]))\
                .then_inc(rows_ready, 1)
            dve.wait_ge(gain_ready, 1)

            def scale(n):
                dve.wait_ge(wide_ready, n + 1)
                nc.vector.scalar_tensor_tensor(out=o[:, n % DH], in0=o[:, n % DH], scalar=gain[:],
                                               in1=wide_bank[n % 2][:], op0=ALU.mult, op1=ALU.mult)\
                    .then_inc(scaled, 1)

            def low(n):
                half, h = divmod(n, DH)
                cols = slice(half * NCOL, (half + 1) * NCOL)
                dve.wait_ge(hi_ready, n + 1)
                nc.vector.tensor_tensor(c.Xlo[:, h, cols], o[:, h], c.Xhi[:, h, cols].bitcast(F32), ALU.subtract)\
                    .then_inc(lo_ready, 1)

            def add(n):
                half, g, t = outs[n]
                cols = slice(g * NCOL, (g + 1) * NCOL)
                dve.wait_ge(result_ready, n + 1)
                bank = banks[n % BANKS][:]
                nc.vector.tensor_tensor(bank, bank, gate[:, cols], ALU.mult).then_inc(gated, 1)
                dve.wait_ge(gated, n + 1)
                nc.vector.tensor_tensor(c.H[:, t, cols], c.H[:, t, cols], bank, ALU.add).then_inc(added, 1)

            for h in range(DH):
                scale(h)
                if h:
                    low(h - 1)
            low(DH - 1)
            dve.wait_ge(gate_loaded, 16)
            add(0)
            add(1)
            add(2)
            for h in range(DH):
                scale(DH + h)
                if h:
                    low(DH + h - 1)
                if h % 2:
                    add(EARLY + h // 2)
            low(2 * DH - 1)
            for n in range(EARLY + DH // 2, len(outs)):
                add(n)


def final_norm(nc, chip, a, out):
    c = chip
    with ExitStack() as ctx:
        sb = lambda n, s, dt=F32: c.sb("fn_" + n, s, dt, ctx=ctx)
        sem = lambda n: c.sem("fn_" + n, ctx)
        gain, ms, rs = sb("gain", [P, D]), sb("ms", [P, TT]), sb("rs", [P, TT])
        loaded, ms_ready, rs_ready, y_ready = (sem(x) for x in ("loaded", "ms_ready", "rs_ready", "y_ready"))
        block = ctx.enter_context(nc.Block())

        @block.gpsimd
        def _(pool):
            for h in range(2):
                cols = slice(4 * h, 4 * h + 4)
                nc.gpsimd.tensor_scalar(ms[:, cols], c.sums[:, cols], 1.0 / D, EPS, ALU.mult, ALU.add).then_inc(ms_ready, 1)
                pool.wait_ge(ms_ready, h + 1)
                nc.gpsimd.tensor_tensor(rs[:, cols], ms[:, cols], c.minus_half[:, 0:4], ALU.pow).then_inc(rs_ready, 1)

        @block.vector
        def _(dve):
            dve.wait_ge(loaded, 16)
            for t in range(TT):
                dve.wait_ge(rs_ready, t // 4 + 1)
                nc.vector.scalar_tensor_tensor(out=c.H[:, t, :], in0=c.H[:, t, :], scalar=rs[:, t:t + 1], in1=gain[:],
                                               op0=ALU.mult, op1=ALU.mult).then_inc(y_ready, 1)

        @block.sync
        def _(sp):
            sp.dma_start(gain[:], a["final_gain_2"].rearrange("(a n) -> a n", a=1).to_broadcast([P, D]))\
                .then_inc(loaded, 16)
            for t in range(TT):
                sp.wait_ge(y_ready, t + 1)
                sp.dma_start(out[0, t * P:(t + 1) * P, :], c.H[:, t, :]).then_inc(c.out_stored, 16)
            sp.wait_ge(c.out_stored, 16 * TT)


def program(nc, a, out):
    with ExitStack() as ctx:
        ctx.enter_context(nc.allow_non_contiguous_dma(reason="gains and transposed results"))
        c = Chip(nc, ctx)

        def scratch(name, shape):
            return nc.dram_tensor(name, shape, F32, kind="Internal").ap()

        d = {
            "zc": scratch("zc", [TT, P, 432]), "gqk": scratch("gqk", [4, P, S]),
            "gv": scratch("gv", [TT, P, NCOL]), "gr": scratch("gr", [TT, P, NCOL]),
            "mqk_hi": scratch("mqk_hi", [2, MH, MQK, S]), "mqk_lo": scratch("mqk_lo", [2, MH, MQK, S]),
            "mv_hi": scratch("mv_hi", [MH, TT, P, MV]), "mv_lo": scratch("mv_lo", [MH, TT, P, MV]),
            "dq": scratch("dq", [DH, 2, P, S]),
            "dk_hi": scratch("dk_hi", [DH, 2, DD, S + CTX]), "dk_lo": scratch("dk_lo", [DH, 2, DD, S + CTX]),
            "dv_hi": scratch("dv_hi", [DH, P, TT + CT, P]), "dv_lo": scratch("dv_lo", [DH, P, TT + CT, P]),
            "dz": scratch("dz", [DH, P, S]), "do": scratch("do", [DH, P, S]),
            "mod_row": scratch("mod_row", [2, 3 * D]),
        }
        constants(nc, c, a)
        with ExitStack() as x_ctx:
            c.hold_x("x1", x_ctx)
            norm_transpose(nc, c, "n1", half_parts(c, c.gains[:, 0], load=a["x"][0]))

            w_in = a["w_in"][0]
            rows = [slice(k * P, (k + 1) * P) for k in range(KT)]
            g_low = GH * GDK * 2 + GH * GDV
            g_r = g_low + GR
            c_q = g_r + GH * GDV
            one = lambda o: 1.0
            tok_place = lambda name, width: (lambda o: [(d[name][o], slice(0, width))])
            groups = [
                ([[w_in[r, g_low:g_r], w_in[r, c_q:c_q + MQR + MKVR + MROPE]] for r in rows], False,
                 tok_place("zc", 432), ACT.Copy, one),
                ([w_in[r, 0:NCOL] for r in rows], True,
                 lambda o: [(d["gqk"][o // HALVES, :, (o % HALVES) * NCOL:(o % HALVES + 1) * NCOL], slice(0, NCOL))],
                 ACT.Copy, lambda o: GDK ** -0.5 if o < TT // 2 else 1.0),
                ([w_in[r, NCOL:2 * NCOL] for r in rows], False, tok_place("gv", NCOL), ACT.Copy, one),
                ([w_in[r, g_r:c_q] for r in rows], False, tok_place("gr", NCOL), ACT.Silu, one),
            ]
            project_to_dram(nc, c, "p1", groups)
        latent_prepare(nc, c, a, d)
        with ExitStack() as x_ctx:
            c.hold_x("xa", x_ctx, halves=(0,))
            gated_linear_attention(nc, c, a, d)
            c.hold_x("xb", x_ctx, halves=(1,))
            c.renew_semaphores()
            latent_attention(nc, c, a, d)
            project_into_residual(nc, c, "wo", a["w_out"][0])
            norm_transpose(nc, c, "n2", half_parts(c, c.gains[:, 1]))
            c.renew_semaphores()
            mlp(nc, c, a)
            norm_transpose(nc, c, "n3", half_parts(c, c.gains[:, 2]))
            ple(nc, c, a)
            c.renew_semaphores()
            with ExitStack() as inner:
                ctx_hi, ctx_lo = (c.sb(f"ctx_{x}", [P, KT, CTX], F32R, ctx=inner) for x in ("hi", "lo"))
                with ExitStack() as load_ctx:
                    raw = c.sb("ctx_raw", [P, CT, D], ctx=load_ctx)
                    context = [(raw[:, t, :], a["ctx_2"][0, t * P:(t + 1) * P, :]) for t in range(CT)]
                    norm_transpose(nc, c, "n4", half_parts(c, c.mod_gain[:, 0], c.mod_bias[:, 0]) +
                                   [(context, c.mod_gain[:, 1], c.mod_bias[:, 1], (ctx_hi, ctx_lo), 0)])
                differential_project(nc, c, a, d, ctx_hi, ctx_lo)
        c.renew_semaphores()
        differential_attention(nc, c, a, d)
        with ExitStack() as x_ctx:
            c.hold_x("x2", x_ctx)
            head_norm_project(nc, c, a, d)
            final_norm(nc, c, a, out)


_INS = ["x", "p", "positions", "attn_norm", "w_in", "gla_gate_w2", "gla_gate_b", "gla_out_norm", "mla_q_norm",
        "mla_w_uq", "mla_kv_norm", "mla_w_ukv", "qk_norm_q", "qk_norm_k", "w_out", "mlp_norm", "w_mlp_up",
        "w_mlp_down", "ple_norm", "w_ple_gate", "b_ple_gate", "w_ple_proj", "c_2", "ctx_2", "c_ctx_2",
        "norm_gain_2", "ada_w_2", "ada_b_2", "final_gain_2", "da_w_in_2", "da_lam_q_2", "da_lam_k_2",
        "da_subln_gain_2", "da_w_out_2"]


def shape_constants():
    import numpy as np
    f = np.float32
    inv = (f(10000.0) ** (-np.arange(0, MROPE, 2, dtype=f) / f(MROPE))).astype(f)
    n = np.arange(S)
    axis = (f(10000.0) ** (-np.arange(0, 32, 2, dtype=f) / f(32))).astype(f)
    ang = np.concatenate([(n // 64).astype(f)[:, None] * axis, (n % 64).astype(f)[:, None] * axis], axis=1)
    s, t = np.arange(P)[:, None], np.arange(P)[None, :]
    masks = [(s // (2 * h) == t // (2 * h)) & (s % (2 * h) < h) & (t % (2 * h) >= h) for h in (64, 32, 16)]
    masks.append((s // 16 == t // 16) & (s <= t))
    return {"inv_freq": inv[None], "da_cos": np.cos(ang).astype(f), "da_sin": np.sin(ang).astype(f),
            "gla_masks": np.stack(masks, axis=1).astype(f)}


def kernel(**inputs):
    import numpy as np
    import concourse.bacc as bacc
    from concourse.bass_utils import run_bass_kernel_spmd

    nc = bacc.Bacc("TRN2", target_bir_lowering=False, num_devices=1)
    arrays, args = {}, {}
    for name, array in [(n, inputs[n]) for n in _INS] + list(shape_constants().items()):
        array = np.ascontiguousarray(array)
        arrays[f"in_{name}"] = array
        args[name] = nc.dram_tensor(f"in_{name}", array.shape, mybir.dt.from_np(array.dtype),
                                    kind="ExternalInput").ap()
    out = nc.dram_tensor("out", (1, S, D), F32, kind="ExternalOutput").ap()
    program(nc, args, out)
    result = run_bass_kernel_spmd(nc, [arrays], core_ids=[0])
    return result.results[0]["out"]
```
